# Optimizing a Trainium2 kernel written in Bass

```python
import jax, jax.numpy as jnp
from jax import lax
import numpy as np

D_MODEL = 1024
BATCH = 1
SEQ = 1024
DEPTH = 1

H_R = 8
N_R = 64
C_R = H_R * N_R
DECAY_LORA = 64
AAA_LORA = 64
GATE_LORA = 128
RW_SIZES = (C_R, C_R, C_R, DECAY_LORA, AAA_LORA, GATE_LORA)
RW_COLS = sum(RW_SIZES)
LNX_EPS = 64e-5

H_M = 4
DK_M = 64
DV_M = 128
C_MQK = H_M * DK_M
C_MV = H_M * DV_M
ML_SIZES = (C_MQK, C_MQK, C_MV, C_MV, H_M, H_M)
ML_COLS = sum(ML_SIZES)
QK_CONV = 4
CHUNK = 64
GATE_CAP = 15.0

N_IN = RW_COLS + ML_COLS
D_MIX = C_R + C_MV

D_FF = 2816
FFN_CONV = 3
NORM_EPS = 1e-6


def _split(t, sizes):
    idx = np.cumsum(sizes)[:-1].tolist()
    return jnp.split(t, idx, axis=-1)

def rmsnorm(x, g):
    xf = x.astype(jnp.float32)
    y = xf * lax.rsqrt(jnp.mean(xf * xf, axis=-1, keepdims=True) + NORM_EPS)
    return y.astype(x.dtype) * g

def head_layernorm(y, eps):
    yf = y.astype(jnp.float32)
    mu = jnp.mean(yf, axis=-1, keepdims=True)
    var = jnp.mean(jnp.square(yf - mu), axis=-1, keepdims=True)
    return (yf - mu) * lax.rsqrt(var + eps)

def head_rmsnorm(y):
    yf = y.astype(jnp.float32)
    return yf * lax.rsqrt(jnp.mean(yf * yf, axis=-1, keepdims=True) + NORM_EPS)

def token_shift(t):
    return jnp.pad(t, ((0, 0), (1, 0), (0, 0)))[:, :-1]

def causal_dwconv(t, w, b):
    K = w.shape[0]
    T = t.shape[1]
    tp = jnp.pad(t, ((0, 0), (K - 1, 0), (0, 0)))
    out = b + tp[:, 0:T] * w[0]
    for j in range(1, K):
        out = out + tp[:, j:j + T] * w[j]
    return out

def softcap(t):
    return GATE_CAP * jnp.tanh(t / GATE_CAP)

def rwkv7_scan(r, w, k, v, a, b):
    Bn, T, H, N = r.shape

    def step(S, inp):
        r_t, w_t, k_t, v_t, a_t, b_t = inp
        sa = jnp.einsum('bhij,bhj->bhi', S, a_t)
        S = S * w_t[:, :, None, :] + sa[..., None] * b_t[:, :, None, :] + v_t[..., :, None] * k_t[..., None, :]
        y = jnp.einsum('bhij,bhj->bhi', S, r_t)
        return S, y

    S0 = jnp.zeros((Bn, H, N, N), jnp.float32)
    xs = tuple(jnp.moveaxis(t, 1, 0) for t in (r, w, k, v, a, b))
    _, y = lax.scan(step, S0, xs)
    return jnp.moveaxis(y, 0, 1)

def rwkv7_group(p, mu, w0, w_up_decay, a0, w_up_a, w_up_g, k_k, k_a, r_k, lnx_w, lnx_b):
    Bn, T, _ = p.shape
    p = p + (token_shift(p) - p) * mu
    r, k, v, w_lo, a_lo, g_lo = _split(p, RW_SIZES)
    log_w = -jax.nn.softplus(-(w0 + jnp.tanh(w_lo) @ w_up_decay)) - 0.5
    decay = jnp.exp(-jnp.exp(log_w.astype(jnp.float32)))
    a = jax.nn.sigmoid(a0 + a_lo @ w_up_a)
    g = jax.nn.sigmoid(g_lo) @ w_up_g
    heads = lambda t: t.reshape(Bn, T, H_R, N_R)
    kk = heads(k * k_k).astype(jnp.float32)
    kk = kk / jnp.maximum(jnp.sqrt(jnp.sum(kk * kk, axis=-1, keepdims=True)), 1e-12)
    k = k * (1 + (a - 1) * k_a)
    r_h, k_h, v_h, a_h = heads(r), heads(k), heads(v), heads(a)
    y = rwkv7_scan(r_h, heads(decay), k_h, v_h, -kk, kk * a_h)
    y = head_layernorm(y, LNX_EPS).reshape(Bn, T, C_R) * lnx_w + lnx_b
    bonus = jnp.sum(r_h * k_h * r_k, axis=-1, keepdims=True) * v_h
    return ((y + bonus.reshape(Bn, T, C_R)) * g).astype(p.dtype)

def mlstm_chunkwise(q, k, v, ig, logf):
    Bn, T, H, _ = q.shape
    nc = T // CHUNK

    def to_chunks(t):
        t = t.reshape(Bn, nc, CHUNK, H, *t.shape[3:])
        return jnp.moveaxis(t, (1, 3), (0, 2))

    causal = jnp.tril(jnp.ones((CHUNK, CHUNK), dtype=bool))

    def step(carry, inp):
        C, n, m = carry
        qc, kc, vc, ic, fc = inp
        b = jnp.cumsum(fc, axis=-1)
        log_d = jnp.where(causal, b[..., :, None] - b[..., None, :] + ic[..., None, :], -jnp.inf)
        m_inter = b + m[..., None]
        m_t = jnp.maximum(jnp.max(log_d, axis=-1), m_inter)
        d = jnp.exp(log_d - m_t[..., None])
        s = jnp.einsum('bhtd,bhsd->bhts', qc, kc) * d
        sc = jnp.exp(m_inter - m_t)
        num = jnp.einsum('bhts,bhsv->bhtv', s, vc) + sc[..., None] * jnp.einsum('bhtd,bhdv->bhtv', qc, C)
        den = jnp.sum(s, axis=-1) + sc * jnp.einsum('bhtd,bhd->bht', qc, n)
        h = num / jnp.maximum(jnp.abs(den), jnp.exp(-m_t))[..., None]
        b_last = b[..., -1]
        a_w = b_last[..., None] - b + ic
        m_new = jnp.maximum(b_last + m, jnp.max(a_w, axis=-1))
        w_s = jnp.exp(a_w - m_new[..., None])
        dec = jnp.exp(b_last + m - m_new)
        C = dec[..., None, None] * C + jnp.einsum('bhs,bhsd,bhsv->bhdv', w_s, kc, vc)
        n = dec[..., None] * n + jnp.einsum('bhs,bhsd->bhd', w_s, kc)
        return (C, n, m_new), h

    carry0 = (jnp.zeros((Bn, H, q.shape[-1], v.shape[-1]), jnp.float32),
              jnp.zeros((Bn, H, q.shape[-1]), jnp.float32),
              jnp.zeros((Bn, H), jnp.float32))
    xs = tuple(to_chunks(t) for t in (q, k, v, ig, logf))
    _, h = lax.scan(step, carry0, xs)
    h = jnp.moveaxis(h, (0, 2), (1, 3))
    return h.reshape(Bn, T, H, v.shape[-1])

def mlstm_group(p, qk_conv_w, qk_conv_b, i_bias, f_bias, mh_norm_g):
    Bn, T, _ = p.shape
    q, k, v, o, ig, fg = _split(p, ML_SIZES)
    qk = jax.nn.silu(causal_dwconv(jnp.concatenate([q, k], axis=-1), qk_conv_w, qk_conv_b))
    q, k = qk[..., :C_MQK], qk[..., C_MQK:]
    ig = softcap((ig + i_bias).astype(jnp.float32))
    logf = jax.nn.log_sigmoid(softcap((fg + f_bias).astype(jnp.float32)))
    h = mlstm_chunkwise(q.reshape(Bn, T, H_M, DK_M) * (DK_M ** -0.5),
                        k.reshape(Bn, T, H_M, DK_M),
                        v.reshape(Bn, T, H_M, DV_M), ig, logf)
    h = head_rmsnorm(h).reshape(Bn, T, C_MV) * mh_norm_g * jax.nn.sigmoid(o)
    return h.astype(p.dtype)

def first_inputs(seed: int = 0) -> dict:
    key = jax.random.key(seed)
    ks = jax.random.split(key, 26)
    f32 = jnp.float32
    nrm = lambda k, s, sc: jax.random.normal(k, s, f32) * sc
    gain = lambda k, s: 1.0 + 0.02 * jax.random.normal(k, s, f32)
    L = DEPTH
    return {
        "x": jax.random.normal(ks[0], (BATCH, SEQ, D_MODEL), f32),
        "norm1_g": gain(ks[1], (L, D_MODEL)),
        "w_in": nrm(ks[2], (L, D_MODEL, N_IN), D_MODEL ** -0.5),
        "rw_mu": jax.random.uniform(ks[3], (L, RW_COLS), f32),
        "w0": jax.random.uniform(ks[4], (L, C_R), f32, -6.0, 0.0),
        "w_up_decay": nrm(ks[5], (L, DECAY_LORA, C_R), 0.1 * DECAY_LORA ** -0.5),
        "a0": nrm(ks[6], (L, C_R), 0.1),
        "w_up_a": nrm(ks[7], (L, AAA_LORA, C_R), 0.1 * AAA_LORA ** -0.5),
        "w_up_g": nrm(ks[8], (L, GATE_LORA, C_R), GATE_LORA ** -0.5),
        "k_k": 0.85 + 0.02 * jax.random.normal(ks[9], (L, C_R), f32),
        "k_a": gain(ks[10], (L, C_R)),
        "r_k": nrm(ks[11], (L, H_R, N_R), 0.1),
        "lnx_w": gain(ks[12], (L, C_R)),
        "lnx_b": nrm(ks[13], (L, C_R), 0.02),
        "qk_conv_w": nrm(ks[14], (L, QK_CONV, 2 * C_MQK), QK_CONV ** -0.5),
        "qk_conv_b": nrm(ks[15], (L, 2 * C_MQK), 0.02),
        "i_bias": nrm(ks[16], (L, H_M), 0.1),
        "f_bias": jax.random.uniform(ks[17], (L, H_M), f32, 3.0, 6.0),
        "mh_norm_g": gain(ks[18], (L, C_MV)),
        "w_out": nrm(ks[19], (L, D_MIX, D_MODEL), D_MIX ** -0.5),
        "norm2_g": gain(ks[20], (L, D_MODEL)),
        "w_ffn_up": nrm(ks[21], (L, D_MODEL, 2 * D_FF), D_MODEL ** -0.5),
        "ffn_conv_w": nrm(ks[22], (L, FFN_CONV, D_FF), FFN_CONV ** -0.5),
        "ffn_conv_b": nrm(ks[23], (L, D_FF), 0.02),
        "w_ffn_down": nrm(ks[24], (L, D_FF, D_MODEL), D_FF ** -0.5),
        "norm_f_g": gain(ks[25], (D_MODEL,)),
    }

def first_block(x, norm1_g, w_in, rw_mu, w0, w_up_decay, a0, w_up_a, w_up_g, k_k, k_a, r_k,
              lnx_w, lnx_b, qk_conv_w, qk_conv_b, i_bias, f_bias, mh_norm_g, w_out,
              norm2_g, w_ffn_up, ffn_conv_w, ffn_conv_b, w_ffn_down, norm_f_g):
    for l in range(DEPTH):
        h = rmsnorm(x, norm1_g[l])
        proj = h @ w_in[l]
        p_rw, p_ml = proj[..., :RW_COLS], proj[..., RW_COLS:]
        y_rw = rwkv7_group(p_rw, rw_mu[l], w0[l], w_up_decay[l], a0[l], w_up_a[l], w_up_g[l],
                           k_k[l], k_a[l], r_k[l], lnx_w[l], lnx_b[l])
        y_ml = mlstm_group(p_ml, qk_conv_w[l], qk_conv_b[l], i_bias[l], f_bias[l],
                           mh_norm_g[l])
        x = x + jnp.concatenate([y_rw, y_ml], axis=-1) @ w_out[l]
        h = rmsnorm(x, norm2_g[l])
        u = h @ w_ffn_up[l]
        a, b = u[..., :D_FF], u[..., D_FF:]
        a = causal_dwconv(a, ffn_conv_w[l], ffn_conv_b[l])
        x = x + (jax.nn.silu(a) * b) @ w_ffn_down[l]
    return rmsnorm(x, norm_f_g)


_first_inputs = first_inputs


def first_inputs(seed=0):
    import zlib

    import numpy as np

    out = dict(_first_inputs(seed))
    spreads = {}
    factors = {'w_up_decay': 8.0,
     'a0': 3.27,
     'w_up_a': 3.66,
     'k_k': 7.825,
     'k_a': 6.811,
     'lnx_w': 7.469,
     'lnx_b': 7.435,
     'qk_conv_b': 6.182,
     'i_bias': 8.0,
     'mh_norm_g': 7.774,
     'norm2_g': 4.338,
     'ffn_conv_b': 6.207,
     'norm_f_g': 2.804}
    for name, (base, spread) in spreads.items():
        noise = np.random.default_rng([zlib.crc32(name.encode()), seed]).standard_normal(out[name].shape)
        drawn = base * np.exp(spread * noise) if base else spread * noise
        out[name] = __import__('jax').numpy.asarray(drawn.astype(out[name].dtype))
    for name, factor in factors.items():
        out[name] = (out[name] * factor).astype(out[name].dtype)
    return out


_narrow_inputs = first_inputs


def first_inputs(seed=0):

    out = dict(_narrow_inputs(seed))
    wider = {'k_k': 3.76,
     'lnx_w': 3.37,
     'lnx_b': 3.41,
     'i_bias': 12.0,
     'mh_norm_g': 3.38,
     'norm_f_g': 3.15}
    for name, times in wider.items():
        mean = out[name].mean()
        out[name] = (mean + times * (out[name] - mean)).astype(out[name].dtype)
    return out


D_RNN = 1024
RNN_BLOCKS = 8
RNN_BLOCK_W = D_RNN // RNN_BLOCKS
CONV_W = 4
LRU_C = 8.0
N_HEADS = 8
QK_NOPE = 128
QK_ROPE = 64
QK_DIM = QK_NOPE + QK_ROPE
V_DIM = 128
Q_LORA = 256
KV_LORA = 256
ROPE_THETA = 10000.0
Q_BLOCK = 128
N_GROUPS = 8
EXPERTS_PER_GROUP = 8
N_EXPERTS = N_GROUPS * EXPERTS_PER_GROUP
TOP_K = 2
D_EXPERT = 256
MOE_BLOCK = 128
EPS = 1e-6

IN_SPLITS = (D_RNN, D_RNN, Q_LORA, KV_LORA, QK_ROPE, D_MODEL, D_MODEL)
D_IN = D_RNN + D_RNN + Q_LORA + KV_LORA + QK_ROPE + D_MODEL + D_MODEL


def rmsnorm_2(x, g):
    xf = x.astype(jnp.float32)
    y = xf * lax.rsqrt(jnp.mean(xf * xf, axis=-1, keepdims=True) + EPS)
    return (y * g.astype(jnp.float32)).astype(x.dtype)

def causal_depthwise_conv(x, w, b):
    y = lax.conv_general_dilated(
        x, w[:, None, :].astype(x.dtype), window_strides=(1,),
        padding=[(CONV_W - 1, 0)], dimension_numbers=("NWC", "WIO", "NWC"),
        feature_group_count=x.shape[-1])
    return y + b.astype(x.dtype)

def rg_lru(x, wa, ba, wx, bx, lam):
    B, S, C = x.shape
    xb = x.reshape(B, S, RNN_BLOCKS, RNN_BLOCK_W)
    r = jax.nn.sigmoid(jnp.einsum("bsnk,nkj->bsnj", xb, wa).reshape(B, S, C) + ba)
    i = jax.nn.sigmoid(jnp.einsum("bsnk,nkj->bsnj", xb, wx).reshape(B, S, C) + bx)
    log_a = -LRU_C * r.astype(jnp.float32) * jax.nn.softplus(-lam.astype(jnp.float32))
    a = jnp.exp(log_a)
    mult = jnp.sqrt(-jnp.expm1(2.0 * log_a))
    b_in = x.astype(jnp.float32) * i.astype(jnp.float32) * mult

    def combine(left, right):
        a1, b1 = left
        a2, b2 = right
        return a1 * a2, a2 * b1 + b2

    _, h = lax.associative_scan(combine, (a, b_in), axis=1)
    return h.astype(x.dtype)

def apply_rope(x, cos, sin):
    half = x.shape[-1] // 2
    x1, x2 = x[..., :half], x[..., half:]
    return jnp.concatenate([x1 * cos - x2 * sin, x2 * cos + x1 * sin], axis=-1)

def mla_attention(c_q, c_kv, k_pe, positions, q_norm_g, w_uq, kv_norm_g, w_ukv,
                  qk_q_g, qk_k_g, w_mla_o):
    B, S, _ = c_q.shape
    q = (rmsnorm_2(c_q, q_norm_g) @ w_uq).reshape(B, S, N_HEADS, QK_DIM)
    kv = (rmsnorm_2(c_kv, kv_norm_g) @ w_ukv).reshape(B, S, N_HEADS, QK_NOPE + V_DIM)
    k_nope, v = kv[..., :QK_NOPE], kv[..., QK_NOPE:]
    k_pe_h = jnp.broadcast_to(k_pe[:, :, None, :], (B, S, N_HEADS, QK_ROPE))
    k = jnp.concatenate([k_nope, k_pe_h], axis=-1)
    q = rmsnorm_2(q, qk_q_g)
    k = rmsnorm_2(k, qk_k_g)
    inv_freq = ROPE_THETA ** (-jnp.arange(0, QK_ROPE, 2, dtype=jnp.float32) / QK_ROPE)
    ang = positions.astype(jnp.float32)[..., None] * inv_freq
    cos = jnp.cos(ang)[:, :, None, :].astype(q.dtype)
    sin = jnp.sin(ang)[:, :, None, :].astype(q.dtype)
    q = jnp.concatenate([q[..., :QK_NOPE], apply_rope(q[..., QK_NOPE:], cos, sin)], axis=-1)
    k = jnp.concatenate([k[..., :QK_NOPE], apply_rope(k[..., QK_NOPE:], cos, sin)], axis=-1)
    scale = QK_DIM ** -0.5
    outs = []
    for s0 in range(0, S, Q_BLOCK):
        e = s0 + Q_BLOCK
        s = jnp.einsum("bqhd,bkhd->bhqk", q[:, s0:e], k[:, :e]).astype(jnp.float32) * scale
        mask = jnp.arange(e)[None, :] <= (s0 + jnp.arange(Q_BLOCK))[:, None]
        p = jax.nn.softmax(jnp.where(mask, s, -jnp.inf), axis=-1).astype(v.dtype)
        outs.append(jnp.einsum("bhqk,bkhd->bqhd", p, v[:, :e]))
    o = jnp.concatenate(outs, axis=1).reshape(B, S, N_HEADS * V_DIM)
    return o @ w_mla_o

def hier_moe(u, wg, bg, we, be, w1, w3, w2):
    B, S, D = u.shape
    N = B * S
    xf = u.reshape(N, D)
    g_logits = (xf @ wg).astype(jnp.float32) + bg.astype(jnp.float32)
    g_prob = jax.nn.softmax(g_logits, axis=-1)
    g_sel = jnp.argmax(g_logits, axis=-1).astype(jnp.int32)
    e_logits = ((xf @ we).astype(jnp.float32) + be.astype(jnp.float32)).reshape(N, N_GROUPS, EXPERTS_PER_GROUP)
    e_in_group = jnp.take_along_axis(e_logits, g_sel[:, None, None], axis=1)[:, 0]
    e_prob = jax.nn.softmax(e_in_group, axis=-1)
    top_p, top_j = lax.top_k(e_prob, TOP_K)
    gate = jnp.take_along_axis(g_prob, g_sel[:, None], axis=1) * top_p / jnp.sum(top_p, axis=-1, keepdims=True)
    expert_id = g_sel[:, None] * EXPERTS_PER_GROUP + top_j.astype(jnp.int32)
    M = N * TOP_K
    flat_e = expert_id.reshape(M)
    flat_tok = jnp.repeat(jnp.arange(N, dtype=jnp.int32), TOP_K)
    flat_w = gate.reshape(M)
    order = jnp.argsort(flat_e)
    sorted_e = flat_e[order]
    counts = jnp.bincount(flat_e, length=N_EXPERTS)
    padded = ((counts + MOE_BLOCK - 1) // MOE_BLOCK) * MOE_BLOCK
    start = jnp.cumsum(counts) - counts
    pad_end = jnp.cumsum(padded)
    pad_start = pad_end - padded
    dest = pad_start[sorted_e] + (jnp.arange(M, dtype=jnp.int32) - start[sorted_e])
    m_pad = M + N_EXPERTS * MOE_BLOCK
    n_blocks = m_pad // MOE_BLOCK
    tok_buf = jnp.full((m_pad,), N, dtype=jnp.int32).at[dest].set(flat_tok[order])
    w_buf = jnp.zeros((m_pad,), dtype=jnp.float32).at[dest].set(flat_w[order])
    block_e = jnp.minimum(
        jnp.searchsorted(pad_end, jnp.arange(n_blocks, dtype=jnp.int32) * MOE_BLOCK, side="right"),
        N_EXPERTS - 1).astype(jnp.int32)
    x_pad = jnp.concatenate([xf, jnp.zeros((1, D), xf.dtype)], axis=0)[tok_buf]
    x_pad = x_pad.reshape(n_blocks, MOE_BLOCK, D)

    def expert_block(args):
        xb, e = args
        h = jax.nn.silu(xb @ w1[e]) * (xb @ w3[e])
        return h @ w2[e]

    y_pad = lax.map(expert_block, (x_pad, block_e)).reshape(m_pad, D)
    y = jax.ops.segment_sum(y_pad * w_buf[:, None].astype(y_pad.dtype), tok_buf, num_segments=N + 1)[:N]
    return y.reshape(B, S, D)

def second_inputs(seed: int = 0) -> dict:
    key = jax.random.key(seed)
    ks = jax.random.split(key, 32)
    L, D, f32 = DEPTH, D_MODEL, jnp.float32

    def nrm(k, shape, fan_in):
        return jax.random.normal(k, shape, f32) * (fan_in ** -0.5)

    def gain(k, shape):
        return 1.0 + 0.1 * jax.random.normal(k, shape, f32)

    def bias(k, shape):
        return 0.01 * jax.random.normal(k, shape, f32)

    x = jax.random.normal(ks[0], (BATCH, SEQ, D), f32)
    offset = jax.random.randint(ks[1], (BATCH, 1), 0, 4096, dtype=jnp.int32)
    positions = offset + jnp.arange(SEQ, dtype=jnp.int32)[None, :]
    a0 = jax.random.uniform(ks[2], (L, D_RNN), f32, 0.9, 0.999)
    s0 = a0 ** (1.0 / LRU_C)
    lru_lambda = jnp.log(s0) - jnp.log1p(-s0)
    return {
        "x": x,
        "positions": positions,
        "norm1_g": gain(ks[3], (L, D)),
        "w_in": nrm(ks[4], (L, D, D_IN), D),
        "conv_w": nrm(ks[5], (L, CONV_W, D_RNN), CONV_W),
        "conv_b": bias(ks[6], (L, D_RNN)),
        "lru_wa": nrm(ks[7], (L, RNN_BLOCKS, RNN_BLOCK_W, RNN_BLOCK_W), RNN_BLOCK_W),
        "lru_ba": bias(ks[8], (L, D_RNN)),
        "lru_wx": nrm(ks[9], (L, RNN_BLOCKS, RNN_BLOCK_W, RNN_BLOCK_W), RNN_BLOCK_W),
        "lru_bx": bias(ks[10], (L, D_RNN)),
        "lru_lambda": lru_lambda,
        "w_rnn_o": nrm(ks[11], (L, D_RNN, D), D_RNN),
        "q_norm_g": gain(ks[12], (L, Q_LORA)),
        "w_uq": nrm(ks[13], (L, Q_LORA, N_HEADS * QK_DIM), Q_LORA),
        "kv_norm_g": gain(ks[14], (L, KV_LORA)),
        "w_ukv": nrm(ks[15], (L, KV_LORA, N_HEADS * (QK_NOPE + V_DIM)), KV_LORA),
        "qk_norm_q_g": gain(ks[16], (L, QK_DIM)),
        "qk_norm_k_g": gain(ks[17], (L, QK_DIM)),
        "w_mla_o": nrm(ks[18], (L, N_HEADS * V_DIM, D), N_HEADS * V_DIM),
        "w_out": nrm(ks[19], (L, D, D), D),
        "norm2_g": gain(ks[20], (L, D)),
        "router_wg": nrm(ks[21], (L, D, N_GROUPS), D),
        "router_bg": bias(ks[22], (L, N_GROUPS)),
        "router_we": nrm(ks[23], (L, D, N_EXPERTS), D),
        "router_be": bias(ks[24], (L, N_EXPERTS)),
        "exp_w1": nrm(ks[25], (L, N_EXPERTS, D, D_EXPERT), D),
        "exp_w3": nrm(ks[26], (L, N_EXPERTS, D, D_EXPERT), D),
        "exp_w2": nrm(ks[27], (L, N_EXPERTS, D_EXPERT, D), D_EXPERT),
    }

def second_block(x, positions, norm1_g, w_in, conv_w, conv_b, lru_wa, lru_ba, lru_wx, lru_bx,
              lru_lambda, w_rnn_o, q_norm_g, w_uq, kv_norm_g, w_ukv, qk_norm_q_g, qk_norm_k_g,
              w_mla_o, w_out, norm2_g, router_wg, router_bg, router_we, router_be,
              exp_w1, exp_w3, exp_w2):
    split_points = [int(p) for p in np.cumsum(IN_SPLITS)[:-1]]
    h = x
    for l in range(DEPTH):
        u = rmsnorm_2(h, norm1_g[l])
        proj = u @ w_in[l]
        x_r, y_r, c_q, c_kv, k_pe, g_a, g_b = jnp.split(proj, split_points, axis=-1)
        x_r = causal_depthwise_conv(x_r, conv_w[l], conv_b[l])
        h_r = rg_lru(x_r, lru_wa[l], lru_ba[l], lru_wx[l], lru_bx[l], lru_lambda[l])
        branch_a = (h_r * jax.nn.gelu(y_r, approximate=True)) @ w_rnn_o[l]
        branch_b = mla_attention(c_q, c_kv, k_pe, positions, q_norm_g[l], w_uq[l], kv_norm_g[l],
                                 w_ukv[l], qk_norm_q_g[l], qk_norm_k_g[l], w_mla_o[l])
        merged = jax.nn.sigmoid(g_a) * branch_a + jax.nn.sigmoid(g_b) * branch_b
        h = h + merged @ w_out[l]
        h = h + hier_moe(rmsnorm_2(h, norm2_g[l]), router_wg[l], router_bg[l], router_we[l],
                         router_be[l], exp_w1[l], exp_w3[l], exp_w2[l])
    return h


def setup_inputs(seed=0):
    out = dict(first_inputs(seed))
    for name, value in second_inputs(seed + 1).items():
        if name != "x":
            out[name + "_2"] = value
    return out


def reference(
    x, norm1_g, w_in, rw_mu, w0, w_up_decay, a0, w_up_a, w_up_g, k_k, k_a, r_k, lnx_w, lnx_b,
    qk_conv_w, qk_conv_b, i_bias, f_bias, mh_norm_g, w_out, norm2_g, w_ffn_up, ffn_conv_w,
    ffn_conv_b, w_ffn_down, norm_f_g, positions_2, norm1_g_2, w_in_2, conv_w_2, conv_b_2,
    lru_wa_2, lru_ba_2, lru_wx_2, lru_bx_2, lru_lambda_2, w_rnn_o_2, q_norm_g_2, w_uq_2,
    kv_norm_g_2, w_ukv_2, qk_norm_q_g_2, qk_norm_k_g_2, w_mla_o_2, w_out_2, norm2_g_2,
    router_wg_2, router_bg_2, router_we_2, router_be_2, exp_w1_2, exp_w3_2, exp_w2_2,
):
    x = first_block(
        x, norm1_g, w_in, rw_mu, w0, w_up_decay, a0, w_up_a, w_up_g, k_k, k_a, r_k, lnx_w,
        lnx_b, qk_conv_w, qk_conv_b, i_bias, f_bias, mh_norm_g, w_out, norm2_g, w_ffn_up,
        ffn_conv_w, ffn_conv_b, w_ffn_down, norm_f_g,
    )
    return second_block(
        x, positions_2, norm1_g_2, w_in_2, conv_w_2, conv_b_2, lru_wa_2, lru_ba_2, lru_wx_2,
        lru_bx_2, lru_lambda_2, w_rnn_o_2, q_norm_g_2, w_uq_2, kv_norm_g_2, w_ukv_2,
        qk_norm_q_g_2, qk_norm_k_g_2, w_mla_o_2, w_out_2, norm2_g_2, router_wg_2, router_bg_2,
        router_we_2, router_be_2, exp_w1_2, exp_w3_2, exp_w2_2,
    )


_drawn_inputs = setup_inputs


def setup_inputs(seed=0):
    import zlib

    import numpy as np

    out = dict(_drawn_inputs(seed))
    spreads = {}
    factors = {'conv_b_2': 7.234,
     'lru_ba_2': 64.0,
     'lru_bx_2': 64.0,
     'q_norm_g_2': 8.0,
     'kv_norm_g_2': 8.0,
     'qk_norm_q_g_2': 8.0,
     'qk_norm_k_g_2': 8.0,
     'router_bg_2': 64.0,
     'router_be_2': 64.0,
     'lru_wa_2': 4.461,
     'norm2_g_2': 4.715}
    for name, (base, spread) in spreads.items():
        noise = np.random.default_rng([zlib.crc32(name.encode()), seed]).standard_normal(out[name].shape)
        drawn = base * np.exp(spread * noise) if base else spread * noise
        out[name] = __import__('jax').numpy.asarray(drawn.astype(out[name].dtype))
    for name, factor in factors.items():
        out[name] = (out[name] * factor).astype(out[name].dtype)
    return out
```

```python
from contextlib import ExitStack

import numpy as np

import concourse.bass as bass
from concourse import mybir

F32 = mybir.dt.float32
F32R = mybir.dt.float32r
I32 = mybir.dt.int32
U32 = mybir.dt.uint32
ALU = mybir.AluOpType
ACT = mybir.ActivationFunctionType
AX = mybir.AxisListType

P = 128
SEQ = 1024
HALF = 512
DM = 1024
DT = DM // P


def stage_semaphores(nc, ctx, prefix):
    held = []

    def give_back():
        nc.clear_and_free_semaphores(held)
        nc.all_engine_barrier()

    ctx.callback(give_back)

    def sem(name):
        held.append(nc.alloc_semaphore(f"{prefix}_{name}"))
        return held[-1]

    return sem


def run_loop(eng, n, body):
    body(0, True, n == 1)
    if n > 2:
        with eng.Fori(1, n - 1) as i:
            body(i, False, False)
    if n > 1:
        body(n - 1, False, True)


def split_matmuls(pe, out, w_hi, w_lo, x_hi, x_lo, first, last):
    pe.matmul(out, w_hi, x_hi, start=first, stop=False)
    pe.matmul(out, w_hi, x_lo, start=False, stop=False)
    return pe.matmul(out, w_lo, x_hi, start=False, stop=last)


def dense_stage(nc, name, src, KT, w, NT, out, vecs, consts, tokens=SEQ, norm=None, mode="copy",
                aux=None, aux2=None, norm_out=None):
    PASSES = SEQ // tokens
    NH = tokens // HALF
    N = NT // 2
    with ExitStack() as ctx:
        sb = lambda n, s, d=F32: ctx.enter_context(nc.sbuf_tensor(f"{name}_{n}", s, d))
        psum = lambda n, s: ctx.enter_context(nc.psum_tensor(f"{name}_{n}", s, F32))
        sem = stage_semaphores(nc, ctx, name)
        x_hi = sb("x_hi", [P, KT, tokens], F32R)
        x_lo = sb("x_lo", [P, KT, tokens], F32R)
        w_raw = sb("w_raw", [P, 2, KT * P])
        w_hi = sb("w_hi", [P, 2, KT * P], F32R)
        w_lo = sb("w_lo", [P, 2, KT * P], F32R)
        XS = KT if norm else 2
        x_raw = sb("x_raw", [P, XS, tokens])
        o_buf = sb("o_buf", [P, 2, tokens])
        acc = psum("acc", [P, 4, HALF])
        x_loaded = [sem(f"x_loaded{i}") for i in range(XS)]
        w_loaded = [sem(f"w_loaded{i}") for i in range(2)]
        x_split = sem("x_split")
        x_hi_done = sem("x_hi_done")
        w_hi_done = sem("w_hi_done")
        w_lo_done = sem("w_lo_done")
        acc_ready = sem("acc_ready")
        acc_free = sem("acc_free")
        out_ready = sem("out_ready")
        stored = [sem(f"stored{i}") for i in range(2)]
        if norm:
            gain, eps_col, width = norm
            sq = sb("sq", [P, 2, tokens])
            rstd = sb("rstd", [P, tokens])
            rms = sb("rms", [P, tokens])
            ss = psum("ss", [P, 2, HALF])
            sq_ready = sem("sq_ready")
            ss_ready = sem("ss_ready")
            rms_ready = sem("rms_ready")
            rstd_ready = sem("rstd_ready")
            h_ready = sem("h_ready")
        if aux is not None:
            aux_buf = sb("aux", [P, 2, tokens])
            aux_loaded = [sem(f"aux_loaded{i}") for i in range(2)]
            if mode.startswith("gate"):
                sig = sb("sig", [P, 2, tokens])
                sig_ready = sem("sig_ready")
                prod_done = sem("prod_done")
        if aux2 is not None:
            aux2_buf = sb("aux2", [P, 2, tokens])
        if mode == "ffn":
            cw, cb = vecs["ffn_conv"], vecs["ffn_conv_b"]
            a_pad = sb("a_pad", [P, tokens + 2])
            conv = sb("conv", [P, 2, tokens])
            act = sb("act", [P, tokens])
            pad_zero = sem("pad_zero")
            conv_step = sem("conv_step")
            act_ready = sem("act_ready")
            a_copied = sem("a_copied")
        V = vecs["buf"]
        NO = N if mode == "ffn" else NT
        block = ctx.enter_context(nc.Block(no_gpsimd_drain=True))

        @block.sync
        def _(sp):
            for p in range(PASSES):
                tok = slice(p * tokens, (p + 1) * tokens)
                for u in range(2):
                    if p:
                        sp.wait_ge(w_lo_done, p * NT - 1 + u)
                    sp.dma_start(w_raw[:, u, :], w[u]).then_inc(w_loaded[u], 16)
                for k in range(KT):
                    if not norm and p * KT + k >= 2:
                        sp.wait_ge(x_split, p * KT + k - 1)
                    sp.dma_start(x_raw[:, k if norm else k % 2, :], src[k][:, tok]).then_inc(x_loaded[k % XS], 16)
                if N > 1:
                    with sp.Fori(1, N) as i:
                        for u in range(2):
                            sp.wait_ge(w_lo_done, 2 * i + (p * NT + u - 1))
                            sp.dma_start(w_raw[:, u, :], w[2 * i + u]).then_inc(w_loaded[u], 16)

        @block.scalar
        def _(act_e):
            if norm:
                for k in range(KT):
                    act_e.wait_ge(x_loaded[k], 16)
                    if k >= 2:
                        act_e.wait_ge(ss_ready, k - 1)
                    nc.scalar.activation(sq[:, k % 2, :], x_raw[:, k, :], ACT.Square).then_inc(sq_ready, 1)
                act_e.wait_ge(ss_ready, KT)
                nc.scalar.activation(rms[:, :], ss[:, :, :].rearrange("p a b -> p (a b)"), ACT.Sqrt,
                                     bias=consts["buf"][:, eps_col:eps_col + 1], scale=1.0 / width).then_inc(rms_ready, 1)
            for p in range(PASSES):
                for k in range(KT):
                    if norm:
                        act_e.wait_ge(h_ready, k + 1)
                    else:
                        act_e.wait_ge(x_loaded[k % 2], 16 * (p * (KT // 2) + k // 2 + 1))
                        if p and k == 0:
                            act_e.wait_ge(acc_ready, p * NT * NH)
                    nc.scalar.copy(x_hi[:, k, :], x_raw[:, k if norm else k % 2, :]).then_inc(x_hi_done, 1)

                def body(i, first, last, p=p):
                    for u in range(2):
                        act_e.wait_ge(w_loaded[u], 16 * i + 16 * (p * N + 1))
                        if not first:
                            act_e.wait_ge(acc_ready, (2 * NH) * i + (p * NT + u - 1) * NH)
                        nc.scalar.copy(w_hi[:, u, :], w_raw[:, u, :]).then_inc(w_hi_done, 1)
                        if mode.startswith("gate"):
                            act_e.wait_ge(aux_loaded[u], (32 if aux2 is not None else 16) * i + (32 if aux2 is not None else 16))
                            if not first:
                                act_e.wait_ge(prod_done, 2 * i + u - 1)
                            nc.scalar.activation(sig[:, u, :], aux_buf[:, u, :], ACT.Sigmoid).then_inc(sig_ready, 1)
                    if mode == "ffn":
                        act_e.wait_ge(conv_step, 3 * i + 3)
                        if not first:
                            act_e.wait_ge(out_ready, i)
                        nc.scalar.activation(act[:, :], conv[:, 0, :], ACT.Silu).then_inc(act_ready, 1)

                run_loop(act_e, N, body)

        @block.tensor
        def _(pe):
            if norm:
                for k in range(KT):
                    pe.wait_ge(sq_ready, k + 1)
                    for h in range(NH):
                        mm = pe.matmul(ss[:, h, :], consts["ones"], sq[:, k % 2, h * HALF:(h + 1) * HALF],
                                       start=k == 0, stop=k == KT - 1)
                    mm.then_inc(ss_ready, 1)
            for p in range(PASSES):
                pe.wait_ge(x_split, (p + 1) * KT)

                def body(i, first, last, p=p):
                    for u in range(2):
                        pe.wait_ge(w_lo_done, 2 * i + (p * NT + u + 1))
                        for h in range(NH):
                            if not (first and p == 0):
                                pe.wait_ge(acc_free, (2 * NH) * i + (p * NT + u - 2) * NH + h + 1)
                            for k in range(KT):
                                ks = slice(k * P, (k + 1) * P)
                                hs = slice(h * HALF, (h + 1) * HALF)
                                mm = split_matmuls(pe, acc[:, u * NH + h, :], w_hi[:, u, ks], w_lo[:, u, ks],
                                                   x_hi[:, k, hs], x_lo[:, k, hs], k == 0, k == KT - 1)
                            mm.then_inc(acc_ready, 1)

                run_loop(pe, N, body)

        @block.vector
        def _(dve):
            if norm:
                dve.wait_ge(rms_ready, 1)
                nc.vector.reciprocal(rstd[:, :], rms[:, :]).then_inc(rstd_ready, 1)
                dve.wait_ge(rstd_ready, 1)
                for k in range(KT):
                    nc.vector.scalar_tensor_tensor(out=x_raw[:, k, :], in0=x_raw[:, k, :], scalar=V[:, gain + k:gain + k + 1],
                                                   in1=rstd[:, :], op0=ALU.mult, op1=ALU.mult).then_inc(h_ready, 1)
            if mode == "ffn":
                nc.vector.memset(a_pad[:, 0:2], 0.0).then_inc(pad_zero, 1)
                dve.wait_ge(pad_zero, 1)

            def low_part(t_u, t_count):
                dve.wait_ge(w_hi_done, t_count)
                nc.vector.tensor_tensor(w_lo[:, t_u, :], w_raw[:, t_u, :], w_hi[:, t_u, :], ALU.subtract).then_inc(w_lo_done, 1)

            for p in range(PASSES):
                for k in range(KT):
                    dve.wait_ge(x_hi_done, p * KT + k + 1)
                    nc.vector.tensor_tensor(x_lo[:, k, :], x_raw[:, k if norm else k % 2, :], x_hi[:, k, :],
                                            ALU.subtract).then_inc(x_split, 1)
                low_part(0, p * NT + 1)

                def body(i, first, last, p=p):
                    for u in range(2):
                        if not (last and u == 1):
                            low_part(1 - u, 2 * i + (p * NT + u + 2))
                        if mode == "ffn":
                            ffn_part(i, u, first)
                            continue
                        if not (first and p == 0):
                            dve.wait_ge(stored[u], 16 * i + 16 * p * N)
                        if aux is not None and not mode.startswith("gate"):
                            dve.wait_ge(aux_loaded[u], 16 * i + 16 * (p * N + 1))
                        if mode.startswith("gate"):
                            dve.wait_ge(sig_ready, 2 * i + u + 1)
                        for h in range(NH):
                            hs = slice(h * HALF, (h + 1) * HALF)
                            dve.wait_ge(acc_ready, (2 * NH) * i + (p * NT + u) * NH + h + 1)
                            a = acc[:, u * NH + h, :]
                            if mode == "copy":
                                ins = nc.vector.tensor_copy(o_buf[:, u, hs], a)
                            elif mode == "residual":
                                ins = nc.vector.tensor_tensor(o_buf[:, u, hs], a, aux_buf[:, u, hs], ALU.add)
                            else:
                                ins = nc.vector.tensor_tensor(o_buf[:, u, hs], a, sig[:, u, hs], ALU.mult)
                            ins.then_inc(acc_free, 1)
                        if mode == "gate_add":
                            dve.wait_ge(acc_free, (2 * NH) * i + (u + 1) * NH)
                            nc.vector.tensor_tensor(o_buf[:, u, :], o_buf[:, u, :], aux2_buf[:, u, :],
                                                    ALU.add).then_inc(prod_done, 1)
                        elif mode == "gate":
                            dve.wait_ge(acc_free, (2 * NH) * i + (u + 1) * NH)
                            dve.sem_inc(prod_done, 1)

                def ffn_part(i, u, first):
                    if u == 0:
                        for h in range(NH):
                            dve.wait_ge(acc_ready, (2 * NH) * i + h + 1)
                            nc.vector.tensor_copy(a_pad[:, 2 + h * HALF:2 + (h + 1) * HALF], acc[:, h, :]).then_inc(acc_free, 1)
                        dve.wait_ge(acc_free, (2 * NH) * i + NH)
                        nc.vector.tensor_scalar(conv[:, 0, :], a_pad[:, 2:2 + tokens], V[:, bass.ds(cw + 2 * N + i, 1)],
                                                V[:, bass.ds(cb + i, 1)], ALU.mult, ALU.add).then_inc(conv_step, 1)
                        dve.wait_ge(conv_step, 3 * i + 1)
                        nc.vector.scalar_tensor_tensor(out=conv[:, 1, :], in0=a_pad[:, 1:1 + tokens],
                                                       scalar=V[:, bass.ds(cw + N + i, 1)], in1=conv[:, 0, :],
                                                       op0=ALU.mult, op1=ALU.add).then_inc(conv_step, 1)
                        dve.wait_ge(conv_step, 3 * i + 2)
                        nc.vector.scalar_tensor_tensor(out=conv[:, 0, :], in0=a_pad[:, 0:tokens],
                                                       scalar=V[:, bass.ds(cw + i, 1)], in1=conv[:, 1, :],
                                                       op0=ALU.mult, op1=ALU.add).then_inc(conv_step, 1)
                    else:
                        dve.wait_ge(act_ready, i + 1)
                        if not first:
                            dve.wait_ge(stored[0], 16 * i)
                        for h in range(NH):
                            hs = slice(h * HALF, (h + 1) * HALF)
                            dve.wait_ge(acc_ready, (2 * NH) * i + NH + h + 1)
                            nc.vector.tensor_tensor(o_buf[:, 0, hs], acc[:, NH + h, :], act[:, hs],
                                                    ALU.mult).then_inc(acc_free, 1)
                        dve.wait_ge(acc_free, (2 * NH) * i + 2 * NH)
                        dve.sem_inc(out_ready, 1)

                run_loop(dve, N, body)

        @block.gpsimd
        def _(pool):
            for p in range(PASSES):
                tok = slice(p * tokens, (p + 1) * tokens)

                def load_aux(i, u, p=p, tok=tok):
                    pool.dma_start(aux_buf[:, u, :], aux[2 * i + u][:, tok]).then_inc(aux_loaded[u], 16)
                    if aux2 is not None:
                        pool.dma_start(aux2_buf[:, u, :], aux2[2 * i + u][:, tok]).then_inc(aux_loaded[u], 16)

                if aux is not None:
                    for u in range(2):
                        if p:
                            pool.wait_ge(acc_free, (p * NT - 1 + u) * NH)
                        load_aux(0, u)

                def body(i, first, last, p=p, tok=tok, load_aux=load_aux):
                    if mode == "ffn":
                        pool.wait_ge(out_ready, i + 1)
                        pool.dma_start(out[i][:, tok], o_buf[:, 0, :]).then_inc(stored[0], 16)
                        return
                    for u in range(2):
                        if mode == "gate_add":
                            pool.wait_ge(prod_done, 2 * i + u + 1)
                        else:
                            pool.wait_ge(acc_free, (2 * NH) * i + (p * NT + u + 1) * NH)
                        pool.dma_start(out[2 * i + u][:, tok], o_buf[:, u, :]).then_inc(stored[u], 16)
                        if aux is not None and not last:
                            load_aux(i + 1, u)

                run_loop(pool, N, body)
            for u in range(1 if mode == "ffn" else 2):
                pool.wait_ge(stored[u], 16 * N * PASSES)
def _cols(v):
    return np.reshape(v, (-1, P)).T


def _tiles(w):
    K, N = w.shape
    return np.ascontiguousarray(np.transpose(np.reshape(w, (K // P, P, N // P, P)), (2, 1, 0, 3))).reshape(N // P, P, K)


def _vec_table():
    at, table = 0, {}
    for name, n in (("norm1", 8), ("mu", 14), ("w0", 4), ("a0", 4), ("k_k", 4), ("k_a", 4), ("r_k", 4), ("lnx_w", 4),
                    ("lnx_b", 4), ("qk_conv", 16), ("qk_conv_b", 4), ("i_bias", 1), ("f_bias", 1), ("mh_g", 4),
                    ("norm2", 8), ("ffn_conv", 66), ("ffn_conv_b", 22), ("norm_f", 8), ("norm1_2", 8), ("conv_2", 32),
                    ("conv_b_2", 8), ("lru_ba", 8), ("lru_bx", 8), ("lru_lam", 8), ("q_norm", 2), ("kv_norm", 2),
                    ("qg_n", 1), ("qg_r", 1), ("qg_s", 1), ("kg_n", 1), ("kg_r", 1), ("kg_s", 1), ("norm2_2", 8)):
        table[name] = at
        at += n
    return table, at


VEC, NVEC = _vec_table()


def _const_table():
    at, table = 0, {}
    for name, n in (("ones", P), ("ident", P), ("head_ones", P), ("before", P), ("upto", P), ("after", P), ("row_sel", 4 * P),
                    ("eps6", 1), ("eps_ln", 1), ("inv_freq", 1), ("rope_sign", 1), ("one", 1), ("iota64", 64), ("iota8", 8),
                    ("block_start", 1)):
        table[name] = at
        at += n
    return table, at


CONST, NCONST = _const_table()
LEVELS = 7


def constants():
    c = np.zeros((P, NCONST), np.float32)
    r, q = np.arange(P)[:, None], np.arange(P)[None, :]
    put = lambda name, a: c.__setitem__((slice(None), slice(CONST[name], CONST[name] + a.shape[1])), a)
    put("ones", np.ones((P, P)))
    put("ident", r == q)
    put("head_ones", r // 64 == q // 64)
    put("before", r < q)
    put("upto", r <= q)
    put("after", r > q)
    put("row_sel", np.concatenate([np.repeat(r == h, P, 1) for h in range(4)], 1))
    put("eps6", np.full((P, 1), 1e-6))
    put("eps_ln", np.full((P, 1), 64e-5))
    inv = (np.float32(10000.0) ** (-(np.arange(0, 64, 2, dtype=np.float32)) / np.float32(64))).astype(np.float32)
    put("inv_freq", np.tile(inv, 4)[:, None])
    put("rope_sign", np.where(r % 64 < 32, -1.0, 1.0))
    put("one", np.ones((P, 1)))
    put("iota64", np.tile(np.arange(64.0), (P, 1)))
    put("iota8", np.tile(np.arange(8.0), (P, 1)))
    put("block_start", r * float(P))
    lv = []
    for l in range(LEVELS):
        b = 1 << l
        lv.append((r // (2 * b) == q // (2 * b)) & (r // b > q // b))
    masks = np.concatenate(lv + [m.T for m in lv], 1).astype(np.float32)
    return c, masks


def lay_out(a):
    v = np.zeros((P, NVEC), np.float32)

    def put(name, cols):
        v[:, VEC[name]:VEC[name] + cols.shape[1]] = cols

    L = {k: np.asarray(x)[0] for k, x in a.items() if k not in ("x", "norm_f_g", "positions_2")}
    for name, key in (("norm1", "norm1_g"), ("mu", "rw_mu"), ("w0", "w0"), ("a0", "a0"), ("k_k", "k_k"), ("k_a", "k_a"),
                      ("r_k", "r_k"), ("lnx_w", "lnx_w"), ("lnx_b", "lnx_b"), ("qk_conv", "qk_conv_w"),
                      ("qk_conv_b", "qk_conv_b"), ("mh_g", "mh_norm_g"), ("norm2", "norm2_g"), ("ffn_conv", "ffn_conv_w"),
                      ("ffn_conv_b", "ffn_conv_b"), ("norm1_2", "norm1_g_2"), ("conv_2", "conv_w_2"),
                      ("conv_b_2", "conv_b_2"), ("lru_ba", "lru_ba_2"), ("lru_bx", "lru_bx_2"), ("lru_lam", "lru_lambda_2"),
                      ("q_norm", "q_norm_g_2"), ("kv_norm", "kv_norm_g_2"), ("norm2_2", "norm2_g_2")):
        put(name, _cols(L[key]))
    put("norm_f", _cols(np.asarray(a["norm_f_g"])))
    v[0:4, VEC["i_bias"]] = L["i_bias"]
    v[0:4, VEC["f_bias"]] = L["f_bias"]
    swap = np.concatenate([np.arange(32, 64), np.arange(0, 32)])
    for c, key in (("qg", "qk_norm_q_g_2"), ("kg", "qk_norm_k_g_2")):
        v[:, VEC[c + "_n"]] = L[key][:128]
        v[:, VEC[c + "_r"]] = np.concatenate([L[key][128:]] * 2)
        v[:, VEC[c + "_s"]] = np.concatenate([L[key][128:][swap]] * 2)
    z = lambda n: np.zeros((DM, n), np.float32)
    w_in = L["w_in"]
    gates = np.concatenate([w_in[:, 3328:3332], z(28), w_in[:, 3332:3336], z(92)], 1)
    w_in_t = _tiles(np.concatenate([w_in[:, :3328], gates, z(128)], 1))
    up = L["w_ffn_up"]
    up = np.transpose(np.reshape(up, (DM, 2, 22, P)), (0, 2, 1, 3)).reshape(DM, 44 * P)
    w2 = L["w_in_2"]
    kpe = w2[:, 2560:2624]
    w_in2_t = _tiles(np.concatenate([w2[:, :2560], kpe, kpe, kpe[:, swap], kpe[:, swap], w2[:, 2624:]], 1))
    uq = np.reshape(L["w_uq_2"], (256, 8, 192))
    uq_t = _tiles(np.concatenate([uq[:, :, :128].reshape(256, -1), uq[:, :, 128:].reshape(256, -1),
                                  uq[:, :, 128:][:, :, swap].reshape(256, -1)], 1))
    ukv = np.reshape(L["w_ukv_2"], (256, 8, 2, 128))
    ukv_t = _tiles(np.transpose(ukv, (0, 2, 1, 3)).reshape(256, 2048))
    lora = np.concatenate([L["w_up_decay"], L["w_up_a"]], 0)
    router = np.concatenate([L["router_wg_2"], L["router_we_2"]], 1)
    router = np.transpose(np.reshape(router, (8, P, 72)), (1, 0, 2)).reshape(P, 8 * 72)
    w13 = np.concatenate([L["exp_w1_2"], L["exp_w3_2"]], 2)
    w13 = np.ascontiguousarray(np.transpose(np.reshape(w13, (64, 8, P, 512)), (0, 2, 1, 3))).reshape(64 * P, 4096)
    ew2 = np.ascontiguousarray(np.transpose(np.reshape(L["exp_w2_2"], (64, 2, P, DM)), (0, 2, 1, 3))).reshape(64 * P, 2048)
    lru_w = np.concatenate([np.transpose(L["lru_wa_2"], (1, 0, 2)).reshape(P, DM), np.transpose(L["lru_wx_2"], (1, 0, 2)).reshape(P, DM)], 1)
    consts, masks = constants()
    return {
        "xT": np.ascontiguousarray(np.asarray(a["x"])[0].T).reshape(DT, P, SEQ),
        "vecs": v, "consts": consts, "masks": masks,
        "w_in": w_in_t, "w_out": _tiles(L["w_out"]), "w_up": _tiles(up), "w_down": _tiles(L["w_ffn_down"]),
        "w_in2": w_in2_t, "w_rnn_o": _tiles(L["w_rnn_o_2"]), "w_mla_o": _tiles(L["w_mla_o_2"]), "w_out2": _tiles(L["w_out_2"]),
        "w_uq": uq_t, "w_ukv": ukv_t, "lora": lora, "w_up_g": L["w_up_g"], "router": router,
        "router_b": np.concatenate([L["router_bg_2"], L["router_be_2"]])[None, :],
        "w13": w13, "ew2": ew2, "lru_w": lru_w, "positions": np.asarray(a["positions_2"]),
    }
class Steps:

    def __init__(self, eng, sem):
        self.eng, self.sem, self.n = eng, sem, 0

    def __call__(self, ins):
        ins.then_inc(self.sem, 1)
        self.n += 1
        return self.n

    def settle(self):
        self.eng.wait_ge(self.sem, self.n)

    def link(self, ins):
        self(ins)
        self.settle()


def mlstm_stage(nc, proj, y_out, V, C):
    NH, DK, CAP = 4, 64, 15.0
    q0, v0, o0, gate = 14, 18, 22, 26
    one = lambda name, h=0: C[:, CONST[name] + h:CONST[name] + h + 1]
    with ExitStack() as ctx:
        sb = lambda n, s, d=F32: ctx.enter_context(nc.sbuf_tensor(f"ml_{n}", s, d))
        sem = stage_semaphores(nc, ctx, "ml")
        qk = sb("qk", [P, 4, SEQ])
        v_tok = sb("v_tok", [P, DT, NH * P])
        g_cols = sb("g_cols", [P, DT, NH])
        neg_G = sb("neg_G", [P, NH, SEQ])
        exp_m = sb("exp_m", [P, NH, SEQ])

        with ExitStack() as ctx1:
            sb1 = lambda n, s, d=F32: ctx1.enter_context(nc.sbuf_tensor(f"ml_{n}", s, d))
            pre = sb1("pre", [P, 4, SEQ + 3])
            conv = sb1("conv", [P, 2, 2, SEQ])
            vT = sb1("vT", [P, 4, SEQ])
            ig = sb1("ig", [NH, SEQ])
            fg = sb1("fg", [NH, SEQ])
            row_t = sb1("row_t", [NH, 4, SEQ])
            ones_row = sb1("ones_row", [NH, SEQ])
            cap_b = sb1("cap_b", [NH, 2])
            tr = ctx1.enter_context(nc.psum_tensor("ml_tr", [P, 2, 512], F32))
            bc = ctx1.enter_context(nc.psum_tensor("ml_bc", [P, 4, 512], F32))
            gc = ctx1.enter_context(nc.psum_tensor("ml_gc", [P, 512], F32))
            qk_loaded = [sem(f"qk_loaded{i}") for i in range(4)]
            v_loaded, gates_loaded, pads = sem("v_loaded"), sem("gates_loaded"), sem("pads")
            conv_done, qk_done, dve_steps = sem("conv_done"), sem("qk_done"), sem("dve_steps")
            bias_ready, tanh_ready, exp_ready, ln_ready = sem("bias_ready"), sem("tanh_ready"), sem("exp_ready"), sem("ln_ready")
            rows_ready, tr_ready, tr_free, bc_ready, bc_free = (sem(n) for n in ("rows_ready", "tr_ready", "tr_free", "bc_ready", "bc_free"))
            gc_ready, bc2_free = sem("gc_ready"), sem("bc2_free")
            block = ctx1.enter_context(nc.Block(no_gpsimd_drain=True))

            @block.sync
            def _(sp):
                sp.dma_start(ig[:, :], proj[gate][0:NH, :]).then_inc(gates_loaded, 16)
                sp.dma_start(fg[:, :], proj[gate][32:32 + NH, :]).then_inc(gates_loaded, 16)
                for j in range(4):
                    sp.dma_start(pre[:, j, 3:], proj[q0 + j]).then_inc(qk_loaded[j], 16)
                for j in range(4):
                    sp.dma_start(vT[:, j, :], proj[v0 + j]).then_inc(v_loaded, 16)

            @block.vector
            def _(dve):
                st = Steps(dve, dve_steps)
                nc.vector.memset(pre[:, :, 0:3], 0.0).then_inc(pads, 1)
                nc.vector.memset(ones_row[:, :], 1.0).then_inc(pads, 1)
                nc.vector.tensor_scalar(cap_b[:, :], V[0:NH, VEC["i_bias"]:VEC["i_bias"] + 2], 1.0 / CAP, None,
                                        ALU.mult).then_inc(bias_ready, 1)
                dve.wait_ge(pads, 2)
                dve.wait_ge(ln_ready, 1)
                st.link(nc.vector.tensor_tensor_scan(row_t[:, 3, :], ones_row[:, :], row_t[:, 2, :], 0.0, ALU.mult, ALU.subtract))
                st.link(nc.vector.scalar_tensor_tensor(out=ig[:, :], in0=row_t[:, 0, :], scalar=CAP, in1=row_t[:, 3, :],
                                                       op0=ALU.mult, op1=ALU.subtract))
                st.link(nc.vector.tensor_tensor_scan(row_t[:, 1, :], ones_row[:, :], ig[:, :], 0.0, ALU.mult, ALU.max))
                st.link(nc.vector.tensor_scalar(row_t[:, 0, :], row_t[:, 1, :], -1.0, None, ALU.mult))
                st.link(nc.vector.tensor_tensor(row_t[:, 2, :], row_t[:, 0, :], row_t[:, 3, :], ALU.subtract))
                dve.sem_inc(rows_ready, 1)
                for h in range(NH):
                    for f in range(2):
                        dve.wait_ge(bc_ready, 2 * h + f + 1)
                        nc.vector.tensor_copy(neg_G[:, h, f * 512:(f + 1) * 512], bc[:, f, :]).then_inc(bc_free, 1)
                for j in range(4):
                    dve.wait_ge(qk_loaded[j], 16)
                    if j >= 2:
                        dve.wait_ge(qk_done, j - 1)
                    w = lambda tap: V[:, VEC["qk_conv"] + 4 * tap + j:VEC["qk_conv"] + 4 * tap + j + 1]
                    st.link(nc.vector.tensor_scalar(conv[:, j % 2, 0, :], pre[:, j, 3:3 + SEQ], w(3),
                                                    V[:, VEC["qk_conv_b"] + j:VEC["qk_conv_b"] + j + 1], ALU.mult, ALU.add))
                    for n, tap in enumerate((2, 1, 0)):
                        st.link(nc.vector.scalar_tensor_tensor(out=conv[:, j % 2, (n + 1) % 2, :], in0=pre[:, j, tap:tap + SEQ],
                                                               scalar=w(tap), in1=conv[:, j % 2, n % 2, :],
                                                               op0=ALU.mult, op1=ALU.add))
                    dve.sem_inc(conv_done, 1)
                dve.wait_ge(gc_ready, 1)
                nc.vector.tensor_copy(g_cols[:, :, :].rearrange("p a b -> p (a b)"), gc[:, 0:DT * NH])

            @block.scalar
            def _(act):
                act.wait_ge(gates_loaded, 32)
                act.wait_ge(bias_ready, 1)
                nc.scalar.activation(row_t[:, 0, :], ig[:, :], ACT.Tanh, bias=cap_b[:, 0:1], scale=1.0 / CAP).then_inc(tanh_ready, 1)
                nc.scalar.activation(row_t[:, 1, :], fg[:, :], ACT.Tanh, bias=cap_b[:, 1:2], scale=1.0 / CAP).then_inc(tanh_ready, 1)
                act.wait_ge(tanh_ready, 2)
                nc.scalar.activation(row_t[:, 3, :], row_t[:, 1, :], ACT.Exp, scale=-CAP).then_inc(exp_ready, 1)
                act.wait_ge(exp_ready, 1)
                nc.scalar.activation(row_t[:, 2, :], row_t[:, 3, :], ACT.Ln, bias=one("one")[0:NH], scale=1.0).then_inc(ln_ready, 1)
                for s in range(DT):
                    act.wait_ge(tr_ready, s + 1)
                    nc.scalar.copy(v_tok[:, s, :], tr[:, s % 2, :]).then_inc(tr_free, 1)
                for h in range(NH):
                    for f in range(2):
                        act.wait_ge(bc_ready, 2 * NH + 2 * h + f + 1)
                        nc.scalar.activation(exp_m[:, h, f * 512:(f + 1) * 512], bc[:, 2 + f, :], ACT.Exp).then_inc(bc2_free, 1)
                for j in range(4):
                    act.wait_ge(conv_done, j + 1)
                    nc.scalar.activation(qk[:, j, :], conv[:, j % 2, 1, :], ACT.Silu).then_inc(qk_done, 1)

            @block.tensor
            def _(pe):
                ident = C[:, CONST["ident"]:CONST["ident"] + P]
                pe.wait_ge(v_loaded, 64)
                for s in range(DT):
                    if s >= 2:
                        pe.wait_ge(tr_free, s - 1)
                    for j in range(4):
                        mm = pe.transpose(tr[:, s % 2, j * P:(j + 1) * P], vT[:, j, s * P:(s + 1) * P], ident)
                    mm.then_inc(tr_ready, 1)
                pe.wait_ge(rows_ready, 1)
                for s in range(DT):
                    mm = pe.matmul(gc[:, s * NH:(s + 1) * NH], ig[:, s * P:(s + 1) * P], C[0:NH, CONST["ident"]:CONST["ident"] + NH],
                                   start=True, stop=True)
                mm.then_inc(gc_ready, 1)
                for r in range(2):
                    for h in range(NH):
                        for f in range(2):
                            if h >= 1:
                                pe.wait_ge(bc2_free if r else bc_free, 2 * (h - 1) + f + 1)
                            sel = C[0:NH, CONST["row_sel"] + h * P:CONST["row_sel"] + (h + 1) * P]
                            pe.matmul(bc[:, 2 * r + f, :], sel, row_t[:, 2 * r, f * 512:(f + 1) * 512],
                                      start=True, stop=True).then_inc(bc_ready, 1)

        with ExitStack() as ctx2:
            sb2 = lambda n, s, d=F32: ctx2.enter_context(nc.sbuf_tensor(f"ml_{n}", s, d))
            NR = 3
            arg = sb2("arg", [P, NR, HALF])
            wgt = sb2("wgt", [P, NR, HALF])
            prod = sb2("prod", [P, NR, HALF])
            den = sb2("den", [P, HALF])
            den2 = sb2("den2", [P, HALF])
            h_buf = sb2("h_buf", [P, 2, HALF])
            sq = sb2("sq", [P, HALF])
            o_raw = sb2("o_raw", [P, 2, HALF])
            o_sig = sb2("o_sig", [P, 2, HALF])
            y = sb2("y", [P, 2, HALF])
            rms = sb2("rms", [P, HALF])
            score = ctx2.enter_context(nc.psum_tensor("ml_score", [P, NR, 512], F32))
            num = ctx2.enter_context(nc.psum_tensor("ml_num", [P, 2, 512], F32))
            dsum = ctx2.enter_context(nc.psum_tensor("ml_dsum", [P, 2, 512], F32))
            ss = ctx2.enter_context(nc.psum_tensor("ml_ss", [P, 512], F32))
            arg_ready, exp_done, score_ready, prod_done = (sem(n) for n in ("arg_ready", "exp_done", "score_ready", "prod_done"))
            prod_used, group_ready, group_free, steps2 = (sem(n) for n in ("prod_used", "group_ready", "group_free", "steps2"))
            h_ready, sq_ready, ss_ready, rms_ready, sig_ready, y_ready = (sem(n) for n in ("h_ready", "sq_ready", "ss_ready", "rms_ready", "sig_ready", "y_ready"))
            o_loaded = [sem(f"o_loaded{i}") for i in range(2)]
            stored = [sem(f"stored{i}") for i in range(2)]
            groups = [(h, f) for h in range(NH) for f in range(2)]
            items = [(n, h, f, s) for n, (h, f) in enumerate(groups) for s in range(4 * f + 4)]
            last_item = {n: max(i for i, it in enumerate(items) if it[0] == n) for n in range(len(groups))}
            span = lambda f, s: (max(0, s * P - f * HALF), HALF)
            block = ctx2.enter_context(nc.Block(no_gpsimd_drain=True))

            @block.vector
            def _(dve):
                st = Steps(dve, steps2)

                def weights(i):
                    n, h, f, s = items[i]
                    a, b = span(f, s)
                    if i >= NR:
                        dve.wait_ge(exp_done, i - NR + 1)
                    nc.vector.tensor_scalar(arg[:, i % NR, a:b], neg_G[:, h, f * HALF + a:f * HALF + b], g_cols[:, s, h:h + 1],
                                            0.0, ALU.add, ALU.min).then_inc(arg_ready, 1)

                def finish(n):
                    h, f = groups[n]
                    dve.wait_ge(group_ready, n + 1)
                    st.link(nc.vector.scalar_tensor_tensor(out=den[:, :], in0=dsum[:, n % 2, :], scalar=-1.0, in1=exp_m[:, h, f * HALF:(f + 1) * HALF],
                                                           op0=ALU.mult, op1=ALU.max))
                    st.link(nc.vector.tensor_tensor(den2[:, :], dsum[:, n % 2, :], den[:, :], ALU.max))
                    st.link(nc.vector.reciprocal(den[:, :], den2[:, :]))
                    st.link(nc.vector.tensor_tensor(h_buf[:, n % 2, :], num[:, n % 2, :], den[:, :], ALU.mult))
                    dve.sem_inc(h_ready, 1)
                    dve.wait_ge(rms_ready, n + 1)
                    st.link(nc.vector.reciprocal(den[:, :], rms[:, :]))
                    dve.wait_ge(sig_ready, n + 1)
                    st.link(nc.vector.scalar_tensor_tensor(out=h_buf[:, n % 2, :], in0=h_buf[:, n % 2, :], scalar=V[:, VEC["mh_g"] + h:VEC["mh_g"] + h + 1],
                                                           in1=den[:, :], op0=ALU.mult, op1=ALU.mult))
                    if n >= 2:
                        dve.wait_ge(stored[n % 2], 16 * (n // 2))
                    nc.vector.tensor_tensor(y[:, n % 2, :], h_buf[:, n % 2, :], o_sig[:, n % 2, :], ALU.mult).then_inc(y_ready, 1)

                weights(0)
                weights(1)
                for i, (n, h, f, s) in enumerate(items):
                    if i + 2 < len(items):
                        weights(i + 2)
                    a, b = span(f, s)
                    dve.wait_ge(exp_done, i + 1)
                    dve.wait_ge(score_ready, i + 1)
                    if i >= NR:
                        dve.wait_ge(prod_used, i - NR + 1)
                    st.link(nc.vector.scalar_tensor_tensor(out=prod[:, i % NR, a:b], in0=score[:, i % NR, a:b], scalar=DK ** -0.5,
                                                           in1=wgt[:, i % NR, a:b], op0=ALU.mult, op1=ALU.mult))
                    if s >= 4 * f:
                        st.link(nc.vector.tensor_tensor(prod[:, i % NR, a:a + P], prod[:, i % NR, a:a + P],
                                                        C[:, CONST["upto"]:CONST["upto"] + P], ALU.mult))
                    dve.sem_inc(prod_done, 1)
                    if i == last_item[n]:
                        finish(n)

            @block.scalar
            def _(act):
                def weight_exp(i):
                    n, h, f, s = items[i]
                    a, b = span(f, s)
                    act.wait_ge(arg_ready, i + 1)
                    if i >= NR:
                        act.wait_ge(prod_done, i - NR + 1)
                    nc.scalar.activation(wgt[:, i % NR, a:b], arg[:, i % NR, a:b], ACT.Exp).then_inc(exp_done, 1)

                for i, (n, h, f, s) in enumerate(items):
                    weight_exp(i)
                    if i == last_item[n]:
                        act.wait_ge(o_loaded[n % 2], 16 * (n // 2 + 1))
                        if n >= 2:
                            act.wait_ge(y_ready, n - 1)
                        nc.scalar.activation(o_sig[:, n % 2, :], o_raw[:, n % 2, :], ACT.Sigmoid).then_inc(sig_ready, 1)
                        act.wait_ge(h_ready, n + 1)
                        nc.scalar.activation(sq[:, :], h_buf[:, n % 2, :], ACT.Square).then_inc(sq_ready, 1)
                        act.wait_ge(ss_ready, n + 1)
                        nc.scalar.activation(rms[:, :], ss[:, :], ACT.Sqrt, bias=one("eps6"), scale=1.0 / P).then_inc(rms_ready, 1)

            @block.tensor
            def _(pe):
                def scores(i):
                    n, h, f, s = items[i]
                    a, b = span(f, s)
                    base = 64 * (h % 2)
                    if i >= NR:
                        pe.wait_ge(prod_done, i - NR + 1)
                    pe.matmul(score[:, i % NR, a:b], qk[base:base + DK, 2 + h // 2, s * P:(s + 1) * P],
                              qk[base:base + DK, h // 2, f * HALF + a:f * HALF + b], start=True, stop=True).then_inc(score_ready, 1)

                scores(0)
                scores(1)
                for i, (n, h, f, s) in enumerate(items):
                    if i + 2 < len(items):
                        scores(i + 2)
                    a, b = span(f, s)
                    pe.wait_ge(prod_done, i + 1)
                    if s == 0 and n >= 2:
                        pe.wait_ge(h_ready, n - 1)
                    end = i == last_item[n]
                    pe.matmul(num[:, n % 2, a:b], v_tok[:, s, h * P:(h + 1) * P], prod[:, i % NR, a:b], start=s == 0, stop=end,
                              skip_group_check=True)
                    pe.matmul(dsum[:, n % 2, a:b], C[:, CONST["ones"]:CONST["ones"] + P], prod[:, i % NR, a:b], start=s == 0,
                              stop=end, skip_group_check=True).then_inc(prod_used, 1)
                    if end:
                        pe.wait_ge(prod_used, i + 1)
                        pe.sem_inc(group_ready, 1)
                        pe.wait_ge(sq_ready, n + 1)
                        pe.matmul(ss[:, :], C[:, CONST["ones"]:CONST["ones"] + P], sq[:, :], start=True, stop=True).then_inc(ss_ready, 1)

            @block.sync
            def _(sp):
                for n, (h, f) in enumerate(groups):
                    if n >= 2:
                        sp.wait_ge(sig_ready, n - 1)
                    sp.dma_start(o_raw[:, n % 2, :], proj[o0 + h][:, f * HALF:(f + 1) * HALF]).then_inc(o_loaded[n % 2], 16)

            @block.gpsimd
            def _(pool):
                for n, (h, f) in enumerate(groups):
                    pool.wait_ge(y_ready, n + 1)
                    pool.dma_start(y_out[h][:, f * HALF:(f + 1) * HALF], y[:, n % 2, :]).then_inc(stored[n % 2], 16)
                for u in range(2):
                    pool.wait_ge(stored[u], 16 * len(groups) // 2)
HR, NR_ = 8, 64
CH = P
NCH = SEQ // CH


def rwkv_prepare_stage(nc, proj, lora, w_up_g, scr, V, C):
    RATE = float(np.exp(-0.5))
    r0, k0, v0, wa0, g0 = 0, 4, 8, 12, 13
    col = lambda name, j=0: V[:, VEC[name] + j:VEC[name] + j + 1]
    with ExitStack() as ctx:
        sb = lambda n, s, d=F32: ctx.enter_context(nc.sbuf_tensor(f"rp_{n}", s, d))
        sem = stage_semaphores(nc, ctx, "rp")
        pre = sb("pre", [P, 2, SEQ + 1])
        kept = sb("kept", [P, 2, SEQ])
        one_mu = sb("one_mu", [P, 14])
        one_ka = sb("one_ka", [P, 4])
        wa = sb("wa", [P, SEQ])
        wt = sb("wt", [64, SEQ])
        gl = sb("gl", [P, SEQ])
        lora_w = sb("lora_w", [P, 512])
        upg_w = sb("upg_w", [P, 512])
        rr, kx, vx = sb("rr", [P, SEQ]), sb("kx", [P, SEQ]), sb("vx", [P, SEQ])
        sg, a_, g_sb = sb("sg", [P, SEQ]), sb("a", [P, SEQ]), sb("g", [P, SEQ])
        kk, sq, nrm = sb("kk", [P, SEQ]), sb("sq", [P, SEQ]), sb("nrm", [P, SEQ])
        cum, dif = sb("cum", [P, SEQ]), sb("dif", [P, SEQ])
        e_pos, e_neg, e_prev = sb("e_pos", [P, SEQ]), sb("e_neg", [P, SEQ]), sb("e_prev", [P, SEQ])
        k2, rk = sb("k2", [P, SEQ]), sb("rk", [P, SEQ])
        reset = sb("reset", [P, SEQ])
        ar, bt, kt, bon = sb("ar", [P, NCH, 2, CH]), sb("bt", [P, SEQ]), sb("kt", [P, SEQ]), sb("bon", [P, SEQ])
        s_arg, s_exp = sb("s_arg", [P, NCH]), sb("s_exp", [P, NCH])
        up = ctx.enter_context(nc.psum_tensor("rp_up", [P, 6, 512], F32))
        hs = ctx.enter_context(nc.psum_tensor("rp_hs", [P, 2, 512], F32))
        loaded = [sem(f"loaded{i}") for i in range(2)]
        w_loaded, pads, kept_done, mixed = sem("w_loaded"), sem("pads"), sem("kept_done"), sem("mixed")
        lo_ready, up_ready, act_done, st_sem, kk_sq, hs_ready, nrm_done = (
            sem(n) for n in ("lo_ready", "up_ready", "act_done", "steps", "kk_sq", "hs_ready", "nrm_done"))
        dif_ready, exp_done, rk_ready, out_ready, stored, mu_ready, g_ready = (
            sem(n) for n in ("dif_ready", "exp_done", "rk_ready", "out_ready", "stored", "mu_ready", "g_ready"))
        order = [wa0, g0]
        for m in range(4):
            order += [r0 + m, k0 + m, v0 + m]
        NST = 7
        block = ctx.enter_context(nc.Block(no_gpsimd_drain=True))

        @block.sync
        def _(sp):
            sp.dma_start(lora_w[:, :], lora).then_inc(w_loaded, 16)
            sp.dma_start(upg_w[:, :], w_up_g).then_inc(w_loaded, 16)
            for n, t in enumerate(order):
                if n >= 2:
                    sp.wait_ge(mixed, n - 1)
                sp.dma_start(pre[:, n % 2, 1:], proj[t]).then_inc(loaded[n % 2], 16)

        @block.scalar
        def _(act):
            def keep(n):
                t = order[n]
                act.wait_ge(loaded[n % 2], 16 * (n // 2 + 1))
                if n >= 2:
                    act.wait_ge(mixed, n - 1)
                nc.scalar.activation(kept[:, n % 2, :], pre[:, n % 2, 1:], ACT.Copy, scale=one_mu[:, t:t + 1]).then_inc(kept_done, 1)

            act.wait_ge(mu_ready, 1)
            keep(0)
            keep(1)
            act.wait_ge(mixed, 2)
            nc.scalar.activation(wt[:, :], wa[0:64, :], ACT.Tanh).then_inc(lo_ready, 1)
            nc.scalar.activation(gl[:, :], gl[:, :], ACT.Sigmoid).then_inc(lo_ready, 1)
            for m in range(4):
                for j in range(3):
                    keep(2 + 3 * m + j)
                for h in range(2):
                    hc = slice(h * HALF, (h + 1) * HALF)
                    act.wait_ge(up_ready, 6 * m + 3 * h + 3)
                    if m and h == 0:
                        act.wait_ge(nrm_done, m)
                        act.wait_ge(stored, 16 * NST * m)
                    nc.scalar.activation(sg[:, hc], up[:, 3 * h, :], ACT.Sigmoid, bias=col("w0", m)).then_inc(act_done, 1)
                    nc.scalar.activation(a_[:, hc], up[:, 3 * h + 1, :], ACT.Sigmoid, bias=col("a0", m)).then_inc(act_done, 1)
                    nc.scalar.copy(g_sb[:, hc], up[:, 3 * h + 2, :]).then_inc(act_done, 1)
                act.wait_ge(kk_sq, 2 * m + 1)
                nc.scalar.activation(sq[:, :], kk[:, :], ACT.Square).then_inc(kk_sq, 1)
                act.wait_ge(hs_ready, 2 * m + 1)
                nc.scalar.activation(nrm[:, :], hs[:, :, :].rearrange("p a b -> p (a b)"), ACT.Sqrt).then_inc(nrm_done, 1)
                act.wait_ge(dif_ready, m + 1)
                nc.scalar.activation(e_pos[:, :], dif[:, :], ACT.Exp).then_inc(exp_done, 1)
                nc.scalar.activation(e_neg[:, :], dif[:, :], ACT.Exp, scale=-1.0).then_inc(exp_done, 1)
                nc.scalar.activation(e_prev[:, :], cum[:, :], ACT.Exp).then_inc(exp_done, 1)
                nc.scalar.activation(s_exp[:, :], s_arg[:, :], ACT.Exp).then_inc(exp_done, 1)

        @block.tensor
        def _(pe):
            pe.wait_ge(w_loaded, 32)
            pe.wait_ge(lo_ready, 2)
            for m in range(4):
                ms = slice(m * P, (m + 1) * P)
                for h in range(2):
                    hc = slice(h * HALF, (h + 1) * HALF)
                    if m:
                        pe.wait_ge(act_done, 6 * (m - 1) + 3 * h + 3)
                    pe.matmul(up[:, 3 * h, :], lora_w[0:64, ms], wt[:, hc], start=True, stop=True).then_inc(up_ready, 1)
                    pe.matmul(up[:, 3 * h + 1, :], lora_w[64:128, ms], wa[64:128, hc], start=True, stop=True).then_inc(up_ready, 1)
                    pe.matmul(up[:, 3 * h + 2, :], upg_w[:, ms], gl[:, hc], start=True, stop=True).then_inc(up_ready, 1)
                pe.wait_ge(kk_sq, 2 * m + 2)
                if m:
                    pe.wait_ge(out_ready, m)
                ones = C[:, CONST["head_ones"]:CONST["head_ones"] + P]
                for h in range(2):
                    mm = pe.matmul(hs[:, h, :], ones, sq[:, h * HALF:(h + 1) * HALF], start=True, stop=True)
                mm.then_inc(hs_ready, 1)
                pe.wait_ge(rk_ready, m + 1)
                pe.wait_ge(nrm_done, m + 1)
                for h in range(2):
                    mm = pe.matmul(hs[:, h, :], ones, rk[:, h * HALF:(h + 1) * HALF], start=True, stop=True)
                mm.then_inc(hs_ready, 1)

        @block.vector
        def _(dve):
            st = Steps(dve, st_sem)
            tt, ts, stt = nc.vector.tensor_tensor, nc.vector.tensor_scalar, nc.vector.scalar_tensor_tensor
            st(nc.vector.memset(pre[:, :, 0:1], 0.0))
            st(nc.vector.memset(reset[:, :], 1.0))
            st.settle()
            st(nc.vector.memset(reset[:, :].rearrange("p (c t) -> p c t", c=NCH)[:, :, 0:1], 0.0))
            st(ts(one_ka[:, :], V[:, VEC["k_a"]:VEC["k_a"] + 4], -1.0, 1.0, ALU.mult, ALU.add))
            ts(one_mu[:, :], V[:, VEC["mu"]:VEC["mu"] + 14], -1.0, 1.0, ALU.mult, ALU.add).then_inc(mu_ready, 1)
            st.settle()

            def mix(n, dst):
                dve.wait_ge(kept_done, n + 1)
                stt(out=dst, in0=pre[:, n % 2, 0:SEQ], scalar=col("mu", order[n]), in1=kept[:, n % 2, :],
                    op0=ALU.mult, op1=ALU.add).then_inc(mixed, 1)

            mix(0, wa[:, :])
            mix(1, gl[:, :])
            for m in range(4):
                if m:
                    dve.wait_ge(stored, 16 * NST * m)
                mix(2 + 3 * m, rr[:, :])
                mix(3 + 3 * m, kx[:, :])
                mix(4 + 3 * m, vx[:, :])
                dve.wait_ge(mixed, 5 + 3 * m)
                ts(kk[:, :], kx[:, :], col("k_k", m), None, ALU.mult).then_inc(kk_sq, 1)
                dve.wait_ge(act_done, 6 * m + 6)
                st.link(ts(sg[:, :], sg[:, :], -RATE, None, ALU.mult))
                st.link(nc.vector.tensor_tensor_scan(cum[:, :], reset[:, :], sg[:, :], 0.0, ALU.mult, ALU.add))
                cum3 = cum[:, :].rearrange("p (c t) -> p c t", c=NCH)
                mid = cum3[:, :, 63:64]
                st(tt(dif[:, :].rearrange("p (c t) -> p c t", c=NCH), cum3, mid.to_broadcast([P, NCH, CH]), ALU.subtract))
                st(tt(s_arg[:, :].unsqueeze(2), cum3[:, :, CH - 1:CH], mid, ALU.subtract))
                st.settle()
                st.link(tt(s_arg[:, 0:NCH - 1], s_arg[:, 0:NCH - 1], cum3[:, 1:NCH, 63:64].rearrange("p c o -> p (c o)"), ALU.add))
                tt(cum[:, :], dif[:, :], sg[:, :], ALU.subtract).then_inc(dif_ready, 1)
                st.link(ts(k2[:, :], a_[:, :], col("k_a", m), one_ka[:, m:m + 1], ALU.mult, ALU.add))
                st.link(tt(k2[:, :], k2[:, :], kx[:, :], ALU.mult))
                stt(out=rk[:, :], in0=rr[:, :], scalar=col("r_k", m), in1=k2[:, :], op0=ALU.mult, op1=ALU.mult).then_inc(rk_ready, 1)
                dve.wait_ge(nrm_done, m + 1)
                st.link(ts(nrm[:, :], nrm[:, :], 1e-12, None, ALU.max))
                st.link(nc.vector.reciprocal(sq[:, :], nrm[:, :]))
                st.link(tt(kk[:, :], kk[:, :], sq[:, :], ALU.mult))
                dve.wait_ge(exp_done, 4 * m + 4)
                c3 = lambda t: t[:, :].rearrange("p (c t) -> p c t", c=NCH)
                st(stt(out=ar[:, :, 0, :], in0=c3(kk), scalar=-1.0, in1=c3(e_prev), op0=ALU.mult, op1=ALU.mult))
                st(tt(ar[:, :, 1, :], c3(rr), c3(e_pos), ALU.mult))
                st(tt(kk[:, :], kk[:, :], a_[:, :], ALU.mult))
                st(tt(kt[:, :], k2[:, :], e_neg[:, :], ALU.mult))
                st.settle()
                st(tt(bt[:, :], kk[:, :], e_neg[:, :], ALU.mult))
                dve.wait_ge(hs_ready, 2 * m + 2)
                st(tt(bon[:, :], hs[:, :, :].rearrange("p a b -> p (a b)"), vx[:, :], ALU.mult))
                st.settle()
                dve.sem_inc(out_ready, 1)

        @block.gpsimd
        def _(pool):
            for m in range(4):
                pool.wait_ge(out_ready, m + 1)
                for dst, s_ in ((scr["ar"][m], ar[:, :, :, :].rearrange("p a b c -> p (a b c)")), (scr["bt"][m], bt[:, :]), (scr["kt"][m], kt[:, :]),
                                (scr["v"][m], vx[:, :]), (scr["bonus"][m], bon[:, :]), (scr["g"][m], g_sb[:, :]), (scr["scale"][m], s_exp[:, :])):
                    pool.dma_start(dst, s_).then_inc(stored, 16)
            pool.wait_ge(stored, 16 * NST * 4)


def rwkv_scan_stage(nc, scr, masks, C):
    with ExitStack() as ctx:
        sb = lambda n, s, d=F32: ctx.enter_context(nc.sbuf_tensor(f"rs_{n}", s, d))
        sem = stage_semaphores(nc, ctx, "rs")
        lv = sb("lv", [P, 2 * LEVELS * P])
        ar = sb("ar", [P, 2, 4, 2 * CH])
        bt, kt, vt = sb("bt", [P, 2, 4, CH]), sb("kt", [P, 2, 4, CH]), sb("vt", [P, 2, 4, CH])
        scale = sb("scale", [P, 4, NCH])
        tok = sb("tok", [P, 3, 512])
        mb = sb("mb", [P, 2, 4, 2 * CH])
        mk = sb("mk", [P, 2, 4, 2 * CH])
        lab = sb("lab", [P, 2, 4, CH])
        X, XT = sb("X", [P, 2, 4, CH]), sb("XT", [P, 2, 4, CH])
        T_ = sb("T", [P, 2, 4, CH])
        zs, us = sb("zs", [P, 512]), sb("us", [P, 512])
        S, S_new = sb("S", [P, 4, P]), sb("S_new", [P, 4, P])
        ybuf = sb("ybuf", [P, 2, 512])
        ps = ctx.enter_context(nc.psum_tensor("rs_ps", [P, 8, 512], F32))
        loaded = [sem(f"loaded{i}") for i in range(2)]
        stored = [sem(f"stored{i}") for i in range(2)]
        c_loaded, s_init, wait_held = sem("c_loaded"), sem("s_init"), sem("wait_held")
        tr_ready, tr_copied, mat_ready, mat_masked, x_init = (sem(n) for n in ("tr_ready", "tr_copied", "mat_ready", "mat_masked", "x_init"))
        t_ready, t_copied, xx_ready, x_done, z_ready, z_copied = (sem(n) for n in ("t_ready", "t_copied", "xx_ready", "x_done", "z_ready", "z_copied"))
        u_ready, u_copied, y_ready, y_copied, ds_ready, ds_done, ds_done_a, steps = (sem(n) for n in ("u_ready", "u_copied", "y_ready", "y_copied", "ds_ready", "ds_done", "ds_done_a", "steps"))
        NL = LEVELS - 1
        lvm = lambda l, t: lv[:, (t * LEVELS + l) * P:(t * LEVELS + l + 1) * P].bitcast(U32).unsqueeze(1).to_broadcast([P, 4, P])
        bank = lambda b: ps[:, b, :].rearrange("p (h t) -> p h t", h=4)
        block = ctx.enter_context(nc.Block(no_gpsimd_drain=True))

        @block.sync
        def _(sp):
            sp.dma_start(lv[:, :], masks).then_inc(c_loaded, 16)
            sp.dma_start(scale[:, :, :], scr["scale"].rearrange("m p c -> p m c")).then_inc(c_loaded, 16)

            def load(c, u):
                arv = scr["ar"].rearrange("m p (c x) -> p m c x", c=NCH)
                sp.dma_start(ar[:, u, :, :], arv[:, :, c, :]).then_inc(loaded[u], 16)
                for dst, s_ in ((bt, "bt"), (kt, "kt"), (vt, "v")):
                    v_ = scr[s_].rearrange("m p (c x) -> p m c x", c=NCH)
                    sp.dma_start(dst[:, u, :, :], v_[:, :, c, :]).then_inc(loaded[u], 16)

            load(0, 0)
            load(1, 1)
            with sp.Fori(1, NCH // 2) as i:
                for u in range(2):
                    sp.wait_ge(ds_ready, 2 * i + (u - 1))
                    sp.wait_ge(y_ready, 2 * i + (u - 1))
                    load(2 * i + u, u)

        @block.tensor
        def _(pe):
            ident = C[:, CONST["ident"]:CONST["ident"] + P]

            def body(i, first, last):
                for u in range(2):
                    c = 2 * i + u
                    fresh = first and u == 0
                    pe.wait_ge(loaded[u], 64 * i + 64)
                    if not fresh:
                        pe.wait_ge(y_copied, c)
                        pe.wait_ge(ds_done, c)
                    for n, src in enumerate((bt, kt, vt)):
                        for m in range(4):
                            mm = pe.transpose(ps[:, 5 + n, m * P:(m + 1) * P], src[:, u, m, :], ident)
                        mm.then_inc(tr_ready, 1)
                    for g in range(2):
                        base = 64 * g
                        if not (fresh and g == 0):
                            pe.wait_ge(mat_masked, 12 * i + (6 * u + 3 * g))
                            if g == 0:
                                pe.wait_ge(x_done, 2 * (2 * NL) * i + 2 * NL * u)
                                pe.wait_ge(z_copied, c)
                        for m in range(4):
                            at_rt = ar[base:base + 64, u, m, :]
                            pe.matmul(ps[:, m // 2, (m % 2) * 256:(m % 2 + 1) * 256], bt[base:base + 64, u, m, :], at_rt,
                                      start=True, stop=True)
                            pe.matmul(ps[:, 2 + m // 2, (m % 2) * 256:(m % 2 + 1) * 256], kt[base:base + 64, u, m, :], at_rt,
                                      start=True, stop=True)
                            mm = pe.matmul(ps[:, 4, m * P:(m + 1) * P], ar[base:base + 64, u, m, 0:CH],
                                           bt[base:base + 64, u, m, :], start=True, stop=True)
                        mm.then_inc(mat_ready, 1)
                    for l in range(NL):
                        for g in range(2):
                            if l == 0:
                                pe.wait_ge(x_init, 4 * i + 2 * u + g + 1)
                                pe.wait_ge(tr_copied, 3 * (2 * i) + 3 * u + 3)
                            else:
                                pe.wait_ge(x_done, 4 * NL * i + 2 * NL * u + 2 * (l - 1) + g + 1)
                            for m in range(4):
                                mm = pe.matmul(ps[:, 5 + g, m * P:(m + 1) * P], mb[:, g, m, 0:CH], X[:, g, m, :], start=True, stop=True)
                            mm.then_inc(t_ready, 1)
                        for g in range(2):
                            pe.wait_ge(t_copied, 4 * NL * i + 2 * NL * u + 2 * l + g + 1)
                            if l == 0 and g == 0:
                                pe.wait_ge(mat_masked, 12 * i + 6 * u + 6)
                            for m in range(4):
                                if l < NL - 1:
                                    pe.matmul(ps[:, 2 * g, m * P:(m + 1) * P], XT[:, g, m, :], T_[:, g, m, :], start=True, stop=True)
                                mm = pe.matmul(ps[:, 2 * g + 1, m * P:(m + 1) * P], T_[:, g, m, :], XT[:, g, m, :], start=True, stop=True)
                            mm.then_inc(xx_ready, 1)
                    if fresh:
                        pe.wait_ge(s_init, 1)
                    pe.wait_ge(tr_copied, 6 * i + 3 * u + 3)
                    for m in range(4):
                        pe.matmul(ps[:, 4, m * P:(m + 1) * P], ar[:, u, m, 0:CH], S[:, m, :], start=True, stop=False, skip_group_check=True)
                        for g in range(2):
                            h = 2 * m + g
                            mm = pe.matmul(ps[:, 4, h * 64:(h + 1) * 64], mk[:, g, m, 0:CH], tok[:, 2, h * 64:(h + 1) * 64],
                                           start=False, stop=True, skip_group_check=True)
                    mm.then_inc(z_ready, 1)
                    pe.wait_ge(z_copied, c + 1)
                    pe.wait_ge(x_done, 4 * NL * i + 2 * NL * (u + 1))
                    for h in range(HR):
                        mm = pe.matmul(ps[:, 7, h * 64:(h + 1) * 64], XT[:, h % 2, h // 2, :], zs[:, h * 64:(h + 1) * 64], start=True, stop=True)
                    mm.then_inc(u_ready, 1)
                    pe.wait_ge(u_copied, c + 1)
                    for m in range(4):
                        pe.matmul(ps[:, 5, m * P:(m + 1) * P], S[:, m, :], ar[:, u, m, CH:], start=True, stop=False, skip_group_check=True)
                        for g in range(2):
                            h = 2 * m + g
                            o = ps[64 * g:64 * g + 64, 5, m * P:(m + 1) * P]
                            pe.matmul(o, us[:, h * 64:(h + 1) * 64], mb[:, g, m, CH:], start=False, stop=False, skip_group_check=True)
                            mm = pe.matmul(o, tok[:, 2, h * 64:(h + 1) * 64], mk[:, g, m, CH:], start=False, stop=True, skip_group_check=True)
                    mm.then_inc(y_ready, 1)
                    for m in range(4):
                        ms = slice(m * P, (m + 1) * P)
                        pe.matmul(ps[:, 6, ms], tok[:, 0, ms], us[:, ms], start=True, stop=False, skip_group_check=True)
                        mm = pe.matmul(ps[:, 6, ms], tok[:, 1, ms], tok[:, 2, ms], start=False, stop=True, skip_group_check=True)
                    mm.then_inc(ds_ready, 1)

            run_loop(pe, NCH // 2, body)

        @block.scalar
        def _(act):
            def body(i, first, last):
                for u in range(2):
                    c = 2 * i + u
                    fresh = first and u == 0
                    for n in range(3):
                        act.wait_ge(tr_ready, 6 * i + 3 * u + n + 1)
                        if n == 0 and not fresh:
                            act.wait_ge(ds_ready, c)
                        nc.scalar.copy(tok[:, n, :], ps[:, 5 + n, :]).then_inc(tr_copied, 1)
                    for l in range(NL):
                        for g in range(2):
                            act.wait_ge(t_ready, 4 * NL * i + 2 * NL * u + 2 * l + g + 1)
                            nc.scalar.copy(T_[:, g, :, :].rearrange("p h t -> p (h t)"), ps[:, 5 + g, :]).then_inc(t_copied, 1)
                    act.wait_ge(z_ready, c + 1)
                    nc.scalar.copy(zs[:, :], ps[:, 4, :]).then_inc(z_copied, 1)
                    act.wait_ge(u_ready, c + 1)
                    nc.scalar.copy(us[:, :], ps[:, 7, :]).then_inc(u_copied, 1)
                    act.wait_ge(y_ready, c + 1)
                    if not first:
                        act.wait_ge(stored[u], 64 * i)
                    nc.scalar.copy(ybuf[:, u, :], ps[:, 5, :]).then_inc(y_copied, 1)

            run_loop(act, NCH // 2, body)

        @block.vector
        def _(dve):
            tt = nc.vector.tensor_tensor
            before = C[:, CONST["before"]:CONST["before"] + 2 * P].unsqueeze(1).to_broadcast([P, 4, 2 * P])
            after = C[:, CONST["after"]:CONST["after"] + P].unsqueeze(1).to_broadcast([P, 4, P])
            ident = C[:, CONST["ident"]:CONST["ident"] + P].unsqueeze(1).to_broadcast([P, 4, P])
            nc.vector.memset(S[:, :, :], 0.0).then_inc(s_init, 1)
            nc.vector.memset(S_new[:, :, :], 0.0).then_inc(s_init, 1)
            dve.wait_ge(s_init, 2)
            dve.wait_ge(c_loaded, 32)

            def body(i, first, last):
                for u in range(2):
                    c = 2 * i + u
                    for g in range(2):
                        n = 12 * i + 6 * u + 3 * g
                        dve.wait_ge(mat_ready, 4 * i + 2 * u + g + 1)
                        if g == 0 and not (first and u == 0):
                            dve.wait_ge(ds_ready, c)
                        m4 = lambda b: ps[:, b:b + 2, :].rearrange("p b (m x) -> p (b m) x", m=2)
                        tt(mb[:, g, :, :], m4(0), before, ALU.mult).then_inc(mat_masked, 1)
                        tt(mk[:, g, :, :], m4(2), before, ALU.mult).then_inc(mat_masked, 1)
                        tt(lab[:, g, :, :], bank(4), after, ALU.mult).then_inc(mat_masked, 1)
                        s0 = 16 * i + 8 * u + 4 * g
                        nc.vector.tensor_copy(X[:, g, :, :], ident).then_inc(steps, 1)
                        nc.vector.tensor_copy(XT[:, g, :, :], ident).then_inc(steps, 1)
                        dve.wait_ge(mat_masked, n + 3)
                        dve.wait_ge(steps, s0 + 2)
                        dve.sem_inc(wait_held, 1)
                        nc.vector.copy_predicated(X[:, g, :, :], lvm(0, 0), lab[:, g, :, :]).then_inc(steps, 1)
                        nc.vector.copy_predicated(XT[:, g, :, :], lvm(0, 1), mb[:, g, :, 0:CH]).then_inc(steps, 1)
                        dve.wait_ge(steps, s0 + 4)
                        dve.sem_inc(x_init, 1)
                    for l in range(NL):
                        for g in range(2):
                            dve.wait_ge(xx_ready, 4 * NL * i + 2 * NL * u + 2 * l + g + 1)
                            dve.sem_inc(wait_held, 1)
                            if l < NL - 1:
                                nc.vector.copy_predicated(X[:, g, :, :], lvm(l + 1, 0), bank(2 * g))
                            nc.vector.copy_predicated(XT[:, g, :, :], lvm(l + 1, 1), bank(2 * g + 1)).then_inc(x_done, 1)
                    dve.wait_ge(ds_ready, c + 1)
                    for g in range(2):
                        b = slice(64 * g, 64 * g + 64)
                        tt(S_new[b, :, b], S[b, :, b], ps[b, 6, :].rearrange("p (m x) -> p m x", m=4)[:, :, b], ALU.add).then_inc(ds_done_a, 1)
                    dve.wait_ge(ds_done_a, 4 * i + 2 * u + 2)
                    for g in range(2):
                        b = slice(64 * g, 64 * g + 64)
                        ins = tt(S[b, :, b], S_new[b, :, b], scale[b, :, bass.ds(c, 1)].to_broadcast([64, 4, 64]), ALU.mult)
                        if g == 1:
                            ins.then_inc(ds_done, 1)

            run_loop(dve, NCH // 2, body)

        @block.gpsimd
        def _(pool):
            def body(i, first, last):
                for u in range(2):
                    c = 2 * i + u
                    pool.wait_ge(y_copied, c + 1)
                    for m in range(4):
                        pool.dma_start(scr["y"][m][:, bass.ts(c, CH)], ybuf[:, u, m * P:(m + 1) * P]).then_inc(stored[u], 16)

            run_loop(pool, NCH // 2, body)
            for u in range(2):
                pool.wait_ge(stored[u], 64 * NCH // 2)


def rwkv_finish_stage(nc, scr, y_out, V, C):
    col = lambda name, j=0: V[:, VEC[name] + j:VEC[name] + j + 1]
    with ExitStack() as ctx:
        sb = lambda n, s, d=F32: ctx.enter_context(nc.sbuf_tensor(f"rf_{n}", s, d))
        sem = stage_semaphores(nc, ctx, "rf")
        y, bon, g_ = sb("y", [P, 2, SEQ]), sb("bon", [P, 2, SEQ]), sb("g", [P, 2, SEQ])
        yc, sq, rms, out = sb("yc", [P, 2, SEQ]), sb("sq", [P, 2, SEQ]), sb("rms", [P, 2, SEQ]), sb("out", [P, 2, SEQ])
        mean = ctx.enter_context(nc.psum_tensor("rf_mean", [P, 2, 2, 512], F32))
        var = ctx.enter_context(nc.psum_tensor("rf_var", [P, 2, 2, 512], F32))
        loaded = [sem(f"loaded{i}") for i in range(2)]
        stored = [sem(f"stored{i}") for i in range(2)]
        mean_ready, yc_ready, sq_ready, var_ready, rms_ready, out_ready, steps = (
            sem(n) for n in ("mean_ready", "yc_ready", "sq_ready", "var_ready", "rms_ready", "out_ready", "steps"))
        flat = lambda t: t.rearrange("p a b -> p (a b)")
        block = ctx.enter_context(nc.Block(no_gpsimd_drain=True))

        @block.sync
        def _(sp):
            for m in range(4):
                if m >= 2:
                    sp.wait_ge(out_ready, m - 1)
                for dst, src in ((y, "y"), (bon, "bonus"), (g_, "g")):
                    sp.dma_start(dst[:, m % 2, :], scr[src][m]).then_inc(loaded[m % 2], 16)

        @block.tensor
        def _(pe):
            ones = C[:, CONST["head_ones"]:CONST["head_ones"] + P]

            def head_sum(dst, src):
                for h in range(2):
                    mm = pe.matmul(dst[:, h, :], ones, src[:, h * HALF:(h + 1) * HALF], start=True, stop=True)
                return mm

            for m in range(4):
                pe.wait_ge(loaded[m % 2], 48 * (m // 2 + 1))
                if m >= 2:
                    pe.wait_ge(yc_ready, m - 1)
                head_sum(mean[:, m % 2, :, :], y[:, m % 2, :]).then_inc(mean_ready, 1)
                if m:
                    pe.wait_ge(sq_ready, m)
                    if m >= 3:
                        pe.wait_ge(rms_ready, m - 2)
                    head_sum(var[:, (m - 1) % 2, :, :], sq[:, (m - 1) % 2, :]).then_inc(var_ready, 1)
            pe.wait_ge(sq_ready, 4)
            pe.wait_ge(rms_ready, 2)
            head_sum(var[:, 1, :, :], sq[:, 1, :]).then_inc(var_ready, 1)

        @block.scalar
        def _(act):
            for m in range(4):
                act.wait_ge(yc_ready, m + 1)
                if m >= 2:
                    act.wait_ge(var_ready, m - 1)
                nc.scalar.activation(sq[:, m % 2, :], yc[:, m % 2, :], ACT.Square).then_inc(sq_ready, 1)
                if m:
                    act.wait_ge(var_ready, m)
                    if m >= 3:
                        act.wait_ge(out_ready, m - 2)
                    nc.scalar.activation(rms[:, (m - 1) % 2, :], flat(var[:, (m - 1) % 2, :, :]), ACT.Sqrt,
                                         bias=C[:, CONST["eps_ln"]:CONST["eps_ln"] + 1], scale=1.0 / NR_).then_inc(rms_ready, 1)
            act.wait_ge(var_ready, 4)
            act.wait_ge(out_ready, 2)
            nc.scalar.activation(rms[:, 1, :], flat(var[:, 1, :, :]), ACT.Sqrt,
                                 bias=C[:, CONST["eps_ln"]:CONST["eps_ln"] + 1], scale=1.0 / NR_).then_inc(rms_ready, 1)

        @block.vector
        def _(dve):
            st = Steps(dve, steps)
            tt, ts, stt = nc.vector.tensor_tensor, nc.vector.tensor_scalar, nc.vector.scalar_tensor_tensor

            def center(m):
                u = m % 2
                dve.wait_ge(mean_ready, m + 1)
                stt(out=yc[:, u, :], in0=flat(mean[:, u, :, :]), scalar=-1.0 / NR_, in1=y[:, u, :], op0=ALU.mult,
                    op1=ALU.add).then_inc(yc_ready, 1)

            def finish(m):
                u = m % 2
                dve.wait_ge(rms_ready, m + 1)
                st.link(nc.vector.reciprocal(rms[:, u, :], rms[:, u, :]))
                st.link(tt(yc[:, u, :], yc[:, u, :], rms[:, u, :], ALU.mult))
                st.link(ts(yc[:, u, :], yc[:, u, :], col("lnx_w", m), col("lnx_b", m), ALU.mult, ALU.add))
                st.link(tt(yc[:, u, :], yc[:, u, :], bon[:, u, :], ALU.add))
                if m >= 2:
                    dve.wait_ge(stored[u], 16)
                tt(out[:, u, :], yc[:, u, :], g_[:, u, :], ALU.mult).then_inc(out_ready, 1)

            center(0)
            for m in range(4):
                if m < 3:
                    center(m + 1)
                finish(m)

        @block.gpsimd
        def _(pool):
            for m in range(4):
                pool.wait_ge(out_ready, m + 1)
                pool.dma_start(y_out[m], out[:, m % 2, :]).then_inc(stored[m % 2], 16)
            for u in range(2):
                pool.wait_ge(stored[u], 32)
def norm_stage(nc, src, dst, gain, eps_col, V, C):
    with ExitStack() as ctx:
        sb = lambda n, s, d=F32: ctx.enter_context(nc.sbuf_tensor(f"nf_{n}", s, d))
        sem = stage_semaphores(nc, ctx, "nf")
        x, sq, rms = sb("x", [P, DT, SEQ]), sb("sq", [P, 2, SEQ]), sb("rms", [P, SEQ])
        ss = ctx.enter_context(nc.psum_tensor("nf_ss", [P, 2, 512], F32))
        loaded = [sem(f"loaded{k}") for k in range(DT)]
        sq_ready, ss_ready, rms_ready, rstd_ready, h_ready, stored = (
            sem(n) for n in ("sq_ready", "ss_ready", "rms_ready", "rstd_ready", "h_ready", "stored"))
        block = ctx.enter_context(nc.Block(no_gpsimd_drain=True))

        @block.sync
        def _(sp):
            for k in range(DT):
                sp.dma_start(x[:, k, :], src[k]).then_inc(loaded[k], 16)
            for k in range(DT):
                sp.wait_ge(h_ready, k + 1)
                sp.dma_start(dst[k], x[:, k, :]).then_inc(stored, 16)
            sp.wait_ge(stored, 16 * DT)

        @block.scalar
        def _(act):
            for k in range(DT):
                act.wait_ge(loaded[k], 16)
                if k >= 2:
                    act.wait_ge(ss_ready, k - 1)
                nc.scalar.activation(sq[:, k % 2, :], x[:, k, :], ACT.Square).then_inc(sq_ready, 1)
            act.wait_ge(ss_ready, DT)
            nc.scalar.activation(rms[:, :], ss[:, :, :].rearrange("p a b -> p (a b)"), ACT.Sqrt,
                                 bias=C[:, eps_col:eps_col + 1], scale=1.0 / DM).then_inc(rms_ready, 1)

        @block.tensor
        def _(pe):
            for k in range(DT):
                pe.wait_ge(sq_ready, k + 1)
                for h in range(2):
                    mm = pe.matmul(ss[:, h, :], C[:, CONST["ones"]:CONST["ones"] + P], sq[:, k % 2, h * HALF:(h + 1) * HALF],
                                   start=k == 0, stop=k == DT - 1)
                mm.then_inc(ss_ready, 1)

        @block.vector
        def _(dve):
            dve.wait_ge(rms_ready, 1)
            nc.vector.reciprocal(rms[:, :], rms[:, :]).then_inc(rstd_ready, 1)
            dve.wait_ge(rstd_ready, 1)
            for k in range(DT):
                nc.vector.scalar_tensor_tensor(out=x[:, k, :], in0=x[:, k, :], scalar=V[:, gain + k:gain + k + 1],
                                               in1=rms[:, :], op0=ALU.mult, op1=ALU.mult).then_inc(h_ready, 1)


def lru_stage(nc, proj, lru_w, out, V, C):
    col = lambda name, j=0: V[:, VEC[name] + j:VEC[name] + j + 1]
    with ExitStack() as ctx:
        sb = lambda n, s, d=F32: ctx.enter_context(nc.sbuf_tensor(f"lr_{n}", s, d))
        sem = stage_semaphores(nc, ctx, "lr")
        W = sb("W", [P, 2 * DM])
        pre, yr = sb("pre", [P, 2, SEQ + 3]), sb("yr", [P, 2, SEQ])
        cv, xc = sb("cv", [P, 2, SEQ]), sb("xc", [P, 2, SEQ])
        rg, ig, gel = sb("rg", [P, 2, SEQ]), sb("ig", [P, 2, SEQ]), sb("gel", [P, 2, SEQ])
        a_, a2, th, mu = sb("a", [P, 2, SEQ]), sb("a2", [P, SEQ]), sb("th", [P, 2, SEQ]), sb("mu", [P, 2, SEQ])
        sq = sb("sq", [P, 2, SEQ])
        bi, h_, o = sb("bi", [P, SEQ]), sb("h", [P, SEQ]), sb("o", [P, 2, SEQ])
        sp_, m8, m16 = sb("sp", [P, 4, DT]), sb("m8", [P, DT]), sb("m16", [P, DT])
        p8 = sb("p8", [P, DT])
        gate = ctx.enter_context(nc.psum_tensor("lr_gate", [P, 2, 4, 512], F32))
        loaded = [sem(f"loaded{i}") for i in range(2)]
        stored = [sem(f"stored{i}") for i in range(2)]
        w_loaded, lam_e, lam_a, rates, conv_ready, gate_ready, sig_done, exps_done = (
            sem(n) for n in ("w_loaded", "lam_e", "lam_a", "rates", "conv_ready", "gate_ready", "sig_done", "exps_done"))
        sq_ready, mu_ready, steps, pads, o_ready = (sem(n) for n in ("sq_ready", "mu_ready", "steps", "pads", "o_ready"))
        block = ctx.enter_context(nc.Block(no_gpsimd_drain=True))

        @block.sync
        def _(sp):
            sp.dma_start(W[:, :], lru_w).then_inc(w_loaded, 16)
            for n in range(DT):
                if n >= 2:
                    sp.wait_ge(o_ready, n - 1)
                sp.dma_start(pre[:, n % 2, 3:], proj[n]).then_inc(loaded[n % 2], 16)
                sp.dma_start(yr[:, n % 2, :], proj[8 + n]).then_inc(loaded[n % 2], 16)

        @block.tensor
        def _(pe):
            pe.wait_ge(w_loaded, 16)
            for n in range(DT):
                u = n % 2
                pe.wait_ge(conv_ready, n + 1)
                if n >= 2:
                    pe.wait_ge(sig_done, 3 * (n - 1))
                for j in range(2):
                    for h in range(2):
                        mm = pe.matmul(gate[:, u, 2 * j + h, :], W[:, j * DM + n * P:j * DM + (n + 1) * P],
                                       xc[:, u, h * HALF:(h + 1) * HALF], start=True, stop=True)
                mm.then_inc(gate_ready, 1)

        @block.scalar
        def _(act):
            act.wait_ge(lam_a, 1)
            nc.scalar.activation(sp_[:, 1, :], sp_[:, 0, :], ACT.Exp, scale=-1.0).then_inc(lam_e, 1)
            act.wait_ge(rates, 1)
            flat = lambda t: t.rearrange("p a b -> p (a b)")

            def root(n):
                u = n % 2
                act.wait_ge(sq_ready, n + 1)
                if n >= 2:
                    act.wait_ge(o_ready, n - 1)
                nc.scalar.activation(mu[:, u, :], sq[:, u, :], ACT.Sqrt).then_inc(mu_ready, 1)

            for n in range(DT):
                u = n % 2
                act.wait_ge(gate_ready, n + 1)
                if n >= 2:
                    act.wait_ge(o_ready, n - 1)
                nc.scalar.activation(rg[:, u, :], flat(gate[:, u, 0:2, :]), ACT.Sigmoid, bias=col("lru_ba", n)).then_inc(sig_done, 1)
                nc.scalar.activation(ig[:, u, :], flat(gate[:, u, 2:4, :]), ACT.Sigmoid, bias=col("lru_bx", n)).then_inc(sig_done, 1)
                nc.scalar.activation(gel[:, u, :], yr[:, u, :], ACT.Gelu_apprx_tanh).then_inc(sig_done, 1)
                act.wait_ge(sig_done, 3 * n + 1)
                if n:
                    act.wait_ge(sq_ready, n)
                nc.scalar.activation(a_[:, u, :], rg[:, u, :], ACT.Exp, scale=m8[:, n:n + 1]).then_inc(exps_done, 1)
                nc.scalar.activation(a2[:, :], rg[:, u, :], ACT.Exp, scale=m16[:, n:n + 1]).then_inc(exps_done, 1)
                nc.scalar.activation(th[:, u, :], rg[:, u, :], ACT.Tanh, scale=p8[:, n:n + 1]).then_inc(exps_done, 1)
                root(n)

        @block.vector
        def _(dve):
            st = Steps(dve, steps)
            tt, ts, stt = nc.vector.tensor_tensor, nc.vector.tensor_scalar, nc.vector.scalar_tensor_tensor
            nc.vector.memset(pre[:, :, 0:3], 0.0).then_inc(pads, 1)
            lam = V[:, VEC["lru_lam"]:VEC["lru_lam"] + DT]
            stt(out=sp_[:, 0, :], in0=lam, scalar=-1.0, in1=lam, op0=ALU.mult, op1=ALU.max).then_inc(lam_a, 1)
            dve.wait_ge(lam_e, 1)
            st.link(ts(sp_[:, 2, :], sp_[:, 1, :], 2.0, None, ALU.add))
            st.link(nc.vector.reciprocal(sp_[:, 3, :], sp_[:, 2, :]))
            st.link(tt(sp_[:, 0, :], sp_[:, 1, :], sp_[:, 3, :], ALU.mult))
            st.link(tt(sp_[:, 1, :], sp_[:, 0, :], sp_[:, 0, :], ALU.mult))
            st.link(ts(sp_[:, 2, :], sp_[:, 1, :], 1.0 / 17, 1.0 / 15, ALU.mult, ALU.add))
            for k in (13, 11, 9, 7, 5, 3, 1):
                st.link(tt(sp_[:, 3, :], sp_[:, 2, :], sp_[:, 1, :], ALU.mult))
                st.link(ts(sp_[:, 2, :], sp_[:, 3, :], 1.0 / k, None, ALU.add))
            st.link(tt(sp_[:, 3, :], sp_[:, 2, :], sp_[:, 0, :], ALU.mult))
            st.link(ts(sp_[:, 0, :], lam, -1.0, 0.0, ALU.mult, ALU.max))
            st.link(stt(out=sp_[:, 1, :], in0=sp_[:, 3, :], scalar=2.0, in1=sp_[:, 0, :], op0=ALU.mult, op1=ALU.add))
            st(ts(m8[:, :], sp_[:, 1, :], -8.0, None, ALU.mult))
            st(ts(m16[:, :], sp_[:, 1, :], -16.0, None, ALU.mult))
            st(ts(p8[:, :], sp_[:, 1, :], 8.0, None, ALU.mult))
            st.settle()
            dve.sem_inc(rates, 1)
            dve.wait_ge(pads, 1)

            def conv(n):
                u = n % 2
                dve.wait_ge(loaded[u], 32 * (n // 2 + 1))
                if n:
                    dve.wait_ge(conv_ready, n)
                w = lambda tap: col("conv_2", 8 * tap + n)
                st.link(ts(cv[:, 0, :], pre[:, u, 3:3 + SEQ], w(3), col("conv_b_2", n), ALU.mult, ALU.add))
                st.link(stt(out=cv[:, 1, :], in0=pre[:, u, 2:2 + SEQ], scalar=w(2), in1=cv[:, 0, :], op0=ALU.mult, op1=ALU.add))
                st.link(stt(out=cv[:, 0, :], in0=pre[:, u, 1:1 + SEQ], scalar=w(1), in1=cv[:, 1, :], op0=ALU.mult, op1=ALU.add))
                if n >= 2:
                    dve.wait_ge(gate_ready, n - 1)
                stt(out=xc[:, u, :], in0=pre[:, u, 0:SEQ], scalar=w(0), in1=cv[:, 0, :], op0=ALU.mult, op1=ALU.add).then_inc(conv_ready, 1)

            conv(0)
            for n in range(DT):
                u = n % 2
                if n + 1 < DT:
                    conv(n + 1)
                dve.wait_ge(exps_done, 3 * n + 3)
                if n >= 2:
                    dve.wait_ge(mu_ready, n - 1)
                stt(out=sq[:, u, :], in0=a2[:, :], scalar=1.0, in1=th[:, u, :], op0=ALU.add, op1=ALU.mult).then_inc(sq_ready, 1)
                dve.wait_ge(sig_done, 3 * n + 3)
                dve.wait_ge(conv_ready, n + 1)
                st.link(tt(bi[:, :], xc[:, u, :], ig[:, u, :], ALU.mult))
                dve.wait_ge(mu_ready, n + 1)
                st.link(tt(bi[:, :], bi[:, :], mu[:, u, :], ALU.mult))
                st.link(nc.vector.tensor_tensor_scan(h_[:, :], a_[:, u, :], bi[:, :], 0.0, ALU.mult, ALU.add))
                if n >= 2:
                    dve.wait_ge(stored[u], 16 * (n // 2))
                tt(o[:, u, :], h_[:, :], gel[:, u, :], ALU.mult).then_inc(o_ready, 1)

        @block.gpsimd
        def _(pool):
            for n in range(DT):
                pool.wait_ge(o_ready, n + 1)
                pool.dma_start(out[n], o[:, n % 2, :]).then_inc(stored[n % 2], 16)
            for u in range(2):
                pool.wait_ge(stored[u], 16 * DT // 2)


def attention_stage(nc, proj, qT, kvT, positions, out, V, C):
    H, QD = 8, 192
    TWO_PI = 6.283185307179586
    MAGIC = 1.5 * 2.0 ** 23
    C1 = 6.28125
    C2 = float(np.float32(np.floor((TWO_PI - C1) * 2.0 ** 20) / 2.0 ** 20))
    C3 = TWO_PI - C1 - C2
    col = lambda name, j=0: V[:, VEC[name] + j:VEC[name] + j + 1]
    ones = C[:, CONST["ones"]:CONST["ones"] + P]
    ident = C[:, CONST["ident"]:CONST["ident"] + P]
    eps = C[:, CONST["eps6"]:CONST["eps6"] + 1]
    with ExitStack() as ctx:
        sb = lambda n, s, d=F32: ctx.enter_context(nc.sbuf_tensor(f"at_{n}", s, d))
        sem = stage_semaphores(nc, ctx, "at")
        pos = sb("pos", [P, SEQ], I32)
        ang, t1, t2, cosb, sinb = (sb(n, [P, SEQ]) for n in ("ang", "t1", "t2", "cos", "sin"))
        kpe, kps, krot, kpe_sq = (sb(n, [P, SEQ]) for n in ("kpe", "kps", "krot", "kpe_sq"))
        qn, kn, vt = sb("qn", [P, 2, SEQ]), sb("kn", [P, 2, SEQ]), sb("vt", [P, 2, SEQ])
        qr, qs = sb("qr", [P, SEQ]), sb("qs", [P, SEQ])
        qr_sq, q_sq, k_sq = sb("qr_sq", [P, SEQ]), sb("q_sq", [P, SEQ]), sb("k_sq", [P, SEQ])
        qrot = sb("qrot", [P, 2, SEQ])
        q_g, k_g, k_r, v_tok = sb("q_g", [P, 2, SEQ]), sb("k_g", [P, 2, SEQ]), sb("k_r", [P, 2, SEQ]), sb("v_tok", [P, 2, SEQ])
        rk = sb("rk", [P, SEQ])
        rq, q_scale, neg_scale = sb("rq", [P, 2, 8]), sb("q_scale", [P, 2, 8]), sb("neg_scale", [P, 2, 8])
        pr = sb("pr", [P, 2, SEQ])
        prT = sb("prT", [P, 2, SEQ])
        mx, bias, total, rinv = (sb(n, [P, 64]) for n in ("mx", "bias", "total", "rinv"))
        o_sb = sb("o_sb", [P, 2, SEQ])
        score = ctx.enter_context(nc.psum_tensor("at_score", [P, 2, 1024], F32))
        tr = ctx.enter_context(nc.psum_tensor("at_tr", [P, 2, 512], F32))
        ob = ctx.enter_context(nc.psum_tensor("at_ob", [P, 512], F32))
        pb = ctx.enter_context(nc.psum_tensor("at_pb", [P, 512], F32))
        g_loaded, steps, ang_ready, trig_ready, kpe_sq_ready = (sem(n) for n in ("g_loaded", "steps", "ang_ready", "trig_ready", "kpe_sq_ready"))
        h_loaded = [sem(f"h_loaded{i}") for i in range(2)]
        r_loaded, rot_done, sq_ready, prep_ready, prep_read, rk_ready, head_ready, rq_done = (
            sem(n) for n in ("r_loaded", "rot_done", "sq_ready", "prep_ready", "prep_read", "rk_ready", "head_ready", "rq_done"))
        score_ready, bias_ready, prob_ready, norm_ready, tr_ready, tr_copied, ob_ready, ob_copied = (
            sem(n) for n in ("score_ready", "bias_ready", "prob_ready", "norm_ready", "tr_ready", "tr_copied", "ob_ready", "ob_copied"))
        stored = [sem(f"stored{i}") for i in range(2)]
        NQ = SEQ // P
        trs = [0]
        for h in range(H):
            for b in range(NQ):
                trs.append(trs[-1] + b // 4 + 1)
        block = ctx.enter_context(nc.Block(no_gpsimd_drain=True))

        @block.sync
        def _(sp):
            sp.dma_start(pos[:, :], positions.partition_broadcast(P)).then_inc(g_loaded, 16)
            sp.dma_start(kpe[:, :], proj[20]).then_inc(g_loaded, 16)
            sp.dma_start(kps[:, :], proj[21]).then_inc(g_loaded, 16)
            for h in range(H):
                u = h % 2
                if h >= 2:
                    sp.wait_ge(head_ready, h - 1)
                    sp.wait_ge(prep_ready, 5 * (h - 1))
                sp.dma_start(qn[:, u, :], qT[h]).then_inc(h_loaded[u], 16)
                sp.dma_start(kn[:, u, :], kvT[h]).then_inc(h_loaded[u], 16)
                sp.dma_start(vt[:, u, :], kvT[8 + h]).then_inc(h_loaded[u], 16)
                if u == 0:
                    if h:
                        sp.wait_ge(rot_done, 1 + h // 2)
                    sp.dma_start(qr[:, :], qT[8 + h // 2]).then_inc(r_loaded, 16)
                    sp.dma_start(qs[:, :], qT[12 + h // 2]).then_inc(r_loaded, 16)

        @block.vector
        def _(dve):
            st = Steps(dve, steps)
            tt, ts, stt = nc.vector.tensor_tensor, nc.vector.tensor_scalar, nc.vector.scalar_tensor_tensor
            dve.wait_ge(g_loaded, 48)
            st.link(nc.vector.tensor_copy(t1[:, :], pos[:, :]))
            st.link(ts(ang[:, :], t1[:, :], C[:, CONST["inv_freq"]:CONST["inv_freq"] + 1], None, ALU.mult))
            st.link(ts(t1[:, :], ang[:, :], 1.0 / TWO_PI, None, ALU.mult))
            st.link(ts(t2[:, :], t1[:, :], MAGIC, None, ALU.add))
            st.link(ts(t1[:, :], t2[:, :], -MAGIC, None, ALU.add))
            for c_ in (C1, C2, C3):
                st.link(stt(out=ang[:, :], in0=t1[:, :], scalar=-c_, in1=ang[:, :], op0=ALU.mult, op1=ALU.add))
            st.link(ts(ang[:, :], ang[:, :], 3.1415925, -3.1415925, ALU.min, ALU.max))
            st.link(stt(out=t1[:, :], in0=ang[:, :], scalar=-1.0, in1=ang[:, :], op0=ALU.mult, op1=ALU.max))
            ts(t2[:, :], t1[:, :], -1.0, TWO_PI / 4, ALU.mult, ALU.add).then_inc(ang_ready, 1)
            dve.wait_ge(trig_ready, 2)
            st.link(ts(sinb[:, :], sinb[:, :], C[:, CONST["rope_sign"]:CONST["rope_sign"] + 1], None, ALU.mult))

            def rotate(dst, a, b, g):
                st(stt(out=t1[:, :], in0=a, scalar=col(g + "_r"), in1=cosb[:, :], op0=ALU.mult, op1=ALU.mult))
                st(stt(out=t2[:, :], in0=b, scalar=col(g + "_s"), in1=sinb[:, :], op0=ALU.mult, op1=ALU.mult))
                st.settle()
                st.link(tt(dst, t1[:, :], t2[:, :], ALU.add))
                dve.sem_inc(rot_done, 1)

            rotate(krot[:, :], kpe[:, :], kps[:, :], "kg")

            def prep(h):
                u = h % 2
                dve.wait_ge(h_loaded[u], 48 * (h // 2 + 1))
                if u == 0:
                    dve.wait_ge(r_loaded, 32 * (h // 2 + 1))
                    dve.wait_ge(sq_ready, 3 * h + 1 - h // 2)
                    rotate(qrot[:, (h // 2) % 2, :], qr[:, :], qs[:, :], "qg")
                if h >= 2:
                    dve.wait_ge(ob_ready, NQ * (h - 1))
                st(ts(q_g[:, u, :], qn[:, u, :], col("qg_n"), None, ALU.mult))
                dve.wait_ge(rk_ready, 2 * h + 2)
                st.link(nc.vector.reciprocal(rk[:, :], rk[:, :]))
                base = 64 * u
                st(stt(out=k_g[:, u, :], in0=kn[:, u, :], scalar=col("kg_n"), in1=rk[:, :], op0=ALU.mult, op1=ALU.mult))
                st(tt(k_r[base:base + 64, u, :], krot[base:base + 64, :], rk[base:base + 64, :], ALU.mult))
                dve.wait_ge(rq_done, h + 1)
                st.link(nc.vector.reciprocal(q_scale[:, u, :], rq[:, u, :]))
                st(ts(neg_scale[:, u, :], q_scale[:, u, :], -(QD ** -0.5), None, ALU.mult))
                st.settle()
                st.link(ts(q_scale[:, u, :], q_scale[:, u, :], QD ** -0.5, None, ALU.mult))
                dve.sem_inc(head_ready, 1)

            def maximum(h, b):
                n = NQ * h + b
                u, w = n % 2, (b + 1) * P
                dve.wait_ge(score_ready, n + 1)
                st.link(stt(out=score[:, u, b * P:w], in0=C[:, CONST["before"]:CONST["before"] + P], scalar=-1e30,
                            in1=score[:, u, b * P:w], op0=ALU.mult, op1=ALU.add))
                st.link(nc.vector.reduce_max(mx[:, n:n + 1], score[:, u, 0:w], AX.X))
                tt(bias[:, n:n + 1], mx[:, n:n + 1], neg_scale[:, h % 2, b:b + 1], ALU.mult).then_inc(bias_ready, 1)

            def normalise(h, b):
                n = NQ * h + b
                u, w = n % 2, (b + 1) * P
                dve.wait_ge(prob_ready, n + 1)
                st.link(nc.vector.reciprocal(rinv[:, n:n + 1], total[:, n:n + 1]))
                ts(pr[:, u, 0:w], pr[:, u, 0:w], rinv[:, n:n + 1], None, ALU.mult).then_inc(norm_ready, 1)

            def outputs(h, b):
                n = NQ * h + b
                dve.wait_ge(ob_ready, n + 1)
                if b == 0 and h >= 2:
                    dve.wait_ge(stored[h % 2], 16 * (h // 2))
                nc.vector.tensor_copy(o_sb[:, h % 2, b * P:(b + 1) * P], ob[:, 0:P]).then_inc(ob_copied, 1)

            prep(0)
            every = [(h, b) for h in range(H) for b in range(NQ)]
            for n, (h, b) in enumerate(every):
                if b == 2 and h + 1 < H:
                    prep(h + 1)
                maximum(h, b)
                if n >= 1:
                    normalise(*every[n - 1])
                if n >= 2:
                    outputs(*every[n - 2])
            normalise(*every[-1])
            outputs(*every[-2])
            outputs(*every[-1])

        @block.scalar
        def _(act):
            act.wait_ge(ang_ready, 1)
            nc.scalar.activation(sinb[:, :], ang[:, :], ACT.Sin).then_inc(trig_ready, 1)
            nc.scalar.activation(cosb[:, :], t2[:, :], ACT.Sin).then_inc(trig_ready, 1)
            act.wait_ge(g_loaded, 48)
            nc.scalar.activation(kpe_sq[:, :], kpe[:, :], ACT.Square).then_inc(kpe_sq_ready, 1)

            def prep(h):
                u = h % 2
                act.wait_ge(h_loaded[u], 48 * (h // 2 + 1))
                if h:
                    act.wait_ge(prep_ready, 5 * h)
                if u == 0:
                    act.wait_ge(r_loaded, 32 * (h // 2 + 1))
                    nc.scalar.activation(qr_sq[:, :], qr[:, :], ACT.Square).then_inc(sq_ready, 1)
                nc.scalar.activation(q_sq[:, :], qn[:, u, :], ACT.Square).then_inc(sq_ready, 1)
                nc.scalar.activation(k_sq[:, :], kn[:, u, :], ACT.Square).then_inc(sq_ready, 1)
                if h >= 1:
                    act.wait_ge(head_ready, h)
                if h >= 2:
                    act.wait_ge(ob_ready, NQ * (h - 1))
                for f in range(2):
                    act.wait_ge(prep_ready, 5 * h + f + 1)
                    nc.scalar.activation(rk[:, f * 512:(f + 1) * 512], pb[:, :], ACT.Sqrt, bias=eps, scale=1.0 / QD).then_inc(rk_ready, 1)
                act.wait_ge(prep_ready, 5 * h + 3)
                nc.scalar.activation(rq[:, u, :], pb[:, 0:8], ACT.Sqrt, bias=eps, scale=1.0 / QD).then_inc(rq_done, 1)
                for f in range(2):
                    act.wait_ge(prep_ready, 5 * h + 4 + f)
                    nc.scalar.copy(v_tok[:, u, f * 512:(f + 1) * 512], pb[:, :]).then_inc(prep_read, 1)

            def probs(h, b):
                n = NQ * h + b
                u, w = n % 2, (b + 1) * P
                act.wait_ge(bias_ready, n + 1)
                if n >= 2:
                    act.wait_ge(tr_ready, trs[n - 1])
                nc.scalar.activation(pr[:, u, 0:w], score[:, u, 0:w], ACT.Exp, bias=bias[:, n:n + 1],
                                     scale=q_scale[:, h % 2, b:b + 1], accum_out=total[:, n:n + 1]).then_inc(prob_ready, 1)

            def copies(h, b):
                n = NQ * h + b
                for k in range(b // 4 + 1):
                    w = min(512, (b + 1) * P - k * 512)
                    act.wait_ge(tr_ready, trs[n] + k + 1)
                    if n >= 2:
                        act.wait_ge(ob_ready, n - 1)
                    nc.scalar.copy(prT[:, n % 2, k * 512:k * 512 + w], tr[:, (trs[n] + k) % 2, 0:w]).then_inc(tr_copied, 1)

            prep(0)
            every = [(h, b) for h in range(H) for b in range(NQ)]
            for n, (h, b) in enumerate(every):
                if b == 2 and h + 1 < H:
                    prep(h + 1)
                probs(h, b)
                if n >= 1:
                    copies(*every[n - 1])
            copies(*every[-1])

        @block.tensor
        def _(pe):
            def prep(h):
                u, base = h % 2, 64 * (h % 2)
                pe.wait_ge(sq_ready, 2 * h + 2 + h // 2 + 1)
                if h == 0:
                    pe.wait_ge(kpe_sq_ready, 1)
                for f in range(2):
                    fs = slice(f * 512, (f + 1) * 512)
                    if f or h:
                        pe.wait_ge(rk_ready, 2 * h + 1) if f else pe.wait_ge(prep_read, 2 * h)
                    pe.matmul(pb[:, :], ones, k_sq[:, fs], start=True, stop=False)
                    pe.matmul(pb[:, :], C[0:64, CONST["ones"]:CONST["ones"] + P], kpe_sq[0:64, fs], start=False, stop=True).then_inc(prep_ready, 1)
                pe.wait_ge(rk_ready, 2 * h + 2)
                for t in range(NQ):
                    tsl = slice(t * P, (t + 1) * P)
                    pe.matmul(pb[:, t:t + 1], q_sq[:, tsl], C[:, CONST["ones"]:CONST["ones"] + 1], start=True, stop=False, skip_group_check=True)
                    mm = pe.matmul(pb[:, t:t + 1], qr_sq[base:base + 64, tsl], C[base:base + 64, CONST["ones"]:CONST["ones"] + 1],
                                   start=False, stop=True, skip_group_check=True)
                mm.then_inc(prep_ready, 1)
                for f in range(2):
                    pe.wait_ge(prep_read, 2 * h + 1) if f else pe.wait_ge(rq_done, h + 1)
                    for t in range(4):
                        mm = pe.transpose(pb[:, t * P:(t + 1) * P], vt[:, u, (4 * f + t) * P:(4 * f + t + 1) * P], ident)
                    mm.then_inc(prep_ready, 1)

            def scores(h, b):
                n = NQ * h + b
                u, base, hu = n % 2, 64 * (h % 2), h % 2
                if b == 0:
                    pe.wait_ge(head_ready, h + 1)
                if n >= 2:
                    pe.wait_ge(prob_ready, n - 1)
                for f in range(b // 4 + 1):
                    w = min(512, (b + 1) * P - f * 512)
                    o = score[:, u, f * 512:f * 512 + w]
                    pe.matmul(o, q_g[:, hu, b * P:(b + 1) * P], k_g[:, hu, f * 512:f * 512 + w], start=True, stop=False)
                    mm = pe.matmul(o, qrot[base:base + 64, (h // 2) % 2, b * P:(b + 1) * P], k_r[base:base + 64, hu, f * 512:f * 512 + w],
                                   start=False, stop=True)
                mm.then_inc(score_ready, 1)

            def transposes(h, b):
                n = NQ * h + b
                pe.wait_ge(norm_ready, n + 1)
                for k in range(b // 4 + 1):
                    g = trs[n] + k
                    if g >= 2:
                        pe.wait_ge(tr_copied, g - 1)
                    for j in range(min(4, b + 1 - 4 * k)):
                        mm = pe.transpose(tr[:, g % 2, j * P:(j + 1) * P], pr[:, n % 2, (4 * k + j) * P:(4 * k + j + 1) * P], ident)
                    mm.then_inc(tr_ready, 1)

            def values(h, b):
                n = NQ * h + b
                pe.wait_ge(tr_copied, trs[n + 1])
                if b == 0:
                    pe.wait_ge(prep_read, 2 * h + 2)
                if n >= 1:
                    pe.wait_ge(ob_copied, n)
                o = ob[:, 0:P]
                for k in range(b + 1):
                    mm = pe.matmul(o, v_tok[:, h % 2, k * P:(k + 1) * P], prT[:, n % 2, k * P:(k + 1) * P], start=k == 0,
                                   stop=k == b, skip_group_check=True)
                mm.then_inc(ob_ready, 1)

            prep(0)
            every = [(h, b) for h in range(H) for b in range(NQ)]
            for n, (h, b) in enumerate(every):
                if b == 2 and h + 1 < H:
                    prep(h + 1)
                scores(h, b)
                if n >= 1:
                    transposes(*every[n - 1])
                if n >= 2:
                    values(*every[n - 2])
            transposes(*every[-1])
            values(*every[-2])
            values(*every[-1])

        @block.gpsimd
        def _(pool):
            for h in range(H):
                pool.wait_ge(ob_copied, NQ * (h + 1))
                pool.dma_start(out[h], o_sb[:, h % 2, :]).then_inc(stored[h % 2], 16)
            for u in range(2):
                pool.wait_ge(stored[u], 16 * H // 2)
N_EXP, GRP, PER = 64, 8, 8
NBLK = 2 * SEQ // P + N_EXP


def router_stage(nc, src, router, router_b, u_tok, table, dest, gates, blk_expert, V, C):
    with ExitStack() as ctx:
        sb = lambda n, s, d=F32: ctx.enter_context(nc.sbuf_tensor(f"ro_{n}", s, d))
        sem = stage_semaphores(nc, ctx, "ro")
        x, sq, rms = sb("x", [P, DT, SEQ]), sb("sq", [P, 2, SEQ]), sb("rms", [P, SEQ])
        wr, br = sb("wr", [P, DT * 72]), sb("br", [P, 72])
        ut = sb("ut", [P, 2, DM])
        lg = sb("lg", [P, DT, 72])
        zero = sb("zero", [P, NBLK], I32)
        g_eq, g_key, g_hot = sb("g_eq", [P, DT, 8]), sb("g_key", [P, DT, 8]), sb("g_hot", [P, DT, 8])
        g_exp = sb("g_exp", [P, DT, 8])
        gmax, gsum, gp, m1, m2, kmin = (sb(n, [P, DT]) for n in ("gmax", "gsum", "gp", "m1", "m2", "kmin"))
        ein, ein2, e_key = sb("ein", [P, DT, 8]), sb("ein2", [P, DT, 8]), sb("e_key", [P, DT, 8])
        e_hot = sb("e_hot", [P, 2, DT, 8])
        big = sb("big", [P, DT, 64])
        hot = sb("hot", [P, 3, DT, 64])
        rat, rden = sb("rat", [P, DT]), sb("rden", [P, DT])
        cnt, padded, pend, pstart = sb("cnt", [P, 64]), sb("padded", [P, 64]), sb("pend", [P, 64]), sb("pstart", [P, 64])
        ci = sb("ci", [P, 2, 64], I32)
        slot = sb("slot", [P, DT, 64])
        dest_f = sb("dest_f", [P, 2, DT])
        be = sb("be", [P, 64])
        bcol = sb("bcol", [P, 2])
        tok_id = sb("tok_id", [P, DT], I32)
        ss = ctx.enter_context(nc.psum_tensor("ro_ss", [P, 2, 512], F32))
        tr = ctx.enter_context(nc.psum_tensor("ro_tr", [P, 4, 512], F32))
        lp = ctx.enter_context(nc.psum_tensor("ro_lp", [P, 2, 512], F32))
        loaded = [sem(f"loaded{k}") for k in range(DT)]
        stored = [sem(f"stored{k}") for k in range(2)]
        w_loaded, sq_ready, ss_ready, rms_ready, rstd_ready, h_ready, steps = (
            sem(n) for n in ("w_loaded", "sq_ready", "ss_ready", "rms_ready", "rstd_ready", "h_ready", "steps"))
        lg_ready, lg_read, tr_ready, tr_copied, table_zero, zero_ready, key_ready, exp_done = (
            sem(n) for n in ("lg_ready", "lg_read", "tr_ready", "tr_copied", "table_zero", "zero_ready", "key_ready", "exp_done"))
        hot_ready, count_ready, bcol_ready, brow_ready, dest_ready, scattered, id_ready, logit_done = (
            sem(n) for n in ("hot_ready", "count_ready", "bcol_ready", "brow_ready", "dest_ready", "scattered", "id_ready", "logit_done"))
        ident = C[:, CONST["ident"]:CONST["ident"] + P]
        ones = C[:, CONST["ones"]:CONST["ones"] + P]
        block = ctx.enter_context(nc.Block(no_gpsimd_drain=True))

        @block.sync
        def _(sp):
            for k in range(DT):
                sp.dma_start(x[:, k, :], src[k]).then_inc(loaded[k], 16)
            sp.dma_start(wr[:, :], router).then_inc(w_loaded, 16)
            sp.dma_start(br[:, :], router_b.partition_broadcast(P)).then_inc(w_loaded, 16)
            sp.wait_ge(zero_ready, 1)
            sp.dma_start(table.rearrange("(p c) o -> p (c o)", p=P), zero[:, :]).then_inc(table_zero, 16)
            for t in range(DT):
                sp.wait_ge(tr_copied, t + 1)
                sp.dma_start(u_tok[t * P:(t + 1) * P, :], ut[:, t % 2, :]).then_inc(stored[t % 2], 16)
            for u in range(2):
                sp.wait_ge(stored[u], 16 * DT // 2)

        @block.scalar
        def _(act):
            for k in range(DT):
                act.wait_ge(loaded[k], 16)
                if k >= 2:
                    act.wait_ge(ss_ready, k - 1)
                nc.scalar.activation(sq[:, k % 2, :], x[:, k, :], ACT.Square).then_inc(sq_ready, 1)
            act.wait_ge(ss_ready, DT)
            nc.scalar.activation(rms[:, :], ss[:, :, :].rearrange("p a b -> p (a b)"), ACT.Sqrt,
                                 bias=C[:, CONST["eps6"]:CONST["eps6"] + 1], scale=1.0 / DM).then_inc(rms_ready, 1)
            for t in range(DT):
                u = t % 2
                act.wait_ge(tr_ready, t + 1)
                if t >= 2:
                    act.wait_ge(stored[u], 16 * (t // 2))
                nc.scalar.copy(ut[:, u, :], tr[:, 2 * u:2 * u + 2, :].rearrange("p a b -> p (a b)")).then_inc(tr_copied, 1)
            act.wait_ge(key_ready, 1)
            nc.scalar.activation(g_exp[:, :, :], g_exp[:, :, :], ACT.Exp).then_inc(exp_done, 1)
            act.wait_ge(key_ready, 2)
            nc.scalar.activation(rat[:, :], rat[:, :], ACT.Exp).then_inc(exp_done, 1)

        @block.tensor
        def _(pe):
            for k in range(DT):
                pe.wait_ge(sq_ready, k + 1)
                for h in range(2):
                    mm = pe.matmul(ss[:, h, :], ones, sq[:, k % 2, h * HALF:(h + 1) * HALF], start=k == 0, stop=k == DT - 1)
                mm.then_inc(ss_ready, 1)
            pe.wait_ge(w_loaded, 32)
            pe.wait_ge(h_ready, DT)
            for t in range(DT):
                u, tsl = t % 2, slice(t * P, (t + 1) * P)
                if t >= 2:
                    pe.wait_ge(lg_read, t - 1)
                    pe.wait_ge(tr_copied, t - 1)
                for k in range(DT):
                    mm = pe.matmul(lp[:, u, 0:72], x[:, k, tsl], wr[:, k * 72:(k + 1) * 72], start=k == 0, stop=k == DT - 1)
                mm.then_inc(lg_ready, 1)
                for k in range(DT):
                    mm = pe.transpose(tr[:, 2 * u + k // 4, (k % 4) * P:(k % 4 + 1) * P], x[:, k, tsl], ident)
                mm.then_inc(tr_ready, 1)
            pe.wait_ge(hot_ready, 1)
            for t in range(DT):
                o = ss[:, 0, t * 64:(t + 1) * 64]
                for e in range(t):
                    pe.matmul(o, ones, hot[:, 2, e, :], start=e == 0, stop=False, skip_group_check=True)
                pe.matmul(o, C[:, CONST["before"]:CONST["before"] + P], hot[:, 2, t, :], start=t == 0, stop=True, skip_group_check=True)
            for t in range(DT):
                mm = pe.matmul(ss[:, 1, 0:64], ones, hot[:, 2, t, :], start=t == 0, stop=t == DT - 1)
            mm.then_inc(count_ready, 1)
            pe.wait_ge(bcol_ready, 1)
            pe.matmul(lp[0:1, 0, 0:P], bcol[:, 1:2], ident, start=True, stop=True).then_inc(brow_ready, 1)

        @block.vector
        def _(dve):
            st = Steps(dve, steps)
            tt, ts, stt = nc.vector.tensor_tensor, nc.vector.tensor_scalar, nc.vector.scalar_tensor_tensor
            bc = lambda t, n: t.unsqueeze(2).to_broadcast([P, DT, n])
            nc.vector.memset(zero[:, :], 0).then_inc(zero_ready, 1)
            dve.wait_ge(rms_ready, 1)
            nc.vector.reciprocal(rms[:, :], rms[:, :]).then_inc(rstd_ready, 1)
            dve.wait_ge(rstd_ready, 1)
            for k in range(DT):
                stt(out=x[:, k, :], in0=x[:, k, :], scalar=V[:, VEC["norm2_2"] + k:VEC["norm2_2"] + k + 1],
                    in1=rms[:, :], op0=ALU.mult, op1=ALU.mult).then_inc(h_ready, 1)
            dve.wait_ge(w_loaded, 32)
            for t in range(DT):
                dve.wait_ge(lg_ready, t + 1)
                tt(lg[:, t, :], lp[:, t % 2, 0:72], br[:, :], ALU.add).then_inc(lg_read, 1)
            dve.wait_ge(lg_read, DT)
            G, E = lg[:, :, 0:8], lg[:, :, 8:72]
            iota = C[:, CONST["iota8"]:CONST["iota8"] + 8].unsqueeze(1).to_broadcast([P, DT, 8])

            def first_hot(hot_out, vals, mx):
                st.link(nc.vector.reduce_max(mx, vals, AX.X))
                st.link(tt(g_eq[:, :, :], vals, bc(mx, 8), ALU.is_equal))
                st.link(stt(out=g_key[:, :, :], in0=g_eq[:, :, :], scalar=-8.0, in1=iota, op0=ALU.mult, op1=ALU.add))
                st.link(nc.vector.tensor_reduce(kmin[:, :], g_key[:, :, :], AX.X, ALU.min))
                st.link(tt(hot_out, g_key[:, :, :], bc(kmin[:, :], 8), ALU.is_equal))

            first_hot(g_hot[:, :, :], G, gmax[:, :])
            st.link(tt(g_exp[:, :, :], G, bc(gmax[:, :], 8), ALU.subtract))
            dve.sem_inc(key_ready, 1)
            big4 = big[:, :, :].rearrange("p t (g e) -> p t g e", g=8)
            gh4 = g_hot[:, :, :].unsqueeze(3).to_broadcast([P, DT, 8, 8])
            for t in range(DT):
                st(tt(big4[:, t, :, :], E[:, t, :].rearrange("p (g e) -> p g e", g=8), gh4[:, t, :, :], ALU.mult))
            st.settle()
            for t in range(DT):
                st(nc.vector.tensor_reduce(ein[:, t, :], big4[:, t, :, :].rearrange("p g e -> p e g"), AX.X, ALU.add))
            st.settle()
            first_hot(e_hot[:, 0, :, :], ein[:, :, :], m1[:, :])
            st.link(stt(out=ein2[:, :, :], in0=e_hot[:, 0, :, :], scalar=-3e38, in1=ein[:, :, :], op0=ALU.mult, op1=ALU.add))
            first_hot(e_hot[:, 1, :, :], ein2[:, :, :], m2[:, :])
            st.link(tt(rat[:, :], m2[:, :], m1[:, :], ALU.subtract))
            dve.sem_inc(key_ready, 1)
            for j in range(2):
                for t in range(DT):
                    st(tt(hot[:, j, t, :].rearrange("p (g e) -> p g e", g=8), gh4[:, t, :, :],
                          e_hot[:, j, t, :].unsqueeze(1).to_broadcast([P, 8, 8]), ALU.mult))
            st.settle()
            tt(hot[:, 2, :, :], hot[:, 0, :, :], hot[:, 1, :, :], ALU.add).then_inc(hot_ready, 1)
            dve.wait_ge(exp_done, 2)
            st.link(nc.vector.reduce_sum(gsum[:, :], g_exp[:, :, :], AX.X))
            st.link(stt(out=rden[:, :], in0=rat[:, :], scalar=1.0, in1=gsum[:, :], op0=ALU.add, op1=ALU.mult))
            st.link(nc.vector.reciprocal(gates[:, 0, :], rden[:, :]))
            st.link(tt(gates[:, 1, :], gates[:, 0, :], rat[:, :], ALU.mult))
            dve.wait_ge(count_ready, 1)
            st.link(ts(cnt[:, :], ss[:, 1, 0:64], float(P - 1), None, ALU.add))
            st.link(nc.vector.tensor_copy(ci[:, 0, :], cnt[:, :]))
            st.link(ts(ci[:, 1, :], ci[:, 0, :], 7, 7, ALU.arith_shift_right, ALU.logical_shift_left))
            st.link(nc.vector.tensor_copy(padded[:, :], ci[:, 1, :]))
            st.link(nc.vector.tensor_tensor_scan(pend[:, :], ones[:, 0:64], padded[:, :], 0.0, ALU.mult, ALU.add))
            st.link(tt(pstart[:, :], pend[:, :], padded[:, :], ALU.subtract))
            st.link(ts(be[:, :], pend[:, :], C[:, CONST["block_start"]:CONST["block_start"] + 1], None, ALU.is_le))
            st.link(nc.vector.reduce_sum(bcol[:, 0:1], be[:, :], AX.X))
            ts(bcol[:, 1:2], bcol[:, 0:1], float(N_EXP - 1), None, ALU.min).then_inc(bcol_ready, 1)
            st.link(tt(slot[:, :, :], ss[:, 0, :].rearrange("p (t e) -> p t e", t=DT), pstart[:, :].unsqueeze(1).to_broadcast([P, DT, 64]), ALU.add))
            for j in range(2):
                st.link(tt(big[:, :, :], slot[:, :, :], hot[:, j, :, :], ALU.mult))
                st.link(nc.vector.reduce_sum(dest_f[:, j, :], big[:, :, :], AX.X))
            nc.vector.tensor_copy(dest[:, :, :], dest_f[:, :, :]).then_inc(dest_ready, 1)
            dve.wait_ge(brow_ready, 1)
            nc.vector.tensor_copy(blk_expert[:, :], lp[0:1, 0, 0:P]).then_inc(dest_ready, 1)

        @block.gpsimd
        def _(pool):
            nc.gpsimd.iota(tok_id[:, :], pattern=[[P, DT]], base=0, channel_multiplier=1).then_inc(id_ready, 1)
            pool.wait_ge(id_ready, 1)
            pool.wait_ge(table_zero, 16)
            pool.wait_ge(dest_ready, 1)
            for j in range(2):
                for t in range(DT):
                    pool.indirect_dma_start(table, bass.IndirectOffsetOnAxis(dest[:, j, t:t + 1], 0), tok_id[:, t:t + 1], None).then_inc(scattered, 16)
            pool.wait_ge(scattered, 16 * 2 * DT)


def expert_stage(nc, u_tok, table, w13, ew2, y_pad, blk_expert, C):
    FE = 256
    with ExitStack() as ctx:
        sb = lambda n, s, d=F32: ctx.enter_context(nc.sbuf_tensor(f"ex_{n}", s, d))
        sem = stage_semaphores(nc, ctx, "ex")
        wa, wb = sb("wa", [P, 2, 8 * 2 * FE]), sb("wb", [P, 2, 2 * DM])
        idx = sb("idx", [P, 2], U32)
        xb, xT = sb("xb", [P, 2, DM]), sb("xT", [P, 2, DM])
        s1, hh, hT = sb("s1", [P, 2, FE]), sb("hh", [P, 2, FE]), sb("hT", [P, 2, FE])
        yb = sb("yb", [P, 2, DM])
        xp = ctx.enter_context(nc.psum_tensor("ex_xp", [P, 2, 512], F32))
        ap_ = ctx.enter_context(nc.psum_tensor("ex_ap", [P, 2, 512], F32))
        hp = ctx.enter_context(nc.psum_tensor("ex_hp", [P, 512], F32))
        yp = ctx.enter_context(nc.psum_tensor("ex_yp", [P, 2, 512], F32))
        wa_loaded = [sem(f"wa_loaded{i}") for i in range(2)]
        wb_loaded = [sem(f"wb_loaded{i}") for i in range(2)]
        i_loaded = [sem(f"i_loaded{i}") for i in range(2)]
        gathered = [sem(f"gathered{i}") for i in range(2)]
        stored = [sem(f"stored{i}") for i in range(2)]
        xp_ready, xT_ready, ap_ready, s1_ready, hh_ready, hp_ready, hT_ready, yp_ready, y_low, y_high = (
            sem(n) for n in ("xp_ready", "xT_ready", "ap_ready", "s1_ready", "hh_ready", "hp_ready", "hT_ready", "yp_ready", "y_low", "y_high"))
        wait_held = sem("wait_held")
        ident = C[:, CONST["ident"]:CONST["ident"] + P]
        N = NBLK // 2
        block = ctx.enter_context(nc.Block(no_gpsimd_drain=True))

        @block.sync
        def _(sp):
            def body(i, first, last):
                for u in range(2):
                    b = 2 * i + u
                    e = sp.value_load(blk_expert[0:1, bass.ds(b, 1)], min_val=0, max_val=N_EXP - 1)
                    if not first:
                        sp.wait_ge(ap_ready, 2 * i + (u - 1))
                    sp.dma_start(wa[:, u, :], w13[bass.ds(e * P, P), :]).then_inc(wa_loaded[u], 16)
                    if not first:
                        sp.wait_ge(yp_ready, 2 * i + (u - 1))
                    sp.dma_start(wb[:, u, :], ew2[bass.ds(e * P, P), :]).then_inc(wb_loaded[u], 16)

            run_loop(sp, N, body)

        @block.gpsimd
        def _(pool):
            def fetch(b, i, u, first):
                if not first:
                    pool.wait_ge(xp_ready, 2 * i + (u - 1))
                pool.dma_start(idx[:, u:u + 1], table[bass.ds(b * P, P), :].bitcast(U32)).then_inc(i_loaded[u], 16)
                pool.wait_ge(i_loaded[u], 16 * i + 16)
                pool.sem_inc(wait_held, 1)
                pool.indirect_dma_start(xb[:, u, :], None, u_tok, bass.IndirectOffsetOnAxis(idx[:, u:u + 1], 0)).then_inc(gathered[u], 16)

            def body(i, first, last):
                for u in range(2):
                    fetch(2 * i + u, i, u, first)

            run_loop(pool, N, body)

        @block.tensor
        def _(pe):
            def turn(i, u):
                pe.wait_ge(gathered[u], 16 * i + 16)
                for k in range(8):
                    mm = pe.transpose(xp[:, k // 4, (k % 4) * P:(k % 4 + 1) * P], xb[:, u, k * P:(k + 1) * P], ident)
                mm.then_inc(xp_ready, 1)

            turn(0, 0)

            def body(i, first, last):
                for u in range(2):
                    b = 2 * i + u
                    pe.wait_ge(xT_ready, 4 * i + 2 * u + 2)
                    pe.wait_ge(wa_loaded[u], 16 * i + 16)
                    if not first:
                        pe.wait_ge(hh_ready, 2 * i + (u - 1))
                    for k in range(8):
                        mm = pe.matmul(ap_[:, u, :], xT[:, u, k * P:(k + 1) * P], wa[:, u, k * 512:(k + 1) * 512], start=k == 0, stop=k == 7)
                    mm.then_inc(ap_ready, 1)
                    if u == 0:
                        turn(i, 1)
                    elif not last:
                        turn(i + 1, 0)
                    pe.wait_ge(hh_ready, b + 1)
                    if not (first and u == 0):
                        pe.wait_ge(hT_ready, b)
                    for k in range(2):
                        mm = pe.transpose(hp[:, k * P:(k + 1) * P], hh[:, u, k * P:(k + 1) * P], ident)
                    mm.then_inc(hp_ready, 1)
                    pe.wait_ge(hT_ready, b + 1)
                    pe.wait_ge(wb_loaded[u], 16 * i + 16)
                    if not (first and u == 0):
                        pe.wait_ge(y_low, b)
                        pe.wait_ge(y_high, b)
                    for n in range(2):
                        for k in range(2):
                            mm = pe.matmul(yp[:, n, :], hT[:, u, k * P:(k + 1) * P], wb[:, u, k * DM + n * 512:k * DM + (n + 1) * 512],
                                           start=k == 0, stop=k == 1)
                    mm.then_inc(yp_ready, 1)

            run_loop(pe, N, body)

        @block.scalar
        def _(act):
            def x_copy(i, u, first):
                act.wait_ge(xp_ready, 2 * i + u + 1)
                if not first:
                    act.wait_ge(ap_ready, 2 * i + (u - 1))
                for n in range(2):
                    nc.scalar.copy(xT[:, u, n * 512:(n + 1) * 512], xp[:, n, :]).then_inc(xT_ready, 1)

            x_copy(0, 0, True)

            def body(i, first, last):
                for u in range(2):
                    b = 2 * i + u
                    if u == 0:
                        x_copy(i, 1, first)
                    elif not last:
                        x_copy(i + 1, 0, False)
                    act.wait_ge(ap_ready, b + 1)
                    if not first:
                        act.wait_ge(hh_ready, 2 * i + (u - 1))
                    nc.scalar.activation(s1[:, u, :], ap_[:, u, 0:FE], ACT.Silu).then_inc(s1_ready, 1)
                    act.wait_ge(yp_ready, b + 1)
                    if not first:
                        act.wait_ge(stored[u], 16 * i)
                    nc.scalar.copy(yb[:, u, 0:512], yp[:, 0, :]).then_inc(y_low, 1)
                    act.wait_ge(y_low, b + 1)
                    act.wait_ge(y_high, b + 1)
                    act.dma_start(y_pad[bass.ds(b * P, P), :], yb[:, u, :]).then_inc(stored[u], 16)

            run_loop(act, N, body)
            for u in range(2):
                act.wait_ge(stored[u], 16 * N)

        @block.vector
        def _(dve):
            def body(i, first, last):
                for u in range(2):
                    b = 2 * i + u
                    dve.wait_ge(s1_ready, b + 1)
                    if not first:
                        dve.wait_ge(hp_ready, 2 * i + (u - 1))
                    nc.vector.tensor_tensor(hh[:, u, :], ap_[:, u, FE:2 * FE], s1[:, u, :], ALU.mult).then_inc(hh_ready, 1)
                    dve.wait_ge(hp_ready, b + 1)
                    if not first:
                        dve.wait_ge(yp_ready, 2 * i + (u - 1))
                    nc.vector.tensor_copy(hT[:, u, :], hp[:, 0:FE]).then_inc(hT_ready, 1)
                    dve.wait_ge(yp_ready, b + 1)
                    if not first:
                        dve.wait_ge(stored[u], 16 * i)
                    nc.vector.tensor_copy(yb[:, u, 512:], yp[:, 1, :]).then_inc(y_high, 1)

            run_loop(dve, N, body)


def combine_stage(nc, resid, y_pad, out, dest, gates, C):
    with ExitStack() as ctx:
        sb = lambda n, s, d=F32: ctx.enter_context(nc.sbuf_tensor(f"co_{n}", s, d))
        sem = stage_semaphores(nc, ctx, "co")
        x = sb("x", [P, DT, SEQ])
        y1, y2, acc, o = sb("y1", [P, 2, DM]), sb("y2", [P, 2, DM]), sb("acc", [P, 2, DM]), sb("o", [P, 2, DM])
        tr = ctx.enter_context(nc.psum_tensor("co_tr", [P, 4, 512], F32))
        loaded, tr_ready, acc_ready, o_ready = (sem(n) for n in ("loaded", "tr_ready", "acc_ready", "o_ready"))
        gathered = [sem(f"gathered{i}") for i in range(2)]
        stored = [sem(f"stored{i}") for i in range(2)]
        block = ctx.enter_context(nc.Block(no_gpsimd_drain=True))

        @block.sync
        def _(sp):
            for k in range(DT):
                sp.dma_start(x[:, k, :], resid[k]).then_inc(loaded, 16)
            for t in range(DT):
                sp.wait_ge(o_ready, t + 1)
                sp.dma_start(out[t * P:(t + 1) * P, :], o[:, t % 2, :]).then_inc(stored[t % 2], 16)
            for u in range(2):
                sp.wait_ge(stored[u], 16 * DT // 2)

        @block.gpsimd
        def _(pool):
            for t in range(DT):
                u = t % 2
                if t >= 2:
                    pool.wait_ge(o_ready, t - 1)
                for j, y in enumerate((y1, y2)):
                    pool.indirect_dma_start(y[:, u, :], None, y_pad, bass.IndirectOffsetOnAxis(dest[:, j, t:t + 1], 0)).then_inc(gathered[u], 16)

        @block.tensor
        def _(pe):
            pe.wait_ge(loaded, 16 * DT)
            for t in range(DT):
                u = t % 2
                if t >= 2:
                    pe.wait_ge(acc_ready, t - 1)
                for k in range(DT):
                    mm = pe.transpose(tr[:, 2 * u + k // 4, (k % 4) * P:(k % 4 + 1) * P], x[:, k, t * P:(t + 1) * P],
                                      C[:, CONST["ident"]:CONST["ident"] + P])
                mm.then_inc(tr_ready, 1)

        @block.vector
        def _(dve):
            for t in range(DT):
                u = t % 2
                dve.wait_ge(gathered[u], 32 * (t // 2 + 1))
                dve.wait_ge(tr_ready, t + 1)
                if t >= 2:
                    dve.wait_ge(o_ready, t - 1)
                nc.vector.scalar_tensor_tensor(out=acc[:, u, :], in0=y1[:, u, :], scalar=gates[:, 0, t:t + 1],
                                               in1=tr[:, 2 * u:2 * u + 2, :].rearrange("p a b -> p (a b)"), op0=ALU.mult, op1=ALU.add).then_inc(acc_ready, 1)
                dve.wait_ge(acc_ready, t + 1)
                if t >= 2:
                    dve.wait_ge(stored[u], 16 * (t // 2))
                nc.vector.scalar_tensor_tensor(out=o[:, u, :], in0=y2[:, u, :], scalar=gates[:, 1, t:t + 1],
                                               in1=acc[:, u, :], op0=ALU.mult, op1=ALU.add).then_inc(o_ready, 1)
def program(nc, a, out):
    scratch = lambda name, *shape, d=F32: nc.dram_tensor(f"s_{name}", shape, d, kind="Internal").ap()
    proj = scratch("proj", 28, P, SEQ)
    cat = scratch("cat", 8, P, SEQ)
    scr = {n: scratch(n, *s) for n, s in (("ar", (4, P, 2 * SEQ)), ("bt", (4, P, SEQ)), ("kt", (4, P, SEQ)), ("v", (4, P, SEQ)),
                                          ("bonus", (4, P, SEQ)), ("g", (4, P, SEQ)), ("scale", (4, P, NCH)), ("y", (4, P, SEQ)))}
    x1, x2, h0, h1 = (scratch(n, DT, P, SEQ) for n in ("x1", "x2", "h0", "h1"))
    ffn = scratch("ffn", 22, P, SEQ)
    proj2 = scratch("proj2", 38, P, SEQ)
    hg, br_a, merged, att = (scratch(n, DT, P, SEQ) for n in ("hg", "br_a", "merged", "att"))
    qT, kvT = scratch("qT", 16, P, SEQ), scratch("kvT", 16, P, SEQ)
    u_tok, y_pad = scratch("u_tok", SEQ, DM), scratch("y_pad", NBLK * P, DM)
    table = scratch("table", NBLK * P, 1, d=I32)
    with ExitStack() as ctx:
        V = ctx.enter_context(nc.sbuf_tensor("vecs_sb", [P, NVEC], F32))
        C = ctx.enter_context(nc.sbuf_tensor("consts_sb", [P, NCONST], F32))
        s = ctx.enter_context(nc.semaphore("params_loaded"))
        with nc.Block(no_gpsimd_drain=True) as block:
            @block.sync
            def _(sp):
                sp.dma_start(V[:], a["vecs"]).then_inc(s, 16)
                sp.dma_start(C[:], a["consts"]).then_inc(s, 16)
                sp.wait_ge(s, 32)
        vecs = {"buf": V, "ffn_conv": VEC["ffn_conv"], "ffn_conv_b": VEC["ffn_conv_b"]}
        consts = {"buf": C, "ones": C[:, CONST["ones"]:CONST["ones"] + P]}
        eps = CONST["eps6"]

        def dense(name, src, KT, w, NT, out_, **kw):
            dense_stage(nc, name, src, KT, a[w], NT, out_, vecs, consts, **kw)

        dense("in1", a["xT"], 8, "w_in", 28, proj, norm=(VEC["norm1"], eps, DM))
        mlstm_stage(nc, proj, cat[4:8], V, C)
        rwkv_prepare_stage(nc, proj, a["lora"], a["w_up_g"], scr, V, C)
        rwkv_scan_stage(nc, scr, a["masks"], C)
        rwkv_finish_stage(nc, scr, cat[0:4], V, C)
        dense("out1", cat, 8, "w_out", 8, x1, mode="residual", aux=a["xT"])
        dense("up", x1, 8, "w_up", 44, ffn, norm=(VEC["norm2"], eps, DM), mode="ffn")
        dense("down", ffn, 22, "w_down", 8, x2, mode="residual", aux=x1, tokens=HALF)
        norm_stage(nc, x2, h0, VEC["norm_f"], eps, V, C)
        dense("in2", h0, 8, "w_in2", 38, proj2, norm=(VEC["norm1_2"], eps, DM))
        lru_stage(nc, proj2, a["lru_w"], hg, V, C)
        dense("uq", proj2[16:18], 2, "w_uq", 16, qT, norm=(VEC["q_norm"], eps, 256))
        dense("ukv", proj2[18:20], 2, "w_ukv", 16, kvT, norm=(VEC["kv_norm"], eps, 256))
        attention_stage(nc, proj2, qT, kvT, a["positions"], att, V, C)
        dense("rnn_o", hg, 8, "w_rnn_o", 8, br_a, mode="gate", aux=proj2[22:30])
        dense("mla_o", att, 8, "w_mla_o", 8, merged, mode="gate_add", aux=proj2[30:38], aux2=br_a)
        dense("out2", merged, 8, "w_out2", 8, h1, mode="residual", aux=h0)
        dest = ctx.enter_context(nc.sbuf_tensor("dest", [P, 2, DT], U32))
        gates = ctx.enter_context(nc.sbuf_tensor("gates", [P, 2, DT], F32))
        blk_expert = ctx.enter_context(nc.sbuf_tensor("blk_expert", [1, P], I32))
        router_stage(nc, h1, a["router"], a["router_b"], u_tok, table, dest, gates, blk_expert, V, C)
        expert_stage(nc, u_tok, table, a["w13"], a["ew2"], y_pad, blk_expert, C)
        combine_stage(nc, h1, y_pad, out, dest, gates, C)


def kernel(**inputs):
    import concourse.bacc as bacc
    from concourse.bass_utils import run_bass_kernel_spmd

    nc = bacc.Bacc("TRN2", target_bir_lowering=False, num_devices=1)
    arrays = {f"in_{k}": v for k, v in lay_out(inputs).items()}
    aps = {k[3:]: nc.dram_tensor(k, v.shape, mybir.dt.from_np(v.dtype), kind="ExternalInput").ap() for k, v in arrays.items()}
    out = nc.dram_tensor("out", (SEQ, DM), F32, kind="ExternalOutput").ap()
    program(nc, aps, out)
    r = run_bass_kernel_spmd(nc, [arrays], core_ids=[0])
    return r.results[0]["out"].reshape(1, SEQ, DM)
```

```python
from contextlib import ExitStack

import numpy as np

import concourse.bass as bass
from concourse import mybir

F32 = mybir.dt.float32
F32R = mybir.dt.float32r
I32 = mybir.dt.int32
U32 = mybir.dt.uint32
ALU = mybir.AluOpType
ACT = mybir.ActivationFunctionType
AX = mybir.AxisListType

P = 128
SEQ = 1024
HALF = 512
DM = 1024
DT = DM // P


def stage_semaphores(nc, ctx, prefix):
    held = []

    def give_back():
        nc.clear_and_free_semaphores(held)
        nc.all_engine_barrier()

    ctx.callback(give_back)

    def sem(name):
        held.append(nc.alloc_semaphore(f"{prefix}_{name}"))
        return held[-1]

    return sem


def run_loop(eng, n, body):
    body(0, True, n == 1)
    if n > 2:
        with eng.Fori(1, n - 1) as i:
            body(i, False, False)
    if n > 1:
        body(n - 1, False, True)


def split_matmuls(pe, out, w_hi, w_lo, x_hi, x_lo, first, last):
    pe.matmul(out, w_hi, x_hi, start=first, stop=False)
    pe.matmul(out, w_hi, x_lo, start=False, stop=False)
    return pe.matmul(out, w_lo, x_hi, start=False, stop=last)


def dense_stage(nc, name, src, KT, w, NT, out, vecs, consts, tokens=SEQ, norm=None, mode="copy",
                aux=None, aux2=None, norm_out=None):
    PASSES = SEQ // tokens
    NH = tokens // HALF
    N = NT // 2
    with ExitStack() as ctx:
        sb = lambda n, s, d=F32: ctx.enter_context(nc.sbuf_tensor(f"{name}_{n}", s, d))
        psum = lambda n, s: ctx.enter_context(nc.psum_tensor(f"{name}_{n}", s, F32))
        sem = stage_semaphores(nc, ctx, name)
        x_hi = sb("x_hi", [P, KT, tokens], F32R)
        x_lo = sb("x_lo", [P, KT, tokens], F32R)
        w_raw = sb("w_raw", [P, 2, KT * P])
        w_hi = sb("w_hi", [P, 2, KT * P], F32R)
        w_lo = sb("w_lo", [P, 2, KT * P], F32R)
        XS = KT if norm else 2
        x_raw = sb("x_raw", [P, XS, tokens])
        o_buf = sb("o_buf", [P, 2, tokens])
        acc = psum("acc", [P, 4, HALF])
        x_loaded = [sem(f"x_loaded{i}") for i in range(XS)]
        w_loaded = [sem(f"w_loaded{i}") for i in range(2)]
        x_split = sem("x_split")
        x_hi_done = sem("x_hi_done")
        w_hi_done = sem("w_hi_done")
        w_lo_done = sem("w_lo_done")
        acc_ready = sem("acc_ready")
        acc_free = sem("acc_free")
        out_ready = sem("out_ready")
        stored = [sem(f"stored{i}") for i in range(2)]
        if norm:
            gain, eps_col, width = norm
            sq = sb("sq", [P, 2, tokens])
            rstd = sb("rstd", [P, tokens])
            rms = sb("rms", [P, tokens])
            ss = psum("ss", [P, 2, HALF])
            sq_ready = sem("sq_ready")
            ss_ready = sem("ss_ready")
            rms_ready = sem("rms_ready")
            rstd_ready = sem("rstd_ready")
            h_ready = sem("h_ready")
        if aux is not None:
            aux_buf = sb("aux", [P, 2, tokens])
            aux_loaded = [sem(f"aux_loaded{i}") for i in range(2)]
            if mode.startswith("gate"):
                sig = sb("sig", [P, 2, tokens])
                sig_ready = sem("sig_ready")
                prod_done = sem("prod_done")
        if aux2 is not None:
            aux2_buf = sb("aux2", [P, 2, tokens])
        if mode == "ffn":
            cw, cb = vecs["ffn_conv"], vecs["ffn_conv_b"]
            a_pad = sb("a_pad", [P, tokens + 2])
            conv = sb("conv", [P, 2, tokens])
            act = sb("act", [P, tokens])
            pad_zero = sem("pad_zero")
            conv_step = sem("conv_step")
            act_ready = sem("act_ready")
            a_copied = sem("a_copied")
        V = vecs["buf"]
        NO = N if mode == "ffn" else NT
        block = ctx.enter_context(nc.Block(no_gpsimd_drain=True))

        @block.sync
        def _(sp):
            for p in range(PASSES):
                tok = slice(p * tokens, (p + 1) * tokens)
                for u in range(2):
                    if p:
                        sp.wait_ge(w_lo_done, p * NT - 1 + u)
                    sp.dma_start(w_raw[:, u, :], w[u]).then_inc(w_loaded[u], 16)
                for k in range(KT):
                    if not norm and p * KT + k >= 2:
                        sp.wait_ge(x_split, p * KT + k - 1)
                    sp.dma_start(x_raw[:, k if norm else k % 2, :], src[k][:, tok]).then_inc(x_loaded[k % XS], 16)
                if N > 1:
                    with sp.Fori(1, N) as i:
                        for u in range(2):
                            sp.wait_ge(w_lo_done, 2 * i + (p * NT + u - 1))
                            sp.dma_start(w_raw[:, u, :], w[2 * i + u]).then_inc(w_loaded[u], 16)

        @block.scalar
        def _(act_e):
            if norm:
                for k in range(KT):
                    act_e.wait_ge(x_loaded[k], 16)
                    if k >= 2:
                        act_e.wait_ge(ss_ready, k - 1)
                    nc.scalar.activation(sq[:, k % 2, :], x_raw[:, k, :], ACT.Square).then_inc(sq_ready, 1)
                act_e.wait_ge(ss_ready, KT)
                nc.scalar.activation(rms[:, :], ss[:, :, :].rearrange("p a b -> p (a b)"), ACT.Sqrt,
                                     bias=consts["buf"][:, eps_col:eps_col + 1], scale=1.0 / width).then_inc(rms_ready, 1)
            for p in range(PASSES):
                for k in range(KT):
                    if norm:
                        act_e.wait_ge(h_ready, k + 1)
                    else:
                        act_e.wait_ge(x_loaded[k % 2], 16 * (p * (KT // 2) + k // 2 + 1))
                        if p and k == 0:
                            act_e.wait_ge(acc_ready, p * NT * NH)
                    nc.scalar.copy(x_hi[:, k, :], x_raw[:, k if norm else k % 2, :]).then_inc(x_hi_done, 1)

                def body(i, first, last, p=p):
                    for u in range(2):
                        act_e.wait_ge(w_loaded[u], 16 * i + 16 * (p * N + 1))
                        if not first:
                            act_e.wait_ge(acc_ready, (2 * NH) * i + (p * NT + u - 1) * NH)
                        nc.scalar.copy(w_hi[:, u, :], w_raw[:, u, :]).then_inc(w_hi_done, 1)
                        if mode.startswith("gate"):
                            act_e.wait_ge(aux_loaded[u], (32 if aux2 is not None else 16) * i + (32 if aux2 is not None else 16))
                            if not first:
                                act_e.wait_ge(prod_done, 2 * i + u - 1)
                            nc.scalar.activation(sig[:, u, :], aux_buf[:, u, :], ACT.Sigmoid).then_inc(sig_ready, 1)
                    if mode == "ffn":
                        act_e.wait_ge(conv_step, 3 * i + 3)
                        if not first:
                            act_e.wait_ge(out_ready, i)
                        nc.scalar.activation(act[:, :], conv[:, 0, :], ACT.Silu).then_inc(act_ready, 1)

                run_loop(act_e, N, body)

        @block.tensor
        def _(pe):
            if norm:
                for k in range(KT):
                    pe.wait_ge(sq_ready, k + 1)
                    for h in range(NH):
                        mm = pe.matmul(ss[:, h, :], consts["ones"], sq[:, k % 2, h * HALF:(h + 1) * HALF],
                                       start=k == 0, stop=k == KT - 1)
                    mm.then_inc(ss_ready, 1)
            for p in range(PASSES):
                pe.wait_ge(x_split, (p + 1) * KT)

                def body(i, first, last, p=p):
                    for u in range(2):
                        pe.wait_ge(w_lo_done, 2 * i + (p * NT + u + 1))
                        for h in range(NH):
                            if not (first and p == 0):
                                pe.wait_ge(acc_free, (2 * NH) * i + (p * NT + u - 2) * NH + h + 1)
                            for k in range(KT):
                                ks = slice(k * P, (k + 1) * P)
                                hs = slice(h * HALF, (h + 1) * HALF)
                                mm = split_matmuls(pe, acc[:, u * NH + h, :], w_hi[:, u, ks], w_lo[:, u, ks],
                                                   x_hi[:, k, hs], x_lo[:, k, hs], k == 0, k == KT - 1)
                            mm.then_inc(acc_ready, 1)

                run_loop(pe, N, body)

        @block.vector
        def _(dve):
            if norm:
                dve.wait_ge(rms_ready, 1)
                nc.vector.reciprocal(rstd[:, :], rms[:, :]).then_inc(rstd_ready, 1)
                dve.wait_ge(rstd_ready, 1)
                for k in range(KT):
                    nc.vector.scalar_tensor_tensor(out=x_raw[:, k, :], in0=x_raw[:, k, :], scalar=V[:, gain + k:gain + k + 1],
                                                   in1=rstd[:, :], op0=ALU.mult, op1=ALU.mult).then_inc(h_ready, 1)
            if mode == "ffn":
                nc.vector.memset(a_pad[:, 0:2], 0.0).then_inc(pad_zero, 1)
                dve.wait_ge(pad_zero, 1)

            def low_part(t_u, t_count):
                dve.wait_ge(w_hi_done, t_count)
                nc.vector.tensor_tensor(w_lo[:, t_u, :], w_raw[:, t_u, :], w_hi[:, t_u, :], ALU.subtract).then_inc(w_lo_done, 1)

            for p in range(PASSES):
                for k in range(KT):
                    dve.wait_ge(x_hi_done, p * KT + k + 1)
                    nc.vector.tensor_tensor(x_lo[:, k, :], x_raw[:, k if norm else k % 2, :], x_hi[:, k, :],
                                            ALU.subtract).then_inc(x_split, 1)
                low_part(0, p * NT + 1)

                def body(i, first, last, p=p):
                    for u in range(2):
                        if not (last and u == 1):
                            low_part(1 - u, 2 * i + (p * NT + u + 2))
                        if mode == "ffn":
                            ffn_part(i, u, first)
                            continue
                        if not (first and p == 0):
                            dve.wait_ge(stored[u], 16 * i + 16 * p * N)
                        if aux is not None and not mode.startswith("gate"):
                            dve.wait_ge(aux_loaded[u], 16 * i + 16 * (p * N + 1))
                        if mode.startswith("gate"):
                            dve.wait_ge(sig_ready, 2 * i + u + 1)
                        for h in range(NH):
                            hs = slice(h * HALF, (h + 1) * HALF)
                            dve.wait_ge(acc_ready, (2 * NH) * i + (p * NT + u) * NH + h + 1)
                            a = acc[:, u * NH + h, :]
                            if mode == "copy":
                                ins = nc.vector.tensor_copy(o_buf[:, u, hs], a)
                            elif mode == "residual":
                                ins = nc.vector.tensor_tensor(o_buf[:, u, hs], a, aux_buf[:, u, hs], ALU.add)
                            else:
                                ins = nc.vector.tensor_tensor(o_buf[:, u, hs], a, sig[:, u, hs], ALU.mult)
                            ins.then_inc(acc_free, 1)
                        if mode == "gate_add":
                            dve.wait_ge(acc_free, (2 * NH) * i + (u + 1) * NH)
                            nc.vector.tensor_tensor(o_buf[:, u, :], o_buf[:, u, :], aux2_buf[:, u, :],
                                                    ALU.add).then_inc(prod_done, 1)
                        elif mode == "gate":
                            dve.wait_ge(acc_free, (2 * NH) * i + (u + 1) * NH)
                            dve.sem_inc(prod_done, 1)

                def ffn_part(i, u, first):
                    if u == 0:
                        for h in range(NH):
                            dve.wait_ge(acc_ready, (2 * NH) * i + h + 1)
                            nc.vector.tensor_copy(a_pad[:, 2 + h * HALF:2 + (h + 1) * HALF], acc[:, h, :]).then_inc(acc_free, 1)
                        dve.wait_ge(acc_free, (2 * NH) * i + NH)
                        nc.vector.tensor_scalar(conv[:, 0, :], a_pad[:, 2:2 + tokens], V[:, bass.ds(cw + 2 * N + i, 1)],
                                                V[:, bass.ds(cb + i, 1)], ALU.mult, ALU.add).then_inc(conv_step, 1)
                        dve.wait_ge(conv_step, 3 * i + 1)
                        nc.vector.scalar_tensor_tensor(out=conv[:, 1, :], in0=a_pad[:, 1:1 + tokens],
                                                       scalar=V[:, bass.ds(cw + N + i, 1)], in1=conv[:, 0, :],
                                                       op0=ALU.mult, op1=ALU.add).then_inc(conv_step, 1)
                        dve.wait_ge(conv_step, 3 * i + 2)
                        nc.vector.scalar_tensor_tensor(out=conv[:, 0, :], in0=a_pad[:, 0:tokens],
                                                       scalar=V[:, bass.ds(cw + i, 1)], in1=conv[:, 1, :],
                                                       op0=ALU.mult, op1=ALU.add).then_inc(conv_step, 1)
                    else:
                        dve.wait_ge(act_ready, i + 1)
                        if not first:
                            dve.wait_ge(stored[0], 16 * i)
                        for h in range(NH):
                            hs = slice(h * HALF, (h + 1) * HALF)
                            dve.wait_ge(acc_ready, (2 * NH) * i + NH + h + 1)
                            nc.vector.tensor_tensor(o_buf[:, 0, hs], acc[:, NH + h, :], act[:, hs],
                                                    ALU.mult).then_inc(acc_free, 1)
                        dve.wait_ge(acc_free, (2 * NH) * i + 2 * NH)
                        dve.sem_inc(out_ready, 1)

                run_loop(dve, N, body)

        @block.gpsimd
        def _(pool):
            for p in range(PASSES):
                tok = slice(p * tokens, (p + 1) * tokens)

                def load_aux(i, u, p=p, tok=tok):
                    pool.dma_start(aux_buf[:, u, :], aux[2 * i + u][:, tok]).then_inc(aux_loaded[u], 16)
                    if aux2 is not None:
                        pool.dma_start(aux2_buf[:, u, :], aux2[2 * i + u][:, tok]).then_inc(aux_loaded[u], 16)

                if aux is not None:
                    for u in range(2):
                        if p:
                            pool.wait_ge(acc_free, (p * NT - 1 + u) * NH)
                        load_aux(0, u)

                def body(i, first, last, p=p, tok=tok, load_aux=load_aux):
                    if mode == "ffn":
                        pool.wait_ge(out_ready, i + 1)
                        pool.dma_start(out[i][:, tok], o_buf[:, 0, :]).then_inc(stored[0], 16)
                        return
                    for u in range(2):
                        if mode == "gate_add":
                            pool.wait_ge(prod_done, 2 * i + u + 1)
                        else:
                            pool.wait_ge(acc_free, (2 * NH) * i + (p * NT + u + 1) * NH)
                        pool.dma_start(out[2 * i + u][:, tok], o_buf[:, u, :]).then_inc(stored[u], 16)
                        if aux is not None and not last:
                            load_aux(i + 1, u)

                run_loop(pool, N, body)
            for u in range(1 if mode == "ffn" else 2):
                pool.wait_ge(stored[u], 16 * N * PASSES)
def _cols(v):
    return np.reshape(v, (-1, P)).T


def _tiles(w):
    K, N = w.shape
    return np.ascontiguousarray(np.transpose(np.reshape(w, (K // P, P, N // P, P)), (2, 1, 0, 3))).reshape(N // P, P, K)


def _vec_table():
    at, table = 0, {}
    for name, n in (("norm1", 8), ("mu", 14), ("w0", 4), ("a0", 4), ("k_k", 4), ("k_a", 4), ("r_k", 4), ("lnx_w", 4),
                    ("lnx_b", 4), ("qk_conv", 16), ("qk_conv_b", 4), ("i_bias", 1), ("f_bias", 1), ("mh_g", 4),
                    ("norm2", 8), ("ffn_conv", 66), ("ffn_conv_b", 22), ("norm_f", 8), ("norm1_2", 8), ("conv_2", 32),
                    ("conv_b_2", 8), ("lru_ba", 8), ("lru_bx", 8), ("lru_lam", 8), ("q_norm", 2), ("kv_norm", 2),
                    ("qg_n", 1), ("qg_r", 1), ("qg_s", 1), ("kg_n", 1), ("kg_r", 1), ("kg_s", 1), ("norm2_2", 8)):
        table[name] = at
        at += n
    return table, at


VEC, NVEC = _vec_table()


def _const_table():
    at, table = 0, {}
    for name, n in (("ones", P), ("ident", P), ("head_ones", P), ("before", P), ("upto", P), ("after", P), ("row_sel", 4 * P),
                    ("eps6", 1), ("eps_ln", 1), ("inv_freq", 1), ("rope_sign", 1), ("one", 1), ("iota64", 64), ("iota8", 8),
                    ("block_start", 1)):
        table[name] = at
        at += n
    return table, at


CONST, NCONST = _const_table()
LEVELS = 7


def constants():
    c = np.zeros((P, NCONST), np.float32)
    r, q = np.arange(P)[:, None], np.arange(P)[None, :]
    put = lambda name, a: c.__setitem__((slice(None), slice(CONST[name], CONST[name] + a.shape[1])), a)
    put("ones", np.ones((P, P)))
    put("ident", r == q)
    put("head_ones", r // 64 == q // 64)
    put("before", r < q)
    put("upto", r <= q)
    put("after", r > q)
    put("row_sel", np.concatenate([np.repeat(r == h, P, 1) for h in range(4)], 1))
    put("eps6", np.full((P, 1), 1e-6))
    put("eps_ln", np.full((P, 1), 64e-5))
    inv = (np.float32(10000.0) ** (-(np.arange(0, 64, 2, dtype=np.float32)) / np.float32(64))).astype(np.float32)
    put("inv_freq", np.tile(inv, 4)[:, None])
    put("rope_sign", np.where(r % 64 < 32, -1.0, 1.0))
    put("one", np.ones((P, 1)))
    put("iota64", np.tile(np.arange(64.0), (P, 1)))
    put("iota8", np.tile(np.arange(8.0), (P, 1)))
    put("block_start", r * 64.0)
    lv = []
    for l in range(LEVELS):
        b = 1 << l
        lv.append((r // (2 * b) == q // (2 * b)) & (r // b > q // b))
    masks = np.concatenate(lv + [m.T for m in lv], 1).astype(np.float32)
    return c, masks


def lay_out(a):
    v = np.zeros((P, NVEC), np.float32)

    def put(name, cols):
        v[:, VEC[name]:VEC[name] + cols.shape[1]] = cols

    L = {k: np.asarray(x)[0] for k, x in a.items() if k not in ("x", "norm_f_g", "positions_2")}
    for name, key in (("norm1", "norm1_g"), ("mu", "rw_mu"), ("w0", "w0"), ("a0", "a0"), ("k_k", "k_k"), ("k_a", "k_a"),
                      ("r_k", "r_k"), ("lnx_w", "lnx_w"), ("lnx_b", "lnx_b"), ("qk_conv", "qk_conv_w"),
                      ("qk_conv_b", "qk_conv_b"), ("mh_g", "mh_norm_g"), ("norm2", "norm2_g"), ("ffn_conv", "ffn_conv_w"),
                      ("ffn_conv_b", "ffn_conv_b"), ("norm1_2", "norm1_g_2"), ("conv_2", "conv_w_2"),
                      ("conv_b_2", "conv_b_2"), ("lru_ba", "lru_ba_2"), ("lru_bx", "lru_bx_2"), ("lru_lam", "lru_lambda_2"),
                      ("q_norm", "q_norm_g_2"), ("kv_norm", "kv_norm_g_2"), ("norm2_2", "norm2_g_2")):
        put(name, _cols(L[key]))
    put("norm_f", _cols(np.asarray(a["norm_f_g"])))
    v[0:4, VEC["i_bias"]] = L["i_bias"]
    v[0:4, VEC["f_bias"]] = L["f_bias"]
    swap = np.concatenate([np.arange(32, 64), np.arange(0, 32)])
    for c, key in (("qg", "qk_norm_q_g_2"), ("kg", "qk_norm_k_g_2")):
        v[:, VEC[c + "_n"]] = L[key][:128]
        v[:, VEC[c + "_r"]] = np.concatenate([L[key][128:]] * 2)
        v[:, VEC[c + "_s"]] = np.concatenate([L[key][128:][swap]] * 2)
    z = lambda n: np.zeros((DM, n), np.float32)
    w_in = L["w_in"]
    gates = np.concatenate([w_in[:, 3328:3332], z(28), w_in[:, 3332:3336], z(92)], 1)
    w_in_t = _tiles(np.concatenate([w_in[:, :3328], gates, z(128)], 1))
    up = L["w_ffn_up"]
    up = np.transpose(np.reshape(up, (DM, 2, 22, P)), (0, 2, 1, 3)).reshape(DM, 44 * P)
    w2 = L["w_in_2"]
    kpe = w2[:, 2560:2624]
    w_in2_t = _tiles(np.concatenate([w2[:, :2560], kpe, kpe, kpe[:, swap], kpe[:, swap], w2[:, 2624:]], 1))
    uq = np.reshape(L["w_uq_2"], (256, 8, 192))
    uq_t = _tiles(np.concatenate([uq[:, :, :128].reshape(256, -1), uq[:, :, 128:].reshape(256, -1),
                                  uq[:, :, 128:][:, :, swap].reshape(256, -1)], 1))
    ukv = np.reshape(L["w_ukv_2"], (256, 8, 2, 128))
    ukv_t = _tiles(np.transpose(ukv, (0, 2, 1, 3)).reshape(256, 2048))
    lora = np.concatenate([L["w_up_decay"], L["w_up_a"]], 0)
    router = np.concatenate([L["router_wg_2"], L["router_we_2"]], 1)
    router = np.transpose(np.reshape(router, (8, P, 72)), (1, 0, 2)).reshape(P, 8 * 72)
    w13 = np.concatenate([L["exp_w1_2"], L["exp_w3_2"]], 2)
    w13 = np.ascontiguousarray(np.transpose(np.reshape(w13, (64, 8, P, 512)), (0, 2, 1, 3))).reshape(64 * P, 4096)
    ew2 = np.ascontiguousarray(np.transpose(np.reshape(L["exp_w2_2"], (64, 2, P, DM)), (0, 2, 1, 3))).reshape(64 * P, 2048)
    lru_w = np.concatenate([np.transpose(L["lru_wa_2"], (1, 0, 2)).reshape(P, DM), np.transpose(L["lru_wx_2"], (1, 0, 2)).reshape(P, DM)], 1)
    consts, masks = constants()
    return {
        "xT": np.ascontiguousarray(np.asarray(a["x"])[0].T).reshape(DT, P, SEQ),
        "vecs": v, "consts": consts, "masks": masks,
        "w_in": w_in_t, "w_out": _tiles(L["w_out"]), "w_up": _tiles(up), "w_down": _tiles(L["w_ffn_down"]),
        "w_in2": w_in2_t, "w_rnn_o": _tiles(L["w_rnn_o_2"]), "w_mla_o": _tiles(L["w_mla_o_2"]), "w_out2": _tiles(L["w_out_2"]),
        "w_uq": uq_t, "w_ukv": ukv_t, "lora": lora, "w_up_g": L["w_up_g"], "router": router,
        "router_b": np.concatenate([L["router_bg_2"], L["router_be_2"]])[None, :],
        "w13": w13, "ew2": ew2, "lru_w": lru_w, "positions": np.asarray(a["positions_2"]),
    }
class Steps:

    def __init__(self, eng, sem):
        self.eng, self.sem, self.n = eng, sem, 0

    def __call__(self, ins):
        ins.then_inc(self.sem, 1)
        self.n += 1
        return self.n

    def settle(self):
        self.eng.wait_ge(self.sem, self.n)

    def link(self, ins):
        self(ins)
        self.settle()


def mlstm_stage(nc, proj, y_out, V, C):
    NH, DK, CAP = 4, 64, 15.0
    q0, v0, o0, gate = 14, 18, 22, 26
    one = lambda name, h=0: C[:, CONST[name] + h:CONST[name] + h + 1]
    with ExitStack() as ctx:
        sb = lambda n, s, d=F32: ctx.enter_context(nc.sbuf_tensor(f"ml_{n}", s, d))
        sem = stage_semaphores(nc, ctx, "ml")
        qk = sb("qk", [P, 4, SEQ])
        v_tok = sb("v_tok", [P, DT, NH * P])
        g_cols = sb("g_cols", [P, DT, NH])
        neg_G = sb("neg_G", [P, NH, SEQ])
        exp_m = sb("exp_m", [P, NH, SEQ])

        with ExitStack() as ctx1:
            sb1 = lambda n, s, d=F32: ctx1.enter_context(nc.sbuf_tensor(f"ml_{n}", s, d))
            pre = sb1("pre", [P, 4, SEQ + 3])
            conv = sb1("conv", [P, 2, 2, SEQ])
            vT = sb1("vT", [P, 4, SEQ])
            ig = sb1("ig", [NH, SEQ])
            fg = sb1("fg", [NH, SEQ])
            row_t = sb1("row_t", [NH, 4, SEQ])
            ones_row = sb1("ones_row", [NH, SEQ])
            cap_b = sb1("cap_b", [NH, 2])
            tr = ctx1.enter_context(nc.psum_tensor("ml_tr", [P, 2, 512], F32))
            bc = ctx1.enter_context(nc.psum_tensor("ml_bc", [P, 4, 512], F32))
            gc = ctx1.enter_context(nc.psum_tensor("ml_gc", [P, 512], F32))
            qk_loaded = [sem(f"qk_loaded{i}") for i in range(4)]
            v_loaded, gates_loaded, pads = sem("v_loaded"), sem("gates_loaded"), sem("pads")
            conv_done, qk_done, dve_steps = sem("conv_done"), sem("qk_done"), sem("dve_steps")
            bias_ready, tanh_ready, exp_ready, ln_ready = sem("bias_ready"), sem("tanh_ready"), sem("exp_ready"), sem("ln_ready")
            rows_ready, tr_ready, tr_free, bc_ready, bc_free = (sem(n) for n in ("rows_ready", "tr_ready", "tr_free", "bc_ready", "bc_free"))
            gc_ready, bc2_free = sem("gc_ready"), sem("bc2_free")
            block = ctx1.enter_context(nc.Block(no_gpsimd_drain=True))

            @block.sync
            def _(sp):
                sp.dma_start(ig[:, :], proj[gate][0:NH, :]).then_inc(gates_loaded, 16)
                sp.dma_start(fg[:, :], proj[gate][32:32 + NH, :]).then_inc(gates_loaded, 16)
                for j in range(4):
                    sp.dma_start(pre[:, j, 3:], proj[q0 + j]).then_inc(qk_loaded[j], 16)
                for j in range(4):
                    sp.dma_start(vT[:, j, :], proj[v0 + j]).then_inc(v_loaded, 16)

            @block.vector
            def _(dve):
                st = Steps(dve, dve_steps)
                nc.vector.memset(pre[:, :, 0:3], 0.0).then_inc(pads, 1)
                nc.vector.memset(ones_row[:, :], 1.0).then_inc(pads, 1)
                nc.vector.tensor_scalar(cap_b[:, :], V[0:NH, VEC["i_bias"]:VEC["i_bias"] + 2], 1.0 / CAP, None,
                                        ALU.mult).then_inc(bias_ready, 1)
                dve.wait_ge(pads, 2)
                dve.wait_ge(ln_ready, 1)
                st.link(nc.vector.tensor_tensor_scan(row_t[:, 3, :], ones_row[:, :], row_t[:, 2, :], 0.0, ALU.mult, ALU.subtract))
                st.link(nc.vector.scalar_tensor_tensor(out=ig[:, :], in0=row_t[:, 0, :], scalar=CAP, in1=row_t[:, 3, :],
                                                       op0=ALU.mult, op1=ALU.subtract))
                st.link(nc.vector.tensor_tensor_scan(row_t[:, 1, :], ones_row[:, :], ig[:, :], 0.0, ALU.mult, ALU.max))
                st.link(nc.vector.tensor_scalar(row_t[:, 0, :], row_t[:, 1, :], -1.0, None, ALU.mult))
                st.link(nc.vector.tensor_tensor(row_t[:, 2, :], row_t[:, 0, :], row_t[:, 3, :], ALU.subtract))
                dve.sem_inc(rows_ready, 1)
                for h in range(NH):
                    for f in range(2):
                        dve.wait_ge(bc_ready, 2 * h + f + 1)
                        nc.vector.tensor_copy(neg_G[:, h, f * 512:(f + 1) * 512], bc[:, f, :]).then_inc(bc_free, 1)
                for j in range(4):
                    dve.wait_ge(qk_loaded[j], 16)
                    if j >= 2:
                        dve.wait_ge(qk_done, j - 1)
                    w = lambda tap: V[:, VEC["qk_conv"] + 4 * tap + j:VEC["qk_conv"] + 4 * tap + j + 1]
                    st.link(nc.vector.tensor_scalar(conv[:, j % 2, 0, :], pre[:, j, 3:3 + SEQ], w(3),
                                                    V[:, VEC["qk_conv_b"] + j:VEC["qk_conv_b"] + j + 1], ALU.mult, ALU.add))
                    for n, tap in enumerate((2, 1, 0)):
                        st.link(nc.vector.scalar_tensor_tensor(out=conv[:, j % 2, (n + 1) % 2, :], in0=pre[:, j, tap:tap + SEQ],
                                                               scalar=w(tap), in1=conv[:, j % 2, n % 2, :],
                                                               op0=ALU.mult, op1=ALU.add))
                    dve.sem_inc(conv_done, 1)
                dve.wait_ge(gc_ready, 1)
                nc.vector.tensor_copy(g_cols[:, :, :].rearrange("p a b -> p (a b)"), gc[:, 0:DT * NH])

            @block.scalar
            def _(act):
                act.wait_ge(gates_loaded, 32)
                act.wait_ge(bias_ready, 1)
                nc.scalar.activation(row_t[:, 0, :], ig[:, :], ACT.Tanh, bias=cap_b[:, 0:1], scale=1.0 / CAP).then_inc(tanh_ready, 1)
                nc.scalar.activation(row_t[:, 1, :], fg[:, :], ACT.Tanh, bias=cap_b[:, 1:2], scale=1.0 / CAP).then_inc(tanh_ready, 1)
                act.wait_ge(tanh_ready, 2)
                nc.scalar.activation(row_t[:, 3, :], row_t[:, 1, :], ACT.Exp, scale=-CAP).then_inc(exp_ready, 1)
                act.wait_ge(exp_ready, 1)
                nc.scalar.activation(row_t[:, 2, :], row_t[:, 3, :], ACT.Ln, bias=one("one")[0:NH], scale=1.0).then_inc(ln_ready, 1)
                for s in range(DT):
                    act.wait_ge(tr_ready, s + 1)
                    nc.scalar.copy(v_tok[:, s, :], tr[:, s % 2, :]).then_inc(tr_free, 1)
                for h in range(NH):
                    for f in range(2):
                        act.wait_ge(bc_ready, 2 * NH + 2 * h + f + 1)
                        nc.scalar.activation(exp_m[:, h, f * 512:(f + 1) * 512], bc[:, 2 + f, :], ACT.Exp).then_inc(bc2_free, 1)
                for j in range(4):
                    act.wait_ge(conv_done, j + 1)
                    nc.scalar.activation(qk[:, j, :], conv[:, j % 2, 1, :], ACT.Silu).then_inc(qk_done, 1)

            @block.tensor
            def _(pe):
                ident = C[:, CONST["ident"]:CONST["ident"] + P]
                pe.wait_ge(v_loaded, 64)
                for s in range(DT):
                    if s >= 2:
                        pe.wait_ge(tr_free, s - 1)
                    for j in range(4):
                        mm = pe.transpose(tr[:, s % 2, j * P:(j + 1) * P], vT[:, j, s * P:(s + 1) * P], ident)
                    mm.then_inc(tr_ready, 1)
                pe.wait_ge(rows_ready, 1)
                for s in range(DT):
                    mm = pe.matmul(gc[:, s * NH:(s + 1) * NH], ig[:, s * P:(s + 1) * P], C[0:NH, CONST["ident"]:CONST["ident"] + NH],
                                   start=True, stop=True)
                mm.then_inc(gc_ready, 1)
                for r in range(2):
                    for h in range(NH):
                        for f in range(2):
                            if h >= 1:
                                pe.wait_ge(bc2_free if r else bc_free, 2 * (h - 1) + f + 1)
                            sel = C[0:NH, CONST["row_sel"] + h * P:CONST["row_sel"] + (h + 1) * P]
                            pe.matmul(bc[:, 2 * r + f, :], sel, row_t[:, 2 * r, f * 512:(f + 1) * 512],
                                      start=True, stop=True).then_inc(bc_ready, 1)

        with ExitStack() as ctx2:
            sb2 = lambda n, s, d=F32: ctx2.enter_context(nc.sbuf_tensor(f"ml_{n}", s, d))
            NR = 3
            arg = sb2("arg", [P, NR, HALF])
            wgt = sb2("wgt", [P, NR, HALF])
            prod = sb2("prod", [P, NR, HALF])
            den = sb2("den", [P, HALF])
            den2 = sb2("den2", [P, HALF])
            h_buf = sb2("h_buf", [P, 2, HALF])
            sq = sb2("sq", [P, HALF])
            o_raw = sb2("o_raw", [P, 2, HALF])
            o_sig = sb2("o_sig", [P, 2, HALF])
            y = sb2("y", [P, 2, HALF])
            rms = sb2("rms", [P, HALF])
            score = ctx2.enter_context(nc.psum_tensor("ml_score", [P, NR, 512], F32))
            num = ctx2.enter_context(nc.psum_tensor("ml_num", [P, 2, 512], F32))
            dsum = ctx2.enter_context(nc.psum_tensor("ml_dsum", [P, 2, 512], F32))
            ss = ctx2.enter_context(nc.psum_tensor("ml_ss", [P, 512], F32))
            arg_ready, exp_done, score_ready, prod_done = (sem(n) for n in ("arg_ready", "exp_done", "score_ready", "prod_done"))
            prod_used, group_ready, group_free, steps2 = (sem(n) for n in ("prod_used", "group_ready", "group_free", "steps2"))
            h_ready, sq_ready, ss_ready, rms_ready, sig_ready, y_ready = (sem(n) for n in ("h_ready", "sq_ready", "ss_ready", "rms_ready", "sig_ready", "y_ready"))
            o_loaded = [sem(f"o_loaded{i}") for i in range(2)]
            stored = [sem(f"stored{i}") for i in range(2)]
            groups = [(h, f) for h in range(NH) for f in range(2)]
            items = [(n, h, f, s) for n, (h, f) in enumerate(groups) for s in range(4 * f + 4)]
            last_item = {n: max(i for i, it in enumerate(items) if it[0] == n) for n in range(len(groups))}
            span = lambda f, s: (max(0, s * P - f * HALF), HALF)
            block = ctx2.enter_context(nc.Block(no_gpsimd_drain=True))

            @block.vector
            def _(dve):
                st = Steps(dve, steps2)

                def weights(i):
                    n, h, f, s = items[i]
                    a, b = span(f, s)
                    if i >= NR:
                        dve.wait_ge(exp_done, i - NR + 1)
                    nc.vector.tensor_scalar(arg[:, i % NR, a:b], neg_G[:, h, f * HALF + a:f * HALF + b], g_cols[:, s, h:h + 1],
                                            0.0, ALU.add, ALU.min).then_inc(arg_ready, 1)

                def finish(n):
                    h, f = groups[n]
                    dve.wait_ge(group_ready, n + 1)
                    st.link(nc.vector.scalar_tensor_tensor(out=den[:, :], in0=dsum[:, n % 2, :], scalar=-1.0, in1=exp_m[:, h, f * HALF:(f + 1) * HALF],
                                                           op0=ALU.mult, op1=ALU.max))
                    st.link(nc.vector.tensor_tensor(den2[:, :], dsum[:, n % 2, :], den[:, :], ALU.max))
                    st.link(nc.vector.reciprocal(den[:, :], den2[:, :]))
                    st.link(nc.vector.tensor_tensor(h_buf[:, n % 2, :], num[:, n % 2, :], den[:, :], ALU.mult))
                    dve.sem_inc(h_ready, 1)
                    dve.wait_ge(rms_ready, n + 1)
                    st.link(nc.vector.reciprocal(den[:, :], rms[:, :]))
                    dve.wait_ge(sig_ready, n + 1)
                    st.link(nc.vector.scalar_tensor_tensor(out=h_buf[:, n % 2, :], in0=h_buf[:, n % 2, :], scalar=V[:, VEC["mh_g"] + h:VEC["mh_g"] + h + 1],
                                                           in1=den[:, :], op0=ALU.mult, op1=ALU.mult))
                    if n >= 2:
                        dve.wait_ge(stored[n % 2], 16 * (n // 2))
                    nc.vector.tensor_tensor(y[:, n % 2, :], h_buf[:, n % 2, :], o_sig[:, n % 2, :], ALU.mult).then_inc(y_ready, 1)

                weights(0)
                weights(1)
                for i, (n, h, f, s) in enumerate(items):
                    if i + 2 < len(items):
                        weights(i + 2)
                    a, b = span(f, s)
                    dve.wait_ge(exp_done, i + 1)
                    dve.wait_ge(score_ready, i + 1)
                    if i >= NR:
                        dve.wait_ge(prod_used, i - NR + 1)
                    st.link(nc.vector.scalar_tensor_tensor(out=prod[:, i % NR, a:b], in0=score[:, i % NR, a:b], scalar=DK ** -0.5,
                                                           in1=wgt[:, i % NR, a:b], op0=ALU.mult, op1=ALU.mult))
                    if s >= 4 * f:
                        st.link(nc.vector.tensor_tensor(prod[:, i % NR, a:a + P], prod[:, i % NR, a:a + P],
                                                        C[:, CONST["upto"]:CONST["upto"] + P], ALU.mult))
                    dve.sem_inc(prod_done, 1)
                    if i == last_item[n]:
                        finish(n)

            @block.scalar
            def _(act):
                def weight_exp(i):
                    n, h, f, s = items[i]
                    a, b = span(f, s)
                    act.wait_ge(arg_ready, i + 1)
                    if i >= NR:
                        act.wait_ge(prod_done, i - NR + 1)
                    nc.scalar.activation(wgt[:, i % NR, a:b], arg[:, i % NR, a:b], ACT.Exp).then_inc(exp_done, 1)

                for i, (n, h, f, s) in enumerate(items):
                    weight_exp(i)
                    if i == last_item[n]:
                        act.wait_ge(o_loaded[n % 2], 16 * (n // 2 + 1))
                        if n >= 2:
                            act.wait_ge(y_ready, n - 1)
                        nc.scalar.activation(o_sig[:, n % 2, :], o_raw[:, n % 2, :], ACT.Sigmoid).then_inc(sig_ready, 1)
                        act.wait_ge(h_ready, n + 1)
                        nc.scalar.activation(sq[:, :], h_buf[:, n % 2, :], ACT.Square).then_inc(sq_ready, 1)
                        act.wait_ge(ss_ready, n + 1)
                        nc.scalar.activation(rms[:, :], ss[:, :], ACT.Sqrt, bias=one("eps6"), scale=1.0 / P).then_inc(rms_ready, 1)

            @block.tensor
            def _(pe):
                def scores(i):
                    n, h, f, s = items[i]
                    a, b = span(f, s)
                    base = 64 * (h % 2)
                    if i >= NR:
                        pe.wait_ge(prod_done, i - NR + 1)
                    pe.matmul(score[:, i % NR, a:b], qk[base:base + DK, 2 + h // 2, s * P:(s + 1) * P],
                              qk[base:base + DK, h // 2, f * HALF + a:f * HALF + b], start=True, stop=True).then_inc(score_ready, 1)

                scores(0)
                scores(1)
                for i, (n, h, f, s) in enumerate(items):
                    if i + 2 < len(items):
                        scores(i + 2)
                    a, b = span(f, s)
                    pe.wait_ge(prod_done, i + 1)
                    if s == 0 and n >= 2:
                        pe.wait_ge(h_ready, n - 1)
                    end = i == last_item[n]
                    pe.matmul(num[:, n % 2, a:b], v_tok[:, s, h * P:(h + 1) * P], prod[:, i % NR, a:b], start=s == 0, stop=end,
                              skip_group_check=True)
                    pe.matmul(dsum[:, n % 2, a:b], C[:, CONST["ones"]:CONST["ones"] + P], prod[:, i % NR, a:b], start=s == 0,
                              stop=end, skip_group_check=True).then_inc(prod_used, 1)
                    if end:
                        pe.wait_ge(prod_used, i + 1)
                        pe.sem_inc(group_ready, 1)
                        pe.wait_ge(sq_ready, n + 1)
                        pe.matmul(ss[:, :], C[:, CONST["ones"]:CONST["ones"] + P], sq[:, :], start=True, stop=True).then_inc(ss_ready, 1)

            @block.sync
            def _(sp):
                for n, (h, f) in enumerate(groups):
                    if n >= 2:
                        sp.wait_ge(sig_ready, n - 1)
                    sp.dma_start(o_raw[:, n % 2, :], proj[o0 + h][:, f * HALF:(f + 1) * HALF]).then_inc(o_loaded[n % 2], 16)

            @block.gpsimd
            def _(pool):
                for n, (h, f) in enumerate(groups):
                    pool.wait_ge(y_ready, n + 1)
                    pool.dma_start(y_out[h][:, f * HALF:(f + 1) * HALF], y[:, n % 2, :]).then_inc(stored[n % 2], 16)
                for u in range(2):
                    pool.wait_ge(stored[u], 16 * len(groups) // 2)
HR, NR_ = 8, 64
CH = P
NCH = SEQ // CH


def rwkv_prepare_stage(nc, proj, lora, w_up_g, scr, V, C):
    RATE = float(np.exp(-0.5))
    r0, k0, v0, wa0, g0 = 0, 4, 8, 12, 13
    col = lambda name, j=0: V[:, VEC[name] + j:VEC[name] + j + 1]
    with ExitStack() as ctx:
        sb = lambda n, s, d=F32: ctx.enter_context(nc.sbuf_tensor(f"rp_{n}", s, d))
        sem = stage_semaphores(nc, ctx, "rp")
        pre = sb("pre", [P, 2, SEQ + 1])
        kept = sb("kept", [P, 2, SEQ])
        one_mu = sb("one_mu", [P, 14])
        one_ka = sb("one_ka", [P, 4])
        wa = sb("wa", [P, SEQ])
        wt = sb("wt", [64, SEQ])
        gl = sb("gl", [P, SEQ])
        lora_w = sb("lora_w", [P, 512])
        upg_w = sb("upg_w", [P, 512])
        rr, kx, vx = sb("rr", [P, SEQ]), sb("kx", [P, SEQ]), sb("vx", [P, SEQ])
        sg, a_, g_sb = sb("sg", [P, SEQ]), sb("a", [P, SEQ]), sb("g", [P, SEQ])
        kk, sq, nrm = sb("kk", [P, SEQ]), sb("sq", [P, SEQ]), sb("nrm", [P, SEQ])
        cum, dif = sb("cum", [P, SEQ]), sb("dif", [P, SEQ])
        e_pos, e_neg, e_prev = sb("e_pos", [P, SEQ]), sb("e_neg", [P, SEQ]), sb("e_prev", [P, SEQ])
        k2, rk = sb("k2", [P, SEQ]), sb("rk", [P, SEQ])
        reset = sb("reset", [P, SEQ])
        ar, bt, kt, bon = sb("ar", [P, NCH, 2, CH]), sb("bt", [P, SEQ]), sb("kt", [P, SEQ]), sb("bon", [P, SEQ])
        s_arg, s_exp = sb("s_arg", [P, NCH]), sb("s_exp", [P, NCH])
        up = ctx.enter_context(nc.psum_tensor("rp_up", [P, 6, 512], F32))
        hs = ctx.enter_context(nc.psum_tensor("rp_hs", [P, 2, 512], F32))
        loaded = [sem(f"loaded{i}") for i in range(2)]
        w_loaded, pads, kept_done, mixed = sem("w_loaded"), sem("pads"), sem("kept_done"), sem("mixed")
        lo_ready, up_ready, act_done, st_sem, kk_sq, hs_ready, nrm_done = (
            sem(n) for n in ("lo_ready", "up_ready", "act_done", "steps", "kk_sq", "hs_ready", "nrm_done"))
        dif_ready, exp_done, rk_ready, out_ready, stored, mu_ready, g_ready = (
            sem(n) for n in ("dif_ready", "exp_done", "rk_ready", "out_ready", "stored", "mu_ready", "g_ready"))
        order = [wa0, g0]
        for m in range(4):
            order += [r0 + m, k0 + m, v0 + m]
        NST = 7
        block = ctx.enter_context(nc.Block(no_gpsimd_drain=True))

        @block.sync
        def _(sp):
            sp.dma_start(lora_w[:, :], lora).then_inc(w_loaded, 16)
            sp.dma_start(upg_w[:, :], w_up_g).then_inc(w_loaded, 16)
            for n, t in enumerate(order):
                if n >= 2:
                    sp.wait_ge(mixed, n - 1)
                sp.dma_start(pre[:, n % 2, 1:], proj[t]).then_inc(loaded[n % 2], 16)

        @block.scalar
        def _(act):
            def keep(n):
                t = order[n]
                act.wait_ge(loaded[n % 2], 16 * (n // 2 + 1))
                if n >= 2:
                    act.wait_ge(mixed, n - 1)
                nc.scalar.activation(kept[:, n % 2, :], pre[:, n % 2, 1:], ACT.Copy, scale=one_mu[:, t:t + 1]).then_inc(kept_done, 1)

            act.wait_ge(mu_ready, 1)
            keep(0)
            keep(1)
            act.wait_ge(mixed, 2)
            nc.scalar.activation(wt[:, :], wa[0:64, :], ACT.Tanh).then_inc(lo_ready, 1)
            nc.scalar.activation(gl[:, :], gl[:, :], ACT.Sigmoid).then_inc(lo_ready, 1)
            for m in range(4):
                for j in range(3):
                    keep(2 + 3 * m + j)
                for h in range(2):
                    hc = slice(h * HALF, (h + 1) * HALF)
                    act.wait_ge(up_ready, 6 * m + 3 * h + 3)
                    if m and h == 0:
                        act.wait_ge(nrm_done, m)
                        act.wait_ge(stored, 16 * NST * m)
                    nc.scalar.activation(sg[:, hc], up[:, 3 * h, :], ACT.Sigmoid, bias=col("w0", m)).then_inc(act_done, 1)
                    nc.scalar.activation(a_[:, hc], up[:, 3 * h + 1, :], ACT.Sigmoid, bias=col("a0", m)).then_inc(act_done, 1)
                    nc.scalar.copy(g_sb[:, hc], up[:, 3 * h + 2, :]).then_inc(act_done, 1)
                act.wait_ge(kk_sq, 2 * m + 1)
                nc.scalar.activation(sq[:, :], kk[:, :], ACT.Square).then_inc(kk_sq, 1)
                act.wait_ge(hs_ready, 2 * m + 1)
                nc.scalar.activation(nrm[:, :], hs[:, :, :].rearrange("p a b -> p (a b)"), ACT.Sqrt).then_inc(nrm_done, 1)
                act.wait_ge(dif_ready, m + 1)
                nc.scalar.activation(e_pos[:, :], dif[:, :], ACT.Exp).then_inc(exp_done, 1)
                nc.scalar.activation(e_neg[:, :], dif[:, :], ACT.Exp, scale=-1.0).then_inc(exp_done, 1)
                nc.scalar.activation(e_prev[:, :], cum[:, :], ACT.Exp).then_inc(exp_done, 1)
                nc.scalar.activation(s_exp[:, :], s_arg[:, :], ACT.Exp).then_inc(exp_done, 1)

        @block.tensor
        def _(pe):
            pe.wait_ge(w_loaded, 32)
            pe.wait_ge(lo_ready, 2)
            for m in range(4):
                ms = slice(m * P, (m + 1) * P)
                for h in range(2):
                    hc = slice(h * HALF, (h + 1) * HALF)
                    if m:
                        pe.wait_ge(act_done, 6 * (m - 1) + 3 * h + 3)
                    pe.matmul(up[:, 3 * h, :], lora_w[0:64, ms], wt[:, hc], start=True, stop=True).then_inc(up_ready, 1)
                    pe.matmul(up[:, 3 * h + 1, :], lora_w[64:128, ms], wa[64:128, hc], start=True, stop=True).then_inc(up_ready, 1)
                    pe.matmul(up[:, 3 * h + 2, :], upg_w[:, ms], gl[:, hc], start=True, stop=True).then_inc(up_ready, 1)
                pe.wait_ge(kk_sq, 2 * m + 2)
                if m:
                    pe.wait_ge(out_ready, m)
                ones = C[:, CONST["head_ones"]:CONST["head_ones"] + P]
                for h in range(2):
                    mm = pe.matmul(hs[:, h, :], ones, sq[:, h * HALF:(h + 1) * HALF], start=True, stop=True)
                mm.then_inc(hs_ready, 1)
                pe.wait_ge(rk_ready, m + 1)
                pe.wait_ge(nrm_done, m + 1)
                for h in range(2):
                    mm = pe.matmul(hs[:, h, :], ones, rk[:, h * HALF:(h + 1) * HALF], start=True, stop=True)
                mm.then_inc(hs_ready, 1)

        @block.vector
        def _(dve):
            st = Steps(dve, st_sem)
            tt, ts, stt = nc.vector.tensor_tensor, nc.vector.tensor_scalar, nc.vector.scalar_tensor_tensor
            st(nc.vector.memset(pre[:, :, 0:1], 0.0))
            st(nc.vector.memset(reset[:, :], 1.0))
            st.settle()
            st(nc.vector.memset(reset[:, :].rearrange("p (c t) -> p c t", c=NCH)[:, :, 0:1], 0.0))
            st(ts(one_ka[:, :], V[:, VEC["k_a"]:VEC["k_a"] + 4], -1.0, 1.0, ALU.mult, ALU.add))
            ts(one_mu[:, :], V[:, VEC["mu"]:VEC["mu"] + 14], -1.0, 1.0, ALU.mult, ALU.add).then_inc(mu_ready, 1)
            st.settle()

            def mix(n, dst):
                dve.wait_ge(kept_done, n + 1)
                stt(out=dst, in0=pre[:, n % 2, 0:SEQ], scalar=col("mu", order[n]), in1=kept[:, n % 2, :],
                    op0=ALU.mult, op1=ALU.add).then_inc(mixed, 1)

            mix(0, wa[:, :])
            mix(1, gl[:, :])
            for m in range(4):
                if m:
                    dve.wait_ge(stored, 16 * NST * m)
                mix(2 + 3 * m, rr[:, :])
                mix(3 + 3 * m, kx[:, :])
                mix(4 + 3 * m, vx[:, :])
                dve.wait_ge(mixed, 5 + 3 * m)
                ts(kk[:, :], kx[:, :], col("k_k", m), None, ALU.mult).then_inc(kk_sq, 1)
                dve.wait_ge(act_done, 6 * m + 6)
                st.link(ts(sg[:, :], sg[:, :], -RATE, None, ALU.mult))
                st.link(nc.vector.tensor_tensor_scan(cum[:, :], reset[:, :], sg[:, :], 0.0, ALU.mult, ALU.add))
                cum3 = cum[:, :].rearrange("p (c t) -> p c t", c=NCH)
                mid = cum3[:, :, 63:64]
                st(tt(dif[:, :].rearrange("p (c t) -> p c t", c=NCH), cum3, mid.to_broadcast([P, NCH, CH]), ALU.subtract))
                st(tt(s_arg[:, :].unsqueeze(2), cum3[:, :, CH - 1:CH], mid, ALU.subtract))
                st.settle()
                st.link(tt(s_arg[:, 0:NCH - 1], s_arg[:, 0:NCH - 1], cum3[:, 1:NCH, 63:64].rearrange("p c o -> p (c o)"), ALU.add))
                tt(cum[:, :], dif[:, :], sg[:, :], ALU.subtract).then_inc(dif_ready, 1)
                st.link(ts(k2[:, :], a_[:, :], col("k_a", m), one_ka[:, m:m + 1], ALU.mult, ALU.add))
                st.link(tt(k2[:, :], k2[:, :], kx[:, :], ALU.mult))
                stt(out=rk[:, :], in0=rr[:, :], scalar=col("r_k", m), in1=k2[:, :], op0=ALU.mult, op1=ALU.mult).then_inc(rk_ready, 1)
                dve.wait_ge(nrm_done, m + 1)
                st.link(ts(nrm[:, :], nrm[:, :], 1e-12, None, ALU.max))
                st.link(nc.vector.reciprocal(sq[:, :], nrm[:, :]))
                st.link(tt(kk[:, :], kk[:, :], sq[:, :], ALU.mult))
                dve.wait_ge(exp_done, 4 * m + 4)
                c3 = lambda t: t[:, :].rearrange("p (c t) -> p c t", c=NCH)
                st(stt(out=ar[:, :, 0, :], in0=c3(kk), scalar=-1.0, in1=c3(e_prev), op0=ALU.mult, op1=ALU.mult))
                st(tt(ar[:, :, 1, :], c3(rr), c3(e_pos), ALU.mult))
                st(tt(kk[:, :], kk[:, :], a_[:, :], ALU.mult))
                st(tt(kt[:, :], k2[:, :], e_neg[:, :], ALU.mult))
                st.settle()
                st(tt(bt[:, :], kk[:, :], e_neg[:, :], ALU.mult))
                dve.wait_ge(hs_ready, 2 * m + 2)
                st(tt(bon[:, :], hs[:, :, :].rearrange("p a b -> p (a b)"), vx[:, :], ALU.mult))
                st.settle()
                dve.sem_inc(out_ready, 1)

        @block.gpsimd
        def _(pool):
            for m in range(4):
                pool.wait_ge(out_ready, m + 1)
                for dst, s_ in ((scr["ar"][m], ar[:, :, :, :].rearrange("p a b c -> p (a b c)")), (scr["bt"][m], bt[:, :]), (scr["kt"][m], kt[:, :]),
                                (scr["v"][m], vx[:, :]), (scr["bonus"][m], bon[:, :]), (scr["g"][m], g_sb[:, :]), (scr["scale"][m], s_exp[:, :])):
                    pool.dma_start(dst, s_).then_inc(stored, 16)
            pool.wait_ge(stored, 16 * NST * 4)


def rwkv_scan_stage(nc, scr, masks, C):
    with ExitStack() as ctx:
        sb = lambda n, s, d=F32: ctx.enter_context(nc.sbuf_tensor(f"rs_{n}", s, d))
        sem = stage_semaphores(nc, ctx, "rs")
        lv = sb("lv", [P, 2 * LEVELS * P])
        ar = sb("ar", [P, 2, 4, 2 * CH])
        bt, kt, vt = sb("bt", [P, 2, 4, CH]), sb("kt", [P, 2, 4, CH]), sb("vt", [P, 2, 4, CH])
        scale = sb("scale", [P, 4, NCH])
        tok = sb("tok", [P, 3, 512])
        mb = sb("mb", [P, 2, 4, 2 * CH])
        mk = sb("mk", [P, 2, 4, 2 * CH])
        lab = sb("lab", [P, 2, 4, CH])
        X, XT = sb("X", [P, 2, 4, CH]), sb("XT", [P, 2, 4, CH])
        T_ = sb("T", [P, 2, 4, CH])
        zs, us = sb("zs", [P, 512]), sb("us", [P, 512])
        S, S_new = sb("S", [P, 4, P]), sb("S_new", [P, 4, P])
        ybuf = sb("ybuf", [P, 2, 512])
        ps = ctx.enter_context(nc.psum_tensor("rs_ps", [P, 8, 512], F32))
        loaded = [sem(f"loaded{i}") for i in range(2)]
        stored = [sem(f"stored{i}") for i in range(2)]
        c_loaded, s_init, wait_held = sem("c_loaded"), sem("s_init"), sem("wait_held")
        tr_ready, tr_copied, mat_ready, mat_masked, x_init = (sem(n) for n in ("tr_ready", "tr_copied", "mat_ready", "mat_masked", "x_init"))
        t_ready, t_copied, xx_ready, x_done, z_ready, z_copied = (sem(n) for n in ("t_ready", "t_copied", "xx_ready", "x_done", "z_ready", "z_copied"))
        u_ready, u_copied, y_ready, y_copied, ds_ready, ds_done, ds_done_a, steps = (sem(n) for n in ("u_ready", "u_copied", "y_ready", "y_copied", "ds_ready", "ds_done", "ds_done_a", "steps"))
        NL = LEVELS - 1
        lvm = lambda l, t: lv[:, (t * LEVELS + l) * P:(t * LEVELS + l + 1) * P].bitcast(U32).unsqueeze(1).to_broadcast([P, 4, P])
        bank = lambda b: ps[:, b, :].rearrange("p (h t) -> p h t", h=4)
        block = ctx.enter_context(nc.Block(no_gpsimd_drain=True))

        @block.sync
        def _(sp):
            sp.dma_start(lv[:, :], masks).then_inc(c_loaded, 16)
            sp.dma_start(scale[:, :, :], scr["scale"].rearrange("m p c -> p m c")).then_inc(c_loaded, 16)

            def load(c, u):
                arv = scr["ar"].rearrange("m p (c x) -> p m c x", c=NCH)
                sp.dma_start(ar[:, u, :, :], arv[:, :, c, :]).then_inc(loaded[u], 16)
                for dst, s_ in ((bt, "bt"), (kt, "kt"), (vt, "v")):
                    v_ = scr[s_].rearrange("m p (c x) -> p m c x", c=NCH)
                    sp.dma_start(dst[:, u, :, :], v_[:, :, c, :]).then_inc(loaded[u], 16)

            load(0, 0)
            load(1, 1)
            with sp.Fori(1, NCH // 2) as i:
                for u in range(2):
                    sp.wait_ge(ds_ready, 2 * i + (u - 1))
                    sp.wait_ge(y_ready, 2 * i + (u - 1))
                    load(2 * i + u, u)

        @block.tensor
        def _(pe):
            ident = C[:, CONST["ident"]:CONST["ident"] + P]

            def body(i, first, last):
                for u in range(2):
                    c = 2 * i + u
                    fresh = first and u == 0
                    pe.wait_ge(loaded[u], 64 * i + 64)
                    if not fresh:
                        pe.wait_ge(y_copied, c)
                        pe.wait_ge(ds_done, c)
                    for n, src in enumerate((bt, kt, vt)):
                        for m in range(4):
                            mm = pe.transpose(ps[:, 5 + n, m * P:(m + 1) * P], src[:, u, m, :], ident)
                        mm.then_inc(tr_ready, 1)
                    for g in range(2):
                        base = 64 * g
                        if not (fresh and g == 0):
                            pe.wait_ge(mat_masked, 12 * i + (6 * u + 3 * g))
                            if g == 0:
                                pe.wait_ge(x_done, 2 * (2 * NL) * i + 2 * NL * u)
                                pe.wait_ge(z_copied, c)
                        for m in range(4):
                            at_rt = ar[base:base + 64, u, m, :]
                            pe.matmul(ps[:, m // 2, (m % 2) * 256:(m % 2 + 1) * 256], bt[base:base + 64, u, m, :], at_rt,
                                      start=True, stop=True)
                            pe.matmul(ps[:, 2 + m // 2, (m % 2) * 256:(m % 2 + 1) * 256], kt[base:base + 64, u, m, :], at_rt,
                                      start=True, stop=True)
                            mm = pe.matmul(ps[:, 4, m * P:(m + 1) * P], ar[base:base + 64, u, m, 0:CH],
                                           bt[base:base + 64, u, m, :], start=True, stop=True)
                        mm.then_inc(mat_ready, 1)
                    for l in range(NL):
                        for g in range(2):
                            if l == 0:
                                pe.wait_ge(x_init, 4 * i + 2 * u + g + 1)
                                pe.wait_ge(tr_copied, 3 * (2 * i) + 3 * u + 3)
                            else:
                                pe.wait_ge(x_done, 4 * NL * i + 2 * NL * u + 2 * (l - 1) + g + 1)
                            for m in range(4):
                                mm = pe.matmul(ps[:, 5 + g, m * P:(m + 1) * P], mb[:, g, m, 0:CH], X[:, g, m, :], start=True, stop=True)
                            mm.then_inc(t_ready, 1)
                        for g in range(2):
                            pe.wait_ge(t_copied, 4 * NL * i + 2 * NL * u + 2 * l + g + 1)
                            if l == 0 and g == 0:
                                pe.wait_ge(mat_masked, 12 * i + 6 * u + 6)
                            for m in range(4):
                                if l < NL - 1:
                                    pe.matmul(ps[:, 2 * g, m * P:(m + 1) * P], XT[:, g, m, :], T_[:, g, m, :], start=True, stop=True)
                                mm = pe.matmul(ps[:, 2 * g + 1, m * P:(m + 1) * P], T_[:, g, m, :], XT[:, g, m, :], start=True, stop=True)
                            mm.then_inc(xx_ready, 1)
                    if fresh:
                        pe.wait_ge(s_init, 1)
                    pe.wait_ge(tr_copied, 6 * i + 3 * u + 3)
                    for m in range(4):
                        pe.matmul(ps[:, 4, m * P:(m + 1) * P], ar[:, u, m, 0:CH], S[:, m, :], start=True, stop=False, skip_group_check=True)
                        for g in range(2):
                            h = 2 * m + g
                            mm = pe.matmul(ps[:, 4, h * 64:(h + 1) * 64], mk[:, g, m, 0:CH], tok[:, 2, h * 64:(h + 1) * 64],
                                           start=False, stop=True, skip_group_check=True)
                    mm.then_inc(z_ready, 1)
                    pe.wait_ge(z_copied, c + 1)
                    pe.wait_ge(x_done, 4 * NL * i + 2 * NL * (u + 1))
                    for h in range(HR):
                        mm = pe.matmul(ps[:, 7, h * 64:(h + 1) * 64], XT[:, h % 2, h // 2, :], zs[:, h * 64:(h + 1) * 64], start=True, stop=True)
                    mm.then_inc(u_ready, 1)
                    pe.wait_ge(u_copied, c + 1)
                    for m in range(4):
                        pe.matmul(ps[:, 5, m * P:(m + 1) * P], S[:, m, :], ar[:, u, m, CH:], start=True, stop=False, skip_group_check=True)
                        for g in range(2):
                            h = 2 * m + g
                            o = ps[64 * g:64 * g + 64, 5, m * P:(m + 1) * P]
                            pe.matmul(o, us[:, h * 64:(h + 1) * 64], mb[:, g, m, CH:], start=False, stop=False, skip_group_check=True)
                            mm = pe.matmul(o, tok[:, 2, h * 64:(h + 1) * 64], mk[:, g, m, CH:], start=False, stop=True, skip_group_check=True)
                    mm.then_inc(y_ready, 1)
                    for m in range(4):
                        ms = slice(m * P, (m + 1) * P)
                        pe.matmul(ps[:, 6, ms], tok[:, 0, ms], us[:, ms], start=True, stop=False, skip_group_check=True)
                        mm = pe.matmul(ps[:, 6, ms], tok[:, 1, ms], tok[:, 2, ms], start=False, stop=True, skip_group_check=True)
                    mm.then_inc(ds_ready, 1)

            run_loop(pe, NCH // 2, body)

        @block.scalar
        def _(act):
            def body(i, first, last):
                for u in range(2):
                    c = 2 * i + u
                    fresh = first and u == 0
                    for n in range(3):
                        act.wait_ge(tr_ready, 6 * i + 3 * u + n + 1)
                        if n == 0 and not fresh:
                            act.wait_ge(ds_ready, c)
                        nc.scalar.copy(tok[:, n, :], ps[:, 5 + n, :]).then_inc(tr_copied, 1)
                    for l in range(NL):
                        for g in range(2):
                            act.wait_ge(t_ready, 4 * NL * i + 2 * NL * u + 2 * l + g + 1)
                            nc.scalar.copy(T_[:, g, :, :].rearrange("p h t -> p (h t)"), ps[:, 5 + g, :]).then_inc(t_copied, 1)
                    act.wait_ge(z_ready, c + 1)
                    nc.scalar.copy(zs[:, :], ps[:, 4, :]).then_inc(z_copied, 1)
                    act.wait_ge(u_ready, c + 1)
                    nc.scalar.copy(us[:, :], ps[:, 7, :]).then_inc(u_copied, 1)
                    act.wait_ge(y_ready, c + 1)
                    if not first:
                        act.wait_ge(stored[u], 64 * i)
                    nc.scalar.copy(ybuf[:, u, :], ps[:, 5, :]).then_inc(y_copied, 1)

            run_loop(act, NCH // 2, body)

        @block.vector
        def _(dve):
            tt = nc.vector.tensor_tensor
            before = C[:, CONST["before"]:CONST["before"] + 2 * P].unsqueeze(1).to_broadcast([P, 4, 2 * P])
            after = C[:, CONST["after"]:CONST["after"] + P].unsqueeze(1).to_broadcast([P, 4, P])
            ident = C[:, CONST["ident"]:CONST["ident"] + P].unsqueeze(1).to_broadcast([P, 4, P])
            nc.vector.memset(S[:, :, :], 0.0).then_inc(s_init, 1)
            nc.vector.memset(S_new[:, :, :], 0.0).then_inc(s_init, 1)
            dve.wait_ge(s_init, 2)
            dve.wait_ge(c_loaded, 32)

            def body(i, first, last):
                for u in range(2):
                    c = 2 * i + u
                    for g in range(2):
                        n = 12 * i + 6 * u + 3 * g
                        dve.wait_ge(mat_ready, 4 * i + 2 * u + g + 1)
                        if g == 0 and not (first and u == 0):
                            dve.wait_ge(ds_ready, c)
                        m4 = lambda b: ps[:, b:b + 2, :].rearrange("p b (m x) -> p (b m) x", m=2)
                        tt(mb[:, g, :, :], m4(0), before, ALU.mult).then_inc(mat_masked, 1)
                        tt(mk[:, g, :, :], m4(2), before, ALU.mult).then_inc(mat_masked, 1)
                        tt(lab[:, g, :, :], bank(4), after, ALU.mult).then_inc(mat_masked, 1)
                        s0 = 16 * i + 8 * u + 4 * g
                        nc.vector.tensor_copy(X[:, g, :, :], ident).then_inc(steps, 1)
                        nc.vector.tensor_copy(XT[:, g, :, :], ident).then_inc(steps, 1)
                        dve.wait_ge(mat_masked, n + 3)
                        dve.wait_ge(steps, s0 + 2)
                        dve.sem_inc(wait_held, 1)
                        nc.vector.copy_predicated(X[:, g, :, :], lvm(0, 0), lab[:, g, :, :]).then_inc(steps, 1)
                        nc.vector.copy_predicated(XT[:, g, :, :], lvm(0, 1), mb[:, g, :, 0:CH]).then_inc(steps, 1)
                        dve.wait_ge(steps, s0 + 4)
                        dve.sem_inc(x_init, 1)
                    for l in range(NL):
                        for g in range(2):
                            dve.wait_ge(xx_ready, 4 * NL * i + 2 * NL * u + 2 * l + g + 1)
                            dve.sem_inc(wait_held, 1)
                            if l < NL - 1:
                                nc.vector.copy_predicated(X[:, g, :, :], lvm(l + 1, 0), bank(2 * g))
                            nc.vector.copy_predicated(XT[:, g, :, :], lvm(l + 1, 1), bank(2 * g + 1)).then_inc(x_done, 1)
                    dve.wait_ge(ds_ready, c + 1)
                    for g in range(2):
                        b = slice(64 * g, 64 * g + 64)
                        tt(S_new[b, :, b], S[b, :, b], ps[b, 6, :].rearrange("p (m x) -> p m x", m=4)[:, :, b], ALU.add).then_inc(ds_done_a, 1)
                    dve.wait_ge(ds_done_a, 4 * i + 2 * u + 2)
                    for g in range(2):
                        b = slice(64 * g, 64 * g + 64)
                        ins = tt(S[b, :, b], S_new[b, :, b], scale[b, :, bass.ds(c, 1)].to_broadcast([64, 4, 64]), ALU.mult)
                        if g == 1:
                            ins.then_inc(ds_done, 1)

            run_loop(dve, NCH // 2, body)

        @block.gpsimd
        def _(pool):
            def body(i, first, last):
                for u in range(2):
                    c = 2 * i + u
                    pool.wait_ge(y_copied, c + 1)
                    for m in range(4):
                        pool.dma_start(scr["y"][m][:, bass.ts(c, CH)], ybuf[:, u, m * P:(m + 1) * P]).then_inc(stored[u], 16)

            run_loop(pool, NCH // 2, body)
            for u in range(2):
                pool.wait_ge(stored[u], 64 * NCH // 2)


def rwkv_finish_stage(nc, scr, y_out, V, C):
    col = lambda name, j=0: V[:, VEC[name] + j:VEC[name] + j + 1]
    with ExitStack() as ctx:
        sb = lambda n, s, d=F32: ctx.enter_context(nc.sbuf_tensor(f"rf_{n}", s, d))
        sem = stage_semaphores(nc, ctx, "rf")
        y, bon, g_ = sb("y", [P, 2, SEQ]), sb("bon", [P, 2, SEQ]), sb("g", [P, 2, SEQ])
        yc, sq, rms, out = sb("yc", [P, 2, SEQ]), sb("sq", [P, 2, SEQ]), sb("rms", [P, 2, SEQ]), sb("out", [P, 2, SEQ])
        mean = ctx.enter_context(nc.psum_tensor("rf_mean", [P, 2, 2, 512], F32))
        var = ctx.enter_context(nc.psum_tensor("rf_var", [P, 2, 2, 512], F32))
        loaded = [sem(f"loaded{i}") for i in range(2)]
        stored = [sem(f"stored{i}") for i in range(2)]
        mean_ready, yc_ready, sq_ready, var_ready, rms_ready, out_ready, steps = (
            sem(n) for n in ("mean_ready", "yc_ready", "sq_ready", "var_ready", "rms_ready", "out_ready", "steps"))
        flat = lambda t: t.rearrange("p a b -> p (a b)")
        block = ctx.enter_context(nc.Block(no_gpsimd_drain=True))

        @block.sync
        def _(sp):
            for m in range(4):
                if m >= 2:
                    sp.wait_ge(out_ready, m - 1)
                for dst, src in ((y, "y"), (bon, "bonus"), (g_, "g")):
                    sp.dma_start(dst[:, m % 2, :], scr[src][m]).then_inc(loaded[m % 2], 16)

        @block.tensor
        def _(pe):
            ones = C[:, CONST["head_ones"]:CONST["head_ones"] + P]

            def head_sum(dst, src):
                for h in range(2):
                    mm = pe.matmul(dst[:, h, :], ones, src[:, h * HALF:(h + 1) * HALF], start=True, stop=True)
                return mm

            for m in range(4):
                pe.wait_ge(loaded[m % 2], 48 * (m // 2 + 1))
                if m >= 2:
                    pe.wait_ge(yc_ready, m - 1)
                head_sum(mean[:, m % 2, :, :], y[:, m % 2, :]).then_inc(mean_ready, 1)
                if m:
                    pe.wait_ge(sq_ready, m)
                    if m >= 3:
                        pe.wait_ge(rms_ready, m - 2)
                    head_sum(var[:, (m - 1) % 2, :, :], sq[:, (m - 1) % 2, :]).then_inc(var_ready, 1)
            pe.wait_ge(sq_ready, 4)
            pe.wait_ge(rms_ready, 2)
            head_sum(var[:, 1, :, :], sq[:, 1, :]).then_inc(var_ready, 1)

        @block.scalar
        def _(act):
            for m in range(4):
                act.wait_ge(yc_ready, m + 1)
                if m >= 2:
                    act.wait_ge(var_ready, m - 1)
                nc.scalar.activation(sq[:, m % 2, :], yc[:, m % 2, :], ACT.Square).then_inc(sq_ready, 1)
                if m:
                    act.wait_ge(var_ready, m)
                    if m >= 3:
                        act.wait_ge(out_ready, m - 2)
                    nc.scalar.activation(rms[:, (m - 1) % 2, :], flat(var[:, (m - 1) % 2, :, :]), ACT.Sqrt,
                                         bias=C[:, CONST["eps_ln"]:CONST["eps_ln"] + 1], scale=1.0 / NR_).then_inc(rms_ready, 1)
            act.wait_ge(var_ready, 4)
            act.wait_ge(out_ready, 2)
            nc.scalar.activation(rms[:, 1, :], flat(var[:, 1, :, :]), ACT.Sqrt,
                                 bias=C[:, CONST["eps_ln"]:CONST["eps_ln"] + 1], scale=1.0 / NR_).then_inc(rms_ready, 1)

        @block.vector
        def _(dve):
            st = Steps(dve, steps)
            tt, ts, stt = nc.vector.tensor_tensor, nc.vector.tensor_scalar, nc.vector.scalar_tensor_tensor

            def center(m):
                u = m % 2
                dve.wait_ge(mean_ready, m + 1)
                stt(out=yc[:, u, :], in0=flat(mean[:, u, :, :]), scalar=-1.0 / NR_, in1=y[:, u, :], op0=ALU.mult,
                    op1=ALU.add).then_inc(yc_ready, 1)

            def finish(m):
                u = m % 2
                dve.wait_ge(rms_ready, m + 1)
                st.link(nc.vector.reciprocal(rms[:, u, :], rms[:, u, :]))
                st.link(tt(yc[:, u, :], yc[:, u, :], rms[:, u, :], ALU.mult))
                st.link(ts(yc[:, u, :], yc[:, u, :], col("lnx_w", m), col("lnx_b", m), ALU.mult, ALU.add))
                st.link(tt(yc[:, u, :], yc[:, u, :], bon[:, u, :], ALU.add))
                if m >= 2:
                    dve.wait_ge(stored[u], 16)
                tt(out[:, u, :], yc[:, u, :], g_[:, u, :], ALU.mult).then_inc(out_ready, 1)

            center(0)
            for m in range(4):
                if m < 3:
                    center(m + 1)
                finish(m)

        @block.gpsimd
        def _(pool):
            for m in range(4):
                pool.wait_ge(out_ready, m + 1)
                pool.dma_start(y_out[m], out[:, m % 2, :]).then_inc(stored[m % 2], 16)
            for u in range(2):
                pool.wait_ge(stored[u], 32)
def norm_stage(nc, src, dst, gain, eps_col, V, C):
    with ExitStack() as ctx:
        sb = lambda n, s, d=F32: ctx.enter_context(nc.sbuf_tensor(f"nf_{n}", s, d))
        sem = stage_semaphores(nc, ctx, "nf")
        x, sq, rms = sb("x", [P, DT, SEQ]), sb("sq", [P, 2, SEQ]), sb("rms", [P, SEQ])
        ss = ctx.enter_context(nc.psum_tensor("nf_ss", [P, 2, 512], F32))
        loaded = [sem(f"loaded{k}") for k in range(DT)]
        sq_ready, ss_ready, rms_ready, rstd_ready, h_ready, stored = (
            sem(n) for n in ("sq_ready", "ss_ready", "rms_ready", "rstd_ready", "h_ready", "stored"))
        block = ctx.enter_context(nc.Block(no_gpsimd_drain=True))

        @block.sync
        def _(sp):
            for k in range(DT):
                sp.dma_start(x[:, k, :], src[k]).then_inc(loaded[k], 16)
            for k in range(DT):
                sp.wait_ge(h_ready, k + 1)
                sp.dma_start(dst[k], x[:, k, :]).then_inc(stored, 16)
            sp.wait_ge(stored, 16 * DT)

        @block.scalar
        def _(act):
            for k in range(DT):
                act.wait_ge(loaded[k], 16)
                if k >= 2:
                    act.wait_ge(ss_ready, k - 1)
                nc.scalar.activation(sq[:, k % 2, :], x[:, k, :], ACT.Square).then_inc(sq_ready, 1)
            act.wait_ge(ss_ready, DT)
            nc.scalar.activation(rms[:, :], ss[:, :, :].rearrange("p a b -> p (a b)"), ACT.Sqrt,
                                 bias=C[:, eps_col:eps_col + 1], scale=1.0 / DM).then_inc(rms_ready, 1)

        @block.tensor
        def _(pe):
            for k in range(DT):
                pe.wait_ge(sq_ready, k + 1)
                for h in range(2):
                    mm = pe.matmul(ss[:, h, :], C[:, CONST["ones"]:CONST["ones"] + P], sq[:, k % 2, h * HALF:(h + 1) * HALF],
                                   start=k == 0, stop=k == DT - 1)
                mm.then_inc(ss_ready, 1)

        @block.vector
        def _(dve):
            dve.wait_ge(rms_ready, 1)
            nc.vector.reciprocal(rms[:, :], rms[:, :]).then_inc(rstd_ready, 1)
            dve.wait_ge(rstd_ready, 1)
            for k in range(DT):
                nc.vector.scalar_tensor_tensor(out=x[:, k, :], in0=x[:, k, :], scalar=V[:, gain + k:gain + k + 1],
                                               in1=rms[:, :], op0=ALU.mult, op1=ALU.mult).then_inc(h_ready, 1)


def lru_stage(nc, proj, lru_w, out, V, C):
    col = lambda name, j=0: V[:, VEC[name] + j:VEC[name] + j + 1]
    with ExitStack() as ctx:
        sb = lambda n, s, d=F32: ctx.enter_context(nc.sbuf_tensor(f"lr_{n}", s, d))
        sem = stage_semaphores(nc, ctx, "lr")
        W = sb("W", [P, 2 * DM])
        pre, yr = sb("pre", [P, 2, SEQ + 3]), sb("yr", [P, 2, SEQ])
        cv, xc = sb("cv", [P, 2, SEQ]), sb("xc", [P, 2, SEQ])
        rg, ig, gel = sb("rg", [P, 2, SEQ]), sb("ig", [P, 2, SEQ]), sb("gel", [P, 2, SEQ])
        a_, a2, th, mu = sb("a", [P, 2, SEQ]), sb("a2", [P, SEQ]), sb("th", [P, 2, SEQ]), sb("mu", [P, 2, SEQ])
        sq = sb("sq", [P, 2, SEQ])
        bi, h_, o = sb("bi", [P, SEQ]), sb("h", [P, SEQ]), sb("o", [P, 2, SEQ])
        sp_, m8, m16 = sb("sp", [P, 4, DT]), sb("m8", [P, DT]), sb("m16", [P, DT])
        p8 = sb("p8", [P, DT])
        gate = ctx.enter_context(nc.psum_tensor("lr_gate", [P, 2, 4, 512], F32))
        loaded = [sem(f"loaded{i}") for i in range(2)]
        stored = [sem(f"stored{i}") for i in range(2)]
        w_loaded, lam_e, lam_a, rates, conv_ready, gate_ready, sig_done, exps_done = (
            sem(n) for n in ("w_loaded", "lam_e", "lam_a", "rates", "conv_ready", "gate_ready", "sig_done", "exps_done"))
        sq_ready, mu_ready, steps, pads, o_ready = (sem(n) for n in ("sq_ready", "mu_ready", "steps", "pads", "o_ready"))
        block = ctx.enter_context(nc.Block(no_gpsimd_drain=True))

        @block.sync
        def _(sp):
            sp.dma_start(W[:, :], lru_w).then_inc(w_loaded, 16)
            for n in range(DT):
                if n >= 2:
                    sp.wait_ge(o_ready, n - 1)
                sp.dma_start(pre[:, n % 2, 3:], proj[n]).then_inc(loaded[n % 2], 16)
                sp.dma_start(yr[:, n % 2, :], proj[8 + n]).then_inc(loaded[n % 2], 16)

        @block.tensor
        def _(pe):
            pe.wait_ge(w_loaded, 16)
            for n in range(DT):
                u = n % 2
                pe.wait_ge(conv_ready, n + 1)
                if n >= 2:
                    pe.wait_ge(sig_done, 3 * (n - 1))
                for j in range(2):
                    for h in range(2):
                        mm = pe.matmul(gate[:, u, 2 * j + h, :], W[:, j * DM + n * P:j * DM + (n + 1) * P],
                                       xc[:, u, h * HALF:(h + 1) * HALF], start=True, stop=True)
                mm.then_inc(gate_ready, 1)

        @block.scalar
        def _(act):
            act.wait_ge(lam_a, 1)
            nc.scalar.activation(sp_[:, 1, :], sp_[:, 0, :], ACT.Exp, scale=-1.0).then_inc(lam_e, 1)
            act.wait_ge(rates, 1)
            flat = lambda t: t.rearrange("p a b -> p (a b)")

            def root(n):
                u = n % 2
                act.wait_ge(sq_ready, n + 1)
                if n >= 2:
                    act.wait_ge(o_ready, n - 1)
                nc.scalar.activation(mu[:, u, :], sq[:, u, :], ACT.Sqrt).then_inc(mu_ready, 1)

            for n in range(DT):
                u = n % 2
                act.wait_ge(gate_ready, n + 1)
                if n >= 2:
                    act.wait_ge(o_ready, n - 1)
                nc.scalar.activation(rg[:, u, :], flat(gate[:, u, 0:2, :]), ACT.Sigmoid, bias=col("lru_ba", n)).then_inc(sig_done, 1)
                nc.scalar.activation(ig[:, u, :], flat(gate[:, u, 2:4, :]), ACT.Sigmoid, bias=col("lru_bx", n)).then_inc(sig_done, 1)
                nc.scalar.activation(gel[:, u, :], yr[:, u, :], ACT.Gelu_apprx_tanh).then_inc(sig_done, 1)
                act.wait_ge(sig_done, 3 * n + 1)
                if n:
                    act.wait_ge(sq_ready, n)
                nc.scalar.activation(a_[:, u, :], rg[:, u, :], ACT.Exp, scale=m8[:, n:n + 1]).then_inc(exps_done, 1)
                nc.scalar.activation(a2[:, :], rg[:, u, :], ACT.Exp, scale=m16[:, n:n + 1]).then_inc(exps_done, 1)
                nc.scalar.activation(th[:, u, :], rg[:, u, :], ACT.Tanh, scale=p8[:, n:n + 1]).then_inc(exps_done, 1)
                root(n)

        @block.vector
        def _(dve):
            st = Steps(dve, steps)
            tt, ts, stt = nc.vector.tensor_tensor, nc.vector.tensor_scalar, nc.vector.scalar_tensor_tensor
            nc.vector.memset(pre[:, :, 0:3], 0.0).then_inc(pads, 1)
            lam = V[:, VEC["lru_lam"]:VEC["lru_lam"] + DT]
            stt(out=sp_[:, 0, :], in0=lam, scalar=-1.0, in1=lam, op0=ALU.mult, op1=ALU.max).then_inc(lam_a, 1)
            dve.wait_ge(lam_e, 1)
            st.link(ts(sp_[:, 2, :], sp_[:, 1, :], 2.0, None, ALU.add))
            st.link(nc.vector.reciprocal(sp_[:, 3, :], sp_[:, 2, :]))
            st.link(tt(sp_[:, 0, :], sp_[:, 1, :], sp_[:, 3, :], ALU.mult))
            st.link(tt(sp_[:, 1, :], sp_[:, 0, :], sp_[:, 0, :], ALU.mult))
            st.link(ts(sp_[:, 2, :], sp_[:, 1, :], 1.0 / 17, 1.0 / 15, ALU.mult, ALU.add))
            for k in (13, 11, 9, 7, 5, 3, 1):
                st.link(tt(sp_[:, 3, :], sp_[:, 2, :], sp_[:, 1, :], ALU.mult))
                st.link(ts(sp_[:, 2, :], sp_[:, 3, :], 1.0 / k, None, ALU.add))
            st.link(tt(sp_[:, 3, :], sp_[:, 2, :], sp_[:, 0, :], ALU.mult))
            st.link(ts(sp_[:, 0, :], lam, -1.0, 0.0, ALU.mult, ALU.max))
            st.link(stt(out=sp_[:, 1, :], in0=sp_[:, 3, :], scalar=2.0, in1=sp_[:, 0, :], op0=ALU.mult, op1=ALU.add))
            st(ts(m8[:, :], sp_[:, 1, :], -8.0, None, ALU.mult))
            st(ts(m16[:, :], sp_[:, 1, :], -16.0, None, ALU.mult))
            st(ts(p8[:, :], sp_[:, 1, :], 8.0, None, ALU.mult))
            st.settle()
            dve.sem_inc(rates, 1)
            dve.wait_ge(pads, 1)

            def conv(n):
                u = n % 2
                dve.wait_ge(loaded[u], 32 * (n // 2 + 1))
                if n:
                    dve.wait_ge(conv_ready, n)
                w = lambda tap: col("conv_2", 8 * tap + n)
                st.link(ts(cv[:, 0, :], pre[:, u, 3:3 + SEQ], w(3), col("conv_b_2", n), ALU.mult, ALU.add))
                st.link(stt(out=cv[:, 1, :], in0=pre[:, u, 2:2 + SEQ], scalar=w(2), in1=cv[:, 0, :], op0=ALU.mult, op1=ALU.add))
                st.link(stt(out=cv[:, 0, :], in0=pre[:, u, 1:1 + SEQ], scalar=w(1), in1=cv[:, 1, :], op0=ALU.mult, op1=ALU.add))
                if n >= 2:
                    dve.wait_ge(gate_ready, n - 1)
                stt(out=xc[:, u, :], in0=pre[:, u, 0:SEQ], scalar=w(0), in1=cv[:, 0, :], op0=ALU.mult, op1=ALU.add).then_inc(conv_ready, 1)

            conv(0)
            for n in range(DT):
                u = n % 2
                if n + 1 < DT:
                    conv(n + 1)
                dve.wait_ge(exps_done, 3 * n + 3)
                if n >= 2:
                    dve.wait_ge(mu_ready, n - 1)
                stt(out=sq[:, u, :], in0=a2[:, :], scalar=1.0, in1=th[:, u, :], op0=ALU.add, op1=ALU.mult).then_inc(sq_ready, 1)
                dve.wait_ge(sig_done, 3 * n + 3)
                dve.wait_ge(conv_ready, n + 1)
                st.link(tt(bi[:, :], xc[:, u, :], ig[:, u, :], ALU.mult))
                dve.wait_ge(mu_ready, n + 1)
                st.link(tt(bi[:, :], bi[:, :], mu[:, u, :], ALU.mult))
                st.link(nc.vector.tensor_tensor_scan(h_[:, :], a_[:, u, :], bi[:, :], 0.0, ALU.mult, ALU.add))
                if n >= 2:
                    dve.wait_ge(stored[u], 16 * (n // 2))
                tt(o[:, u, :], h_[:, :], gel[:, u, :], ALU.mult).then_inc(o_ready, 1)

        @block.gpsimd
        def _(pool):
            for n in range(DT):
                pool.wait_ge(o_ready, n + 1)
                pool.dma_start(out[n], o[:, n % 2, :]).then_inc(stored[n % 2], 16)
            for u in range(2):
                pool.wait_ge(stored[u], 16 * DT // 2)


def attention_stage(nc, proj, qT, kvT, positions, out, V, C):
    H, QD = 8, 192
    TWO_PI = 6.283185307179586
    MAGIC = 1.5 * 2.0 ** 23
    C1 = 6.28125
    C2 = float(np.float32(np.floor((TWO_PI - C1) * 2.0 ** 20) / 2.0 ** 20))
    C3 = TWO_PI - C1 - C2
    col = lambda name, j=0: V[:, VEC[name] + j:VEC[name] + j + 1]
    ones = C[:, CONST["ones"]:CONST["ones"] + P]
    ident = C[:, CONST["ident"]:CONST["ident"] + P]
    eps = C[:, CONST["eps6"]:CONST["eps6"] + 1]
    NQ = SEQ // P
    with ExitStack() as ctx:
        sb = lambda n, s, d=F32: ctx.enter_context(nc.sbuf_tensor(f"at_{n}", s, d))
        sem = stage_semaphores(nc, ctx, "at")
        pos = sb("pos", [P, SEQ], I32)
        ang, t1, t2, cosb, sinb = (sb(n, [P, SEQ]) for n in ("ang", "t1", "t2", "cos", "sin"))
        kpe, kps, krot, kpe_sq = (sb(n, [P, SEQ]) for n in ("kpe", "kps", "krot", "kpe_sq"))
        qn, kn, vt = sb("qn", [P, 2, SEQ]), sb("kn", [P, 2, SEQ]), sb("vt", [P, 2, SEQ])
        qr, qs = sb("qr", [P, SEQ]), sb("qs", [P, SEQ])
        qr_sq, q_sq, k_sq = sb("qr_sq", [P, SEQ]), sb("q_sq", [P, SEQ]), sb("k_sq", [P, SEQ])
        cos_q, sin_q, pt1, pt2 = (sb(n, [P, SEQ]) for n in ("cos_q", "sin_q", "pt1", "pt2"))
        qrot = sb("qrot", [P, 2, SEQ])
        q_g, k_g, k_r, v_tok = sb("q_g", [P, 2, SEQ]), sb("k_g", [P, 2, SEQ]), sb("k_r", [P, 2, SEQ]), sb("v_tok", [P, 2, SEQ])
        diag = sb("diag", [P, NQ, P])
        rms, inv = sb("rms", [P, 2 * NQ]), sb("inv", [P, 2 * NQ])
        q_scale, neg_scale = sb("q_scale", [P, 2, 8]), sb("neg_scale", [P, 2, 8])
        pr = sb("pr", [P, 2, SEQ])
        prT = sb("prT", [P, 2, SEQ])
        mx, bias, total, rinv = (sb(n, [P, 64]) for n in ("mx", "bias", "total", "rinv"))
        o_sb = sb("o_sb", [P, 2, SEQ])
        score = ctx.enter_context(nc.psum_tensor("at_score", [P, 2, 1024], F32))
        tr = ctx.enter_context(nc.psum_tensor("at_tr", [P, 2, 512], F32))
        ob = ctx.enter_context(nc.psum_tensor("at_ob", [P, 512], F32))
        pb = ctx.enter_context(nc.psum_tensor("at_pb", [P, 512], F32))
        g_loaded, steps, pool_steps, ang_ready, trig_ready, trig_q_ready = (
            sem(n) for n in ("g_loaded", "steps", "pool_steps", "ang_ready", "trig_ready", "trig_q_ready"))
        h_loaded = [sem(f"h_loaded{i}") for i in range(2)]
        r_loaded, rotated, sq_ready, q_ready, sums_ready, rms_ready, diag_ready, bc_ready, k_half, vt_ready, v_copied = (
            sem(n) for n in ("r_loaded", "rotated", "sq_ready", "q_ready", "sums_ready", "rms_ready", "diag_ready",
                             "bc_ready", "k_half", "vt_ready", "v_copied"))
        score_ready, bias_ready, prob_ready, norm_ready, tr_ready, tr_copied, ob_ready, ob_copied = (
            sem(n) for n in ("score_ready", "bias_ready", "prob_ready", "norm_ready", "tr_ready", "tr_copied", "ob_ready", "ob_copied"))
        stored = [sem(f"stored{i}") for i in range(2)]
        trs = [0]
        for h in range(H):
            for b in range(NQ):
                trs.append(trs[-1] + b // 4 + 1)
        block = ctx.enter_context(nc.Block(no_gpsimd_drain=True))

        @block.sync
        def _(sp):
            sp.dma_start(pos[:, :], positions.partition_broadcast(P)).then_inc(g_loaded, 16)
            sp.dma_start(kpe[:, :], proj[20]).then_inc(g_loaded, 16)
            sp.dma_start(kps[:, :], proj[21]).then_inc(g_loaded, 16)

            def store(h):
                sp.wait_ge(ob_copied, NQ * (h + 1))
                sp.dma_start(out[h], o_sb[:, h % 2, :]).then_inc(stored[h % 2], 16)

            for h in range(H):
                u = h % 2
                if h >= 2:
                    sp.wait_ge(q_ready, h - 1)
                    sp.wait_ge(k_half, 2 * (h - 1))
                    sp.wait_ge(vt_ready, 2 * (h - 1))
                sp.dma_start(qn[:, u, :], qT[h]).then_inc(h_loaded[u], 16)
                sp.dma_start(kn[:, u, :], kvT[h]).then_inc(h_loaded[u], 16)
                sp.dma_start(vt[:, u, :], kvT[8 + h]).then_inc(h_loaded[u], 16)
                if u == 0:
                    if h:
                        sp.wait_ge(rotated, h // 2)
                    sp.dma_start(qr[:, :], qT[8 + h // 2]).then_inc(r_loaded, 16)
                    sp.dma_start(qs[:, :], qT[12 + h // 2]).then_inc(r_loaded, 16)
                if h >= 3:
                    store(h - 3)
            for h in range(H - 3, H):
                store(h)
            for u in range(2):
                sp.wait_ge(stored[u], 16 * H // 2)

        @block.vector
        def _(dve):
            st = Steps(dve, steps)
            tt, ts, stt = nc.vector.tensor_tensor, nc.vector.tensor_scalar, nc.vector.scalar_tensor_tensor
            dve.wait_ge(g_loaded, 48)
            st.link(nc.vector.tensor_copy(t1[:, :], pos[:, :]))
            st.link(ts(ang[:, :], t1[:, :], C[:, CONST["inv_freq"]:CONST["inv_freq"] + 1], None, ALU.mult))
            st.link(ts(t1[:, :], ang[:, :], 1.0 / TWO_PI, None, ALU.mult))
            st.link(ts(t2[:, :], t1[:, :], MAGIC, None, ALU.add))
            st.link(ts(t1[:, :], t2[:, :], -MAGIC, None, ALU.add))
            for c_ in (C1, C2, C3):
                st.link(stt(out=ang[:, :], in0=t1[:, :], scalar=-c_, in1=ang[:, :], op0=ALU.mult, op1=ALU.add))
            st.link(ts(ang[:, :], ang[:, :], 3.1415925, -3.1415925, ALU.min, ALU.max))
            st.link(stt(out=t1[:, :], in0=ang[:, :], scalar=-1.0, in1=ang[:, :], op0=ALU.mult, op1=ALU.max))
            ts(t2[:, :], t1[:, :], -1.0, TWO_PI / 4, ALU.mult, ALU.add).then_inc(ang_ready, 1)
            dve.wait_ge(trig_ready, 2)
            st.link(ts(sinb[:, :], sinb[:, :], C[:, CONST["rope_sign"]:CONST["rope_sign"] + 1], None, ALU.mult))

            tt(cos_q[:, :], cosb[:, :], col("qg_r").to_broadcast([P, SEQ]), ALU.mult).then_inc(trig_q_ready, 1)
            tt(sin_q[:, :], sinb[:, :], col("qg_s").to_broadcast([P, SEQ]), ALU.mult).then_inc(trig_q_ready, 1)
            st(stt(out=t1[:, :], in0=kpe[:, :], scalar=col("kg_r"), in1=cosb[:, :], op0=ALU.mult, op1=ALU.mult))
            st(stt(out=t2[:, :], in0=kps[:, :], scalar=col("kg_s"), in1=sinb[:, :], op0=ALU.mult, op1=ALU.mult))
            st.settle()
            st.link(tt(krot[:, :], t1[:, :], t2[:, :], ALU.add))

            def inverses(h):
                u = h % 2
                dve.wait_ge(rms_ready, h + 1)
                if h >= 1:
                    dve.wait_ge(bc_ready, 2 * h)
                if h >= 2:
                    dve.wait_ge(prob_ready, NQ * (h - 1))
                st.link(nc.vector.reciprocal(inv[:, :], rms[:, :]))
                st(ts(neg_scale[:, u, :], inv[:, 0:NQ], -(QD ** -0.5), None, ALU.mult))
                st(ts(q_scale[:, u, :], inv[:, 0:NQ], QD ** -0.5, None, ALU.mult))
                st.settle()
                tt(diag[:, :, :], ident.unsqueeze(1).to_broadcast([P, NQ, P]), inv[:, NQ:2 * NQ].unsqueeze(2).to_broadcast([P, NQ, P]),
                   ALU.mult).then_inc(diag_ready, 1)

            def key_half(h, f):
                u, base, fs = h % 2, 64 * (h % 2), slice(f * 512, (f + 1) * 512)
                if f == 0:
                    dve.wait_ge(h_loaded[u], 48 * (h // 2 + 1))
                if h >= 2 and f == 0:
                    dve.wait_ge(score_ready, NQ * (h - 1))
                dve.wait_ge(bc_ready, 2 * h + f + 1)
                st(stt(out=k_g[:, u, fs], in0=kn[:, u, fs], scalar=col("kg_n"), in1=pb[:, :], op0=ALU.mult, op1=ALU.mult))
                st(tt(k_r[base:base + 64, u, fs], krot[base:base + 64, fs], pb[base:base + 64, :], ALU.mult))
                st.settle()
                dve.sem_inc(k_half, 1)

            def maximum(h, b):
                n = NQ * h + b
                u, w = n % 2, (b + 1) * P
                dve.wait_ge(score_ready, n + 1)
                st.link(stt(out=score[:, u, b * P:w], in0=C[:, CONST["before"]:CONST["before"] + P], scalar=-1e30,
                            in1=score[:, u, b * P:w], op0=ALU.mult, op1=ALU.add))
                st.link(nc.vector.reduce_max(mx[:, n:n + 1], score[:, u, 0:w], AX.X))
                tt(bias[:, n:n + 1], mx[:, n:n + 1], neg_scale[:, h % 2, b:b + 1], ALU.mult).then_inc(bias_ready, 1)

            def normalise(h, b):
                n = NQ * h + b
                u, w = n % 2, (b + 1) * P
                dve.wait_ge(prob_ready, n + 1)
                st.link(nc.vector.reciprocal(rinv[:, n:n + 1], total[:, n:n + 1]))
                ts(pr[:, u, 0:w], pr[:, u, 0:w], rinv[:, n:n + 1], None, ALU.mult).then_inc(norm_ready, 1)

            def outputs(h, b):
                n = NQ * h + b
                dve.wait_ge(ob_ready, n + 1)
                if b == 0 and h >= 2:
                    dve.wait_ge(stored[h % 2], 16 * (h // 2))
                nc.vector.tensor_copy(o_sb[:, h % 2, b * P:(b + 1) * P], ob[:, 0:P]).then_inc(ob_copied, 1)

            inverses(0)
            key_half(0, 0)
            key_half(0, 1)
            every = [(h, b) for h in range(H) for b in range(NQ)]
            for n, (h, b) in enumerate(every):
                if n >= 3:
                    outputs(*every[n - 3])
                if n >= 1:
                    normalise(*every[n - 1])
                if b in (4, 5) and h + 1 < H:
                    key_half(h + 1, b - 4)
                maximum(h, b)
                if b == 2 and h + 1 < H:
                    inverses(h + 1)
            normalise(*every[-1])
            for last in every[-3:]:
                outputs(*last)

        @block.scalar
        def _(act):
            act.wait_ge(ang_ready, 1)
            nc.scalar.activation(sinb[:, :], ang[:, :], ACT.Sin).then_inc(trig_ready, 1)
            nc.scalar.activation(cosb[:, :], t2[:, :], ACT.Sin).then_inc(trig_ready, 1)

            def norms(h):
                act.wait_ge(sums_ready, h + 1)
                if h >= 1:
                    act.wait_ge(diag_ready, h)
                nc.scalar.activation(rms[:, :], pb[:, 0:2 * NQ], ACT.Sqrt, bias=eps, scale=1.0 / QD).then_inc(rms_ready, 1)

            def value_half(h, f):
                if h >= 2 and f == 0:
                    act.wait_ge(ob_ready, NQ * (h - 1))
                act.wait_ge(vt_ready, 2 * h + f + 1)
                nc.scalar.copy(v_tok[:, h % 2, f * 512:(f + 1) * 512], pb[:, :]).then_inc(v_copied, 1)

            def probs(h, b):
                n = NQ * h + b
                u, w = n % 2, (b + 1) * P
                act.wait_ge(bias_ready, n + 1)
                if n >= 2:
                    act.wait_ge(tr_ready, trs[n - 1])
                nc.scalar.activation(pr[:, u, 0:w], score[:, u, 0:w], ACT.Exp, bias=bias[:, n:n + 1],
                                     scale=q_scale[:, h % 2, b:b + 1], accum_out=total[:, n:n + 1]).then_inc(prob_ready, 1)

            def copies(h, b):
                n = NQ * h + b
                for k in range(b // 4 + 1):
                    w = min(512, (b + 1) * P - k * 512)
                    act.wait_ge(tr_ready, trs[n] + k + 1)
                    if n >= 2:
                        act.wait_ge(ob_ready, n - 1)
                    nc.scalar.copy(prT[:, n % 2, k * 512:k * 512 + w], tr[:, (trs[n] + k) % 2, 0:w]).then_inc(tr_copied, 1)

            norms(0)
            value_half(0, 0)
            value_half(0, 1)
            every = [(h, b) for h in range(H) for b in range(NQ)]
            for n, (h, b) in enumerate(every):
                if b == 2 and h + 1 < H:
                    norms(h + 1)
                if b >= 6 and h + 1 < H:
                    value_half(h + 1, b - 6)
                probs(h, b)
                if n >= 1:
                    copies(*every[n - 1])
            copies(*every[-1])

        @block.tensor
        def _(pe):
            def sums(h):
                pe.wait_ge(sq_ready, h + 1)
                if h:
                    pe.wait_ge(v_copied, 2 * h)
                for t in range(NQ):
                    for j, sq in enumerate((q_sq, k_sq)):
                        mm = pe.matmul(pb[:, j * NQ + t:j * NQ + t + 1], sq[:, t * P:(t + 1) * P], C[:, CONST["ones"]:CONST["ones"] + 1],
                                       start=True, stop=True, skip_group_check=True)
                mm.then_inc(sums_ready, 1)

            def spread(h, f):
                pe.wait_ge(k_half, 2 * h + 1) if f else pe.wait_ge(diag_ready, h + 1)
                pe.matmul(pb[:, :], ones, diag[:, 4 * f:4 * f + 4, :].rearrange("p a b -> p (a b)"), start=True, stop=True).then_inc(bc_ready, 1)

            def turn_values(h, f):
                pe.wait_ge(v_copied, 2 * h + 1) if f else pe.wait_ge(k_half, 2 * h + 2)
                for t in range(4):
                    mm = pe.transpose(pb[:, t * P:(t + 1) * P], vt[:, h % 2, (4 * f + t) * P:(4 * f + t + 1) * P], ident)
                mm.then_inc(vt_ready, 1)

            prep = (lambda h: sums(h), lambda h: spread(h, 0), lambda h: spread(h, 1),
                    lambda h: turn_values(h, 0), lambda h: turn_values(h, 1))
            at_step = {1: 0, 3: 1, 4: 2, 5: 3, 6: 4}

            def scores(h, b):
                n = NQ * h + b
                u, base, hu = n % 2, 64 * (h % 2), h % 2
                if b == 0:
                    pe.wait_ge(k_half, 2 * h + 2)
                    pe.wait_ge(q_ready, h + 1)
                if n >= 2:
                    pe.wait_ge(prob_ready, n - 1)
                for f in range(b // 4 + 1):
                    w = min(512, (b + 1) * P - f * 512)
                    o = score[:, u, f * 512:f * 512 + w]
                    pe.matmul(o, q_g[:, hu, b * P:(b + 1) * P], k_g[:, hu, f * 512:f * 512 + w], start=True, stop=False)
                    mm = pe.matmul(o, qrot[base:base + 64, (h // 2) % 2, b * P:(b + 1) * P], k_r[base:base + 64, hu, f * 512:f * 512 + w],
                                   start=False, stop=True)
                mm.then_inc(score_ready, 1)

            def transposes(h, b):
                n = NQ * h + b
                pe.wait_ge(norm_ready, n + 1)
                for k in range(b // 4 + 1):
                    g = trs[n] + k
                    if g >= 2:
                        pe.wait_ge(tr_copied, g - 1)
                    for j in range(min(4, b + 1 - 4 * k)):
                        mm = pe.transpose(tr[:, g % 2, j * P:(j + 1) * P], pr[:, n % 2, (4 * k + j) * P:(4 * k + j + 1) * P], ident)
                    mm.then_inc(tr_ready, 1)

            def values(h, b):
                n = NQ * h + b
                pe.wait_ge(tr_copied, trs[n + 1])
                if b == 0:
                    pe.wait_ge(v_copied, 2 * h + 2)
                if n >= 1:
                    pe.wait_ge(ob_copied, n)
                o = ob[:, 0:P]
                for k in range(b + 1):
                    mm = pe.matmul(o, v_tok[:, h % 2, k * P:(k + 1) * P], prT[:, n % 2, k * P:(k + 1) * P], start=k == 0,
                                   stop=k == b, skip_group_check=True)
                mm.then_inc(ob_ready, 1)

            for part in prep:
                part(0)
            every = [(h, b) for h in range(H) for b in range(NQ)]
            scores(0, 0)
            for n, (h, b) in enumerate(every):
                if n + 1 < len(every):
                    scores(*every[n + 1])
                if n >= 1:
                    transposes(*every[n - 1])
                if n >= 2:
                    values(*every[n - 2])
                if b in at_step and h + 1 < H:
                    prep[at_step[b]](h + 1)
            transposes(*every[-1])
            values(*every[-2])
            values(*every[-1])

        @block.gpsimd
        def _(pool):
            st = Steps(pool, pool_steps)
            tt = nc.gpsimd.tensor_tensor
            pool.wait_ge(g_loaded, 48)
            st(tt(kpe_sq[:, :], kpe[:, :], kpe[:, :], ALU.mult))
            for h in range(H):
                u, base = h % 2, 64 * (h % 2)
                pool.wait_ge(h_loaded[u], 48 * (h // 2 + 1))
                if h:
                    pool.wait_ge(sums_ready, h)
                st(tt(q_sq[:, :], qn[:, u, :], qn[:, u, :], ALU.mult))
                st(tt(k_sq[:, :], kn[:, u, :], kn[:, u, :], ALU.mult))
                if u == 0:
                    pool.wait_ge(r_loaded, 32 * (h // 2 + 1))
                    st(tt(qr_sq[:, :], qr[:, :], qr[:, :], ALU.mult))
                st.settle()
                st(tt(q_sq[base:base + 64, :], q_sq[base:base + 64, :], qr_sq[base:base + 64, :], ALU.add))
                st(tt(k_sq[0:64, :], k_sq[0:64, :], kpe_sq[0:64, :], ALU.add))
                st.settle()
                pool.sem_inc(sq_ready, 1)
                if h >= 2:
                    pool.wait_ge(score_ready, NQ * (h - 1))
                st(tt(q_g[:, u, :], qn[:, u, :], col("qg_n").to_broadcast([P, SEQ]), ALU.mult))
                if u == 0:
                    if h == 0:
                        pool.wait_ge(trig_q_ready, 2)
                    st(tt(pt1[:, :], qr[:, :], cos_q[:, :], ALU.mult))
                    st(tt(pt2[:, :], qs[:, :], sin_q[:, :], ALU.mult))
                    st.settle()
                    pool.sem_inc(rotated, 1)
                    st(tt(qrot[:, (h // 2) % 2, :], pt1[:, :], pt2[:, :], ALU.add))
                st.settle()
                pool.sem_inc(q_ready, 1)
N_EXP, GRP, PER = 64, 8, 8
BS = 64
NBLK = 2 * SEQ // BS + N_EXP
MIN_PAIRS = 2 * SEQ // BS // 2


def router_stage(nc, src, router, router_b, u_tok, table, y_pad, dest, gates, blk_expert, V, C):
    with ExitStack() as ctx:
        sb = lambda n, s, d=F32: ctx.enter_context(nc.sbuf_tensor(f"ro_{n}", s, d))
        sem = stage_semaphores(nc, ctx, "ro")
        x, sq, rms = sb("x", [P, DT, SEQ]), sb("sq", [P, 2, SEQ]), sb("rms", [P, SEQ])
        wr, br = sb("wr", [P, DT * 72]), sb("br", [P, 72])
        ut = sb("ut", [P, 2, DM])
        lg = sb("lg", [P, DT, 72])
        zero = sb("zero", [P, NBLK * BS // P], I32)
        zero_y = sb("zero_y", [P, DM])
        pairs_i = sb("pairs_i", [1, 2], I32)
        g_eq, g_key, g_hot = sb("g_eq", [P, DT, 8]), sb("g_key", [P, DT, 8]), sb("g_hot", [P, DT, 8])
        g_exp = sb("g_exp", [P, DT, 8])
        gmax, gsum, gp, m1, m2, kmin = (sb(n, [P, DT]) for n in ("gmax", "gsum", "gp", "m1", "m2", "kmin"))
        ein, ein2, e_key = sb("ein", [P, DT, 8]), sb("ein2", [P, DT, 8]), sb("e_key", [P, DT, 8])
        e_hot = sb("e_hot", [P, 2, DT, 8])
        big = sb("big", [P, DT, 64])
        hot = sb("hot", [P, 3, DT, 64])
        rat, rden = sb("rat", [P, DT]), sb("rden", [P, DT])
        cnt, padded, pend, pstart = sb("cnt", [P, 64]), sb("padded", [P, 64]), sb("pend", [P, 64]), sb("pstart", [P, 64])
        ci = sb("ci", [P, 2, 64], I32)
        slot = sb("slot", [P, DT, 64])
        dest_f = sb("dest_f", [P, 2, DT])
        be = sb("be", [P, 64])
        bcol = sb("bcol", [P, 2])
        tok_id = sb("tok_id", [P, DT], I32)
        ss = ctx.enter_context(nc.psum_tensor("ro_ss", [P, 2, 512], F32))
        tr = ctx.enter_context(nc.psum_tensor("ro_tr", [P, 4, 512], F32))
        lp = ctx.enter_context(nc.psum_tensor("ro_lp", [P, 2, 512], F32))
        loaded = [sem(f"loaded{k}") for k in range(DT)]
        stored = [sem(f"stored{k}") for k in range(2)]
        w_loaded, sq_ready, ss_ready, rms_ready, rstd_ready, h_ready, steps = (
            sem(n) for n in ("w_loaded", "sq_ready", "ss_ready", "rms_ready", "rstd_ready", "h_ready", "steps"))
        lg_ready, lg_read, tr_ready, tr_copied, table_zero, zero_ready, key_ready, exp_done = (
            sem(n) for n in ("lg_ready", "lg_read", "tr_ready", "tr_copied", "table_zero", "zero_ready", "key_ready", "exp_done"))
        hot_ready, count_ready, bcol_ready, brow_ready, dest_ready, scattered, id_ready, y_zero = (
            sem(n) for n in ("hot_ready", "count_ready", "bcol_ready", "brow_ready", "dest_ready", "scattered", "id_ready", "y_zero"))
        ident = C[:, CONST["ident"]:CONST["ident"] + P]
        ones = C[:, CONST["ones"]:CONST["ones"] + P]
        block = ctx.enter_context(nc.Block(no_gpsimd_drain=True))

        @block.sync
        def _(sp):
            for k in range(DT):
                sp.dma_start(x[:, k, :], src[k]).then_inc(loaded[k], 16)
            sp.dma_start(wr[:, :], router).then_inc(w_loaded, 16)
            sp.dma_start(br[:, :], router_b.partition_broadcast(P)).then_inc(w_loaded, 16)
            sp.wait_ge(zero_ready, 2)
            sp.dma_start(table.rearrange("(p c) o -> p (c o)", p=P), zero[:, :]).then_inc(table_zero, 16)
            with sp.Fori(MIN_PAIRS, NBLK // 2) as i:
                sp.dma_start(y_pad[bass.ds(i * P, P), :], zero_y[:, :]).then_inc(y_zero, 16)
            for t in range(DT):
                sp.wait_ge(tr_copied, t + 1)
                sp.dma_start(u_tok[t * P:(t + 1) * P, :], ut[:, t % 2, :]).then_inc(stored[t % 2], 16)
            for u in range(2):
                sp.wait_ge(stored[u], 16 * DT // 2)
            sp.wait_ge(y_zero, 16 * (NBLK // 2 - MIN_PAIRS))

        @block.scalar
        def _(act):
            for k in range(DT):
                act.wait_ge(loaded[k], 16)
                if k >= 2:
                    act.wait_ge(ss_ready, k - 1)
                nc.scalar.activation(sq[:, k % 2, :], x[:, k, :], ACT.Square).then_inc(sq_ready, 1)
            act.wait_ge(ss_ready, DT)
            nc.scalar.activation(rms[:, :], ss[:, :, :].rearrange("p a b -> p (a b)"), ACT.Sqrt,
                                 bias=C[:, CONST["eps6"]:CONST["eps6"] + 1], scale=1.0 / DM).then_inc(rms_ready, 1)
            for t in range(DT):
                u = t % 2
                act.wait_ge(tr_ready, t + 1)
                if t >= 2:
                    act.wait_ge(stored[u], 16 * (t // 2))
                nc.scalar.copy(ut[:, u, :], tr[:, 2 * u:2 * u + 2, :].rearrange("p a b -> p (a b)")).then_inc(tr_copied, 1)
            act.wait_ge(key_ready, 1)
            nc.scalar.activation(g_exp[:, :, :], g_exp[:, :, :], ACT.Exp).then_inc(exp_done, 1)
            act.wait_ge(key_ready, 2)
            nc.scalar.activation(rat[:, :], rat[:, :], ACT.Exp).then_inc(exp_done, 1)

        @block.tensor
        def _(pe):
            for k in range(DT):
                pe.wait_ge(sq_ready, k + 1)
                for h in range(2):
                    mm = pe.matmul(ss[:, h, :], ones, sq[:, k % 2, h * HALF:(h + 1) * HALF], start=k == 0, stop=k == DT - 1)
                mm.then_inc(ss_ready, 1)
            pe.wait_ge(w_loaded, 32)
            pe.wait_ge(h_ready, DT)
            for t in range(DT):
                u, tsl = t % 2, slice(t * P, (t + 1) * P)
                if t >= 2:
                    pe.wait_ge(lg_read, t - 1)
                    pe.wait_ge(tr_copied, t - 1)
                for k in range(DT):
                    mm = pe.matmul(lp[:, u, 0:72], x[:, k, tsl], wr[:, k * 72:(k + 1) * 72], start=k == 0, stop=k == DT - 1)
                mm.then_inc(lg_ready, 1)
                for k in range(DT):
                    mm = pe.transpose(tr[:, 2 * u + k // 4, (k % 4) * P:(k % 4 + 1) * P], x[:, k, tsl], ident)
                mm.then_inc(tr_ready, 1)
            pe.wait_ge(hot_ready, 1)
            for t in range(DT):
                o = ss[:, 0, t * 64:(t + 1) * 64]
                for e in range(t):
                    pe.matmul(o, ones, hot[:, 2, e, :], start=e == 0, stop=False, skip_group_check=True)
                pe.matmul(o, C[:, CONST["before"]:CONST["before"] + P], hot[:, 2, t, :], start=t == 0, stop=True, skip_group_check=True)
            for t in range(DT):
                mm = pe.matmul(ss[:, 1, 0:64], ones, hot[:, 2, t, :], start=t == 0, stop=t == DT - 1)
            mm.then_inc(count_ready, 1)
            pe.wait_ge(bcol_ready, 1)
            pe.matmul(lp[0:1, 0, 0:P], bcol[:, 1:2], ident, start=True, stop=True).then_inc(brow_ready, 1)

        @block.vector
        def _(dve):
            st = Steps(dve, steps)
            tt, ts, stt = nc.vector.tensor_tensor, nc.vector.tensor_scalar, nc.vector.scalar_tensor_tensor
            bc = lambda t, n: t.unsqueeze(2).to_broadcast([P, DT, n])
            nc.vector.memset(zero[:, :], 0).then_inc(zero_ready, 1)
            nc.vector.memset(zero_y[:, :], 0.0).then_inc(zero_ready, 1)
            dve.wait_ge(rms_ready, 1)
            nc.vector.reciprocal(rms[:, :], rms[:, :]).then_inc(rstd_ready, 1)
            dve.wait_ge(rstd_ready, 1)
            for k in range(DT):
                stt(out=x[:, k, :], in0=x[:, k, :], scalar=V[:, VEC["norm2_2"] + k:VEC["norm2_2"] + k + 1],
                    in1=rms[:, :], op0=ALU.mult, op1=ALU.mult).then_inc(h_ready, 1)
            dve.wait_ge(w_loaded, 32)
            for t in range(DT):
                dve.wait_ge(lg_ready, t + 1)
                tt(lg[:, t, :], lp[:, t % 2, 0:72], br[:, :], ALU.add).then_inc(lg_read, 1)
            dve.wait_ge(lg_read, DT)
            G, E = lg[:, :, 0:8], lg[:, :, 8:72]
            iota = C[:, CONST["iota8"]:CONST["iota8"] + 8].unsqueeze(1).to_broadcast([P, DT, 8])

            def first_hot(hot_out, vals, mx):
                st.link(nc.vector.reduce_max(mx, vals, AX.X))
                st.link(tt(g_eq[:, :, :], vals, bc(mx, 8), ALU.is_equal))
                st.link(stt(out=g_key[:, :, :], in0=g_eq[:, :, :], scalar=-8.0, in1=iota, op0=ALU.mult, op1=ALU.add))
                st.link(nc.vector.tensor_reduce(kmin[:, :], g_key[:, :, :], AX.X, ALU.min))
                st.link(tt(hot_out, g_key[:, :, :], bc(kmin[:, :], 8), ALU.is_equal))

            first_hot(g_hot[:, :, :], G, gmax[:, :])
            st.link(tt(g_exp[:, :, :], G, bc(gmax[:, :], 8), ALU.subtract))
            dve.sem_inc(key_ready, 1)
            big4 = big[:, :, :].rearrange("p t (g e) -> p t g e", g=8)
            gh4 = g_hot[:, :, :].unsqueeze(3).to_broadcast([P, DT, 8, 8])
            for t in range(DT):
                st(tt(big4[:, t, :, :], E[:, t, :].rearrange("p (g e) -> p g e", g=8), gh4[:, t, :, :], ALU.mult))
            st.settle()
            for t in range(DT):
                st(nc.vector.tensor_reduce(ein[:, t, :], big4[:, t, :, :].rearrange("p g e -> p e g"), AX.X, ALU.add))
            st.settle()
            first_hot(e_hot[:, 0, :, :], ein[:, :, :], m1[:, :])
            st.link(stt(out=ein2[:, :, :], in0=e_hot[:, 0, :, :], scalar=-3e38, in1=ein[:, :, :], op0=ALU.mult, op1=ALU.add))
            first_hot(e_hot[:, 1, :, :], ein2[:, :, :], m2[:, :])
            st.link(tt(rat[:, :], m2[:, :], m1[:, :], ALU.subtract))
            dve.sem_inc(key_ready, 1)
            for j in range(2):
                for t in range(DT):
                    st(tt(hot[:, j, t, :].rearrange("p (g e) -> p g e", g=8), gh4[:, t, :, :],
                          e_hot[:, j, t, :].unsqueeze(1).to_broadcast([P, 8, 8]), ALU.mult))
            st.settle()
            tt(hot[:, 2, :, :], hot[:, 0, :, :], hot[:, 1, :, :], ALU.add).then_inc(hot_ready, 1)
            dve.wait_ge(exp_done, 2)
            st.link(nc.vector.reduce_sum(gsum[:, :], g_exp[:, :, :], AX.X))
            st.link(stt(out=rden[:, :], in0=rat[:, :], scalar=1.0, in1=gsum[:, :], op0=ALU.add, op1=ALU.mult))
            st.link(nc.vector.reciprocal(gates[:, 0, :], rden[:, :]))
            st.link(tt(gates[:, 1, :], gates[:, 0, :], rat[:, :], ALU.mult))
            dve.wait_ge(count_ready, 1)
            st.link(ts(cnt[:, :], ss[:, 1, 0:64], float(BS - 1), None, ALU.add))
            st.link(nc.vector.tensor_copy(ci[:, 0, :], cnt[:, :]))
            st.link(ts(ci[:, 1, :], ci[:, 0, :], 6, 6, ALU.arith_shift_right, ALU.logical_shift_left))
            st.link(nc.vector.tensor_copy(padded[:, :], ci[:, 1, :]))
            st.link(nc.vector.tensor_tensor_scan(pend[:, :], ones[:, 0:64], padded[:, :], 0.0, ALU.mult, ALU.add))
            st.link(tt(pstart[:, :], pend[:, :], padded[:, :], ALU.subtract))
            st.link(ts(be[:, :], pend[:, :], C[:, CONST["block_start"]:CONST["block_start"] + 1], None, ALU.is_le))
            st.link(nc.vector.reduce_sum(bcol[:, 0:1], be[:, :], AX.X))
            ts(bcol[:, 1:2], bcol[:, 0:1], float(N_EXP - 1), None, ALU.min).then_inc(bcol_ready, 1)
            st.link(tt(slot[:, :, :], ss[:, 0, :].rearrange("p (t e) -> p t e", t=DT), pstart[:, :].unsqueeze(1).to_broadcast([P, DT, 64]), ALU.add))
            for j in range(2):
                st.link(tt(big[:, :, :], slot[:, :, :], hot[:, j, :, :], ALU.mult))
                st.link(nc.vector.reduce_sum(dest_f[:, j, :], big[:, :, :], AX.X))
            nc.vector.tensor_copy(dest[:, :, :], dest_f[:, :, :]).then_inc(dest_ready, 1)
            dve.wait_ge(brow_ready, 1)
            nc.vector.tensor_copy(blk_expert[:, 0:P], lp[0:1, 0, 0:P]).then_inc(dest_ready, 1)
            st.link(ts(be[0:1, 0:1], pend[0:1, 63:64], float(-1 - 2 * BS), None, ALU.add))
            st.link(nc.vector.tensor_copy(pairs_i[:, 0:1], be[0:1, 0:1]))
            ts(blk_expert[:, P:P + 1], pairs_i[:, 0:1], 7, None, ALU.arith_shift_right).then_inc(dest_ready, 1)

        @block.gpsimd
        def _(pool):
            nc.gpsimd.iota(tok_id[:, :], pattern=[[P, DT]], base=0, channel_multiplier=1).then_inc(id_ready, 1)
            pool.wait_ge(id_ready, 1)
            pool.wait_ge(table_zero, 16)
            pool.wait_ge(dest_ready, 1)
            for j in range(2):
                for t in range(DT):
                    pool.indirect_dma_start(table, bass.IndirectOffsetOnAxis(dest[:, j, t:t + 1], 0), tok_id[:, t:t + 1], None).then_inc(scattered, 16)
            pool.wait_ge(scattered, 16 * 2 * DT)


def expert_stage(nc, u_tok, table, w13, ew2, y_pad, blk_expert, C):
    FE = 256
    FC = 2 * FE // P
    with ExitStack() as ctx:
        sb = lambda n, s, d=F32: ctx.enter_context(nc.sbuf_tensor(f"ex_{n}", s, d))
        sem = stage_semaphores(nc, ctx, "ex")
        wa, wb = sb("wa", [P, 2, DT * 2 * FE]), sb("wb", [P, 2, 2 * DM])
        idx = sb("idx", [P, 1], U32)
        xb, xT = sb("xb", [P, DM]), sb("xT", [P, DT * P])
        s1, hT = sb("s1", [P, 2, 2 * BS]), sb("hT", [P, 2, 2 * BS])
        yb = sb("yb", [BS, 2, DM])
        xp = ctx.enter_context(nc.psum_tensor("ex_xp", [P, 2, 512], F32))
        ap_ = ctx.enter_context(nc.psum_tensor("ex_ap", [P, 2, 512], F32))
        yp = ctx.enter_context(nc.psum_tensor("ex_yp", [P, 4, 512], F32))
        wa_loaded = [sem(f"wa_loaded{i}") for i in range(2)]
        wb_loaded = [sem(f"wb_loaded{i}") for i in range(2)]
        stored = [sem(f"stored{i}") for i in range(2)]
        i_loaded, gathered, xp_ready, xT_low, xT_high, ap_ready, s1_ready, hT_ready, yp_ready, y_low, y_high, wait_held = (
            sem(n) for n in ("i_loaded", "gathered", "xp_ready", "xT_low", "xT_high", "ap_ready", "s1_ready", "hT_ready",
                             "yp_ready", "y_low", "y_high", "wait_held"))
        ident = C[:, CONST["ident"]:CONST["ident"] + P]

        def last_pair(eng):
            return eng.value_load(blk_expert[0:1, P:P + 1], min_val=MIN_PAIRS - 2, max_val=NBLK // 2 - 2) + 1

        def pair_loop(eng, end, body):
            body(0, True, False, False)
            body(1, False, True, False)
            with eng.Fori(2, end) as i:
                body(i, False, False, False)
            body(end, False, False, True)

        block = ctx.enter_context(nc.Block(no_gpsimd_drain=True))

        @block.sync
        def _(sp):
            def expert_of(i, u):
                return sp.value_load(blk_expert[0:1, bass.ds(2 * i + u, 1)], min_val=0, max_val=N_EXP - 1)

            def load_up(i, u, first):
                e = expert_of(i, u)
                if not first:
                    sp.wait_ge(ap_ready, 2 * i + (u - 1))
                sp.dma_start(wa[:, u, :], w13[bass.ds(e * P, P), :]).then_inc(wa_loaded[u], 16)

            def load_down(i, u, first):
                e = expert_of(i, u)
                if not first:
                    sp.wait_ge(yp_ready, 2 * i + (u - 1))
                sp.dma_start(wb[:, u, :], ew2[bass.ds(e * P, P), :]).then_inc(wb_loaded[u], 16)

            def body(i, first, second, last):
                load_up(i, 0, first)
                if not first:
                    load_down(i - 1, 1, second)
                load_up(i, 1, first)
                load_down(i, 0, first)

            end = last_pair(sp)
            pair_loop(sp, end, body)
            load_down(end, 1, False)

        @block.gpsimd
        def _(pool):
            def fetch(i, first):
                if not first:
                    pool.wait_ge(xp_ready, i)
                pool.dma_start(idx[:, :], table[bass.ds(i * P, P), :].bitcast(U32)).then_inc(i_loaded, 16)
                pool.wait_ge(i_loaded, 16 * i + 16)
                pool.sem_inc(wait_held, 1)
                pool.indirect_dma_start(xb[:, :], None, u_tok, bass.IndirectOffsetOnAxis(idx[:, 0:1], 0)).then_inc(gathered, 16)

            def store(i, u):
                pool.wait_ge(y_low, 2 * i + (u + 1))
                pool.wait_ge(y_high, 2 * i + (u + 1))
                pool.dma_start(y_pad[bass.ds(i * (2 * BS) + u * BS, BS), :], yb[:, u, :]).then_inc(stored[u], 16)

            fetch(0, True)

            def body(i, first, second, last):
                if not last:
                    fetch(i + 1, False)
                if not first:
                    store(i - 1, 1)
                store(i, 0)

            end = last_pair(pool)
            pair_loop(pool, end, body)
            store(end, 1)
            for u in range(2):
                pool.wait_ge(stored[u], 16 * end + 16)

        @block.tensor
        def _(pe):
            def turn(i, first):
                pe.wait_ge(gathered, 16 * i + 16)
                if not first:
                    pe.wait_ge(xT_low, i)
                    pe.wait_ge(xT_high, i)
                for k in range(DT):
                    mm = pe.transpose(xp[:, k // 4, (k % 4) * P:(k % 4 + 1) * P], xb[:, k * P:(k + 1) * P], ident)
                mm.then_inc(xp_ready, 1)

            def up(i, u, first):
                if u == 0:
                    pe.wait_ge(xT_low, i + 1)
                    pe.wait_ge(xT_high, i + 1)
                pe.wait_ge(wa_loaded[u], 16 * i + 16)
                if not first:
                    pe.wait_ge(hT_ready, 2 * i + (u - 1))
                for c in range(FC):
                    for k in range(DT):
                        mm = pe.matmul(ap_[:, u, c * BS:(c + 1) * BS], wa[:, u, k * 512 + c * P:k * 512 + (c + 1) * P],
                                       xT[:, k * P + u * BS:k * P + (u + 1) * BS], start=k == 0, stop=k == DT - 1)
                mm.then_inc(ap_ready, 1)

            def down(i, u, first):
                pe.wait_ge(hT_ready, 2 * i + (u + 1))
                pe.wait_ge(wb_loaded[u], 16 * i + 16)
                if not first:
                    pe.wait_ge(y_low, 2 * i + (u - 1))
                    pe.wait_ge(y_high, 2 * i + (u - 1))
                for n in range(2):
                    for k in range(2):
                        mm = pe.matmul(yp[0:BS, 2 * u + n, :], hT[:, u, k * BS:(k + 1) * BS], wb[:, u, k * DM + n * 512:k * DM + (n + 1) * 512],
                                       start=k == 0, stop=k == 1)
                mm.then_inc(yp_ready, 1)

            turn(0, True)

            def body(i, first, second, last):
                up(i, 0, first)
                if not first:
                    down(i - 1, 1, second)
                up(i, 1, first)
                if not last:
                    turn(i + 1, False)
                down(i, 0, first)

            end = last_pair(pe)
            pair_loop(pe, end, body)
            down(end, 1, False)

        @block.scalar
        def _(act):
            def x_copy(i):
                act.wait_ge(xp_ready, i + 1)
                nc.scalar.copy(xT[:, 0:512], xp[:, 0, :]).then_inc(xT_low, 1)

            def gate(i, u, first):
                act.wait_ge(ap_ready, 2 * i + (u + 1))
                if not first:
                    act.wait_ge(hT_ready, 2 * i + (u - 1))
                nc.scalar.activation(s1[:, u, :], ap_[:, u, 0:2 * BS], ACT.Silu).then_inc(s1_ready, 1)

            def y_copy(i, u, first):
                act.wait_ge(yp_ready, 2 * i + (u + 1))
                if not first:
                    act.wait_ge(stored[u], 16 * i)
                nc.scalar.copy(yb[:, u, 0:512], yp[0:BS, 2 * u, :]).then_inc(y_low, 1)

            x_copy(0)

            def body(i, first, second, last):
                gate(i, 0, first)
                if not first:
                    y_copy(i - 1, 1, second)
                gate(i, 1, first)
                if not last:
                    x_copy(i + 1)
                y_copy(i, 0, first)

            end = last_pair(act)
            pair_loop(act, end, body)
            y_copy(end, 1, False)

        @block.vector
        def _(dve):
            def x_copy(i):
                dve.wait_ge(xp_ready, i + 1)
                nc.vector.tensor_copy(xT[:, 512:], xp[:, 1, :]).then_inc(xT_high, 1)

            def product(i, u, first):
                dve.wait_ge(s1_ready, 2 * i + (u + 1))
                if not first:
                    dve.wait_ge(yp_ready, 2 * i + (u - 1))
                nc.vector.tensor_tensor(hT[:, u, :], ap_[:, u, 2 * BS:4 * BS], s1[:, u, :], ALU.mult).then_inc(hT_ready, 1)

            def y_copy(i, u, first):
                dve.wait_ge(yp_ready, 2 * i + (u + 1))
                if not first:
                    dve.wait_ge(stored[u], 16 * i)
                nc.vector.tensor_copy(yb[:, u, 512:], yp[0:BS, 2 * u + 1, :]).then_inc(y_high, 1)

            x_copy(0)

            def body(i, first, second, last):
                product(i, 0, first)
                if not first:
                    y_copy(i - 1, 1, second)
                product(i, 1, first)
                if not last:
                    x_copy(i + 1)
                y_copy(i, 0, first)

            end = last_pair(dve)
            pair_loop(dve, end, body)
            y_copy(end, 1, False)


def combine_stage(nc, resid, y_pad, out, dest, gates, C):
    with ExitStack() as ctx:
        sb = lambda n, s, d=F32: ctx.enter_context(nc.sbuf_tensor(f"co_{n}", s, d))
        sem = stage_semaphores(nc, ctx, "co")
        x = sb("x", [P, DT, SEQ])
        y1, y2, acc, o = sb("y1", [P, 2, DM]), sb("y2", [P, 2, DM]), sb("acc", [P, 2, DM]), sb("o", [P, 2, DM])
        tr = ctx.enter_context(nc.psum_tensor("co_tr", [P, 4, 512], F32))
        loaded, tr_ready, acc_ready, o_ready = (sem(n) for n in ("loaded", "tr_ready", "acc_ready", "o_ready"))
        gathered = [sem(f"gathered{i}") for i in range(2)]
        stored = [sem(f"stored{i}") for i in range(2)]
        block = ctx.enter_context(nc.Block(no_gpsimd_drain=True))

        @block.sync
        def _(sp):
            for k in range(DT):
                sp.dma_start(x[:, k, :], resid[k]).then_inc(loaded, 16)
            for t in range(DT):
                sp.wait_ge(o_ready, t + 1)
                sp.dma_start(out[t * P:(t + 1) * P, :], o[:, t % 2, :]).then_inc(stored[t % 2], 16)
            for u in range(2):
                sp.wait_ge(stored[u], 16 * DT // 2)

        @block.gpsimd
        def _(pool):
            for t in range(DT):
                u = t % 2
                if t >= 2:
                    pool.wait_ge(o_ready, t - 1)
                for j, y in enumerate((y1, y2)):
                    pool.indirect_dma_start(y[:, u, :], None, y_pad, bass.IndirectOffsetOnAxis(dest[:, j, t:t + 1], 0)).then_inc(gathered[u], 16)

        @block.tensor
        def _(pe):
            pe.wait_ge(loaded, 16 * DT)
            for t in range(DT):
                u = t % 2
                if t >= 2:
                    pe.wait_ge(acc_ready, t - 1)
                for k in range(DT):
                    mm = pe.transpose(tr[:, 2 * u + k // 4, (k % 4) * P:(k % 4 + 1) * P], x[:, k, t * P:(t + 1) * P],
                                      C[:, CONST["ident"]:CONST["ident"] + P])
                mm.then_inc(tr_ready, 1)

        @block.vector
        def _(dve):
            for t in range(DT):
                u = t % 2
                dve.wait_ge(gathered[u], 32 * (t // 2 + 1))
                dve.wait_ge(tr_ready, t + 1)
                if t >= 2:
                    dve.wait_ge(o_ready, t - 1)
                nc.vector.scalar_tensor_tensor(out=acc[:, u, :], in0=y1[:, u, :], scalar=gates[:, 0, t:t + 1],
                                               in1=tr[:, 2 * u:2 * u + 2, :].rearrange("p a b -> p (a b)"), op0=ALU.mult, op1=ALU.add).then_inc(acc_ready, 1)
                dve.wait_ge(acc_ready, t + 1)
                if t >= 2:
                    dve.wait_ge(stored[u], 16 * (t // 2))
                nc.vector.scalar_tensor_tensor(out=o[:, u, :], in0=y2[:, u, :], scalar=gates[:, 1, t:t + 1],
                                               in1=acc[:, u, :], op0=ALU.mult, op1=ALU.add).then_inc(o_ready, 1)
def program(nc, a, out):
    scratch = lambda name, *shape, d=F32: nc.dram_tensor(f"s_{name}", shape, d, kind="Internal").ap()
    proj = scratch("proj", 28, P, SEQ)
    cat = scratch("cat", 8, P, SEQ)
    scr = {n: scratch(n, *s) for n, s in (("ar", (4, P, 2 * SEQ)), ("bt", (4, P, SEQ)), ("kt", (4, P, SEQ)), ("v", (4, P, SEQ)),
                                          ("bonus", (4, P, SEQ)), ("g", (4, P, SEQ)), ("scale", (4, P, NCH)), ("y", (4, P, SEQ)))}
    x1, x2, h0, h1 = (scratch(n, DT, P, SEQ) for n in ("x1", "x2", "h0", "h1"))
    ffn = scratch("ffn", 22, P, SEQ)
    proj2 = scratch("proj2", 38, P, SEQ)
    hg, br_a, merged, att = (scratch(n, DT, P, SEQ) for n in ("hg", "br_a", "merged", "att"))
    qT, kvT = scratch("qT", 16, P, SEQ), scratch("kvT", 16, P, SEQ)
    u_tok, y_pad = scratch("u_tok", SEQ, DM), scratch("y_pad", NBLK * BS, DM)
    table = scratch("table", NBLK * BS, 1, d=I32)
    with ExitStack() as ctx:
        V = ctx.enter_context(nc.sbuf_tensor("vecs_sb", [P, NVEC], F32))
        C = ctx.enter_context(nc.sbuf_tensor("consts_sb", [P, NCONST], F32))
        s = ctx.enter_context(nc.semaphore("params_loaded"))
        with nc.Block(no_gpsimd_drain=True) as block:
            @block.sync
            def _(sp):
                sp.dma_start(V[:], a["vecs"]).then_inc(s, 16)
                sp.dma_start(C[:], a["consts"]).then_inc(s, 16)
                sp.wait_ge(s, 32)
        vecs = {"buf": V, "ffn_conv": VEC["ffn_conv"], "ffn_conv_b": VEC["ffn_conv_b"]}
        consts = {"buf": C, "ones": C[:, CONST["ones"]:CONST["ones"] + P]}
        eps = CONST["eps6"]

        def dense(name, src, KT, w, NT, out_, **kw):
            dense_stage(nc, name, src, KT, a[w], NT, out_, vecs, consts, **kw)

        dense("in1", a["xT"], 8, "w_in", 28, proj, norm=(VEC["norm1"], eps, DM))
        mlstm_stage(nc, proj, cat[4:8], V, C)
        rwkv_prepare_stage(nc, proj, a["lora"], a["w_up_g"], scr, V, C)
        rwkv_scan_stage(nc, scr, a["masks"], C)
        rwkv_finish_stage(nc, scr, cat[0:4], V, C)
        dense("out1", cat, 8, "w_out", 8, x1, mode="residual", aux=a["xT"])
        dense("up", x1, 8, "w_up", 44, ffn, norm=(VEC["norm2"], eps, DM), mode="ffn")
        dense("down", ffn, 22, "w_down", 8, x2, mode="residual", aux=x1, tokens=HALF)
        norm_stage(nc, x2, h0, VEC["norm_f"], eps, V, C)
        dense("in2", h0, 8, "w_in2", 38, proj2, norm=(VEC["norm1_2"], eps, DM))
        lru_stage(nc, proj2, a["lru_w"], hg, V, C)
        dense("uq", proj2[16:18], 2, "w_uq", 16, qT, norm=(VEC["q_norm"], eps, 256))
        dense("ukv", proj2[18:20], 2, "w_ukv", 16, kvT, norm=(VEC["kv_norm"], eps, 256))
        attention_stage(nc, proj2, qT, kvT, a["positions"], att, V, C)
        dense("rnn_o", hg, 8, "w_rnn_o", 8, br_a, mode="gate", aux=proj2[22:30])
        dense("mla_o", att, 8, "w_mla_o", 8, merged, mode="gate_add", aux=proj2[30:38], aux2=br_a)
        dense("out2", merged, 8, "w_out2", 8, h1, mode="residual", aux=h0)
        dest = ctx.enter_context(nc.sbuf_tensor("dest", [P, 2, DT], U32))
        gates = ctx.enter_context(nc.sbuf_tensor("gates", [P, 2, DT], F32))
        blk_expert = ctx.enter_context(nc.sbuf_tensor("blk_expert", [1, P + 1], I32))
        router_stage(nc, h1, a["router"], a["router_b"], u_tok, table, y_pad, dest, gates, blk_expert, V, C)
        expert_stage(nc, u_tok, table, a["w13"], a["ew2"], y_pad, blk_expert, C)
        combine_stage(nc, h1, y_pad, out, dest, gates, C)


def kernel(**inputs):
    import concourse.bacc as bacc
    from concourse.bass_utils import run_bass_kernel_spmd

    nc = bacc.Bacc("TRN2", target_bir_lowering=False, num_devices=1)
    arrays = {f"in_{k}": v for k, v in lay_out(inputs).items()}
    aps = {k[3:]: nc.dram_tensor(k, v.shape, mybir.dt.from_np(v.dtype), kind="ExternalInput").ap() for k, v in arrays.items()}
    out = nc.dram_tensor("out", (SEQ, DM), F32, kind="ExternalOutput").ap()
    program(nc, aps, out)
    r = run_bass_kernel_spmd(nc, [arrays], core_ids=[0])
    return r.results[0]["out"].reshape(1, SEQ, DM)
```

```python
from contextlib import ExitStack

import numpy as np

import concourse.bass as bass
from concourse import mybir

F32 = mybir.dt.float32
F32R = mybir.dt.float32r
I32 = mybir.dt.int32
U32 = mybir.dt.uint32
ALU = mybir.AluOpType
ACT = mybir.ActivationFunctionType
AX = mybir.AxisListType

P = 128
SEQ = 1024
HALF = 512
DM = 1024
DT = DM // P


def stage_semaphores(nc, ctx, prefix):
    held = []

    def give_back():
        nc.clear_and_free_semaphores(held)
        nc.all_engine_barrier()

    ctx.callback(give_back)

    def sem(name):
        held.append(nc.alloc_semaphore(f"{prefix}_{name}"))
        return held[-1]

    return sem


def run_loop(eng, n, body):
    body(0, True, n == 1)
    if n > 2:
        with eng.Fori(1, n - 1) as i:
            body(i, False, False)
    if n > 1:
        body(n - 1, False, True)


def split_matmuls(pe, out, w_hi, w_lo, x_hi, x_lo, first, last):
    pe.matmul(out, w_hi, x_hi, start=first, stop=False)
    pe.matmul(out, w_hi, x_lo, start=False, stop=False)
    return pe.matmul(out, w_lo, x_hi, start=False, stop=last)


def dense_stage(nc, name, src, KT, w, NT, out, vecs, consts, tokens=SEQ, norm=None, mode="copy",
                aux=None, aux2=None, norm_out=None):
    PASSES = SEQ // tokens
    NH = tokens // HALF
    N = NT // 2
    TT = tokens // P
    with ExitStack() as ctx:
        sb = lambda n, s, d=F32: ctx.enter_context(nc.sbuf_tensor(f"{name}_{n}", s, d))
        psum = lambda n, s: ctx.enter_context(nc.psum_tensor(f"{name}_{n}", s, F32))
        sem = stage_semaphores(nc, ctx, name)
        x_hi = sb("x_hi", [P, KT, tokens], F32R)
        x_lo = sb("x_lo", [P, KT, tokens], F32R)
        w_raw = sb("w_raw", [P, 2, KT * P])
        OWN = 2 if PASSES == 1 else 0
        w_hi = sb("w_hi", [P, 2 + OWN, KT * P], F32R)
        w_lo = sb("w_lo", [P, 2 + OWN, KT * P], F32R)
        XS = KT if PASSES == 1 else 6
        x_raw = sb("x_raw", [P, XS, tokens])
        o_buf = sb("o_buf", [P, 1 if mode == "ffn" else 2, tokens])
        acc = psum("acc", [P, 4, HALF])
        x_loaded = [sem(f"x_loaded{i}") for i in range(XS)]
        w_loaded = [sem(f"w_loaded{i}") for i in range(2)]
        x_split = sem("x_split")
        x_hi_done = sem("x_hi_done")
        w_hi_done = sem("w_hi_done")
        w_lo_done = sem("w_lo_done")
        acc_ready = sem("acc_ready")
        acc_free = sem("acc_free")
        out_ready = sem("out_ready")
        stored = [sem(f"stored{i}") for i in range(2)]
        if norm:
            gain, eps_col, width = norm
            sq = sb("sq", [P, 3, tokens])
            sq_sum = sb("sq_sum", [P, tokens])
            rms, inv = sb("rms", [P, TT]), sb("inv", [P, TT])
            diag = sb("diag", [P, TT, P])
            rstd = sb("rstd", [P, tokens])
            ss = psum("ss", [P, HALF])
            spread = psum("spread", [P, 2, HALF])
            sq_ready, sum_ready, ss_ready, rms_ready, inv_ready, diag_ready, spread_ready, rstd_ready = (
                sem(n) for n in ("sq_ready", "sum_ready", "ss_ready", "rms_ready", "inv_ready", "diag_ready", "spread_ready", "rstd_ready"))
        if aux is not None:
            aux_buf = sb("aux", [P, 2, tokens])
            aux_loaded = [sem(f"aux_loaded{i}") for i in range(2)]
            if mode.startswith("gate"):
                sig = sb("sig", [P, 2, tokens])
                sig_ready = sem("sig_ready")
                prod_done = sem("prod_done")
        if aux2 is not None:
            aux2_buf = sb("aux2", [P, 2, tokens])
        if mode == "ffn":
            cw, cb = vecs["ffn_conv"], vecs["ffn_conv_b"]
            a_pad = sb("a_pad", [P, tokens + 2])
            conv = sb("conv", [P, 2, tokens])
            act, act_n = sb("act", [P, tokens]), sb("act_n", [P, tokens])
            pad_zero = sem("pad_zero")
            conv_step = sem("conv_step")
            act_ready = sem("act_ready")
            act_scaled = sem("act_scaled")
            a_copied = sem("a_copied")
        V = vecs["buf"]
        NO = N if mode == "ffn" else NT
        block = ctx.enter_context(nc.Block(no_gpsimd_drain=True))

        @block.sync
        def _(sp):
            for p in range(PASSES):
                tok = slice(p * tokens, (p + 1) * tokens)
                for u in range(2):
                    if p:
                        sp.wait_ge(w_lo_done, p * NT - 1 + u)
                    sp.dma_start(w_raw[:, u, :], w[u]).then_inc(w_loaded[u], 16)
                for k in range(KT):
                    if p * KT + k >= XS:
                        sp.wait_ge(x_split, p * KT + k - XS + 1)
                    sp.dma_start(x_raw[:, (p * KT + k) % XS, :], src[k][:, tok]).then_inc(x_loaded[(p * KT + k) % XS], 16)
                if N > 1:
                    with sp.Fori(1, N) as i:
                        for u in range(2):
                            sp.wait_ge(w_lo_done, 2 * i + (p * NT + u - 1))
                            sp.dma_start(w_raw[:, u, :], w[2 * i + u]).then_inc(w_loaded[u], 16)

        @block.scalar
        def _(act_e):
            def high_part(u, w_count, last_use, slot):
                act_e.wait_ge(w_loaded[u], w_count)
                if last_use is not None:
                    act_e.wait_ge(acc_ready, last_use)
                nc.scalar.copy(w_hi[:, slot, :], w_raw[:, u, :]).then_inc(w_hi_done, 1)

            for p in range(PASSES):
                for u in range(2):
                    high_part(u, 16 * (p * N + 1), (p * NT - 1 + u) * NH if p else None, OWN + u)
                for k in range(KT):
                    act_e.wait_ge(x_loaded[(p * KT + k) % XS], 16 * ((p * KT + k) // XS + 1))
                    if p and k == 0:
                        act_e.wait_ge(acc_ready, p * NT * NH)
                    if norm:
                        nc.scalar.activation(x_hi[:, k, :], x_raw[:, k, :], ACT.Copy, scale=V[:, gain + k:gain + k + 1]).then_inc(x_hi_done, 1)
                        if k >= 3:
                            act_e.wait_ge(sum_ready, k - 2)
                        nc.scalar.activation(sq[:, k % 3, :], x_raw[:, k, :], ACT.Square).then_inc(sq_ready, 1)
                    else:
                        nc.scalar.copy(x_hi[:, k, :], x_raw[:, (p * KT + k) % XS, :]).then_inc(x_hi_done, 1)
                for u in range(OWN):
                    high_part(u, 32, None, u)
                if norm:
                    act_e.wait_ge(ss_ready, 1)
                    nc.scalar.activation(rms[:, :], ss[:, 0:TT], ACT.Sqrt, bias=consts["buf"][:, eps_col:eps_col + 1],
                                         scale=1.0 / width).then_inc(rms_ready, 1)
                    act_e.wait_ge(spread_ready, 1)
                    nc.scalar.copy(rstd[:, :], spread[:, :, :].rearrange("p a b -> p (a b)")).then_inc(rstd_ready, 1)

                def body(i, first, last, p=p):
                    for u in range(2):
                        if mode.startswith("gate"):
                            act_e.wait_ge(aux_loaded[u], (32 if aux2 is not None else 16) * i + (32 if aux2 is not None else 16))
                            if not first:
                                act_e.wait_ge(prod_done, 2 * i + u - 1)
                            nc.scalar.activation(sig[:, u, :], aux_buf[:, u, :], ACT.Sigmoid).then_inc(sig_ready, 1)
                        if not last and not (first and OWN):
                            high_part(u, 16 * i + 16 * (p * N + 2), (2 * NH) * i + (p * NT + u + 1) * NH, u)
                        if mode == "ffn" and u == 0:
                            act_e.wait_ge(conv_step, 3 * i + 3)
                            if not first:
                                act_e.wait_ge(act_scaled, i)
                            nc.scalar.activation(act[:, :], conv[:, 0, :], ACT.Silu).then_inc(act_ready, 1)

                run_loop(act_e, N, body)

        @block.tensor
        def _(pe):
            def products(u, h, k, slot):
                ks, hs = slice(k * P, (k + 1) * P), slice(h * HALF, (h + 1) * HALF)
                return split_matmuls(pe, acc[:, u * NH + h, :], w_hi[:, slot, ks], w_lo[:, slot, ks],
                                     x_hi[:, k, hs], x_lo[:, k, hs], k == 0, k == KT - 1)

            for p in range(PASSES):
                def first_turn(p=p):
                    pe.wait_ge(w_lo_done, p * NT + 2)
                    if p:
                        pe.wait_ge(acc_free, p * NT * NH)
                    for k in range(KT):
                        if norm and k == KT - 1:
                            pe.wait_ge(sum_ready, KT - 1)
                            for t in range(TT):
                                mm = pe.matmul(ss[:, t:t + 1], sq_sum[:, t * P:(t + 1) * P], consts["ones"][:, 0:1],
                                               start=True, stop=True, skip_group_check=True)
                            mm.then_inc(ss_ready, 1)
                        pe.wait_ge(x_split, p * KT + k + 1)
                        for u in range(2):
                            for h in range(NH):
                                mm = products(u, h, k, OWN + u)
                                if k == KT - 1:
                                    mm.then_inc(acc_ready, 1)
                    if norm:
                        pe.wait_ge(diag_ready, 1)
                        for h in range(NH):
                            mm = pe.matmul(spread[:, h, :], consts["ones"], diag[:, 4 * h:4 * h + 4, :].rearrange("p a b -> p (a b)"),
                                           start=True, stop=True)
                        mm.then_inc(spread_ready, 1)

                def body(i, first, last, p=p, first_turn=first_turn):
                    if first:
                        first_turn()
                        return
                    for u in range(2):
                        pe.wait_ge(w_lo_done, 2 * i + (p * NT + u + 1))
                        for h in range(NH):
                            pe.wait_ge(acc_free, (2 * NH) * i + (p * NT + u - 2) * NH + h + 1)
                            for k in range(KT):
                                mm = products(u, h, k, u)
                            mm.then_inc(acc_ready, 1)

                run_loop(pe, N, body)

        @block.vector
        def _(dve):
            if mode == "ffn":
                nc.vector.memset(a_pad[:, 0:2], 0.0).then_inc(pad_zero, 1)
                dve.wait_ge(pad_zero, 1)

            def low_part(t_u, t_count, slot):
                dve.wait_ge(w_hi_done, t_count)
                nc.vector.tensor_tensor(w_lo[:, slot, :], w_raw[:, t_u, :], w_hi[:, slot, :], ALU.subtract).then_inc(w_lo_done, 1)

            for p in range(PASSES):
                for u in range(2):
                    low_part(u, p * NT + u + 1, OWN + u)
                for k in range(KT):
                    dve.wait_ge(x_hi_done, p * KT + k + 1)
                    if norm:
                        nc.vector.scalar_tensor_tensor(out=x_lo[:, k, :], in0=x_raw[:, k, :], scalar=V[:, gain + k:gain + k + 1],
                                                       in1=x_hi[:, k, :], op0=ALU.mult, op1=ALU.subtract).then_inc(x_split, 1)
                    else:
                        nc.vector.tensor_tensor(x_lo[:, k, :], x_raw[:, (p * KT + k) % XS, :], x_hi[:, k, :], ALU.subtract).then_inc(x_split, 1)
                for u in range(OWN):
                    low_part(u, u + 3, u)
                if norm:
                    dve.wait_ge(rms_ready, 1)
                    nc.vector.reciprocal(inv[:, :], rms[:, :]).then_inc(inv_ready, 1)
                    dve.wait_ge(inv_ready, 1)
                    nc.vector.tensor_tensor(diag[:, :, :], consts["ident"].unsqueeze(1).to_broadcast([P, TT, P]),
                                            inv[:, :].unsqueeze(2).to_broadcast([P, TT, P]), ALU.mult).then_inc(diag_ready, 1)
                    dve.wait_ge(rstd_ready, 1)

                def body(i, first, last, p=p):
                    for u in range(2):
                        if mode == "ffn":
                            ffn_part(i, u, first, last)
                            continue
                        if not (first and p == 0):
                            dve.wait_ge(stored[u], 16 * i + 16 * p * N)
                        if aux is not None and not mode.startswith("gate"):
                            dve.wait_ge(aux_loaded[u], 16 * i + 16 * (p * N + 1))
                        if mode.startswith("gate"):
                            dve.wait_ge(sig_ready, 2 * i + u + 1)
                        for h in range(NH):
                            hs = slice(h * HALF, (h + 1) * HALF)
                            dve.wait_ge(acc_ready, (2 * NH) * i + (p * NT + u) * NH + h + 1)
                            a = acc[:, u * NH + h, :]
                            if mode == "copy" and norm:
                                ins = nc.vector.tensor_tensor(o_buf[:, u, hs], a, rstd[:, hs], ALU.mult)
                            elif mode == "copy":
                                ins = nc.vector.tensor_copy(o_buf[:, u, hs], a)
                            elif mode == "residual":
                                ins = nc.vector.tensor_tensor(o_buf[:, u, hs], a, aux_buf[:, u, hs], ALU.add)
                            else:
                                ins = nc.vector.tensor_tensor(o_buf[:, u, hs], a, sig[:, u, hs], ALU.mult)
                            ins.then_inc(acc_free, 1)
                        if mode == "gate_add":
                            dve.wait_ge(acc_free, (2 * NH) * i + (u + 1) * NH)
                            nc.vector.tensor_tensor(o_buf[:, u, :], o_buf[:, u, :], aux2_buf[:, u, :],
                                                    ALU.add).then_inc(prod_done, 1)
                        elif mode == "gate":
                            dve.wait_ge(acc_free, (2 * NH) * i + (u + 1) * NH)
                            dve.sem_inc(prod_done, 1)
                        if not last and not (first and OWN):
                            low_part(u, 2 * i + (p * NT + u + 3), u)

                def ffn_part(i, u, first, last):
                    if u == 0:
                        for h in range(NH):
                            dve.wait_ge(acc_ready, (2 * NH) * i + h + 1)
                            nc.vector.tensor_tensor(a_pad[:, 2 + h * HALF:2 + (h + 1) * HALF], acc[:, h, :],
                                                    rstd[:, h * HALF:(h + 1) * HALF], ALU.mult).then_inc(acc_free, 1)
                        if not last and not (first and OWN):
                            low_part(0, 2 * i + 3, 0)
                        dve.wait_ge(acc_free, (2 * NH) * i + NH)
                        nc.vector.tensor_scalar(conv[:, 0, :], a_pad[:, 2:2 + tokens], V[:, bass.ds(cw + 2 * N + i, 1)],
                                                V[:, bass.ds(cb + i, 1)], ALU.mult, ALU.add).then_inc(conv_step, 1)
                        dve.wait_ge(conv_step, 3 * i + 1)
                        nc.vector.scalar_tensor_tensor(out=conv[:, 1, :], in0=a_pad[:, 1:1 + tokens],
                                                       scalar=V[:, bass.ds(cw + N + i, 1)], in1=conv[:, 0, :],
                                                       op0=ALU.mult, op1=ALU.add).then_inc(conv_step, 1)
                        dve.wait_ge(conv_step, 3 * i + 2)
                        nc.vector.scalar_tensor_tensor(out=conv[:, 0, :], in0=a_pad[:, 0:tokens],
                                                       scalar=V[:, bass.ds(cw + i, 1)], in1=conv[:, 1, :],
                                                       op0=ALU.mult, op1=ALU.add).then_inc(conv_step, 1)
                    else:
                        dve.wait_ge(act_ready, i + 1)
                        if not first:
                            dve.wait_ge(out_ready, i)
                        nc.vector.tensor_tensor(act_n[:, :], act[:, :], rstd[:, :], ALU.mult).then_inc(act_scaled, 1)
                        dve.wait_ge(act_scaled, i + 1)
                        if not first:
                            dve.wait_ge(stored[0], 16 * i)
                        for h in range(NH):
                            hs = slice(h * HALF, (h + 1) * HALF)
                            dve.wait_ge(acc_ready, (2 * NH) * i + NH + h + 1)
                            nc.vector.tensor_tensor(o_buf[:, 0, hs], acc[:, NH + h, :], act_n[:, hs],
                                                    ALU.mult).then_inc(acc_free, 1)
                        dve.wait_ge(acc_free, (2 * NH) * i + 2 * NH)
                        dve.sem_inc(out_ready, 1)
                        if not last and not (first and OWN):
                            low_part(1, 2 * i + 4, 1)

                run_loop(dve, N, body)

        @block.gpsimd
        def _(pool):
            if norm:
                for k in range(1, KT):
                    pool.wait_ge(sq_ready, k + 1)
                    if k >= 2:
                        pool.wait_ge(sum_ready, k - 1)
                    nc.gpsimd.tensor_tensor(sq_sum[:, :], sq[:, 0, :] if k == 1 else sq_sum[:, :], sq[:, k % 3, :],
                                            ALU.add).then_inc(sum_ready, 1)
            for p in range(PASSES):
                tok = slice(p * tokens, (p + 1) * tokens)

                def load_aux(i, u, p=p, tok=tok):
                    pool.dma_start(aux_buf[:, u, :], aux[2 * i + u][:, tok]).then_inc(aux_loaded[u], 16)
                    if aux2 is not None:
                        pool.dma_start(aux2_buf[:, u, :], aux2[2 * i + u][:, tok]).then_inc(aux_loaded[u], 16)

                if aux is not None:
                    for u in range(2):
                        if p:
                            pool.wait_ge(acc_free, (p * NT - 1 + u) * NH)
                        load_aux(0, u)

                def body(i, first, last, p=p, tok=tok, load_aux=load_aux):
                    if mode == "ffn":
                        pool.wait_ge(out_ready, i + 1)
                        pool.dma_start(out[i][:, tok], o_buf[:, 0, :]).then_inc(stored[0], 16)
                        return
                    for u in range(2):
                        if mode == "gate_add":
                            pool.wait_ge(prod_done, 2 * i + u + 1)
                        else:
                            pool.wait_ge(acc_free, (2 * NH) * i + (p * NT + u + 1) * NH)
                        pool.dma_start(out[2 * i + u][:, tok], o_buf[:, u, :]).then_inc(stored[u], 16)
                        if aux is not None and not last:
                            load_aux(i + 1, u)

                run_loop(pool, N, body)
            for u in range(1 if mode == "ffn" else 2):
                pool.wait_ge(stored[u], 16 * N * PASSES)
def _cols(v):
    return np.reshape(v, (-1, P)).T


def _tiles(w):
    K, N = w.shape
    return np.ascontiguousarray(np.transpose(np.reshape(w, (K // P, P, N // P, P)), (2, 1, 0, 3))).reshape(N // P, P, K)


def _vec_table():
    at, table = 0, {}
    for name, n in (("norm1", 8), ("mu", 14), ("w0", 4), ("a0", 4), ("k_k", 4), ("k_a", 4), ("r_k", 4), ("lnx_w", 4),
                    ("lnx_b", 4), ("qk_conv", 16), ("qk_conv_b", 4), ("i_bias", 1), ("f_bias", 1), ("mh_g", 4),
                    ("norm2", 8), ("ffn_conv", 66), ("ffn_conv_b", 22), ("norm_f", 8), ("norm1_2", 8), ("conv_2", 32),
                    ("conv_b_2", 8), ("lru_ba", 8), ("lru_bx", 8), ("lru_lam", 8), ("q_norm", 2), ("kv_norm", 2),
                    ("qg_n", 1), ("qg_r", 1), ("qg_s", 1), ("kg_n", 1), ("kg_r", 1), ("kg_s", 1), ("norm2_2", 8)):
        table[name] = at
        at += n
    return table, at


VEC, NVEC = _vec_table()


def _const_table():
    at, table = 0, {}
    for name, n in (("ones", P), ("ident", P), ("head_ones", P), ("before", P), ("upto", P), ("after", P), ("row_sel", 4 * P),
                    ("eps6", 1), ("eps_ln", 1), ("inv_freq", 1), ("rope_sign", 1), ("one", 1), ("iota64", 64), ("iota8", 8),
                    ("block_start", 1)):
        table[name] = at
        at += n
    return table, at


CONST, NCONST = _const_table()
LEVELS = 7


def constants():
    c = np.zeros((P, NCONST), np.float32)
    r, q = np.arange(P)[:, None], np.arange(P)[None, :]
    put = lambda name, a: c.__setitem__((slice(None), slice(CONST[name], CONST[name] + a.shape[1])), a)
    put("ones", np.ones((P, P)))
    put("ident", r == q)
    put("head_ones", r // 64 == q // 64)
    put("before", r < q)
    put("upto", r <= q)
    put("after", r > q)
    put("row_sel", np.concatenate([np.repeat(r == h, P, 1) for h in range(4)], 1))
    put("eps6", np.full((P, 1), 1e-6))
    put("eps_ln", np.full((P, 1), 64e-5))
    inv = (np.float32(10000.0) ** (-(np.arange(0, 64, 2, dtype=np.float32)) / np.float32(64))).astype(np.float32)
    put("inv_freq", np.tile(inv, 4)[:, None])
    put("rope_sign", np.where(r % 64 < 32, -1.0, 1.0))
    put("one", np.ones((P, 1)))
    put("iota64", np.tile(np.arange(64.0), (P, 1)))
    put("iota8", np.tile(np.arange(8.0), (P, 1)))
    put("block_start", r * 64.0)
    lv = []
    for l in range(LEVELS):
        b = 1 << l
        lv.append((r // (2 * b) == q // (2 * b)) & (r // b > q // b))
    masks = np.concatenate(lv + [m.T for m in lv], 1).astype(np.float32)
    return c, masks


def lay_out(a):
    v = np.zeros((P, NVEC), np.float32)

    def put(name, cols):
        v[:, VEC[name]:VEC[name] + cols.shape[1]] = cols

    L = {k: np.asarray(x)[0] for k, x in a.items() if k not in ("x", "norm_f_g", "positions_2")}
    for name, key in (("norm1", "norm1_g"), ("mu", "rw_mu"), ("w0", "w0"), ("a0", "a0"), ("k_k", "k_k"), ("k_a", "k_a"),
                      ("r_k", "r_k"), ("lnx_w", "lnx_w"), ("lnx_b", "lnx_b"), ("qk_conv", "qk_conv_w"),
                      ("qk_conv_b", "qk_conv_b"), ("mh_g", "mh_norm_g"), ("norm2", "norm2_g"), ("ffn_conv", "ffn_conv_w"),
                      ("ffn_conv_b", "ffn_conv_b"), ("norm1_2", "norm1_g_2"), ("conv_2", "conv_w_2"),
                      ("conv_b_2", "conv_b_2"), ("lru_ba", "lru_ba_2"), ("lru_bx", "lru_bx_2"), ("lru_lam", "lru_lambda_2"),
                      ("q_norm", "q_norm_g_2"), ("kv_norm", "kv_norm_g_2"), ("norm2_2", "norm2_g_2")):
        put(name, _cols(L[key]))
    put("norm_f", _cols(np.asarray(a["norm_f_g"])))
    v[0:4, VEC["i_bias"]] = L["i_bias"]
    v[0:4, VEC["f_bias"]] = L["f_bias"]
    swap = np.concatenate([np.arange(32, 64), np.arange(0, 32)])
    for c, key in (("qg", "qk_norm_q_g_2"), ("kg", "qk_norm_k_g_2")):
        v[:, VEC[c + "_n"]] = L[key][:128]
        v[:, VEC[c + "_r"]] = np.concatenate([L[key][128:]] * 2)
        v[:, VEC[c + "_s"]] = np.concatenate([L[key][128:][swap]] * 2)
    z = lambda n: np.zeros((DM, n), np.float32)
    w_in = L["w_in"]
    gates = np.concatenate([w_in[:, 3328:3332], z(28), w_in[:, 3332:3336], z(92)], 1)
    w_in_t = _tiles(np.concatenate([w_in[:, :3328], gates, z(128)], 1))
    up = L["w_ffn_up"]
    up = np.transpose(np.reshape(up, (DM, 2, 22, P)), (0, 2, 1, 3)).reshape(DM, 44 * P)
    w2 = L["w_in_2"]
    kpe = w2[:, 2560:2624]
    w_in2_t = _tiles(np.concatenate([w2[:, :2560], kpe, kpe, kpe[:, swap], kpe[:, swap], w2[:, 2624:]], 1))
    uq = np.reshape(L["w_uq_2"], (256, 8, 192))
    uq_t = _tiles(np.concatenate([uq[:, :, :128].reshape(256, -1), uq[:, :, 128:].reshape(256, -1),
                                  uq[:, :, 128:][:, :, swap].reshape(256, -1)], 1))
    ukv = np.reshape(L["w_ukv_2"], (256, 8, 2, 128))
    ukv_t = _tiles(np.transpose(ukv, (0, 2, 1, 3)).reshape(256, 2048))
    lora = np.concatenate([L["w_up_decay"], L["w_up_a"]], 0)
    router = np.concatenate([L["router_wg_2"], L["router_we_2"]], 1)
    router = np.transpose(np.reshape(router, (8, P, 72)), (1, 0, 2)).reshape(P, 8 * 72)
    w13 = np.concatenate([L["exp_w1_2"], L["exp_w3_2"]], 2)
    w13 = np.ascontiguousarray(np.transpose(np.reshape(w13, (64, 8, P, 512)), (0, 2, 1, 3))).reshape(64 * P, 4096)
    ew2 = np.ascontiguousarray(np.transpose(np.reshape(L["exp_w2_2"], (64, 2, P, DM)), (0, 2, 1, 3))).reshape(64 * P, 2048)
    lru_w = np.concatenate([np.transpose(L["lru_wa_2"], (1, 0, 2)).reshape(P, DM), np.transpose(L["lru_wx_2"], (1, 0, 2)).reshape(P, DM)], 1)
    consts, masks = constants()
    return {
        "xT": np.ascontiguousarray(np.asarray(a["x"])[0].T).reshape(DT, P, SEQ),
        "vecs": v, "consts": consts, "masks": masks,
        "w_in": w_in_t, "w_out": _tiles(L["w_out"]), "w_up": _tiles(up), "w_down": _tiles(L["w_ffn_down"]),
        "w_in2": w_in2_t, "w_rnn_o": _tiles(L["w_rnn_o_2"]), "w_mla_o": _tiles(L["w_mla_o_2"]), "w_out2": _tiles(L["w_out_2"]),
        "w_uq": uq_t, "w_ukv": ukv_t, "lora": lora, "w_up_g": L["w_up_g"], "router": router,
        "router_b": np.concatenate([L["router_bg_2"], L["router_be_2"]])[None, :],
        "w13": w13, "ew2": ew2, "lru_w": lru_w, "positions": np.asarray(a["positions_2"]),
    }
class Steps:

    def __init__(self, eng, sem):
        self.eng, self.sem, self.n = eng, sem, 0

    def __call__(self, ins):
        ins.then_inc(self.sem, 1)
        self.n += 1
        return self.n

    def settle(self):
        self.eng.wait_ge(self.sem, self.n)

    def link(self, ins):
        self(ins)
        self.settle()


def mlstm_stage(nc, proj, y_out, V, C):
    NH, DK, CAP = 4, 64, 15.0
    q0, v0, o0, gate = 14, 18, 22, 26
    one = lambda name, h=0: C[:, CONST[name] + h:CONST[name] + h + 1]
    with ExitStack() as ctx:
        sb = lambda n, s, d=F32: ctx.enter_context(nc.sbuf_tensor(f"ml_{n}", s, d))
        sem = stage_semaphores(nc, ctx, "ml")
        qk = sb("qk", [P, 4, SEQ])
        v_tok = sb("v_tok", [P, DT, NH * P])
        g_cols = sb("g_cols", [P, DT, NH])
        neg_G = sb("neg_G", [P, NH, SEQ])
        exp_m = sb("exp_m", [P, NH, SEQ])

        with ExitStack() as ctx1:
            sb1 = lambda n, s, d=F32: ctx1.enter_context(nc.sbuf_tensor(f"ml_{n}", s, d))
            pre = sb1("pre", [P, 4, SEQ + 3])
            conv = sb1("conv", [P, 2, 2, SEQ])
            vT = sb1("vT", [P, 4, SEQ])
            ig = sb1("ig", [NH, SEQ])
            fg = sb1("fg", [NH, SEQ])
            row_t = sb1("row_t", [NH, 4, SEQ])
            ones_row = sb1("ones_row", [NH, SEQ])
            cap_b = sb1("cap_b", [NH, 2])
            tr = ctx1.enter_context(nc.psum_tensor("ml_tr", [P, 2, 512], F32))
            bc = ctx1.enter_context(nc.psum_tensor("ml_bc", [P, 4, 512], F32))
            gc = ctx1.enter_context(nc.psum_tensor("ml_gc", [P, 512], F32))
            qk_loaded = [sem(f"qk_loaded{i}") for i in range(4)]
            v_loaded, gates_loaded, pads = sem("v_loaded"), sem("gates_loaded"), sem("pads")
            conv_done, qk_done, dve_steps = sem("conv_done"), sem("qk_done"), sem("dve_steps")
            bias_ready, tanh_ready, exp_ready, ln_ready = sem("bias_ready"), sem("tanh_ready"), sem("exp_ready"), sem("ln_ready")
            rows_ready, tr_ready, tr_free, bc_ready, bc_free = (sem(n) for n in ("rows_ready", "tr_ready", "tr_free", "bc_ready", "bc_free"))
            gc_ready, bc2_free = sem("gc_ready"), sem("bc2_free")
            block = ctx1.enter_context(nc.Block(no_gpsimd_drain=True))

            @block.sync
            def _(sp):
                sp.dma_start(ig[:, :], proj[gate][0:NH, :]).then_inc(gates_loaded, 16)
                sp.dma_start(fg[:, :], proj[gate][32:32 + NH, :]).then_inc(gates_loaded, 16)
                for j in range(4):
                    sp.dma_start(pre[:, j, 3:], proj[q0 + j]).then_inc(qk_loaded[j], 16)
                for j in range(4):
                    sp.dma_start(vT[:, j, :], proj[v0 + j]).then_inc(v_loaded, 16)

            @block.vector
            def _(dve):
                st = Steps(dve, dve_steps)
                nc.vector.memset(pre[:, :, 0:3], 0.0).then_inc(pads, 1)
                nc.vector.memset(ones_row[:, :], 1.0).then_inc(pads, 1)
                nc.vector.tensor_scalar(cap_b[:, :], V[0:NH, VEC["i_bias"]:VEC["i_bias"] + 2], 1.0 / CAP, None,
                                        ALU.mult).then_inc(bias_ready, 1)
                dve.wait_ge(pads, 2)
                dve.wait_ge(ln_ready, 1)
                st.link(nc.vector.tensor_tensor_scan(row_t[:, 3, :], ones_row[:, :], row_t[:, 2, :], 0.0, ALU.mult, ALU.subtract))
                st.link(nc.vector.scalar_tensor_tensor(out=ig[:, :], in0=row_t[:, 0, :], scalar=CAP, in1=row_t[:, 3, :],
                                                       op0=ALU.mult, op1=ALU.subtract))
                st.link(nc.vector.tensor_tensor_scan(row_t[:, 1, :], ones_row[:, :], ig[:, :], 0.0, ALU.mult, ALU.max))
                st.link(nc.vector.tensor_scalar(row_t[:, 0, :], row_t[:, 1, :], -1.0, None, ALU.mult))
                st.link(nc.vector.tensor_tensor(row_t[:, 2, :], row_t[:, 0, :], row_t[:, 3, :], ALU.subtract))
                dve.sem_inc(rows_ready, 1)

                def conv_tile(j):
                    dve.wait_ge(qk_loaded[j], 16)
                    if j >= 2:
                        dve.wait_ge(qk_done, j - 1)
                    w = lambda tap: V[:, VEC["qk_conv"] + 4 * tap + j:VEC["qk_conv"] + 4 * tap + j + 1]
                    st.link(nc.vector.tensor_scalar(conv[:, j % 2, 0, :], pre[:, j, 3:3 + SEQ], w(3),
                                                    V[:, VEC["qk_conv_b"] + j:VEC["qk_conv_b"] + j + 1], ALU.mult, ALU.add))
                    for n, tap in enumerate((2, 1, 0)):
                        st.link(nc.vector.scalar_tensor_tensor(out=conv[:, j % 2, (n + 1) % 2, :], in0=pre[:, j, tap:tap + SEQ],
                                                               scalar=w(tap), in1=conv[:, j % 2, n % 2, :],
                                                               op0=ALU.mult, op1=ALU.add))
                    dve.sem_inc(conv_done, 1)

                conv_tile(0)
                conv_tile(1)
                for h in range(NH):
                    for f in range(2):
                        dve.wait_ge(bc_ready, 2 * h + f + 1)
                        nc.vector.tensor_copy(neg_G[:, h, f * 512:(f + 1) * 512], bc[:, f, :]).then_inc(bc_free, 1)
                conv_tile(2)
                conv_tile(3)
                dve.wait_ge(gc_ready, 1)
                nc.vector.tensor_copy(g_cols[:, :, :].rearrange("p a b -> p (a b)"), gc[:, 0:DT * NH])

            @block.scalar
            def _(act):
                act.wait_ge(gates_loaded, 32)
                act.wait_ge(bias_ready, 1)
                nc.scalar.activation(row_t[:, 0, :], ig[:, :], ACT.Tanh, bias=cap_b[:, 0:1], scale=1.0 / CAP).then_inc(tanh_ready, 1)
                nc.scalar.activation(row_t[:, 1, :], fg[:, :], ACT.Tanh, bias=cap_b[:, 1:2], scale=1.0 / CAP).then_inc(tanh_ready, 1)
                act.wait_ge(tanh_ready, 2)
                nc.scalar.activation(row_t[:, 3, :], row_t[:, 1, :], ACT.Exp, scale=-CAP).then_inc(exp_ready, 1)
                act.wait_ge(exp_ready, 1)
                nc.scalar.activation(row_t[:, 2, :], row_t[:, 3, :], ACT.Ln, bias=one("one")[0:NH], scale=1.0).then_inc(ln_ready, 1)
                for s in range(DT):
                    act.wait_ge(tr_ready, s + 1)
                    nc.scalar.copy(v_tok[:, s, :], tr[:, s % 2, :]).then_inc(tr_free, 1)

                def qk_silu(j):
                    act.wait_ge(conv_done, j + 1)
                    nc.scalar.activation(qk[:, j, :], conv[:, j % 2, 1, :], ACT.Silu).then_inc(qk_done, 1)

                qk_silu(0)
                qk_silu(1)
                for h in range(NH):
                    for f in range(2):
                        act.wait_ge(bc_ready, 2 * NH + 2 * h + f + 1)
                        nc.scalar.activation(exp_m[:, h, f * 512:(f + 1) * 512], bc[:, 2 + f, :], ACT.Exp).then_inc(bc2_free, 1)
                qk_silu(2)
                qk_silu(3)

            @block.tensor
            def _(pe):
                ident = C[:, CONST["ident"]:CONST["ident"] + P]
                pe.wait_ge(v_loaded, 64)
                for s in range(DT):
                    if s >= 2:
                        pe.wait_ge(tr_free, s - 1)
                    for j in range(4):
                        mm = pe.transpose(tr[:, s % 2, j * P:(j + 1) * P], vT[:, j, s * P:(s + 1) * P], ident)
                    mm.then_inc(tr_ready, 1)
                pe.wait_ge(rows_ready, 1)
                for s in range(DT):
                    mm = pe.matmul(gc[:, s * NH:(s + 1) * NH], ig[:, s * P:(s + 1) * P], C[0:NH, CONST["ident"]:CONST["ident"] + NH],
                                   start=True, stop=True)
                mm.then_inc(gc_ready, 1)
                for r in range(2):
                    for h in range(NH):
                        for f in range(2):
                            if h >= 1:
                                pe.wait_ge(bc2_free if r else bc_free, 2 * (h - 1) + f + 1)
                            sel = C[0:NH, CONST["row_sel"] + h * P:CONST["row_sel"] + (h + 1) * P]
                            pe.matmul(bc[:, 2 * r + f, :], sel, row_t[:, 2 * r, f * 512:(f + 1) * 512],
                                      start=True, stop=True).then_inc(bc_ready, 1)

        with ExitStack() as ctx2:
            sb2 = lambda n, s, d=F32: ctx2.enter_context(nc.sbuf_tensor(f"ml_{n}", s, d))
            NR = 3
            arg = sb2("arg", [P, NR, HALF])
            wgt = sb2("wgt", [P, NR, HALF])
            prod = sb2("prod", [P, NR, HALF])
            num_sb = sb2("num_sb", [P, 2, HALF])
            den = sb2("den", [P, HALF])
            den2 = sb2("den2", [P, HALF])
            den_sq = sb2("den_sq", [P, HALF])
            inv = sb2("inv", [P, HALF])
            h_buf = sb2("h_buf", [P, HALF])
            v_sum = sb2("v_sum", [P, HALF])
            sq = sb2("sq", [P, HALF])
            o_raw = sb2("o_raw", [P, 2, HALF])
            o_sig = sb2("o_sig", [P, 2, HALF])
            y = sb2("y", [P, 2, HALF])
            rms = sb2("rms", [P, HALF])
            score = ctx2.enter_context(nc.psum_tensor("ml_score", [P, NR, 512], F32))
            num = ctx2.enter_context(nc.psum_tensor("ml_num", [P, 2, 512], F32))
            dsum = ctx2.enter_context(nc.psum_tensor("ml_dsum", [P, 2, 512], F32))
            ss = ctx2.enter_context(nc.psum_tensor("ml_ss", [P, 512], F32))
            arg_ready, exp_done, score_ready, prod_done = (sem(n) for n in ("arg_ready", "exp_done", "score_ready", "prod_done"))
            prod_used, group_ready, group_free, steps2 = (sem(n) for n in ("prod_used", "group_ready", "group_free", "steps2"))
            den_ready, num_copied, sq_ready, ss_ready, sum_ready, rms_ready, sig_ready, y_ready = (
                sem(n) for n in ("den_ready", "num_copied", "sq_ready", "ss_ready", "sum_ready", "rms_ready", "sig_ready", "y_ready"))
            o_loaded = [sem(f"o_loaded{i}") for i in range(2)]
            stored = [sem(f"stored{i}") for i in range(2)]
            groups = [(h, f) for h in range(NH) for f in range(2)]
            items = [(n, h, f, s) for n, (h, f) in enumerate(groups) for s in range(4 * f + 4)]
            last_item = {n: max(i for i, it in enumerate(items) if it[0] == n) for n in range(len(groups))}
            span = lambda f, s: (max(0, s * P - f * HALF), HALF)
            block = ctx2.enter_context(nc.Block(no_gpsimd_drain=True))

            @block.vector
            def _(dve):
                st = Steps(dve, steps2)

                def weights(i):
                    n, h, f, s = items[i]
                    a, b = span(f, s)
                    if i >= NR:
                        dve.wait_ge(exp_done, i - NR + 1)
                    nc.vector.tensor_scalar(arg[:, i % NR, a:b], neg_G[:, h, f * HALF + a:f * HALF + b], g_cols[:, s, h:h + 1],
                                            0.0, ALU.add, ALU.min).then_inc(arg_ready, 1)

                def denominator(n):
                    h, f = groups[n]
                    dve.wait_ge(group_ready, n + 1)
                    nc.vector.tensor_copy(num_sb[:, n % 2, :], num[:, n % 2, :]).then_inc(num_copied, 1)
                    st.link(nc.vector.scalar_tensor_tensor(out=den[:, :], in0=dsum[:, n % 2, :], scalar=-1.0, in1=exp_m[:, h, f * HALF:(f + 1) * HALF],
                                                           op0=ALU.mult, op1=ALU.max))
                    if n:
                        dve.wait_ge(sq_ready, 2 * n)
                    nc.vector.tensor_tensor(den2[:, :], dsum[:, n % 2, :], den[:, :], ALU.max).then_inc(den_ready, 1)

                def mean_square(n):
                    dve.wait_ge(ss_ready, n + 1)
                    dve.wait_ge(sq_ready, 2 * n + 2)
                    if n:
                        dve.wait_ge(rms_ready, n)
                    nc.vector.scalar_tensor_tensor(out=v_sum[:, :], in0=ss[:, :], scalar=1.0 / P, in1=den_sq[:, :],
                                                   op0=ALU.mult, op1=ALU.add).then_inc(sum_ready, 1)

                def finish(n):
                    h, f = groups[n]
                    dve.wait_ge(rms_ready, n + 1)
                    st.link(nc.vector.reciprocal(inv[:, :], rms[:, :]))
                    st.link(nc.vector.scalar_tensor_tensor(out=h_buf[:, :], in0=num_sb[:, n % 2, :], scalar=V[:, VEC["mh_g"] + h:VEC["mh_g"] + h + 1],
                                                           in1=inv[:, :], op0=ALU.mult, op1=ALU.mult))
                    dve.wait_ge(sig_ready, n + 1)
                    if n >= 2:
                        dve.wait_ge(stored[n % 2], 16 * (n // 2))
                    nc.vector.tensor_tensor(y[:, n % 2, :], h_buf[:, :], o_sig[:, n % 2, :], ALU.mult).then_inc(y_ready, 1)

                weights(0)
                weights(1)
                for i, (n, h, f, s) in enumerate(items):
                    if i + 2 < len(items):
                        weights(i + 2)
                    a, b = span(f, s)
                    dve.wait_ge(exp_done, i + 1)
                    dve.wait_ge(score_ready, i + 1)
                    if i >= NR:
                        dve.wait_ge(prod_used, i - NR + 1)
                    st.link(nc.vector.scalar_tensor_tensor(out=prod[:, i % NR, a:b], in0=score[:, i % NR, a:b], scalar=DK ** -0.5,
                                                           in1=wgt[:, i % NR, a:b], op0=ALU.mult, op1=ALU.mult))
                    if s >= 4 * f:
                        st.link(nc.vector.tensor_tensor(prod[:, i % NR, a:a + P], prod[:, i % NR, a:a + P],
                                                        C[:, CONST["upto"]:CONST["upto"] + P], ALU.mult))
                    dve.sem_inc(prod_done, 1)
                    if n and s < 3:
                        (denominator, mean_square, finish)[s](n - 1)
                for part in (denominator, mean_square, finish):
                    part(len(groups) - 1)

            @block.scalar
            def _(act):
                def weight_exp(i):
                    n, h, f, s = items[i]
                    a, b = span(f, s)
                    act.wait_ge(arg_ready, i + 1)
                    if i >= NR:
                        act.wait_ge(prod_done, i - NR + 1)
                    nc.scalar.activation(wgt[:, i % NR, a:b], arg[:, i % NR, a:b], ACT.Exp).then_inc(exp_done, 1)

                def squares(n):
                    act.wait_ge(num_copied, n + 1)
                    if n:
                        act.wait_ge(ss_ready, n)
                        act.wait_ge(sum_ready, n)
                    nc.scalar.activation(sq[:, :], num_sb[:, n % 2, :], ACT.Square).then_inc(sq_ready, 1)
                    act.wait_ge(den_ready, n + 1)
                    nc.scalar.activation(den_sq[:, :], den2[:, :], ACT.Square, scale=1e-3).then_inc(sq_ready, 1)

                def root(n):
                    act.wait_ge(sum_ready, n + 1)
                    if n:
                        act.wait_ge(y_ready, n)
                    nc.scalar.activation(rms[:, :], v_sum[:, :], ACT.Sqrt).then_inc(rms_ready, 1)

                def out_gate(n):
                    act.wait_ge(o_loaded[n % 2], 16 * (n // 2 + 1))
                    if n >= 2:
                        act.wait_ge(y_ready, n - 1)
                    nc.scalar.activation(o_sig[:, n % 2, :], o_raw[:, n % 2, :], ACT.Sigmoid).then_inc(sig_ready, 1)

                weight_exp(0)
                weight_exp(1)
                for i, (n, h, f, s) in enumerate(items):
                    if i + 2 < len(items):
                        weight_exp(i + 2)
                    if n and s < 3:
                        (squares, root, out_gate)[s](n - 1)
                for part in (squares, root, out_gate):
                    part(len(groups) - 1)

            @block.tensor
            def _(pe):
                def scores(i):
                    n, h, f, s = items[i]
                    a, b = span(f, s)
                    base = 64 * (h % 2)
                    if i >= NR:
                        pe.wait_ge(prod_done, i - NR + 1)
                    pe.matmul(score[:, i % NR, a:b], qk[base:base + DK, 2 + h // 2, s * P:(s + 1) * P],
                              qk[base:base + DK, h // 2, f * HALF + a:f * HALF + b], start=True, stop=True).then_inc(score_ready, 1)

                def sum_squares(n):
                    pe.wait_ge(sq_ready, 2 * n + 1)
                    if n:
                        pe.wait_ge(sum_ready, n)
                    pe.matmul(ss[:, :], C[:, CONST["ones"]:CONST["ones"] + P], sq[:, :], start=True, stop=True).then_inc(ss_ready, 1)

                scores(0)
                scores(1)
                for i, (n, h, f, s) in enumerate(items):
                    if i + 2 < len(items):
                        scores(i + 2)
                    a, b = span(f, s)
                    pe.wait_ge(prod_done, i + 1)
                    if s == 0 and n >= 2:
                        pe.wait_ge(num_copied, n - 1)
                        pe.wait_ge(den_ready, n - 1)
                    end = i == last_item[n]
                    pe.matmul(num[:, n % 2, a:b], v_tok[:, s, h * P:(h + 1) * P], prod[:, i % NR, a:b], start=s == 0, stop=end,
                              skip_group_check=True)
                    pe.matmul(dsum[:, n % 2, a:b], C[:, CONST["ones"]:CONST["ones"] + P], prod[:, i % NR, a:b], start=s == 0,
                              stop=end, skip_group_check=True).then_inc(prod_used, 1)
                    if end:
                        pe.wait_ge(prod_used, i + 1)
                        pe.sem_inc(group_ready, 1)
                    if n and s == 0:
                        sum_squares(n - 1)
                sum_squares(len(groups) - 1)

            @block.sync
            def _(sp):
                for n, (h, f) in enumerate(groups):
                    if n >= 2:
                        sp.wait_ge(sig_ready, n - 1)
                    sp.dma_start(o_raw[:, n % 2, :], proj[o0 + h][:, f * HALF:(f + 1) * HALF]).then_inc(o_loaded[n % 2], 16)

            @block.gpsimd
            def _(pool):
                for n, (h, f) in enumerate(groups):
                    pool.wait_ge(y_ready, n + 1)
                    pool.dma_start(y_out[h][:, f * HALF:(f + 1) * HALF], y[:, n % 2, :]).then_inc(stored[n % 2], 16)
                for u in range(2):
                    pool.wait_ge(stored[u], 16 * len(groups) // 2)
HR, NR_ = 8, 64
CH = P
NCH = SEQ // CH


def rwkv_prepare_stage(nc, proj, lora, w_up_g, scr, V, C):
    RATE = float(np.exp(-0.5))
    r0, k0, v0, wa0, g0 = 0, 4, 8, 12, 13
    col = lambda name, j=0: V[:, VEC[name] + j:VEC[name] + j + 1]
    with ExitStack() as ctx:
        sb = lambda n, s, d=F32: ctx.enter_context(nc.sbuf_tensor(f"rp_{n}", s, d))
        sem = stage_semaphores(nc, ctx, "rp")
        pre = sb("pre", [P, 2, SEQ + 1])
        kept = sb("kept", [P, 2, SEQ])
        one_mu = sb("one_mu", [P, 14])
        one_ka = sb("one_ka", [P, 4])
        wa = sb("wa", [P, SEQ])
        wt = sb("wt", [64, SEQ])
        gl = sb("gl", [P, SEQ])
        lora_w = sb("lora_w", [P, 512])
        upg_w = sb("upg_w", [P, 512])
        rr, kx, vx = sb("rr", [P, SEQ]), sb("kx", [P, SEQ]), sb("vx", [P, 2, SEQ])
        sg, a_, g_sb = sb("sg", [P, SEQ]), sb("a", [P, SEQ]), sb("g", [P, 2, SEQ])
        kk, kka, sq = sb("kk", [P, SEQ]), sb("kka", [P, SEQ]), sb("sq", [P, SEQ])
        nrm, inv, inv_b = sb("nrm", [P, 2 * DT]), sb("inv", [P, 2 * DT]), sb("inv_b", [P, DT, 2, NR_])
        cum, dif = sb("cum", [P, SEQ]), sb("dif", [P, SEQ])
        e_pos, e_neg, e_prev = sb("e_pos", [P, SEQ]), sb("e_neg", [P, SEQ]), sb("e_prev", [P, SEQ])
        k2, rk = sb("k2", [P, SEQ]), sb("rk", [P, SEQ])
        reset = sb("reset", [P, SEQ])
        ar = sb("ar", [P, 2, NCH, 2, CH])
        bt, kt, bon = sb("bt", [P, 2, SEQ]), sb("kt", [P, 2, SEQ]), sb("bon", [P, 2, SEQ])
        s_arg, s_exp = sb("s_arg", [P, NCH]), sb("s_exp", [P, 2, NCH])
        up = ctx.enter_context(nc.psum_tensor("rp_up", [P, 6, 512], F32))
        hs = ctx.enter_context(nc.psum_tensor("rp_hs", [P, 2, 512], F32))
        loaded = [sem(f"loaded{i}") for i in range(2)]
        w_loaded, pads, kept_done, mixed = sem("w_loaded"), sem("pads"), sem("kept_done"), sem("mixed")
        lo_ready, up_ready, act_done, st_sem, kk_sq, hs_ready, nrm_done = (
            sem(n) for n in ("lo_ready", "up_ready", "act_done", "steps", "kk_sq", "hs_ready", "nrm_done"))
        dif_ready, exp_done, rk_ready, out_ready, mu_ready, inv_ready, kk_ready, ab_ready = (
            sem(n) for n in ("dif_ready", "exp_done", "rk_ready", "out_ready", "mu_ready", "inv_ready", "kk_ready", "ab_ready"))
        kt_done = sem("kt_done")
        stored = [sem(f"stored{i}") for i in range(2)]
        order = [wa0, g0]
        for m in range(4):
            order += [r0 + m, k0 + m, v0 + m]
        NST = 7
        block = ctx.enter_context(nc.Block(no_gpsimd_drain=True))

        @block.sync
        def _(sp):
            sp.dma_start(lora_w[:, :], lora).then_inc(w_loaded, 16)
            sp.dma_start(upg_w[:, :], w_up_g).then_inc(w_loaded, 16)
            for n, t in enumerate(order):
                if n >= 2:
                    sp.wait_ge(mixed, n - 1)
                sp.dma_start(pre[:, n % 2, 1:], proj[t]).then_inc(loaded[n % 2], 16)

        @block.scalar
        def _(act):
            def keep(n):
                t = order[n]
                act.wait_ge(loaded[n % 2], 16 * (n // 2 + 1))
                if n >= 2:
                    act.wait_ge(mixed, n - 1)
                nc.scalar.activation(kept[:, n % 2, :], pre[:, n % 2, 1:], ACT.Copy, scale=one_mu[:, t:t + 1]).then_inc(kept_done, 1)

            act.wait_ge(mu_ready, 1)
            keep(0)
            keep(1)
            act.wait_ge(mixed, 2)
            nc.scalar.activation(wt[:, :], wa[0:64, :], ACT.Tanh).then_inc(lo_ready, 1)
            nc.scalar.activation(gl[:, :], gl[:, :], ACT.Sigmoid).then_inc(lo_ready, 1)
            for m in range(4):
                for j in range(3):
                    keep(2 + 3 * m + j)
                for h in range(2):
                    hc = slice(h * HALF, (h + 1) * HALF)
                    act.wait_ge(up_ready, 6 * m + 3 * h + 3)
                    if m and h == 0:
                        act.wait_ge(dif_ready, m)
                        act.wait_ge(ab_ready, m)
                        if m >= 2:
                            act.wait_ge(stored[m % 2], 16 * NST * (m // 2))
                    nc.scalar.activation(sg[:, hc], up[:, 3 * h, :], ACT.Sigmoid, bias=col("w0", m)).then_inc(act_done, 1)
                    nc.scalar.activation(a_[:, hc], up[:, 3 * h + 1, :], ACT.Sigmoid, bias=col("a0", m)).then_inc(act_done, 1)
                    nc.scalar.copy(g_sb[:, m % 2, hc], up[:, 3 * h + 2, :]).then_inc(act_done, 1)
                act.wait_ge(kk_sq, 2 * m + 1)
                nc.scalar.activation(sq[:, :], kk[:, :], ACT.Square).then_inc(kk_sq, 1)
                act.wait_ge(hs_ready, 3 * m + 1)
                nc.scalar.activation(nrm[:, :], hs[:, 0, 0:2 * DT], ACT.Sqrt).then_inc(nrm_done, 1)
                act.wait_ge(dif_ready, m + 1)
                if m:
                    act.wait_ge(out_ready, m)
                    act.wait_ge(kt_done, 2 * m)
                nc.scalar.activation(e_pos[:, :], dif[:, :], ACT.Exp).then_inc(exp_done, 1)
                nc.scalar.activation(e_neg[:, :], dif[:, :], ACT.Exp, scale=-1.0).then_inc(exp_done, 1)
                nc.scalar.activation(e_prev[:, :], cum[:, :], ACT.Exp).then_inc(exp_done, 1)
                nc.scalar.activation(s_exp[:, m % 2, :], s_arg[:, :], ACT.Exp).then_inc(exp_done, 1)

        @block.tensor
        def _(pe):
            pe.wait_ge(w_loaded, 32)
            pe.wait_ge(lo_ready, 2)
            for m in range(4):
                ms = slice(m * P, (m + 1) * P)
                for h in range(2):
                    hc = slice(h * HALF, (h + 1) * HALF)
                    if m:
                        pe.wait_ge(act_done, 6 * (m - 1) + 3 * h + 3)
                    pe.matmul(up[:, 3 * h, :], lora_w[0:64, ms], wt[:, hc], start=True, stop=True).then_inc(up_ready, 1)
                    pe.matmul(up[:, 3 * h + 1, :], lora_w[64:128, ms], wa[64:128, hc], start=True, stop=True).then_inc(up_ready, 1)
                    pe.matmul(up[:, 3 * h + 2, :], upg_w[:, ms], gl[:, hc], start=True, stop=True).then_inc(up_ready, 1)
                pe.wait_ge(kk_sq, 2 * m + 2)
                if m:
                    pe.wait_ge(out_ready, m)
                ones = C[:, CONST["head_ones"]:CONST["head_ones"] + P]
                for t in range(DT):
                    mm = pe.matmul(hs[:, 0, 2 * t:2 * t + 2], sq[:, t * P:(t + 1) * P], ones[:, 0:P:NR_], start=True, stop=True, skip_group_check=True)
                mm.then_inc(hs_ready, 1)
                pe.wait_ge(inv_ready, m + 1)
                for t in range(DT):
                    mm = pe.transpose(hs[:, t // 4, (t % 4) * P:(t % 4 + 1) * P], inv_b[:, t, :, :].rearrange("p a b -> p (a b)"),
                                      C[:, CONST["ident"]:CONST["ident"] + P])
                mm.then_inc(hs_ready, 1)
                pe.wait_ge(rk_ready, m + 1)
                pe.wait_ge(kk_ready, m + 1)
                for h in range(2):
                    mm = pe.matmul(hs[:, h, :], ones, rk[:, h * HALF:(h + 1) * HALF], start=True, stop=True)
                mm.then_inc(hs_ready, 1)

        @block.vector
        def _(dve):
            st = Steps(dve, st_sem)
            tt, ts, stt = nc.vector.tensor_tensor, nc.vector.tensor_scalar, nc.vector.scalar_tensor_tensor
            st(nc.vector.memset(pre[:, :, 0:1], 0.0))
            st(nc.vector.memset(reset[:, :], 1.0))
            st.settle()
            st(nc.vector.memset(reset[:, :].rearrange("p (c t) -> p c t", c=NCH)[:, :, 0:1], 0.0))
            st(ts(one_ka[:, :], V[:, VEC["k_a"]:VEC["k_a"] + 4], -1.0, 1.0, ALU.mult, ALU.add))
            ts(one_mu[:, :], V[:, VEC["mu"]:VEC["mu"] + 14], -1.0, 1.0, ALU.mult, ALU.add).then_inc(mu_ready, 1)
            st.settle()

            def mix(n, dst):
                dve.wait_ge(kept_done, n + 1)
                stt(out=dst, in0=pre[:, n % 2, 0:SEQ], scalar=col("mu", order[n]), in1=kept[:, n % 2, :],
                    op0=ALU.mult, op1=ALU.add).then_inc(mixed, 1)

            mix(0, wa[:, :])
            mix(1, gl[:, :])
            for m in range(4):
                u = m % 2
                if m >= 2:
                    dve.wait_ge(stored[u], 16 * NST * (m // 2))
                mix(2 + 3 * m, rr[:, :])
                mix(3 + 3 * m, kx[:, :])
                mix(4 + 3 * m, vx[:, u, :])
                dve.wait_ge(mixed, 5 + 3 * m)
                if m:
                    dve.wait_ge(ab_ready, m)
                    dve.wait_ge(kt_done, 2 * m)
                ts(kk[:, :], kx[:, :], col("k_k", m), None, ALU.mult).then_inc(kk_sq, 1)
                dve.wait_ge(act_done, 6 * m + 6)
                st.link(ts(sg[:, :], sg[:, :], -RATE, None, ALU.mult))
                st.link(nc.vector.tensor_tensor_scan(cum[:, :], reset[:, :], sg[:, :], 0.0, ALU.mult, ALU.add))
                cum3 = cum[:, :].rearrange("p (c t) -> p c t", c=NCH)
                mid = cum3[:, :, 63:64]
                st(tt(dif[:, :].rearrange("p (c t) -> p c t", c=NCH), cum3, mid.to_broadcast([P, NCH, CH]), ALU.subtract))
                st(tt(s_arg[:, :].unsqueeze(2), cum3[:, :, CH - 1:CH], mid, ALU.subtract))
                st.settle()
                st.link(tt(s_arg[:, 0:NCH - 1], s_arg[:, 0:NCH - 1], cum3[:, 1:NCH, 63:64].rearrange("p c o -> p (c o)"), ALU.add))
                tt(cum[:, :], dif[:, :], sg[:, :], ALU.subtract).then_inc(dif_ready, 1)
                dve.wait_ge(nrm_done, m + 1)
                st.link(ts(nrm[:, :], nrm[:, :], 1e-12, None, ALU.max))
                st.link(nc.vector.reciprocal(inv[:, :], nrm[:, :]))
                nc.vector.tensor_copy(inv_b[:, :, :, :].rearrange("p t h x -> p (t h) x"),
                                      inv[:, :].unsqueeze(2).to_broadcast([P, 2 * DT, NR_])).then_inc(inv_ready, 1)
                st.link(ts(k2[:, :], a_[:, :], col("k_a", m), one_ka[:, m:m + 1], ALU.mult, ALU.add))
                st.link(tt(k2[:, :], k2[:, :], kx[:, :], ALU.mult))
                stt(out=rk[:, :], in0=rr[:, :], scalar=col("r_k", m), in1=k2[:, :], op0=ALU.mult, op1=ALU.mult).then_inc(rk_ready, 1)
                dve.wait_ge(hs_ready, 3 * m + 2)
                tt(kk[:, :], kk[:, :], hs[:, :, :].rearrange("p a b -> p (a b)"), ALU.mult).then_inc(kk_ready, 1)
                dve.wait_ge(kk_ready, m + 1)
                dve.wait_ge(exp_done, 4 * m + 4)
                c3 = lambda t: t[:, :].rearrange("p (c t) -> p c t", c=NCH)
                st(stt(out=ar[:, u, :, 0, :], in0=c3(kk), scalar=-1.0, in1=c3(e_prev), op0=ALU.mult, op1=ALU.mult))
                st(tt(ar[:, u, :, 1, :], c3(rr), c3(e_pos), ALU.mult))
                dve.wait_ge(hs_ready, 3 * m + 3)
                st(tt(bon[:, u, :], hs[:, :, :].rearrange("p a b -> p (a b)"), vx[:, u, :], ALU.mult))
                st.settle()
                dve.sem_inc(out_ready, 1)

        @block.gpsimd
        def _(pool):
            tt = nc.gpsimd.tensor_tensor
            for m in range(4):
                u = m % 2
                pool.wait_ge(kk_ready, m + 1)
                tt(kka[:, :], kk[:, :], a_[:, :], ALU.mult).then_inc(ab_ready, 1)
                if m >= 2:
                    pool.wait_ge(stored[u], 16 * NST * (m // 2))
                pool.wait_ge(exp_done, 4 * m + 4)
                tt(kt[:, u, :], k2[:, :], e_neg[:, :], ALU.mult).then_inc(kt_done, 1)
                pool.wait_ge(ab_ready, m + 1)
                tt(bt[:, u, :], kka[:, :], e_neg[:, :], ALU.mult).then_inc(kt_done, 1)
                pool.wait_ge(kt_done, 2 * m + 2)
                pool.wait_ge(out_ready, m + 1)
                for dst, s_ in ((scr["ar"][m], ar[:, u, :, :, :].rearrange("p a b c -> p (a b c)")), (scr["bt"][m], bt[:, u, :]), (scr["kt"][m], kt[:, u, :]),
                                (scr["v"][m], vx[:, u, :]), (scr["bonus"][m], bon[:, u, :]), (scr["g"][m], g_sb[:, u, :]), (scr["scale"][m], s_exp[:, u, :])):
                    pool.dma_start(dst, s_).then_inc(stored[u], 16)
            for u in range(2):
                pool.wait_ge(stored[u], 16 * NST * 2)


def rwkv_scan_stage(nc, scr, masks, C):
    with ExitStack() as ctx:
        sb = lambda n, s, d=F32: ctx.enter_context(nc.sbuf_tensor(f"rs_{n}", s, d))
        sem = stage_semaphores(nc, ctx, "rs")
        lv = sb("lv", [P, 2 * LEVELS * P])
        ar = sb("ar", [P, 2, 4, 2 * CH])
        bt, kt, vt = sb("bt", [P, 2, 4, CH]), sb("kt", [P, 2, 4, CH]), sb("vt", [P, 2, 4, CH])
        scale = sb("scale", [P, 4, NCH])
        tok = sb("tok", [P, 3, 512])
        mb = sb("mb", [P, 2, 4, CH])
        raw = sb("raw", [P, 2, 3, 4, CH])
        mr = sb("mr", [P, 2, 3, 4, CH])
        lab = sb("lab", [P, 2, 4, CH])
        X, XT = sb("X", [P, 2, 4, CH]), sb("XT", [P, 2, 4, CH])
        T_ = sb("T", [P, 2, 4, CH])
        zs, us = sb("zs", [P, 512]), sb("us", [P, 512])
        S, S_new = sb("S", [P, 4, P]), sb("S_new", [P, 4, P])
        ybuf = sb("ybuf", [P, 2, 512])
        ps = ctx.enter_context(nc.psum_tensor("rs_ps", [P, 8, 512], F32))
        loaded = [sem(f"loaded{i}") for i in range(2)]
        stored = [sem(f"stored{i}") for i in range(2)]
        c_loaded, s_init, wait_held = sem("c_loaded"), sem("s_init"), sem("wait_held")
        tr_ready, tr_copied, mat_ready, mat_masked, x_init, x_ident, raw_ready, raw_copied, raw_masked = (
            sem(n) for n in ("tr_ready", "tr_copied", "mat_ready", "mat_masked", "x_init", "x_ident", "raw_ready", "raw_copied", "raw_masked"))
        t_ready, t_copied, xx_ready, x_done, z_ready, z_copied = (sem(n) for n in ("t_ready", "t_copied", "xx_ready", "x_done", "z_ready", "z_copied"))
        u_ready, u_copied, y_ready, y_copied, ds_ready, ds_done, ds_done_a, steps = (sem(n) for n in ("u_ready", "u_copied", "y_ready", "y_copied", "ds_ready", "ds_done", "ds_done_a", "steps"))
        NL = LEVELS - 1
        lvm = lambda l, t: lv[:, (t * LEVELS + l) * P:(t * LEVELS + l + 1) * P].bitcast(U32).unsqueeze(1).to_broadcast([P, 4, P])
        bank = lambda b: ps[:, b, :].rearrange("p (h t) -> p h t", h=4)
        block = ctx.enter_context(nc.Block(no_gpsimd_drain=True))

        @block.sync
        def _(sp):
            sp.dma_start(lv[:, :], masks).then_inc(c_loaded, 16)
            sp.dma_start(scale[:, :, :], scr["scale"].rearrange("m p c -> p m c")).then_inc(c_loaded, 16)

            def load(c, u):
                arv = scr["ar"].rearrange("m p (c x) -> p m c x", c=NCH)
                sp.dma_start(ar[:, u, :, :], arv[:, :, c, :]).then_inc(loaded[u], 16)
                for dst, s_ in ((bt, "bt"), (kt, "kt"), (vt, "v")):
                    v_ = scr[s_].rearrange("m p (c x) -> p m c x", c=NCH)
                    sp.dma_start(dst[:, u, :, :], v_[:, :, c, :]).then_inc(loaded[u], 16)

            load(0, 0)
            load(1, 1)
            with sp.Fori(1, NCH // 2) as i:
                for u in range(2):
                    sp.wait_ge(ds_ready, 2 * i + (u - 1))
                    sp.wait_ge(y_ready, 2 * i + (u - 1))
                    load(2 * i + u, u)

        @block.tensor
        def _(pe):
            ident = C[:, CONST["ident"]:CONST["ident"] + P]

            def group_products(i, u, g, n):
                base = 64 * g
                if n:
                    pe.wait_ge(raw_copied, 12 * i + (6 * u + 2 * n + g - 1))
                for m in range(4):
                    lhs = (bt, kt, kt)[n][base:base + 64, u, m, :]
                    rhs = ar[base:base + 64, u, m, 0:CH] if n == 1 else ar[base:base + 64, u, m, CH:]
                    mm = pe.matmul(ps[:, 4 + 3 * g, m * P:(m + 1) * P], lhs, rhs, start=True, stop=True)
                mm.then_inc(raw_ready, 1)

            def token_major(i, u, n):
                pe.wait_ge(raw_copied, 12 * i + (6 * u + 6))
                if n == 2:
                    pe.wait_ge(tr_copied, 6 * i + (3 * u + 1))
                for m in range(4):
                    mm = pe.transpose(ps[:, 4 + 3 * (n % 2), m * P:(m + 1) * P], (bt, kt, vt)[n][:, u, m, :], ident)
                mm.then_inc(tr_ready, 1)

            def between(i, u, l, g):
                if l < 2:
                    group_products(i, u, g, l + 1)
                elif l == 2:
                    token_major(i, u, g)
                elif l == 3 and g == 0:
                    token_major(i, u, 2)

            def body(i, first, last):
                for u in range(2):
                    c = 2 * i + u
                    fresh = first and u == 0
                    pe.wait_ge(loaded[u], 64 * i + 64)
                    if not fresh:
                        pe.wait_ge(y_copied, c)
                        pe.wait_ge(ds_done, c)
                    for g in range(2):
                        base = 64 * g
                        if g == 0 and not fresh:
                            pe.wait_ge(x_done, 4 * NL * i + 2 * NL * u)
                            pe.wait_ge(z_copied, c)
                            pe.wait_ge(u_copied, c)
                        for m in range(4):
                            ms = slice(m * P, (m + 1) * P)
                            b_t, a_t, r_t = bt[base:base + 64, u, m, :], ar[base:base + 64, u, m, 0:CH], ar[base:base + 64, u, m, CH:]
                            pe.matmul(ps[:, g, ms], b_t, a_t, start=True, stop=True)
                            mm = pe.matmul(ps[:, 2 + g, ms], a_t, b_t, start=True, stop=True)
                        mm.then_inc(mat_ready, 1)
                    for g in range(2):
                        group_products(i, u, g, 0)
                    for l in range(NL):
                        for g in range(2):
                            if l == 0:
                                pe.wait_ge(x_init, 4 * i + 2 * u + g + 1)
                            else:
                                pe.wait_ge(x_done, 4 * NL * i + 2 * NL * u + 2 * (l - 1) + g + 1)
                            for m in range(4):
                                mm = pe.matmul(ps[:, 5 + g, m * P:(m + 1) * P], mb[:, g, m, :], X[:, g, m, :], start=True, stop=True)
                            mm.then_inc(t_ready, 1)
                            between(i, u, l, g)
                        for g in range(2):
                            if l == 0 and g == 0:
                                pe.wait_ge(mat_masked, 8 * i + (4 * u + 4))
                            pe.wait_ge(t_copied, 4 * NL * i + 2 * NL * u + 2 * l + g + 1)
                            for m in range(4):
                                if l < NL - 1:
                                    pe.matmul(ps[:, 2 * g, m * P:(m + 1) * P], XT[:, g, m, :], T_[:, g, m, :], start=True, stop=True)
                                mm = pe.matmul(ps[:, 2 * g + 1, m * P:(m + 1) * P], T_[:, g, m, :], XT[:, g, m, :], start=True, stop=True)
                            mm.then_inc(xx_ready, 1)
                    if fresh:
                        pe.wait_ge(s_init, 1)
                    pe.wait_ge(tr_copied, 6 * i + 3 * u + 3)
                    pe.wait_ge(raw_masked, 12 * i + 6 * u + 6)
                    for m in range(4):
                        pe.matmul(ps[:, 4, m * P:(m + 1) * P], ar[:, u, m, 0:CH], S[:, m, :], start=True, stop=False, skip_group_check=True)
                        for g in range(2):
                            h = 2 * m + g
                            mm = pe.matmul(ps[:, 4, h * 64:(h + 1) * 64], mr[:, g, 1, m, :], tok[:, 2, h * 64:(h + 1) * 64],
                                           start=False, stop=True, skip_group_check=True)
                    mm.then_inc(z_ready, 1)
                    pe.wait_ge(z_copied, c + 1)
                    pe.wait_ge(x_done, 4 * NL * i + 2 * NL * (u + 1))
                    for h in range(HR):
                        mm = pe.matmul(ps[:, 7, h * 64:(h + 1) * 64], XT[:, h % 2, h // 2, :], zs[:, h * 64:(h + 1) * 64], start=True, stop=True)
                    mm.then_inc(u_ready, 1)
                    pe.wait_ge(u_copied, c + 1)
                    for m in range(4):
                        pe.matmul(ps[:, 5, m * P:(m + 1) * P], S[:, m, :], ar[:, u, m, CH:], start=True, stop=False, skip_group_check=True)
                        for g in range(2):
                            h = 2 * m + g
                            o = ps[64 * g:64 * g + 64, 5, m * P:(m + 1) * P]
                            pe.matmul(o, us[:, h * 64:(h + 1) * 64], mr[:, g, 0, m, :], start=False, stop=False, skip_group_check=True)
                            mm = pe.matmul(o, tok[:, 2, h * 64:(h + 1) * 64], mr[:, g, 2, m, :], start=False, stop=True, skip_group_check=True)
                    mm.then_inc(y_ready, 1)
                    for m in range(4):
                        ms = slice(m * P, (m + 1) * P)
                        pe.matmul(ps[:, 6, ms], tok[:, 0, ms], us[:, ms], start=True, stop=False, skip_group_check=True)
                        mm = pe.matmul(ps[:, 6, ms], tok[:, 1, ms], tok[:, 2, ms], start=False, stop=True, skip_group_check=True)
                    mm.then_inc(ds_ready, 1)

            run_loop(pe, NCH // 2, body)

        @block.scalar
        def _(act):
            def raw_copy(i, u, g, n, fresh):
                act.wait_ge(raw_ready, 12 * i + (6 * u + 2 * n + g + 1))
                if not fresh:
                    act.wait_ge(raw_masked, 12 * i + (6 * u + 2 * n + g - 5))
                nc.scalar.copy(raw[:, g, n, :, :].rearrange("p h t -> p (h t)"), ps[:, 4 + 3 * g, :]).then_inc(raw_copied, 1)

            def token_copy(i, u, n, fresh):
                act.wait_ge(tr_ready, 6 * i + (3 * u + n + 1))
                if n == 0 and not fresh:
                    act.wait_ge(ds_ready, 2 * i + u)
                nc.scalar.copy(tok[:, n, :], ps[:, 4 + 3 * (n % 2), :]).then_inc(tr_copied, 1)

            def body(i, first, last):
                for u in range(2):
                    c = 2 * i + u
                    fresh = first and u == 0
                    for g in range(2):
                        raw_copy(i, u, g, 0, fresh)
                    for l in range(NL):
                        for g in range(2):
                            act.wait_ge(t_ready, 4 * NL * i + 2 * NL * u + 2 * l + g + 1)
                            nc.scalar.copy(T_[:, g, :, :].rearrange("p h t -> p (h t)"), ps[:, 5 + g, :]).then_inc(t_copied, 1)
                            if l < 2:
                                raw_copy(i, u, g, l + 1, fresh)
                            elif l == 2:
                                token_copy(i, u, g, fresh)
                            elif l == 3 and g == 0:
                                token_copy(i, u, 2, fresh)
                    act.wait_ge(z_ready, c + 1)
                    nc.scalar.copy(zs[:, :], ps[:, 4, :]).then_inc(z_copied, 1)
                    act.wait_ge(u_ready, c + 1)
                    nc.scalar.copy(us[:, :], ps[:, 7, :]).then_inc(u_copied, 1)
                    act.wait_ge(y_ready, c + 1)
                    if not first:
                        act.wait_ge(stored[u], 64 * i)
                    nc.scalar.copy(ybuf[:, u, :], ps[:, 5, :]).then_inc(y_copied, 1)

            run_loop(act, NCH // 2, body)

        @block.vector
        def _(dve):
            tt = nc.vector.tensor_tensor
            before = C[:, CONST["before"]:CONST["before"] + P].unsqueeze(1).to_broadcast([P, 4, P])
            after = C[:, CONST["after"]:CONST["after"] + P].unsqueeze(1).to_broadcast([P, 4, P])
            nc.vector.memset(S[:, :, :], 0.0).then_inc(s_init, 1)
            nc.vector.memset(S_new[:, :, :], 0.0).then_inc(s_init, 1)
            dve.wait_ge(s_init, 2)
            dve.wait_ge(c_loaded, 32)

            def body(i, first, last):
                for u in range(2):
                    c = 2 * i + u
                    for g in range(2):
                        dve.wait_ge(mat_ready, 4 * i + 2 * u + g + 1)
                        if g == 0 and not (first and u == 0):
                            dve.wait_ge(ds_ready, c)
                        tt(mb[:, g, :, :], bank(g), before, ALU.mult).then_inc(mat_masked, 1)
                        tt(lab[:, g, :, :], bank(2 + g), after, ALU.mult).then_inc(mat_masked, 1)
                        dve.wait_ge(mat_masked, 8 * i + (4 * u + 2 * g + 2))
                        dve.wait_ge(x_ident, 8 * i + (4 * u + 2 * g + 2))
                        dve.sem_inc(wait_held, 1)
                        nc.vector.copy_predicated(X[:, g, :, :], lvm(0, 0), lab[:, g, :, :]).then_inc(steps, 1)
                        nc.vector.copy_predicated(XT[:, g, :, :], lvm(0, 1), mb[:, g, :, :]).then_inc(steps, 1)
                        dve.wait_ge(steps, 8 * i + (4 * u + 2 * g + 2))
                        dve.sem_inc(x_init, 1)
                    for l in range(NL):
                        for g in range(2):
                            dve.wait_ge(xx_ready, 4 * NL * i + 2 * NL * u + 2 * l + g + 1)
                            dve.sem_inc(wait_held, 1)
                            if l < NL - 1:
                                nc.vector.copy_predicated(X[:, g, :, :], lvm(l + 1, 0), bank(2 * g))
                            nc.vector.copy_predicated(XT[:, g, :, :], lvm(l + 1, 1), bank(2 * g + 1)).then_inc(x_done, 1)
                    dve.wait_ge(ds_ready, c + 1)
                    for g in range(2):
                        b = slice(64 * g, 64 * g + 64)
                        tt(S_new[b, :, b], S[b, :, b], ps[b, 6, :].rearrange("p (m x) -> p m x", m=4)[:, :, b], ALU.add).then_inc(ds_done_a, 1)
                    dve.wait_ge(ds_done_a, 4 * i + 2 * u + 2)
                    for g in range(2):
                        b = slice(64 * g, 64 * g + 64)
                        ins = tt(S[b, :, b], S_new[b, :, b], scale[b, :, bass.ds(c, 1)].to_broadcast([64, 4, 64]), ALU.mult)
                        if g == 1:
                            ins.then_inc(ds_done, 1)

            run_loop(dve, NCH // 2, body)

        @block.gpsimd
        def _(pool):
            before = C[:, CONST["before"]:CONST["before"] + P].unsqueeze(1).to_broadcast([P, 4, P])
            upto = C[:, CONST["upto"]:CONST["upto"] + P].unsqueeze(1).to_broadcast([P, 4, P])
            ident = C[:, CONST["ident"]:CONST["ident"] + P].unsqueeze(1).to_broadcast([P, 4, P])

            def store(i, u):
                pool.wait_ge(y_copied, 2 * i + (u + 1))
                for m in range(4):
                    pool.dma_start(scr["y"][m][:, bass.ds(i * (2 * CH) + u * CH, CH)], ybuf[:, u, m * P:(m + 1) * P]).then_inc(stored[u], 16)

            def body(i, first, last):
                for u in range(2):
                    fresh = first and u == 0
                    if not fresh:
                        pool.wait_ge(u_ready, 2 * i + u)
                        pool.sem_inc(wait_held, 1)
                    for g in range(2):
                        nc.gpsimd.tensor_copy(X[:, g, :, :], ident).then_inc(x_ident, 1)
                        nc.gpsimd.tensor_copy(XT[:, g, :, :], ident).then_inc(x_ident, 1)
                    if not fresh:
                        store(i, 0) if u else store(i - 1, 1)
                        pool.wait_ge(ds_ready, 2 * i + u)
                    for n, mask in enumerate((upto, before, upto)):
                        for g in range(2):
                            pool.wait_ge(raw_copied, 12 * i + (6 * u + 2 * n + g + 1))
                            nc.gpsimd.tensor_tensor(mr[:, g, n, :, :], raw[:, g, n, :, :], mask, ALU.mult).then_inc(raw_masked, 1)

            run_loop(pool, NCH // 2, body)
            store(NCH // 2 - 1, 1)
            for u in range(2):
                pool.wait_ge(stored[u], 64 * NCH // 2)


def rwkv_finish_stage(nc, scr, y_out, V, C):
    col = lambda name, j=0: V[:, VEC[name] + j:VEC[name] + j + 1]
    with ExitStack() as ctx:
        sb = lambda n, s, d=F32: ctx.enter_context(nc.sbuf_tensor(f"rf_{n}", s, d))
        sem = stage_semaphores(nc, ctx, "rf")
        y, bon, g_ = sb("y", [P, 2, SEQ]), sb("bon", [P, 2, SEQ]), sb("g", [P, 2, SEQ])
        yc, sq, out = sb("yc", [P, 2, SEQ]), sb("sq", [P, 2, SEQ]), sb("out", [P, 2, SEQ])
        rms, inv, inv_b = sb("rms", [P, 2, 2 * DT]), sb("inv", [P, 2 * DT]), sb("inv_b", [P, 2, 2 * DT, NR_])
        mean = ctx.enter_context(nc.psum_tensor("rf_mean", [P, 2, 2, 512], F32))
        var = ctx.enter_context(nc.psum_tensor("rf_var", [P, 2, 2, 512], F32))
        loaded = [sem(f"loaded{i}") for i in range(2)]
        stored = [sem(f"stored{i}") for i in range(2)]
        mean_ready, yc_ready, sq_ready, var_ready, rms_ready, inv_ready, spread_ready, scaled, out_ready, steps = (
            sem(n) for n in ("mean_ready", "yc_ready", "sq_ready", "var_ready", "rms_ready", "inv_ready", "spread_ready",
                             "scaled", "out_ready", "steps"))
        flat = lambda t: t.rearrange("p a b -> p (a b)")
        block = ctx.enter_context(nc.Block(no_gpsimd_drain=True))

        @block.sync
        def _(sp):
            for m in range(4):
                if m >= 2:
                    sp.wait_ge(out_ready, m - 1)
                for dst, src in ((y, "y"), (bon, "bonus"), (g_, "g")):
                    sp.dma_start(dst[:, m % 2, :], scr[src][m]).then_inc(loaded[m % 2], 16)

        @block.tensor
        def _(pe):
            ones = C[:, CONST["head_ones"]:CONST["head_ones"] + P]

            def head_sum(dst, src):
                for h in range(2):
                    mm = pe.matmul(dst[:, h, :], ones, src[:, h * HALF:(h + 1) * HALF], start=True, stop=True)
                return mm

            def means(m):
                pe.wait_ge(loaded[m % 2], 48 * (m // 2 + 1))
                if m >= 2:
                    pe.wait_ge(yc_ready, m - 1)
                head_sum(mean[:, m % 2, :, :], y[:, m % 2, :]).then_inc(mean_ready, 1)

            def variances(m):
                pe.wait_ge(sq_ready, m + 1)
                if m >= 2:
                    pe.wait_ge(scaled, m - 1)
                for t in range(DT):
                    mm = pe.matmul(var[:, m % 2, 0, 2 * t:2 * t + 2], sq[:, m % 2, t * P:(t + 1) * P], ones[:, 0:P:NR_],
                                   start=True, stop=True, skip_group_check=True)
                mm.then_inc(var_ready, 1)

            def spread(m):
                pe.wait_ge(inv_ready, m + 1)
                for t in range(DT):
                    mm = pe.transpose(var[:, m % 2, t // 4, (t % 4) * P:(t % 4 + 1) * P],
                                      inv_b[:, m % 2, 2 * t:2 * t + 2, :].rearrange("p a b -> p (a b)"), C[:, CONST["ident"]:CONST["ident"] + P])
                mm.then_inc(spread_ready, 1)

            means(0)
            for m in range(4):
                if m < 3:
                    means(m + 1)
                variances(m)
                spread(m)

        @block.scalar
        def _(act):
            def squares(m):
                act.wait_ge(yc_ready, m + 1)
                if m >= 2:
                    act.wait_ge(var_ready, m - 1)
                nc.scalar.activation(sq[:, m % 2, :], yc[:, m % 2, :], ACT.Square).then_inc(sq_ready, 1)

            squares(0)
            for m in range(4):
                act.wait_ge(var_ready, m + 1)
                if m >= 2:
                    act.wait_ge(inv_ready, m - 1)
                nc.scalar.activation(rms[:, m % 2, :], var[:, m % 2, 0, 0:2 * DT], ACT.Sqrt,
                                     bias=C[:, CONST["eps_ln"]:CONST["eps_ln"] + 1], scale=1.0 / NR_).then_inc(rms_ready, 1)
                if m < 3:
                    squares(m + 1)

        @block.vector
        def _(dve):
            st = Steps(dve, steps)
            tt, ts, stt = nc.vector.tensor_tensor, nc.vector.tensor_scalar, nc.vector.scalar_tensor_tensor

            def center(m):
                u = m % 2
                dve.wait_ge(mean_ready, m + 1)
                stt(out=yc[:, u, :], in0=flat(mean[:, u, :, :]), scalar=-1.0 / NR_, in1=y[:, u, :], op0=ALU.mult,
                    op1=ALU.add).then_inc(yc_ready, 1)

            def inverse(m):
                dve.wait_ge(rms_ready, m + 1)
                st.link(nc.vector.reciprocal(inv[:, :], rms[:, m % 2, :]))
                if m >= 2:
                    dve.wait_ge(spread_ready, m - 1)
                nc.vector.tensor_copy(inv_b[:, m % 2, :, :], inv[:, :].unsqueeze(2).to_broadcast([P, 2 * DT, NR_])).then_inc(inv_ready, 1)

            def finish(m):
                u = m % 2
                dve.wait_ge(spread_ready, m + 1)
                tt(yc[:, u, :], yc[:, u, :], flat(var[:, u, :, :]), ALU.mult).then_inc(scaled, 1)
                dve.wait_ge(scaled, m + 1)
                st.link(ts(yc[:, u, :], yc[:, u, :], col("lnx_w", m), col("lnx_b", m), ALU.mult, ALU.add))
                st.link(tt(yc[:, u, :], yc[:, u, :], bon[:, u, :], ALU.add))
                if m >= 2:
                    dve.wait_ge(stored[u], 16)
                tt(out[:, u, :], yc[:, u, :], g_[:, u, :], ALU.mult).then_inc(out_ready, 1)

            center(0)
            for m in range(4):
                inverse(m)
                if m < 3:
                    center(m + 1)
                finish(m)

        @block.gpsimd
        def _(pool):
            for m in range(4):
                pool.wait_ge(out_ready, m + 1)
                pool.dma_start(y_out[m], out[:, m % 2, :]).then_inc(stored[m % 2], 16)
            for u in range(2):
                pool.wait_ge(stored[u], 32)
N_EXP, GRP, PER = 64, 8, 8
BS = 64
NBLK = 2 * SEQ // BS + N_EXP
MIN_PAIRS = 2 * SEQ // BS // 2


def norm_stage(nc, src, dst, gain, eps_col, V, C):
    with ExitStack() as ctx:
        sb = lambda n, s, d=F32: ctx.enter_context(nc.sbuf_tensor(f"nf_{n}", s, d))
        sem = stage_semaphores(nc, ctx, "nf")
        x, sq = sb("x", [P, DT, SEQ]), sb("sq", [P, 3, SEQ])
        sq_sum, rms, inv, diag = sb("sq_sum", [P, SEQ]), sb("rms", [P, DT]), sb("inv", [P, DT]), sb("diag", [P, DT, P])
        ss = ctx.enter_context(nc.psum_tensor("nf_ss", [P, 512], F32))
        spread = ctx.enter_context(nc.psum_tensor("nf_spread", [P, 2, 512], F32))
        loaded = [sem(f"loaded{k}") for k in range(DT)]
        sq_ready, sum_ready, ss_ready, rms_ready, inv_ready, diag_ready, spread_ready, h_ready, stored = (
            sem(n) for n in ("sq_ready", "sum_ready", "ss_ready", "rms_ready", "inv_ready", "diag_ready", "spread_ready", "h_ready", "stored"))
        ones = C[:, CONST["ones"]:CONST["ones"] + P]
        block = ctx.enter_context(nc.Block(no_gpsimd_drain=True))

        @block.sync
        def _(sp):
            for k in range(DT):
                sp.dma_start(x[:, k, :], src[k]).then_inc(loaded[k], 16)
            for k in range(DT):
                sp.wait_ge(h_ready, k + 1)
                sp.dma_start(dst[k], x[:, k, :]).then_inc(stored, 16)
            sp.wait_ge(stored, 16 * DT)

        @block.scalar
        def _(act):
            for k in range(DT):
                act.wait_ge(loaded[k], 16)
                if k >= 3:
                    act.wait_ge(sum_ready, k - 2)
                nc.scalar.activation(sq[:, k % 3, :], x[:, k, :], ACT.Square).then_inc(sq_ready, 1)
            act.wait_ge(ss_ready, 1)
            nc.scalar.activation(rms[:, :], ss[:, 0:DT], ACT.Sqrt, bias=C[:, eps_col:eps_col + 1], scale=1.0 / DM).then_inc(rms_ready, 1)

        @block.tensor
        def _(pe):
            pe.wait_ge(sum_ready, DT - 1)
            for t in range(DT):
                mm = pe.matmul(ss[:, t:t + 1], sq_sum[:, t * P:(t + 1) * P], ones[:, 0:1], start=True, stop=True, skip_group_check=True)
            mm.then_inc(ss_ready, 1)
            pe.wait_ge(diag_ready, 1)
            for h in range(2):
                mm = pe.matmul(spread[:, h, :], ones, diag[:, 4 * h:4 * h + 4, :].rearrange("p a b -> p (a b)"), start=True, stop=True)
            mm.then_inc(spread_ready, 1)

        @block.vector
        def _(dve):
            for k in range(1, DT):
                dve.wait_ge(sq_ready, k + 1)
                if k >= 2:
                    dve.wait_ge(sum_ready, k - 1)
                nc.vector.tensor_tensor(sq_sum[:, :], sq[:, 0, :] if k == 1 else sq_sum[:, :], sq[:, k % 3, :], ALU.add).then_inc(sum_ready, 1)
            dve.wait_ge(rms_ready, 1)
            nc.vector.reciprocal(inv[:, :], rms[:, :]).then_inc(inv_ready, 1)
            dve.wait_ge(inv_ready, 1)
            nc.vector.tensor_tensor(diag[:, :, :], C[:, CONST["ident"]:CONST["ident"] + P].unsqueeze(1).to_broadcast([P, DT, P]),
                                    inv[:, :].unsqueeze(2).to_broadcast([P, DT, P]), ALU.mult).then_inc(diag_ready, 1)
            dve.wait_ge(spread_ready, 1)
            for k in range(DT):
                nc.vector.scalar_tensor_tensor(out=x[:, k, :], in0=x[:, k, :], scalar=V[:, gain + k:gain + k + 1],
                                               in1=spread[:, :, :].rearrange("p a b -> p (a b)"), op0=ALU.mult, op1=ALU.mult).then_inc(h_ready, 1)


def lru_stage(nc, proj, lru_w, out, V, C):
    col = lambda name, j=0: V[:, VEC[name] + j:VEC[name] + j + 1]
    with ExitStack() as ctx:
        sb = lambda n, s, d=F32: ctx.enter_context(nc.sbuf_tensor(f"lr_{n}", s, d))
        sem = stage_semaphores(nc, ctx, "lr")
        W = sb("W", [P, 2 * DM])
        pre, yr = sb("pre", [P, 2, SEQ + 3]), sb("yr", [P, 2, SEQ])
        cv, xc = sb("cv", [P, 2, SEQ]), sb("xc", [P, 3, SEQ])
        rg, ig, gel = sb("rg", [P, 2, SEQ]), sb("ig", [P, 2, SEQ]), sb("gel", [P, 2, SEQ])
        a_, a2, th, mu = sb("a", [P, 2, SEQ]), sb("a2", [P, SEQ]), sb("th", [P, 2, SEQ]), sb("mu", [P, 2, SEQ])
        sq = sb("sq", [P, 2, SEQ])
        bi, h_, o = sb("bi", [P, SEQ]), sb("h", [P, SEQ]), sb("o", [P, 2, SEQ])
        sp_, m8, m16 = sb("sp", [P, 4, DT]), sb("m8", [P, DT]), sb("m16", [P, DT])
        p8 = sb("p8", [P, DT])
        gate = ctx.enter_context(nc.psum_tensor("lr_gate", [P, 2, 4, 512], F32))
        loaded = [sem(f"loaded{i}") for i in range(2)]
        y_loaded = [sem(f"y_loaded{i}") for i in range(2)]
        stored = [sem(f"stored{i}") for i in range(2)]
        w_loaded, lam_e, lam_a, rates, conv_ready, gate_ready, sig_done, exps_done = (
            sem(n) for n in ("w_loaded", "lam_e", "lam_a", "rates", "conv_ready", "gate_ready", "sig_done", "exps_done"))
        sq_ready, mu_ready, steps, pads, o_ready = (sem(n) for n in ("sq_ready", "mu_ready", "steps", "pads", "o_ready"))
        block = ctx.enter_context(nc.Block(no_gpsimd_drain=True))

        @block.sync
        def _(sp):
            sp.dma_start(W[:, :], lru_w).then_inc(w_loaded, 16)
            for n in range(DT):
                if n >= 2:
                    sp.wait_ge(conv_ready, n - 1)
                sp.dma_start(pre[:, n % 2, 3:], proj[n]).then_inc(loaded[n % 2], 16)
                if n >= 2:
                    sp.wait_ge(sig_done, 3 * (n - 1))
                sp.dma_start(yr[:, n % 2, :], proj[8 + n]).then_inc(y_loaded[n % 2], 16)

        @block.tensor
        def _(pe):
            pe.wait_ge(w_loaded, 16)
            for n in range(DT):
                u = n % 2
                pe.wait_ge(conv_ready, n + 1)
                if n >= 2:
                    pe.wait_ge(sig_done, 3 * (n - 1))
                for j in range(2):
                    for h in range(2):
                        mm = pe.matmul(gate[:, u, 2 * j + h, :], W[:, j * DM + n * P:j * DM + (n + 1) * P],
                                       xc[:, n % 3, h * HALF:(h + 1) * HALF], start=True, stop=True)
                mm.then_inc(gate_ready, 1)

        @block.scalar
        def _(act):
            act.wait_ge(lam_a, 1)
            nc.scalar.activation(sp_[:, 1, :], sp_[:, 0, :], ACT.Exp, scale=-1.0).then_inc(lam_e, 1)
            act.wait_ge(rates, 1)
            flat = lambda t: t.rearrange("p a b -> p (a b)")

            def root(n):
                u = n % 2
                act.wait_ge(sq_ready, n + 1)
                if n >= 2:
                    act.wait_ge(o_ready, n - 1)
                nc.scalar.activation(mu[:, u, :], sq[:, u, :], ACT.Sqrt).then_inc(mu_ready, 1)

            for n in range(DT):
                u = n % 2
                act.wait_ge(gate_ready, n + 1)
                if n >= 2:
                    act.wait_ge(o_ready, n - 1)
                nc.scalar.activation(rg[:, u, :], flat(gate[:, u, 0:2, :]), ACT.Sigmoid, bias=col("lru_ba", n)).then_inc(sig_done, 1)
                nc.scalar.activation(ig[:, u, :], flat(gate[:, u, 2:4, :]), ACT.Sigmoid, bias=col("lru_bx", n)).then_inc(sig_done, 1)
                act.wait_ge(y_loaded[u], 16 * (n // 2 + 1))
                nc.scalar.activation(gel[:, u, :], yr[:, u, :], ACT.Gelu_apprx_tanh).then_inc(sig_done, 1)
                act.wait_ge(sig_done, 3 * n + 1)
                if n:
                    act.wait_ge(sq_ready, n)
                nc.scalar.activation(a_[:, u, :], rg[:, u, :], ACT.Exp, scale=m8[:, n:n + 1]).then_inc(exps_done, 1)
                nc.scalar.activation(a2[:, :], rg[:, u, :], ACT.Exp, scale=m16[:, n:n + 1]).then_inc(exps_done, 1)
                nc.scalar.activation(th[:, u, :], rg[:, u, :], ACT.Tanh, scale=p8[:, n:n + 1]).then_inc(exps_done, 1)
                root(n)

        @block.vector
        def _(dve):
            st = Steps(dve, steps)
            tt, ts, stt = nc.vector.tensor_tensor, nc.vector.tensor_scalar, nc.vector.scalar_tensor_tensor
            nc.vector.memset(pre[:, :, 0:3], 0.0).then_inc(pads, 1)
            lam = V[:, VEC["lru_lam"]:VEC["lru_lam"] + DT]
            stt(out=sp_[:, 0, :], in0=lam, scalar=-1.0, in1=lam, op0=ALU.mult, op1=ALU.max).then_inc(lam_a, 1)
            dve.wait_ge(lam_e, 1)
            st.link(ts(sp_[:, 2, :], sp_[:, 1, :], 2.0, None, ALU.add))
            st.link(nc.vector.reciprocal(sp_[:, 3, :], sp_[:, 2, :]))
            st.link(tt(sp_[:, 0, :], sp_[:, 1, :], sp_[:, 3, :], ALU.mult))
            st.link(tt(sp_[:, 1, :], sp_[:, 0, :], sp_[:, 0, :], ALU.mult))
            st.link(ts(sp_[:, 2, :], sp_[:, 1, :], 1.0 / 17, 1.0 / 15, ALU.mult, ALU.add))
            for k in (13, 11, 9, 7, 5, 3, 1):
                st.link(tt(sp_[:, 3, :], sp_[:, 2, :], sp_[:, 1, :], ALU.mult))
                st.link(ts(sp_[:, 2, :], sp_[:, 3, :], 1.0 / k, None, ALU.add))
            st.link(tt(sp_[:, 3, :], sp_[:, 2, :], sp_[:, 0, :], ALU.mult))
            st.link(ts(sp_[:, 0, :], lam, -1.0, 0.0, ALU.mult, ALU.max))
            st.link(stt(out=sp_[:, 1, :], in0=sp_[:, 3, :], scalar=2.0, in1=sp_[:, 0, :], op0=ALU.mult, op1=ALU.add))
            st(ts(m8[:, :], sp_[:, 1, :], -8.0, None, ALU.mult))
            st(ts(m16[:, :], sp_[:, 1, :], -16.0, None, ALU.mult))
            st(ts(p8[:, :], sp_[:, 1, :], 8.0, None, ALU.mult))
            st.settle()
            dve.sem_inc(rates, 1)
            dve.wait_ge(pads, 1)

            def conv(n):
                u = n % 2
                dve.wait_ge(loaded[u], 16 * (n // 2 + 1))
                if n:
                    dve.wait_ge(conv_ready, n)
                w = lambda tap: col("conv_2", 8 * tap + n)
                st.link(ts(cv[:, 0, :], pre[:, u, 3:3 + SEQ], w(3), col("conv_b_2", n), ALU.mult, ALU.add))
                st.link(stt(out=cv[:, 1, :], in0=pre[:, u, 2:2 + SEQ], scalar=w(2), in1=cv[:, 0, :], op0=ALU.mult, op1=ALU.add))
                st.link(stt(out=cv[:, 0, :], in0=pre[:, u, 1:1 + SEQ], scalar=w(1), in1=cv[:, 1, :], op0=ALU.mult, op1=ALU.add))
                if n >= 3:
                    dve.wait_ge(gate_ready, n - 2)
                stt(out=xc[:, n % 3, :], in0=pre[:, u, 0:SEQ], scalar=w(0), in1=cv[:, 0, :], op0=ALU.mult, op1=ALU.add).then_inc(conv_ready, 1)

            conv(0)
            conv(1)
            for n in range(DT):
                u = n % 2
                dve.wait_ge(exps_done, 3 * n + 3)
                if n >= 2:
                    dve.wait_ge(mu_ready, n - 1)
                stt(out=sq[:, u, :], in0=a2[:, :], scalar=1.0, in1=th[:, u, :], op0=ALU.add, op1=ALU.mult).then_inc(sq_ready, 1)
                dve.wait_ge(sig_done, 3 * n + 3)
                dve.wait_ge(conv_ready, n + 1)
                st.link(tt(bi[:, :], xc[:, n % 3, :], ig[:, u, :], ALU.mult))
                if n + 2 < DT:
                    conv(n + 2)
                dve.wait_ge(mu_ready, n + 1)
                st.link(tt(bi[:, :], bi[:, :], mu[:, u, :], ALU.mult))
                st.link(nc.vector.tensor_tensor_scan(h_[:, :], a_[:, u, :], bi[:, :], 0.0, ALU.mult, ALU.add))
                if n >= 2:
                    dve.wait_ge(stored[u], 16 * (n // 2))
                tt(o[:, u, :], h_[:, :], gel[:, u, :], ALU.mult).then_inc(o_ready, 1)

        @block.gpsimd
        def _(pool):
            for n in range(DT):
                pool.wait_ge(o_ready, n + 1)
                pool.dma_start(out[n], o[:, n % 2, :]).then_inc(stored[n % 2], 16)
            for u in range(2):
                pool.wait_ge(stored[u], 16 * DT // 2)


def attention_stage(nc, proj, qT, kvT, positions, out, y_pad, V, C):
    H, QD = 8, 192
    TWO_PI = 6.283185307179586
    MAGIC = 1.5 * 2.0 ** 23
    C1 = 6.28125
    C2 = float(np.float32(np.floor((TWO_PI - C1) * 2.0 ** 20) / 2.0 ** 20))
    C3 = TWO_PI - C1 - C2
    col = lambda name, j=0: V[:, VEC[name] + j:VEC[name] + j + 1]
    ones = C[:, CONST["ones"]:CONST["ones"] + P]
    ident = C[:, CONST["ident"]:CONST["ident"] + P]
    eps = C[:, CONST["eps6"]:CONST["eps6"] + 1]
    NQ = SEQ // P
    with ExitStack() as ctx:
        sb = lambda n, s, d=F32: ctx.enter_context(nc.sbuf_tensor(f"at_{n}", s, d))
        sem = stage_semaphores(nc, ctx, "at")
        pos = sb("pos", [P, SEQ], I32)
        ang, t1, t2, cosb, sinb = (sb(n, [P, SEQ]) for n in ("ang", "t1", "t2", "cos", "sin"))
        kpe, kps, krot, kpe_sq = (sb(n, [P, SEQ]) for n in ("kpe", "kps", "krot", "kpe_sq"))
        qn, kn, vt = sb("qn", [P, 2, SEQ]), sb("kn", [P, 2, SEQ]), sb("vt", [P, 2, SEQ])
        qr, qs = sb("qr", [P, SEQ]), sb("qs", [P, SEQ])
        qr_sq, q_sq, k_sq = sb("qr_sq", [P, SEQ]), sb("q_sq", [P, SEQ]), sb("k_sq", [P, SEQ])
        cos_q, sin_q, pt1, pt2 = (sb(n, [P, SEQ]) for n in ("cos_q", "sin_q", "pt1", "pt2"))
        qrot = sb("qrot", [P, 2, SEQ])
        q_g, k_g, k_r, v_tok = sb("q_g", [P, 2, SEQ]), sb("k_g", [P, 2, SEQ]), sb("k_r", [P, 2, SEQ]), sb("v_tok", [P, 2, SEQ])
        diag = sb("diag", [P, NQ, P])
        rms, inv = sb("rms", [P, 2 * NQ]), sb("inv", [P, 2 * NQ])
        q_scale, neg_scale = sb("q_scale", [P, 2, 8]), sb("neg_scale", [P, 2, 8])
        pr = sb("pr", [P, 2, SEQ])
        prT = sb("prT", [P, 2, SEQ])
        mx, bias, total, rinv = (sb(n, [P, 64]) for n in ("mx", "bias", "total", "rinv"))
        o_sb = sb("o_sb", [P, 2, SEQ])
        zeros = sb("zeros", [P, DM])
        y_zero = sem("y_zero")
        score = ctx.enter_context(nc.psum_tensor("at_score", [P, 2, 1024], F32))
        tr = ctx.enter_context(nc.psum_tensor("at_tr", [P, 2, 512], F32))
        ob = ctx.enter_context(nc.psum_tensor("at_ob", [P, 512], F32))
        pb = ctx.enter_context(nc.psum_tensor("at_pb", [P, 512], F32))
        g_loaded, steps, pool_steps, ang_ready, trig_ready, trig_q_ready = (
            sem(n) for n in ("g_loaded", "steps", "pool_steps", "ang_ready", "trig_ready", "trig_q_ready"))
        h_loaded = [sem(f"h_loaded{i}") for i in range(2)]
        r_loaded, rotated, sq_ready, q_ready, sums_ready, rms_ready, diag_ready, bc_ready, k_half, vt_ready, v_copied = (
            sem(n) for n in ("r_loaded", "rotated", "sq_ready", "q_ready", "sums_ready", "rms_ready", "diag_ready",
                             "bc_ready", "k_half", "vt_ready", "v_copied"))
        score_ready, bias_ready, prob_ready, norm_ready, tr_ready, tr_copied, ob_ready, ob_copied = (
            sem(n) for n in ("score_ready", "bias_ready", "prob_ready", "norm_ready", "tr_ready", "tr_copied", "ob_ready", "ob_copied"))
        stored = [sem(f"stored{i}") for i in range(2)]
        trs = [0]
        for h in range(H):
            for b in range(NQ):
                trs.append(trs[-1] + b // 4 + 1)
        block = ctx.enter_context(nc.Block(no_gpsimd_drain=True))

        @block.sync
        def _(sp):
            sp.dma_start(pos[:, :], positions.partition_broadcast(P)).then_inc(g_loaded, 16)
            sp.dma_start(kpe[:, :], proj[20]).then_inc(g_loaded, 16)
            sp.dma_start(kps[:, :], proj[21]).then_inc(g_loaded, 16)

            def store(h):
                sp.wait_ge(ob_copied, NQ * (h + 1))
                sp.dma_start(out[h], o_sb[:, h % 2, :]).then_inc(stored[h % 2], 16)

            for h in range(H):
                u = h % 2
                if h >= 2:
                    sp.wait_ge(q_ready, h - 1)
                    sp.wait_ge(k_half, 2 * (h - 1))
                    sp.wait_ge(vt_ready, 2 * (h - 1))
                sp.dma_start(qn[:, u, :], qT[h]).then_inc(h_loaded[u], 16)
                sp.dma_start(kn[:, u, :], kvT[h]).then_inc(h_loaded[u], 16)
                sp.dma_start(vt[:, u, :], kvT[8 + h]).then_inc(h_loaded[u], 16)
                if u == 0:
                    if h:
                        sp.wait_ge(rotated, h // 2)
                    sp.dma_start(qr[:, :], qT[8 + h // 2]).then_inc(r_loaded, 16)
                    sp.dma_start(qs[:, :], qT[12 + h // 2]).then_inc(r_loaded, 16)
                if h >= 3:
                    store(h - 3)
            for h in range(H - 3, H):
                store(h)
            for u in range(2):
                sp.wait_ge(stored[u], 16 * H // 2)

        @block.vector
        def _(dve):
            st = Steps(dve, steps)
            tt, ts, stt = nc.vector.tensor_tensor, nc.vector.tensor_scalar, nc.vector.scalar_tensor_tensor
            dve.wait_ge(g_loaded, 48)
            st.link(nc.vector.tensor_copy(t1[:, :], pos[:, :]))
            st.link(ts(ang[:, :], t1[:, :], C[:, CONST["inv_freq"]:CONST["inv_freq"] + 1], None, ALU.mult))
            st.link(ts(t1[:, :], ang[:, :], 1.0 / TWO_PI, None, ALU.mult))
            st.link(ts(t2[:, :], t1[:, :], MAGIC, None, ALU.add))
            st.link(ts(t1[:, :], t2[:, :], -MAGIC, None, ALU.add))
            for c_ in (C1, C2, C3):
                st.link(stt(out=ang[:, :], in0=t1[:, :], scalar=-c_, in1=ang[:, :], op0=ALU.mult, op1=ALU.add))
            st.link(ts(ang[:, :], ang[:, :], 3.1415925, -3.1415925, ALU.min, ALU.max))
            st.link(stt(out=t1[:, :], in0=ang[:, :], scalar=-1.0, in1=ang[:, :], op0=ALU.mult, op1=ALU.max))
            ts(t2[:, :], t1[:, :], -1.0, TWO_PI / 4, ALU.mult, ALU.add).then_inc(ang_ready, 1)
            dve.wait_ge(trig_ready, 2)
            st.link(ts(sinb[:, :], sinb[:, :], C[:, CONST["rope_sign"]:CONST["rope_sign"] + 1], None, ALU.mult))

            tt(cos_q[:, :], cosb[:, :], col("qg_r").to_broadcast([P, SEQ]), ALU.mult).then_inc(trig_q_ready, 1)
            tt(sin_q[:, :], sinb[:, :], col("qg_s").to_broadcast([P, SEQ]), ALU.mult).then_inc(trig_q_ready, 1)
            st(stt(out=t1[:, :], in0=kpe[:, :], scalar=col("kg_r"), in1=cosb[:, :], op0=ALU.mult, op1=ALU.mult))
            st(stt(out=t2[:, :], in0=kps[:, :], scalar=col("kg_s"), in1=sinb[:, :], op0=ALU.mult, op1=ALU.mult))
            st.settle()
            st.link(tt(krot[:, :], t1[:, :], t2[:, :], ALU.add))

            def inverses(h):
                u = h % 2
                dve.wait_ge(rms_ready, h + 1)
                if h >= 1:
                    dve.wait_ge(bc_ready, 2 * h)
                if h >= 2:
                    dve.wait_ge(prob_ready, NQ * (h - 1))
                st.link(nc.vector.reciprocal(inv[:, :], rms[:, :]))
                st(ts(neg_scale[:, u, :], inv[:, 0:NQ], -(QD ** -0.5), None, ALU.mult))
                st(ts(q_scale[:, u, :], inv[:, 0:NQ], QD ** -0.5, None, ALU.mult))
                st.settle()
                tt(diag[:, :, :], ident.unsqueeze(1).to_broadcast([P, NQ, P]), inv[:, NQ:2 * NQ].unsqueeze(2).to_broadcast([P, NQ, P]),
                   ALU.mult).then_inc(diag_ready, 1)

            def key_half(h, f):
                u, base, fs = h % 2, 64 * (h % 2), slice(f * 512, (f + 1) * 512)
                if f == 0:
                    dve.wait_ge(h_loaded[u], 48 * (h // 2 + 1))
                if h >= 2 and f == 0:
                    dve.wait_ge(score_ready, NQ * (h - 1))
                dve.wait_ge(bc_ready, 2 * h + f + 1)
                st(stt(out=k_g[:, u, fs], in0=kn[:, u, fs], scalar=col("kg_n"), in1=pb[:, :], op0=ALU.mult, op1=ALU.mult))
                st(tt(k_r[base:base + 64, u, fs], krot[base:base + 64, fs], pb[base:base + 64, :], ALU.mult))
                st.settle()
                dve.sem_inc(k_half, 1)

            def maximum(h, b):
                n = NQ * h + b
                u, w = n % 2, (b + 1) * P
                dve.wait_ge(score_ready, n + 1)
                st.link(stt(out=score[:, u, b * P:w], in0=C[:, CONST["before"]:CONST["before"] + P], scalar=-1e30,
                            in1=score[:, u, b * P:w], op0=ALU.mult, op1=ALU.add))
                st.link(nc.vector.reduce_max(mx[:, n:n + 1], score[:, u, 0:w], AX.X))
                tt(bias[:, n:n + 1], mx[:, n:n + 1], neg_scale[:, h % 2, b:b + 1], ALU.mult).then_inc(bias_ready, 1)

            def normalise(h, b):
                n = NQ * h + b
                u, w = n % 2, (b + 1) * P
                dve.wait_ge(prob_ready, n + 1)
                st.link(nc.vector.reciprocal(rinv[:, n:n + 1], total[:, n:n + 1]))
                ts(pr[:, u, 0:w], pr[:, u, 0:w], rinv[:, n:n + 1], None, ALU.mult).then_inc(norm_ready, 1)

            def outputs(h, b):
                n = NQ * h + b
                dve.wait_ge(ob_ready, n + 1)
                if b == 0 and h >= 2:
                    dve.wait_ge(stored[h % 2], 16 * (h // 2))
                nc.vector.tensor_copy(o_sb[:, h % 2, b * P:(b + 1) * P], ob[:, 0:P]).then_inc(ob_copied, 1)

            inverses(0)
            key_half(0, 0)
            key_half(0, 1)
            every = [(h, b) for h in range(H) for b in range(NQ)]
            for n, (h, b) in enumerate(every):
                if n >= 3:
                    outputs(*every[n - 3])
                if n >= 1:
                    normalise(*every[n - 1])
                if b in (4, 5) and h + 1 < H:
                    key_half(h + 1, b - 4)
                maximum(h, b)
                if b == 2 and h + 1 < H:
                    inverses(h + 1)
            normalise(*every[-1])
            for last in every[-3:]:
                outputs(*last)

        @block.scalar
        def _(act):
            act.wait_ge(ang_ready, 1)
            nc.scalar.activation(sinb[:, :], ang[:, :], ACT.Sin).then_inc(trig_ready, 1)
            nc.scalar.activation(cosb[:, :], t2[:, :], ACT.Sin).then_inc(trig_ready, 1)

            def norms(h):
                act.wait_ge(sums_ready, h + 1)
                if h >= 1:
                    act.wait_ge(diag_ready, h)
                nc.scalar.activation(rms[:, :], pb[:, 0:2 * NQ], ACT.Sqrt, bias=eps, scale=1.0 / QD).then_inc(rms_ready, 1)

            def value_half(h, f):
                if h >= 2 and f == 0:
                    act.wait_ge(ob_ready, NQ * (h - 1))
                act.wait_ge(vt_ready, 2 * h + f + 1)
                nc.scalar.copy(v_tok[:, h % 2, f * 512:(f + 1) * 512], pb[:, :]).then_inc(v_copied, 1)

            def probs(h, b):
                n = NQ * h + b
                u, w = n % 2, (b + 1) * P
                act.wait_ge(bias_ready, n + 1)
                if n >= 2:
                    act.wait_ge(tr_ready, trs[n - 1])
                nc.scalar.activation(pr[:, u, 0:w], score[:, u, 0:w], ACT.Exp, bias=bias[:, n:n + 1],
                                     scale=q_scale[:, h % 2, b:b + 1], accum_out=total[:, n:n + 1]).then_inc(prob_ready, 1)

            def copies(h, b):
                n = NQ * h + b
                for k in range(b // 4 + 1):
                    w = min(512, (b + 1) * P - k * 512)
                    act.wait_ge(tr_ready, trs[n] + k + 1)
                    if n >= 2:
                        act.wait_ge(ob_ready, n - 1)
                    nc.scalar.copy(prT[:, n % 2, k * 512:k * 512 + w], tr[:, (trs[n] + k) % 2, 0:w]).then_inc(tr_copied, 1)

            norms(0)
            value_half(0, 0)
            value_half(0, 1)
            every = [(h, b) for h in range(H) for b in range(NQ)]
            for n, (h, b) in enumerate(every):
                if b == 2 and h + 1 < H:
                    norms(h + 1)
                if b >= 6 and h + 1 < H:
                    value_half(h + 1, b - 6)
                probs(h, b)
                if n >= 1:
                    copies(*every[n - 1])
            copies(*every[-1])

        @block.tensor
        def _(pe):
            def sums(h):
                pe.wait_ge(sq_ready, h + 1)
                if h:
                    pe.wait_ge(v_copied, 2 * h)
                for t in range(NQ):
                    for j, sq in enumerate((q_sq, k_sq)):
                        mm = pe.matmul(pb[:, j * NQ + t:j * NQ + t + 1], sq[:, t * P:(t + 1) * P], C[:, CONST["ones"]:CONST["ones"] + 1],
                                       start=True, stop=True, skip_group_check=True)
                mm.then_inc(sums_ready, 1)

            def spread(h, f):
                pe.wait_ge(k_half, 2 * h + 1) if f else pe.wait_ge(diag_ready, h + 1)
                pe.matmul(pb[:, :], ones, diag[:, 4 * f:4 * f + 4, :].rearrange("p a b -> p (a b)"), start=True, stop=True).then_inc(bc_ready, 1)

            def turn_values(h, f):
                pe.wait_ge(v_copied, 2 * h + 1) if f else pe.wait_ge(k_half, 2 * h + 2)
                for t in range(4):
                    mm = pe.transpose(pb[:, t * P:(t + 1) * P], vt[:, h % 2, (4 * f + t) * P:(4 * f + t + 1) * P], ident)
                mm.then_inc(vt_ready, 1)

            prep = (lambda h: sums(h), lambda h: spread(h, 0), lambda h: spread(h, 1),
                    lambda h: turn_values(h, 0), lambda h: turn_values(h, 1))
            at_step = {1: 0, 3: 1, 4: 2, 5: 3, 6: 4}

            def scores(h, b):
                n = NQ * h + b
                u, base, hu = n % 2, 64 * (h % 2), h % 2
                if b == 0:
                    pe.wait_ge(k_half, 2 * h + 2)
                    pe.wait_ge(q_ready, h + 1)
                if n >= 2:
                    pe.wait_ge(prob_ready, n - 1)
                for f in range(b // 4 + 1):
                    w = min(512, (b + 1) * P - f * 512)
                    o = score[:, u, f * 512:f * 512 + w]
                    pe.matmul(o, q_g[:, hu, b * P:(b + 1) * P], k_g[:, hu, f * 512:f * 512 + w], start=True, stop=False)
                    mm = pe.matmul(o, qrot[base:base + 64, (h // 2) % 2, b * P:(b + 1) * P], k_r[base:base + 64, hu, f * 512:f * 512 + w],
                                   start=False, stop=True)
                mm.then_inc(score_ready, 1)

            def transposes(h, b):
                n = NQ * h + b
                pe.wait_ge(norm_ready, n + 1)
                for k in range(b // 4 + 1):
                    g = trs[n] + k
                    if g >= 2:
                        pe.wait_ge(tr_copied, g - 1)
                    for j in range(min(4, b + 1 - 4 * k)):
                        mm = pe.transpose(tr[:, g % 2, j * P:(j + 1) * P], pr[:, n % 2, (4 * k + j) * P:(4 * k + j + 1) * P], ident)
                    mm.then_inc(tr_ready, 1)

            def values(h, b):
                n = NQ * h + b
                pe.wait_ge(tr_copied, trs[n + 1])
                if b == 0:
                    pe.wait_ge(v_copied, 2 * h + 2)
                if n >= 1:
                    pe.wait_ge(ob_copied, n)
                o = ob[:, 0:P]
                for k in range(b + 1):
                    mm = pe.matmul(o, v_tok[:, h % 2, k * P:(k + 1) * P], prT[:, n % 2, k * P:(k + 1) * P], start=k == 0,
                                   stop=k == b, skip_group_check=True)
                mm.then_inc(ob_ready, 1)

            for part in prep:
                part(0)
            every = [(h, b) for h in range(H) for b in range(NQ)]
            scores(0, 0)
            for n, (h, b) in enumerate(every):
                if n + 1 < len(every):
                    scores(*every[n + 1])
                if n >= 1:
                    transposes(*every[n - 1])
                if n >= 2:
                    values(*every[n - 2])
                if b in at_step and h + 1 < H:
                    prep[at_step[b]](h + 1)
            transposes(*every[-1])
            values(*every[-2])
            values(*every[-1])

        @block.gpsimd
        def _(pool):
            st = Steps(pool, pool_steps)
            tt = nc.gpsimd.tensor_tensor
            pool.wait_ge(g_loaded, 48)
            st(tt(kpe_sq[:, :], kpe[:, :], kpe[:, :], ALU.mult))
            for h in range(H):
                u, base = h % 2, 64 * (h % 2)
                pool.wait_ge(h_loaded[u], 48 * (h // 2 + 1))
                if h:
                    pool.wait_ge(sums_ready, h)
                st(tt(q_sq[:, :], qn[:, u, :], qn[:, u, :], ALU.mult))
                st(tt(k_sq[:, :], kn[:, u, :], kn[:, u, :], ALU.mult))
                if u == 0:
                    pool.wait_ge(r_loaded, 32 * (h // 2 + 1))
                    st(tt(qr_sq[:, :], qr[:, :], qr[:, :], ALU.mult))
                st.settle()
                st(tt(q_sq[base:base + 64, :], q_sq[base:base + 64, :], qr_sq[base:base + 64, :], ALU.add))
                st(tt(k_sq[0:64, :], k_sq[0:64, :], kpe_sq[0:64, :], ALU.add))
                st.settle()
                pool.sem_inc(sq_ready, 1)
                if h >= 2:
                    pool.wait_ge(score_ready, NQ * (h - 1))
                st(tt(q_g[:, u, :], qn[:, u, :], col("qg_n").to_broadcast([P, SEQ]), ALU.mult))
                if u == 0:
                    if h == 0:
                        pool.wait_ge(trig_q_ready, 2)
                    st(tt(pt1[:, :], qr[:, :], cos_q[:, :], ALU.mult))
                    st(tt(pt2[:, :], qs[:, :], sin_q[:, :], ALU.mult))
                    st.settle()
                    pool.sem_inc(rotated, 1)
                    st(tt(qrot[:, (h // 2) % 2, :], pt1[:, :], pt2[:, :], ALU.add))
                st.settle()
                pool.sem_inc(q_ready, 1)
            st.link(nc.gpsimd.memset(zeros[:, :], 0.0))
            with pool.Fori(MIN_PAIRS, NBLK // 2) as i:
                pool.dma_start(y_pad[bass.ds(i * P, P), :], zeros[:, :]).then_inc(y_zero, 16)
            pool.wait_ge(y_zero, 16 * (NBLK // 2 - MIN_PAIRS))
def router_stage(nc, src, router, router_b, u_tok, table, dest, gates, blk_expert, V, C):
    with ExitStack() as ctx:
        sb = lambda n, s, d=F32: ctx.enter_context(nc.sbuf_tensor(f"ro_{n}", s, d))
        sem = stage_semaphores(nc, ctx, "ro")
        x, sq, rms = sb("x", [P, DT, SEQ]), sb("sq", [P, 3, SEQ]), sb("rms", [P, DT])
        sq_sum, rstd = sb("sq_sum", [P, SEQ]), sb("rstd", [P, DT])
        wr, br = sb("wr", [P, DT * 72]), sb("br", [P, 72])
        ut = sb("ut", [P, 2, DM])
        lg = sb("lg", [P, DT, 72])
        zero = sb("zero", [P, NBLK * BS // P], I32)
        pairs_i = sb("pairs_i", [1, 2], I32)
        g_eq, g_key, g_hot = sb("g_eq", [P, DT, 8]), sb("g_key", [P, DT, 8]), sb("g_hot", [P, DT, 8])
        g_exp = sb("g_exp", [P, DT, 8])
        gmax, gsum, gp, m1, m2, kmin = (sb(n, [P, DT]) for n in ("gmax", "gsum", "gp", "m1", "m2", "kmin"))
        ein, ein2, e_key = sb("ein", [P, DT, 8]), sb("ein2", [P, DT, 8]), sb("e_key", [P, DT, 8])
        e_hot = sb("e_hot", [P, 2, DT, 8])
        big = sb("big", [P, DT, 64])
        hot = sb("hot", [P, 3, DT, 64])
        rat, rden = sb("rat", [P, DT]), sb("rden", [P, DT])
        cnt, padded, pend, pstart = sb("cnt", [P, 64]), sb("padded", [P, 64]), sb("pend", [P, 64]), sb("pstart", [P, 64])
        ci = sb("ci", [P, 2, 64], I32)
        slot = sb("slot", [P, DT, 64])
        dest_f = sb("dest_f", [P, 2, DT])
        be = sb("be", [P, 64])
        bcol = sb("bcol", [P, 2])
        tok_id = sb("tok_id", [P, DT], I32)
        ss = ctx.enter_context(nc.psum_tensor("ro_ss", [P, 2, 512], F32))
        tr = ctx.enter_context(nc.psum_tensor("ro_tr", [P, 4, 512], F32))
        lp = ctx.enter_context(nc.psum_tensor("ro_lp", [P, 2, 512], F32))
        loaded = [sem(f"loaded{k}") for k in range(DT)]
        stored = [sem(f"stored{k}") for k in range(2)]
        w_loaded, sq_ready, sum_ready, ss_ready, rms_ready, rstd_ready, h_ready, steps = (
            sem(n) for n in ("w_loaded", "sq_ready", "sum_ready", "ss_ready", "rms_ready", "rstd_ready", "h_ready", "steps"))
        lg_ready, lg_read, tr_ready, tr_copied, table_zero, zero_ready, key_ready, exp_done = (
            sem(n) for n in ("lg_ready", "lg_read", "tr_ready", "tr_copied", "table_zero", "zero_ready", "key_ready", "exp_done"))
        hot_ready, count_ready, bcol_ready, brow_ready, dest_ready, scattered, id_ready = (
            sem(n) for n in ("hot_ready", "count_ready", "bcol_ready", "brow_ready", "dest_ready", "scattered", "id_ready"))
        ident = C[:, CONST["ident"]:CONST["ident"] + P]
        ones = C[:, CONST["ones"]:CONST["ones"] + P]
        block = ctx.enter_context(nc.Block(no_gpsimd_drain=True))

        @block.sync
        def _(sp):
            for k in range(DT):
                sp.dma_start(x[:, k, :], src[k]).then_inc(loaded[k], 16)
            sp.dma_start(wr[:, :], router).then_inc(w_loaded, 16)
            sp.dma_start(br[:, :], router_b.partition_broadcast(P)).then_inc(w_loaded, 16)
            sp.wait_ge(zero_ready, 1)
            sp.dma_start(table.rearrange("(p c) o -> p (c o)", p=P), zero[:, :]).then_inc(table_zero, 16)
            for t in range(DT):
                sp.wait_ge(tr_copied, t + 1)
                sp.dma_start(u_tok[t * P:(t + 1) * P, :], ut[:, t % 2, :]).then_inc(stored[t % 2], 16)
            for u in range(2):
                sp.wait_ge(stored[u], 16 * DT // 2)

        @block.scalar
        def _(act):
            for k in range(DT):
                act.wait_ge(loaded[k], 16)
                if k >= 3:
                    act.wait_ge(sum_ready, k - 2)
                nc.scalar.activation(sq[:, k % 3, :], x[:, k, :], ACT.Square).then_inc(sq_ready, 1)
            act.wait_ge(ss_ready, 1)
            nc.scalar.activation(rms[:, :], ss[:, 0, 0:DT], ACT.Sqrt,
                                 bias=C[:, CONST["eps6"]:CONST["eps6"] + 1], scale=1.0 / DM).then_inc(rms_ready, 1)
            act.wait_ge(rstd_ready, 1)
            for t in range(DT):
                u = t % 2
                act.wait_ge(tr_ready, t + 1)
                if t >= 2:
                    act.wait_ge(stored[u], 16 * (t // 2))
                nc.scalar.activation(ut[:, u, :], tr[:, 2 * u:2 * u + 2, :].rearrange("p a b -> p (a b)"), ACT.Copy,
                                     scale=rstd[:, t:t + 1]).then_inc(tr_copied, 1)
            act.wait_ge(key_ready, 1)
            nc.scalar.activation(g_exp[:, :, :], g_exp[:, :, :], ACT.Exp).then_inc(exp_done, 1)
            act.wait_ge(key_ready, 2)
            nc.scalar.activation(rat[:, :], rat[:, :], ACT.Exp).then_inc(exp_done, 1)

        @block.tensor
        def _(pe):
            def square_sums():
                pe.wait_ge(sum_ready, DT - 1)
                for t in range(DT):
                    mm = pe.matmul(ss[:, 0, t:t + 1], sq_sum[:, t * P:(t + 1) * P], ones[:, 0:1], start=True, stop=True, skip_group_check=True)
                mm.then_inc(ss_ready, 1)

            pe.wait_ge(w_loaded, 32)
            pe.wait_ge(h_ready, DT)
            for t in range(DT):
                u, tsl = t % 2, slice(t * P, (t + 1) * P)
                if t == 1:
                    square_sums()
                if t >= 2:
                    pe.wait_ge(lg_read, t - 1)
                    pe.wait_ge(tr_copied, t - 1)
                for k in range(DT):
                    mm = pe.matmul(lp[:, u, 0:72], x[:, k, tsl], wr[:, k * 72:(k + 1) * 72], start=k == 0, stop=k == DT - 1)
                mm.then_inc(lg_ready, 1)
                for k in range(DT):
                    mm = pe.transpose(tr[:, 2 * u + k // 4, (k % 4) * P:(k % 4 + 1) * P], x[:, k, tsl], ident)
                mm.then_inc(tr_ready, 1)
            pe.wait_ge(hot_ready, 1)
            for t in range(DT):
                o = ss[:, 0, t * 64:(t + 1) * 64]
                for e in range(t):
                    pe.matmul(o, ones, hot[:, 2, e, :], start=e == 0, stop=False, skip_group_check=True)
                pe.matmul(o, C[:, CONST["before"]:CONST["before"] + P], hot[:, 2, t, :], start=t == 0, stop=True, skip_group_check=True)
            for t in range(DT):
                mm = pe.matmul(ss[:, 1, 0:64], ones, hot[:, 2, t, :], start=t == 0, stop=t == DT - 1)
            mm.then_inc(count_ready, 1)
            pe.wait_ge(bcol_ready, 1)
            pe.matmul(lp[0:1, 0, 0:P], bcol[:, 1:2], ident, start=True, stop=True).then_inc(brow_ready, 1)

        @block.vector
        def _(dve):
            st = Steps(dve, steps)
            tt, ts, stt = nc.vector.tensor_tensor, nc.vector.tensor_scalar, nc.vector.scalar_tensor_tensor
            bc = lambda t, n: t.unsqueeze(2).to_broadcast([P, DT, n])
            nc.vector.memset(zero[:, :], 0).then_inc(zero_ready, 1)
            for k in range(DT):
                dve.wait_ge(sq_ready, k + 1)
                ts(x[:, k, :], x[:, k, :], V[:, VEC["norm2_2"] + k:VEC["norm2_2"] + k + 1], None, ALU.mult).then_inc(h_ready, 1)
            dve.wait_ge(rms_ready, 1)
            nc.vector.reciprocal(rstd[:, :], rms[:, :]).then_inc(rstd_ready, 1)
            dve.wait_ge(rstd_ready, 1)
            dve.wait_ge(w_loaded, 32)
            for t in range(DT):
                dve.wait_ge(lg_ready, t + 1)
                stt(out=lg[:, t, :], in0=lp[:, t % 2, 0:72], scalar=rstd[:, t:t + 1], in1=br[:, :], op0=ALU.mult, op1=ALU.add).then_inc(lg_read, 1)
            dve.wait_ge(lg_read, DT)
            G, E = lg[:, :, 0:8], lg[:, :, 8:72]
            iota = C[:, CONST["iota8"]:CONST["iota8"] + 8].unsqueeze(1).to_broadcast([P, DT, 8])

            def first_hot(hot_out, vals, mx):
                st.link(nc.vector.reduce_max(mx, vals, AX.X))
                st.link(tt(g_eq[:, :, :], vals, bc(mx, 8), ALU.is_equal))
                st.link(stt(out=g_key[:, :, :], in0=g_eq[:, :, :], scalar=-8.0, in1=iota, op0=ALU.mult, op1=ALU.add))
                st.link(nc.vector.tensor_reduce(kmin[:, :], g_key[:, :, :], AX.X, ALU.min))
                st.link(tt(hot_out, g_key[:, :, :], bc(kmin[:, :], 8), ALU.is_equal))

            first_hot(g_hot[:, :, :], G, gmax[:, :])
            st.link(tt(g_exp[:, :, :], G, bc(gmax[:, :], 8), ALU.subtract))
            dve.sem_inc(key_ready, 1)
            big4 = big[:, :, :].rearrange("p t (g e) -> p t g e", g=8)
            gh4 = g_hot[:, :, :].unsqueeze(3).to_broadcast([P, DT, 8, 8])
            for t in range(DT):
                st(tt(big4[:, t, :, :], E[:, t, :].rearrange("p (g e) -> p g e", g=8), gh4[:, t, :, :], ALU.mult))
            st.settle()
            for t in range(DT):
                st(nc.vector.tensor_reduce(ein[:, t, :], big4[:, t, :, :].rearrange("p g e -> p e g"), AX.X, ALU.add))
            st.settle()
            first_hot(e_hot[:, 0, :, :], ein[:, :, :], m1[:, :])
            st.link(stt(out=ein2[:, :, :], in0=e_hot[:, 0, :, :], scalar=-3e38, in1=ein[:, :, :], op0=ALU.mult, op1=ALU.add))
            first_hot(e_hot[:, 1, :, :], ein2[:, :, :], m2[:, :])
            st.link(tt(rat[:, :], m2[:, :], m1[:, :], ALU.subtract))
            dve.sem_inc(key_ready, 1)
            for j in range(2):
                for t in range(DT):
                    st(tt(hot[:, j, t, :].rearrange("p (g e) -> p g e", g=8), gh4[:, t, :, :],
                          e_hot[:, j, t, :].unsqueeze(1).to_broadcast([P, 8, 8]), ALU.mult))
            st.settle()
            tt(hot[:, 2, :, :], hot[:, 0, :, :], hot[:, 1, :, :], ALU.add).then_inc(hot_ready, 1)
            dve.wait_ge(exp_done, 2)
            st.link(nc.vector.reduce_sum(gsum[:, :], g_exp[:, :, :], AX.X))
            st.link(stt(out=rden[:, :], in0=rat[:, :], scalar=1.0, in1=gsum[:, :], op0=ALU.add, op1=ALU.mult))
            st.link(nc.vector.reciprocal(gates[:, 0, :], rden[:, :]))
            st.link(tt(gates[:, 1, :], gates[:, 0, :], rat[:, :], ALU.mult))
            dve.wait_ge(count_ready, 1)
            st.link(ts(cnt[:, :], ss[:, 1, 0:64], float(BS - 1), None, ALU.add))
            st.link(nc.vector.tensor_copy(ci[:, 0, :], cnt[:, :]))
            st.link(ts(ci[:, 1, :], ci[:, 0, :], 6, 6, ALU.arith_shift_right, ALU.logical_shift_left))
            st.link(nc.vector.tensor_copy(padded[:, :], ci[:, 1, :]))
            st.link(nc.vector.tensor_tensor_scan(pend[:, :], ones[:, 0:64], padded[:, :], 0.0, ALU.mult, ALU.add))
            st.link(tt(pstart[:, :], pend[:, :], padded[:, :], ALU.subtract))
            st.link(ts(be[:, :], pend[:, :], C[:, CONST["block_start"]:CONST["block_start"] + 1], None, ALU.is_le))
            st.link(nc.vector.reduce_sum(bcol[:, 0:1], be[:, :], AX.X))
            ts(bcol[:, 1:2], bcol[:, 0:1], float(N_EXP - 1), None, ALU.min).then_inc(bcol_ready, 1)
            st.link(tt(slot[:, :, :], ss[:, 0, :].rearrange("p (t e) -> p t e", t=DT), pstart[:, :].unsqueeze(1).to_broadcast([P, DT, 64]), ALU.add))
            for j in range(2):
                st.link(tt(big[:, :, :], slot[:, :, :], hot[:, j, :, :], ALU.mult))
                st.link(nc.vector.reduce_sum(dest_f[:, j, :], big[:, :, :], AX.X))
            nc.vector.tensor_copy(dest[:, :, :], dest_f[:, :, :]).then_inc(dest_ready, 1)
            dve.wait_ge(brow_ready, 1)
            nc.vector.tensor_copy(blk_expert[:, 0:P], lp[0:1, 0, 0:P]).then_inc(dest_ready, 1)
            st.link(ts(be[0:1, 0:1], pend[0:1, 63:64], float(-1 - 2 * BS), None, ALU.add))
            st.link(nc.vector.tensor_copy(pairs_i[:, 0:1], be[0:1, 0:1]))
            ts(blk_expert[:, P:P + 1], pairs_i[:, 0:1], 7, None, ALU.arith_shift_right).then_inc(dest_ready, 1)

        @block.gpsimd
        def _(pool):
            for k in range(1, DT):
                pool.wait_ge(sq_ready, k + 1)
                if k >= 2:
                    pool.wait_ge(sum_ready, k - 1)
                nc.gpsimd.tensor_tensor(sq_sum[:, :], sq[:, 0, :] if k == 1 else sq_sum[:, :], sq[:, k % 3, :], ALU.add).then_inc(sum_ready, 1)
            nc.gpsimd.iota(tok_id[:, :], pattern=[[P, DT]], base=0, channel_multiplier=1).then_inc(id_ready, 1)
            pool.wait_ge(id_ready, 1)
            pool.wait_ge(table_zero, 16)
            pool.wait_ge(dest_ready, 1)
            for j in range(2):
                for t in range(DT):
                    pool.indirect_dma_start(table, bass.IndirectOffsetOnAxis(dest[:, j, t:t + 1], 0), tok_id[:, t:t + 1], None).then_inc(scattered, 16)
            pool.wait_ge(scattered, 16 * 2 * DT)


def expert_stage(nc, u_tok, table, w13, ew2, y_pad, blk_expert, C):
    FE = 256
    FC = 2 * FE // P
    with ExitStack() as ctx:
        sb = lambda n, s, d=F32: ctx.enter_context(nc.sbuf_tensor(f"ex_{n}", s, d))
        sem = stage_semaphores(nc, ctx, "ex")
        wa, wb = sb("wa", [P, 2, DT * 2 * FE]), sb("wb", [P, 2, 2 * DM])
        idx = sb("idx", [P, 1], U32)
        xb, xT = sb("xb", [P, DM]), sb("xT", [P, DT * P])
        s1, hT = sb("s1", [P, 2, 2 * BS]), sb("hT", [P, 2, 2 * BS])
        yb = sb("yb", [BS, 2, DM])
        xp = ctx.enter_context(nc.psum_tensor("ex_xp", [P, 2, 512], F32))
        ap_ = ctx.enter_context(nc.psum_tensor("ex_ap", [P, 2, 512], F32))
        yp = ctx.enter_context(nc.psum_tensor("ex_yp", [P, 4, 512], F32))
        wa_loaded = [sem(f"wa_loaded{i}") for i in range(2)]
        wb_loaded = [sem(f"wb_loaded{i}") for i in range(2)]
        stored = [sem(f"stored{i}") for i in range(2)]
        i_loaded, gathered, xp_ready, xT_low, xT_high, ap_ready, s1_ready, hT_ready, yp_ready, y_low, y_high, wait_held = (
            sem(n) for n in ("i_loaded", "gathered", "xp_ready", "xT_low", "xT_high", "ap_ready", "s1_ready", "hT_ready",
                             "yp_ready", "y_low", "y_high", "wait_held"))
        ident = C[:, CONST["ident"]:CONST["ident"] + P]

        def last_pair(eng):
            return eng.value_load(blk_expert[0:1, P:P + 1], min_val=MIN_PAIRS - 2, max_val=NBLK // 2 - 2) + 1

        def pair_loop(eng, end, body):
            body(0, True, False, False)
            body(1, False, True, False)
            with eng.Fori(2, end) as i:
                body(i, False, False, False)
            body(end, False, False, True)

        block = ctx.enter_context(nc.Block(no_gpsimd_drain=True))

        @block.sync
        def _(sp):
            def expert_of(i, u):
                return sp.value_load(blk_expert[0:1, bass.ds(2 * i + u, 1)], min_val=0, max_val=N_EXP - 1)

            def load_up(i, u, first):
                e = expert_of(i, u)
                if not first:
                    sp.wait_ge(ap_ready, 2 * i + (u - 1))
                sp.dma_start(wa[:, u, :], w13[bass.ds(e * P, P), :]).then_inc(wa_loaded[u], 16)

            def load_down(i, u, first):
                e = expert_of(i, u)
                if not first:
                    sp.wait_ge(yp_ready, 2 * i + (u - 1))
                sp.dma_start(wb[:, u, :], ew2[bass.ds(e * P, P), :]).then_inc(wb_loaded[u], 16)

            def body(i, first, second, last):
                load_up(i, 0, first)
                if not first:
                    load_down(i - 1, 1, second)
                load_up(i, 1, first)
                load_down(i, 0, first)

            end = last_pair(sp)
            pair_loop(sp, end, body)
            load_down(end, 1, False)

        @block.gpsimd
        def _(pool):
            def fetch(i, first):
                if not first:
                    pool.wait_ge(xp_ready, i)
                pool.dma_start(idx[:, :], table[bass.ds(i * P, P), :].bitcast(U32)).then_inc(i_loaded, 16)
                pool.wait_ge(i_loaded, 16 * i + 16)
                pool.sem_inc(wait_held, 1)
                pool.indirect_dma_start(xb[:, :], None, u_tok, bass.IndirectOffsetOnAxis(idx[:, 0:1], 0)).then_inc(gathered, 16)

            def store(i, u):
                pool.wait_ge(y_low, 2 * i + (u + 1))
                pool.wait_ge(y_high, 2 * i + (u + 1))
                pool.dma_start(y_pad[bass.ds(i * (2 * BS) + u * BS, BS), :], yb[:, u, :]).then_inc(stored[u], 16)

            fetch(0, True)

            def body(i, first, second, last):
                if not last:
                    fetch(i + 1, False)
                if not first:
                    store(i - 1, 1)
                store(i, 0)

            end = last_pair(pool)
            pair_loop(pool, end, body)
            store(end, 1)
            for u in range(2):
                pool.wait_ge(stored[u], 16 * end + 16)

        @block.tensor
        def _(pe):
            def turn(i, first):
                pe.wait_ge(gathered, 16 * i + 16)
                if not first:
                    pe.wait_ge(xT_low, i)
                    pe.wait_ge(xT_high, i)
                for k in range(DT):
                    mm = pe.transpose(xp[:, k // 4, (k % 4) * P:(k % 4 + 1) * P], xb[:, k * P:(k + 1) * P], ident)
                mm.then_inc(xp_ready, 1)

            def up(i, u, first):
                if u == 0:
                    pe.wait_ge(xT_low, i + 1)
                    pe.wait_ge(xT_high, i + 1)
                pe.wait_ge(wa_loaded[u], 16 * i + 16)
                if not first:
                    pe.wait_ge(hT_ready, 2 * i + (u - 1))
                for c in range(FC):
                    for k in range(DT):
                        mm = pe.matmul(ap_[:, u, c * BS:(c + 1) * BS], wa[:, u, k * 512 + c * P:k * 512 + (c + 1) * P],
                                       xT[:, k * P + u * BS:k * P + (u + 1) * BS], start=k == 0, stop=k == DT - 1)
                mm.then_inc(ap_ready, 1)

            def down(i, u, first):
                pe.wait_ge(hT_ready, 2 * i + (u + 1))
                pe.wait_ge(wb_loaded[u], 16 * i + 16)
                if not first:
                    pe.wait_ge(y_low, 2 * i + (u - 1))
                    pe.wait_ge(y_high, 2 * i + (u - 1))
                for n in range(2):
                    for k in range(2):
                        mm = pe.matmul(yp[0:BS, 2 * u + n, :], hT[:, u, k * BS:(k + 1) * BS], wb[:, u, k * DM + n * 512:k * DM + (n + 1) * 512],
                                       start=k == 0, stop=k == 1)
                mm.then_inc(yp_ready, 1)

            turn(0, True)

            def body(i, first, second, last):
                up(i, 0, first)
                if not first:
                    down(i - 1, 1, second)
                up(i, 1, first)
                if not last:
                    turn(i + 1, False)
                down(i, 0, first)

            end = last_pair(pe)
            pair_loop(pe, end, body)
            down(end, 1, False)

        @block.scalar
        def _(act):
            def x_copy(i):
                act.wait_ge(xp_ready, i + 1)
                nc.scalar.copy(xT[:, 0:512], xp[:, 0, :]).then_inc(xT_low, 1)

            def gate(i, u, first):
                act.wait_ge(ap_ready, 2 * i + (u + 1))
                if not first:
                    act.wait_ge(hT_ready, 2 * i + (u - 1))
                nc.scalar.activation(s1[:, u, :], ap_[:, u, 0:2 * BS], ACT.Silu).then_inc(s1_ready, 1)

            def y_copy(i, u, first):
                act.wait_ge(yp_ready, 2 * i + (u + 1))
                if not first:
                    act.wait_ge(stored[u], 16 * i)
                nc.scalar.copy(yb[:, u, 0:512], yp[0:BS, 2 * u, :]).then_inc(y_low, 1)

            x_copy(0)

            def body(i, first, second, last):
                gate(i, 0, first)
                if not first:
                    y_copy(i - 1, 1, second)
                gate(i, 1, first)
                if not last:
                    x_copy(i + 1)
                y_copy(i, 0, first)

            end = last_pair(act)
            pair_loop(act, end, body)
            y_copy(end, 1, False)

        @block.vector
        def _(dve):
            def x_copy(i):
                dve.wait_ge(xp_ready, i + 1)
                nc.vector.tensor_copy(xT[:, 512:], xp[:, 1, :]).then_inc(xT_high, 1)

            def product(i, u, first):
                dve.wait_ge(s1_ready, 2 * i + (u + 1))
                if not first:
                    dve.wait_ge(yp_ready, 2 * i + (u - 1))
                nc.vector.tensor_tensor(hT[:, u, :], ap_[:, u, 2 * BS:4 * BS], s1[:, u, :], ALU.mult).then_inc(hT_ready, 1)

            def y_copy(i, u, first):
                dve.wait_ge(yp_ready, 2 * i + (u + 1))
                if not first:
                    dve.wait_ge(stored[u], 16 * i)
                nc.vector.tensor_copy(yb[:, u, 512:], yp[0:BS, 2 * u + 1, :]).then_inc(y_high, 1)

            x_copy(0)

            def body(i, first, second, last):
                product(i, 0, first)
                if not first:
                    y_copy(i - 1, 1, second)
                product(i, 1, first)
                if not last:
                    x_copy(i + 1)
                y_copy(i, 0, first)

            end = last_pair(dve)
            pair_loop(dve, end, body)
            y_copy(end, 1, False)


def combine_stage(nc, resid, y_pad, out, dest, gates, C):
    with ExitStack() as ctx:
        sb = lambda n, s, d=F32: ctx.enter_context(nc.sbuf_tensor(f"co_{n}", s, d))
        sem = stage_semaphores(nc, ctx, "co")
        x = sb("x", [P, DT, SEQ])
        y1, y2, acc, o = sb("y1", [P, 2, DM]), sb("y2", [P, 2, DM]), sb("acc", [P, 2, DM]), sb("o", [P, 2, DM])
        tr = ctx.enter_context(nc.psum_tensor("co_tr", [P, 4, 512], F32))
        loaded, tr_ready, acc_ready, o_ready = (sem(n) for n in ("loaded", "tr_ready", "acc_ready", "o_ready"))
        gathered = [sem(f"gathered{i}") for i in range(2)]
        stored = [sem(f"stored{i}") for i in range(2)]
        block = ctx.enter_context(nc.Block(no_gpsimd_drain=True))

        @block.sync
        def _(sp):
            for k in range(DT):
                sp.dma_start(x[:, k, :], resid[k]).then_inc(loaded, 16)
            for t in range(DT):
                sp.wait_ge(o_ready, t + 1)
                sp.dma_start(out[t * P:(t + 1) * P, :], o[:, t % 2, :]).then_inc(stored[t % 2], 16)
            for u in range(2):
                sp.wait_ge(stored[u], 16 * DT // 2)

        @block.gpsimd
        def _(pool):
            for t in range(DT):
                u = t % 2
                if t >= 2:
                    pool.wait_ge(o_ready, t - 1)
                for j, y in enumerate((y1, y2)):
                    pool.indirect_dma_start(y[:, u, :], None, y_pad, bass.IndirectOffsetOnAxis(dest[:, j, t:t + 1], 0)).then_inc(gathered[u], 16)

        @block.tensor
        def _(pe):
            pe.wait_ge(loaded, 16 * DT)
            for t in range(DT):
                u = t % 2
                if t >= 2:
                    pe.wait_ge(acc_ready, t - 1)
                for k in range(DT):
                    mm = pe.transpose(tr[:, 2 * u + k // 4, (k % 4) * P:(k % 4 + 1) * P], x[:, k, t * P:(t + 1) * P],
                                      C[:, CONST["ident"]:CONST["ident"] + P])
                mm.then_inc(tr_ready, 1)

        @block.vector
        def _(dve):
            for t in range(DT):
                u = t % 2
                dve.wait_ge(gathered[u], 32 * (t // 2 + 1))
                dve.wait_ge(tr_ready, t + 1)
                if t >= 2:
                    dve.wait_ge(o_ready, t - 1)
                nc.vector.scalar_tensor_tensor(out=acc[:, u, :], in0=y1[:, u, :], scalar=gates[:, 0, t:t + 1],
                                               in1=tr[:, 2 * u:2 * u + 2, :].rearrange("p a b -> p (a b)"), op0=ALU.mult, op1=ALU.add).then_inc(acc_ready, 1)
                dve.wait_ge(acc_ready, t + 1)
                if t >= 2:
                    dve.wait_ge(stored[u], 16 * (t // 2))
                nc.vector.scalar_tensor_tensor(out=o[:, u, :], in0=y2[:, u, :], scalar=gates[:, 1, t:t + 1],
                                               in1=acc[:, u, :], op0=ALU.mult, op1=ALU.add).then_inc(o_ready, 1)
def program(nc, a, out):
    scratch = lambda name, *shape, d=F32: nc.dram_tensor(f"s_{name}", shape, d, kind="Internal").ap()
    proj = scratch("proj", 28, P, SEQ)
    cat = scratch("cat", 8, P, SEQ)
    scr = {n: scratch(n, *s) for n, s in (("ar", (4, P, 2 * SEQ)), ("bt", (4, P, SEQ)), ("kt", (4, P, SEQ)), ("v", (4, P, SEQ)),
                                          ("bonus", (4, P, SEQ)), ("g", (4, P, SEQ)), ("scale", (4, P, NCH)), ("y", (4, P, SEQ)))}
    x1, x2, h0, h1 = (scratch(n, DT, P, SEQ) for n in ("x1", "x2", "h0", "h1"))
    ffn = scratch("ffn", 22, P, SEQ)
    proj2 = scratch("proj2", 38, P, SEQ)
    hg, br_a, merged, att = (scratch(n, DT, P, SEQ) for n in ("hg", "br_a", "merged", "att"))
    qT, kvT = scratch("qT", 16, P, SEQ), scratch("kvT", 16, P, SEQ)
    u_tok, y_pad = scratch("u_tok", SEQ, DM), scratch("y_pad", NBLK * BS, DM)
    table = scratch("table", NBLK * BS, 1, d=I32)
    with ExitStack() as ctx:
        V = ctx.enter_context(nc.sbuf_tensor("vecs_sb", [P, NVEC], F32))
        C = ctx.enter_context(nc.sbuf_tensor("consts_sb", [P, NCONST], F32))
        s = ctx.enter_context(nc.semaphore("params_loaded"))
        with nc.Block(no_gpsimd_drain=True) as block:
            @block.sync
            def _(sp):
                sp.dma_start(V[:], a["vecs"]).then_inc(s, 16)
                sp.dma_start(C[:], a["consts"]).then_inc(s, 16)
                sp.wait_ge(s, 32)
        vecs = {"buf": V, "ffn_conv": VEC["ffn_conv"], "ffn_conv_b": VEC["ffn_conv_b"]}
        consts = {"buf": C, "ones": C[:, CONST["ones"]:CONST["ones"] + P], "ident": C[:, CONST["ident"]:CONST["ident"] + P]}
        eps = CONST["eps6"]

        def dense(name, src, KT, w, NT, out_, **kw):
            dense_stage(nc, name, src, KT, a[w], NT, out_, vecs, consts, **kw)

        dense("in1", a["xT"], 8, "w_in", 28, proj, norm=(VEC["norm1"], eps, DM))
        mlstm_stage(nc, proj, cat[4:8], V, C)
        rwkv_prepare_stage(nc, proj, a["lora"], a["w_up_g"], scr, V, C)
        rwkv_scan_stage(nc, scr, a["masks"], C)
        rwkv_finish_stage(nc, scr, cat[0:4], V, C)
        dense("out1", cat, 8, "w_out", 8, x1, mode="residual", aux=a["xT"])
        dense("up", x1, 8, "w_up", 44, ffn, norm=(VEC["norm2"], eps, DM), mode="ffn")
        dense("down", ffn, 22, "w_down", 8, x2, mode="residual", aux=x1, tokens=HALF)
        norm_stage(nc, x2, h0, VEC["norm_f"], eps, V, C)
        dense("in2", h0, 8, "w_in2", 38, proj2, norm=(VEC["norm1_2"], eps, DM))
        lru_stage(nc, proj2, a["lru_w"], hg, V, C)
        dense("uq", proj2[16:18], 2, "w_uq", 16, qT, norm=(VEC["q_norm"], eps, 256))
        dense("ukv", proj2[18:20], 2, "w_ukv", 16, kvT, norm=(VEC["kv_norm"], eps, 256))
        attention_stage(nc, proj2, qT, kvT, a["positions"], att, y_pad, V, C)
        dense("rnn_o", hg, 8, "w_rnn_o", 8, br_a, mode="gate", aux=proj2[22:30])
        dense("mla_o", att, 8, "w_mla_o", 8, merged, mode="gate_add", aux=proj2[30:38], aux2=br_a)
        dense("out2", merged, 8, "w_out2", 8, h1, mode="residual", aux=h0)
        dest = ctx.enter_context(nc.sbuf_tensor("dest", [P, 2, DT], U32))
        gates = ctx.enter_context(nc.sbuf_tensor("gates", [P, 2, DT], F32))
        blk_expert = ctx.enter_context(nc.sbuf_tensor("blk_expert", [1, P + 1], I32))
        router_stage(nc, h1, a["router"], a["router_b"], u_tok, table, dest, gates, blk_expert, V, C)
        expert_stage(nc, u_tok, table, a["w13"], a["ew2"], y_pad, blk_expert, C)
        combine_stage(nc, h1, y_pad, out, dest, gates, C)


def kernel(**inputs):
    import concourse.bacc as bacc
    from concourse.bass_utils import run_bass_kernel_spmd

    nc = bacc.Bacc("TRN2", target_bir_lowering=False, num_devices=1)
    arrays = {f"in_{k}": v for k, v in lay_out(inputs).items()}
    aps = {k[3:]: nc.dram_tensor(k, v.shape, mybir.dt.from_np(v.dtype), kind="ExternalInput").ap() for k, v in arrays.items()}
    out = nc.dram_tensor("out", (SEQ, DM), F32, kind="ExternalOutput").ap()
    program(nc, aps, out)
    r = run_bass_kernel_spmd(nc, [arrays], core_ids=[0])
    return r.results[0]["out"].reshape(1, SEQ, DM)
```
